# Optimizing a Trainium2 kernel written in Bass

```python
import math, functools
import jax, jax.numpy as jnp
from jax import lax
import numpy as np

D_MODEL = 1024
BATCH = 1
SEQ = 1024
DEPTH = 2
DEC_BATCH = 8
DEC_SEQ = 4
PAST_LEN = 512
PAGE_SIZE = 128

N_EVEN = (DEPTH + 1) // 2
N_ODD = DEPTH // 2
RET_H = 4
RET_DK = 128
RET_DV = 128
RET_CHUNK = 128
ROPE_BASE = 10000.0
ATT_H = 4
ATT_DH = 128
ATT_BLOCK = 128
IDX_H = 8
IDX_DIM = 64
TOPK_MAX = 256
REL_BUCKETS = 32
REL_MAX_DIST = 128
POOL_WINDOWS = (2, 4, 8, 16)
POOL_GROUPS = 4
POOL_DIM = D_MODEL // 2
POOL_GC = POOL_DIM // POOL_GROUPS
POOL_PAST = 15
D_INNER = D_MODEL // 2
SSM_P = 64
SSM_H = D_INNER // SSM_P
SSM_G = 2
SSM_N = 128
CONV_W = 4
CONV_DIM = D_INNER + 2 * SSM_G * SSM_N
SSD_CHUNK = 128
FF_DIM = -(-8 * D_MODEL // (3 * 256)) * 256
EPS = 1e-6

EVEN_SPLITS = (RET_H * RET_DK, RET_H * RET_DK, RET_H * RET_DV, RET_H * RET_DV,
               ATT_H * ATT_DH, ATT_H * ATT_DH, ATT_H * ATT_DH, IDX_H * IDX_DIM, IDX_DIM, IDX_H)
EVEN_PROJ = sum(EVEN_SPLITS)
ODD_SPLITS = (POOL_DIM, D_INNER, CONV_DIM, SSM_H)
ODD_PROJ = sum(ODD_SPLITS)
MIX_EVEN = RET_H * RET_DV + ATT_H * ATT_DH
MIX_ODD = POOL_DIM + D_INNER

kernel_name = 'hybrid_retention_dsa_pool_ssd_step'

f32 = jnp.float32

def _split(a, sizes):
    return jnp.split(a, np.cumsum(sizes)[:-1].tolist(), axis=-1)

def rmsnorm(x, g):
    xf = x.astype(f32)
    return xf * lax.rsqrt(jnp.mean(xf * xf, -1, keepdims=True) + EPS) * g

def swiglu(h, wg, wu, wd):
    return (jax.nn.silu(h @ wg) * (h @ wu)) @ wd

def rotary(x, pos):
    half = x.shape[-1] // 2
    inv = ROPE_BASE ** (-jnp.linspace(0.0, 1.0, half, dtype=f32))
    ang = pos.astype(f32)[:, None] * inv[None, :]
    cos = jnp.cos(ang)[None, :, None, :]
    sin = jnp.sin(ang)[None, :, None, :]
    x1, x2 = x[..., :half], x[..., half:]
    return jnp.concatenate([x1 * cos - x2 * sin, x1 * sin + x2 * cos], -1)

def _to_chunks(a, q):
    b, l = a.shape[:2]
    return a.reshape(b, l // q, q, *a.shape[2:]).swapaxes(0, 1)

def retention_chunked(q, k, v, R0):
    b, L = q.shape[:2]
    Q = math.gcd(L, RET_CHUNK)
    log_g = jnp.log1p(-jnp.exp2(-5.0 - jnp.arange(RET_H, dtype=f32)))
    idx = jnp.arange(Q, dtype=f32)
    diff = idx[:, None] - idx[None, :]
    dmask = jnp.where(diff[None] >= 0, jnp.exp(log_g[:, None, None] * jnp.maximum(diff, 0.0)[None]), 0.0)
    xi = jnp.exp(log_g[:, None] * (idx + 1.0)[None])
    zeta = jnp.exp(log_g[:, None] * (Q - 1.0 - idx)[None])
    g_chunk = jnp.exp(log_g * Q)

    def step(R, inp):
        qc, kc, vc = inp
        s = jnp.einsum('bihd,bjhd->bhij', qc, kc) * dmask[None]
        inner = jnp.einsum('bhij,bjhe->bihe', s, vc)
        cross = jnp.einsum('bihd,bhde->bihe', qc, R) * xi.T[None, :, :, None]
        R_new = R * g_chunk[None, :, None, None] + jnp.einsum('bjhd,bjhe,hj->bhde', kc, vc, zeta)
        return R_new, inner + cross

    R, o = lax.scan(step, R0, (_to_chunks(q, Q), _to_chunks(k, Q), _to_chunks(v, Q)))
    return o.swapaxes(0, 1).reshape(b, L, RET_H, RET_DV), R

def retention_branch(q, k, v, g, pos, R0):
    b, T = q.shape[:2]
    q = rotary(q.reshape(b, T, RET_H, RET_DK).astype(f32), pos)
    k = rotary(k.reshape(b, T, RET_H, RET_DK).astype(f32), pos) * RET_DK ** -0.5
    v = v.reshape(b, T, RET_H, RET_DV).astype(f32)
    o, R = retention_chunked(q, k, v, R0.astype(f32))
    o = o * lax.rsqrt(jnp.mean(o * o, -1, keepdims=True) + EPS)
    return jax.nn.silu(g.astype(f32)) * o.reshape(b, T, RET_H * RET_DV), R

def t5_bucket(rel):
    n = jnp.maximum(rel, 0)
    max_exact = REL_BUCKETS // 2
    nf = jnp.maximum(n, 1).astype(f32)
    large = max_exact + (jnp.log(nf / max_exact) / math.log(REL_MAX_DIST / max_exact)
                         * (REL_BUCKETS - max_exact)).astype(jnp.int32)
    large = jnp.minimum(large, REL_BUCKETS - 1)
    return jnp.where(n < max_exact, n, large)

def indexer_select(qi, wi, ki, qpos, topk):
    L = ki.shape[1]
    s = jax.nn.relu(jnp.einsum('bthd,bsd->bths', qi, ki))
    score = jnp.einsum('bths,bth->bts', s, wi)
    score = jnp.where(jnp.arange(L)[None, None, :] <= qpos[None, :, None], score, -jnp.inf)
    _, idx = lax.top_k(score, topk)
    valid = idx <= qpos[None, :, None]
    return idx, valid

def sparse_softmax(q, k_sel, v_sel, rel, valid, rel_bias):
    logits = jnp.einsum('bthd,btkhd->bhtk', q.astype(f32), k_sel.astype(f32)) * ATT_DH ** -0.5
    bias = rel_bias.astype(f32)[t5_bucket(rel)]
    logits = logits + jnp.moveaxis(bias, -1, 1)
    logits = jnp.where(valid[:, None], logits, -jnp.inf)
    p = jax.nn.softmax(logits, axis=-1)
    return jnp.einsum('bhtk,btkhd->bthd', p, v_sel.astype(f32))

def attend_prompt(q, k, v, qi, ki, wi, rel_bias):
    b, L = q.shape[:2]
    topk = min(TOPK_MAX, L // 4)
    nb = L // ATT_BLOCK
    pos = jnp.arange(L).reshape(nb, ATT_BLOCK)
    take = jax.vmap(lambda a, i: a[i])

    def one(inp):
        qb, qib, wib, pb = inp
        idx, valid = indexer_select(qib, wib, ki, pb, topk)
        return sparse_softmax(qb, take(k, idx), take(v, idx), pb[None, :, None] - idx, valid, rel_bias)

    o = lax.map(one, (_to_chunks(q, ATT_BLOCK), _to_chunks(qi, ATT_BLOCK), _to_chunks(wi, ATT_BLOCK), pos))
    return o.swapaxes(0, 1).reshape(b, L, ATT_H * ATT_DH)

def gather_paged(pool, page_table, new, idx):
    db, T, K = idx.shape
    n_past = page_table.shape[1] * PAGE_SIZE
    flat = pool.reshape(-1, *pool.shape[2:])
    pi = jnp.minimum(idx, n_past - 1)
    page = jnp.take_along_axis(page_table, (pi // PAGE_SIZE).reshape(db, T * K), axis=1).reshape(db, T, K)
    past = flat[page * PAGE_SIZE + pi % PAGE_SIZE]
    cur = jax.vmap(lambda a, i: a[i])(new, jnp.clip(idx - n_past, 0, new.shape[1] - 1))
    is_past = (idx < n_past).reshape(idx.shape + (1,) * (past.ndim - idx.ndim))
    return jnp.where(is_past, past, cur)

def attend_paged(q, k, v, qi, ki, wi, pool_k, pool_v, pool_ki, page_table, rel_bias):
    db, T = q.shape[:2]
    n_past = page_table.shape[1] * PAGE_SIZE
    L = n_past + T
    topk = min(TOPK_MAX, L // 4)
    qpos = n_past + jnp.arange(T)
    ki_past = pool_ki[page_table].reshape(db, n_past, IDX_DIM).astype(f32)
    ki_all = jnp.concatenate([ki_past, ki], axis=1)
    idx, valid = indexer_select(qi, wi, ki_all, qpos, topk)
    k_sel = gather_paged(pool_k, page_table, k, idx)
    v_sel = gather_paged(pool_v, page_table, v, idx)
    o = sparse_softmax(q, k_sel, v_sel, qpos[None, :, None] - idx, valid, rel_bias)
    return o.reshape(db, T, ATT_H * ATT_DH)

def even_mixer(h, pos, R0, w_in, w_out, q_gain, k_gain, attend):
    b, T = h.shape[:2]
    qr, kr, vr, gr, qa, ka, va, qi, ki, wi = _split(h @ w_in, EVEN_SPLITS)
    ret, R = retention_branch(qr, kr, vr, gr, pos, R0)
    qa = rmsnorm(qa.reshape(b, T, ATT_H, ATT_DH), q_gain)
    ka = rmsnorm(ka.reshape(b, T, ATT_H, ATT_DH), k_gain)
    va = va.reshape(b, T, ATT_H, ATT_DH).astype(f32)
    qi = qi.reshape(b, T, IDX_H, IDX_DIM).astype(f32) * IDX_DIM ** -0.5
    ki = ki.astype(f32)
    wi = wi.astype(f32) * IDX_H ** -0.5
    att = attend(qa, ka, va, qi, ki, wi)
    out = jnp.concatenate([ret, att], -1) @ w_out
    return out, R, ka, va, ki

def multiscale_pool(u, prev, pos):
    T = u.shape[1]
    full = jnp.concatenate([prev.astype(f32), u.astype(f32)], 1)
    cs = jnp.concatenate([jnp.zeros_like(full[:, :1]), jnp.cumsum(full, 1)], 1)
    end = cs[:, POOL_PAST + 1:]
    outs = []
    for g, w in enumerate(POOL_WINDOWS):
        ch = slice(g * POOL_GC, (g + 1) * POOL_GC)
        start = cs[:, POOL_PAST + 1 - w: POOL_PAST + 1 - w + T, ch]
        cnt = jnp.minimum(pos + 1, w).astype(f32)[None, :, None]
        outs.append((end[..., ch] - start) / cnt)
    return jnp.concatenate(outs, -1) - u.astype(f32)

def ssd_chunked(x, dt, A, bm, cm, h0):
    L = x.shape[1]
    Q = math.gcd(L, SSD_CHUNK)
    bh = jnp.repeat(bm, SSM_H // SSM_G, axis=2)
    chh = jnp.repeat(cm, SSM_H // SSM_G, axis=2)
    a = dt * A[None, None, :]
    causal = jnp.tril(jnp.ones((Q, Q), bool))

    def step(h, inp):
        xc, dtc, ac, bc, cc = inp
        cs = jnp.cumsum(ac, axis=1)
        seg = cs[:, :, None, :] - cs[:, None, :, :]
        lm = jnp.exp(jnp.where(causal[None, :, :, None], seg, -jnp.inf))
        sc = jnp.einsum('bihn,bjhn->bijh', cc, bc) * lm * dtc[:, None, :, :]
        y = jnp.einsum('bijh,bjhp->bihp', sc, xc) + jnp.einsum('bihn,bhpn->bihp', cc, h) * jnp.exp(cs)[..., None]
        w_end = jnp.exp(cs[:, -1:, :] - cs) * dtc
        h_new = h * jnp.exp(cs[:, -1, :])[:, :, None, None] + jnp.einsum('bjhn,bjhp,bjh->bhpn', bc, xc, w_end)
        return h_new, y

    hN, y = lax.scan(step, h0, tuple(_to_chunks(t, Q) for t in (x, dt, a, bh, chh)))
    return y.swapaxes(0, 1).reshape(x.shape), hN

def odd_mixer(h, pos, pool_prev, conv_prev, ssm_prev, w_in, w_out, pool_w, pool_scale,
              conv_w, conv_b, dt_bias, a_log, d_skip, ssm_norm):
    b, T = h.shape[:2]
    u, z, xbc, dt = _split(h @ w_in, ODD_SPLITS)
    d = multiscale_pool(u, pool_prev, pos)
    pool_out = jnp.einsum('btgc,gcd->btgd', d.reshape(b, T, POOL_GROUPS, POOL_GC), pool_w).reshape(b, T, POOL_DIM) * pool_scale
    pool_new = jnp.concatenate([pool_prev.astype(f32), u.astype(f32)], 1)[:, -POOL_PAST:]
    full = jnp.concatenate([conv_prev.astype(f32), xbc.astype(f32)], 1)
    conv = conv_b + sum(full[:, j:j + T] * conv_w[j] for j in range(CONV_W))
    conv_new = full[:, -(CONV_W - 1):]
    xs, bm, cm = _split(jax.nn.silu(conv), (D_INNER, SSM_G * SSM_N, SSM_G * SSM_N))
    xs = xs.reshape(b, T, SSM_H, SSM_P)
    dt = jax.nn.softplus(dt.astype(f32) + dt_bias)
    A = -jnp.exp(a_log.astype(f32))
    y, hN = ssd_chunked(xs, dt, A, bm.reshape(b, T, SSM_G, SSM_N), cm.reshape(b, T, SSM_G, SSM_N), ssm_prev.astype(f32))
    y = (y + d_skip[:, None] * xs).reshape(b, T, D_INNER) * jax.nn.silu(z.astype(f32))
    yg = y.reshape(b, T, SSM_G, D_INNER // SSM_G)
    y = (yg * lax.rsqrt(jnp.mean(yg * yg, -1, keepdims=True) + EPS)).reshape(b, T, D_INNER) * ssm_norm
    out = jnp.concatenate([pool_out, y], -1) @ w_out
    return out, pool_new, conv_new, hN

def setup_inputs(seed: int = 0) -> dict:
    key = jax.random.key(seed)
    ks = iter(jax.random.split(key, 48))

    def nrm(shape, scale):
        return jax.random.normal(next(ks), shape, f32) * scale

    n_pages = PAST_LEN // PAGE_SIZE
    n_pool = (DEC_BATCH * n_pages * 5) // 4
    page_table = jax.random.permutation(next(ks), n_pool)[:DEC_BATCH * n_pages].reshape(DEC_BATCH, n_pages).astype(jnp.int32)
    dt0 = jnp.exp(jax.random.uniform(next(ks), (N_ODD, SSM_H), f32, math.log(1e-3), math.log(1e-1)))
    dt_bias = dt0 + jnp.log(-jnp.expm1(-dt0))
    a_log = jnp.log(jax.random.uniform(next(ks), (N_ODD, SSM_H), f32, 1.0, 16.0))
    return {
        'x_prompt': nrm((BATCH, SEQ, D_MODEL), 1.0),
        'x_sample': nrm((DEC_BATCH, DEC_SEQ, D_MODEL), 1.0),
        'cache_k': nrm((N_EVEN, n_pool, PAGE_SIZE, ATT_H, ATT_DH), 1.0),
        'cache_v': nrm((N_EVEN, n_pool, PAGE_SIZE, ATT_H, ATT_DH), 1.0),
        'cache_kidx': nrm((N_EVEN, n_pool, PAGE_SIZE, IDX_DIM), 1.0),
        'state_ret': nrm((N_EVEN, DEC_BATCH, RET_H, RET_DK, RET_DV), 0.5),
        'state_pool': nrm((N_ODD, DEC_BATCH, POOL_PAST, POOL_DIM), 1.0),
        'state_conv': nrm((N_ODD, DEC_BATCH, CONV_W - 1, CONV_DIM), 1.0),
        'state_ssm': nrm((N_ODD, DEC_BATCH, SSM_H, SSM_P, SSM_N), 0.5),
        'page_table': page_table,
        'norm_mix': 1.0 + nrm((DEPTH, D_MODEL), 0.02),
        'norm_ffn': 1.0 + nrm((DEPTH, D_MODEL), 0.02),
        'w_in_even': nrm((N_EVEN, D_MODEL, EVEN_PROJ), D_MODEL ** -0.5),
        'w_out_even': nrm((N_EVEN, MIX_EVEN, D_MODEL), MIX_EVEN ** -0.5),
        'q_norm': 1.0 + nrm((N_EVEN, ATT_DH), 0.02),
        'k_norm': 1.0 + nrm((N_EVEN, ATT_DH), 0.02),
        'rel_bias': nrm((REL_BUCKETS, ATT_H), 0.2),
        'w_in_odd': nrm((N_ODD, D_MODEL, ODD_PROJ), D_MODEL ** -0.5),
        'w_out_odd': nrm((N_ODD, MIX_ODD, D_MODEL), MIX_ODD ** -0.5),
        'pool_w': nrm((N_ODD, POOL_GROUPS, POOL_GC, POOL_GC), POOL_GC ** -0.5),
        'pool_scale': 1.0 + nrm((N_ODD, POOL_DIM), 0.02),
        'conv_w': nrm((N_ODD, CONV_W, CONV_DIM), CONV_W ** -0.5),
        'conv_b': nrm((N_ODD, CONV_DIM), 0.02),
        'dt_bias': dt_bias,
        'a_log': a_log,
        'd_skip': 1.0 + nrm((N_ODD, SSM_H), 0.02),
        'ssm_norm': 1.0 + nrm((N_ODD, D_INNER), 0.02),
        'w_gate': nrm((DEPTH, D_MODEL, FF_DIM), D_MODEL ** -0.5),
        'w_up': nrm((DEPTH, D_MODEL, FF_DIM), D_MODEL ** -0.5),
        'w_down': nrm((DEPTH, FF_DIM, D_MODEL), FF_DIM ** -0.5),
    }

def reference(x_prompt, x_sample, cache_k, cache_v, cache_kidx, state_ret, state_pool, state_conv, state_ssm,
              page_table, norm_mix, norm_ffn, w_in_even, w_out_even, q_norm, k_norm, rel_bias,
              w_in_odd, w_out_odd, pool_w, pool_scale, conv_w, conv_b, dt_bias, a_log, d_skip, ssm_norm,
              w_gate, w_up, w_down):
    bp, sp = x_prompt.shape[:2]
    ts = x_sample.shape[1]
    n_past = page_table.shape[1] * PAGE_SIZE
    pos_p = jnp.arange(sp)
    pos_s = n_past + jnp.arange(ts)
    xp, xs = x_prompt, x_sample
    kp_l, vp_l, kip_l, rp_l, ks_l, vs_l, kis_l, rs_l = [], [], [], [], [], [], [], []
    pp_l, cp_l, hp_l, ps_l, cs_l, hs_l = [], [], [], [], [], []
    for l in range(DEPTH):
        np_ = rmsnorm(xp, norm_mix[l])
        ns_ = rmsnorm(xs, norm_mix[l])
        if l % 2 == 0:
            i = l // 2
            prm = (w_in_even[i], w_out_even[i], q_norm[i], k_norm[i])
            op, rp, kp, vp, kip = even_mixer(np_, pos_p, jnp.zeros((bp, RET_H, RET_DK, RET_DV), f32), *prm,
                                             functools.partial(attend_prompt, rel_bias=rel_bias))
            os_, rs, ks_, vs_, kis = even_mixer(ns_, pos_s, state_ret[i], *prm,
                                                functools.partial(attend_paged, pool_k=cache_k[i], pool_v=cache_v[i],
                                                                  pool_ki=cache_kidx[i], page_table=page_table,
                                                                  rel_bias=rel_bias))
            kp_l.append(kp); vp_l.append(vp); kip_l.append(kip); rp_l.append(rp)
            ks_l.append(ks_); vs_l.append(vs_); kis_l.append(kis); rs_l.append(rs)
        else:
            j = l // 2
            prm = (w_in_odd[j], w_out_odd[j], pool_w[j], pool_scale[j], conv_w[j], conv_b[j],
                   dt_bias[j], a_log[j], d_skip[j], ssm_norm[j])
            op, pp, cp, hp = odd_mixer(np_, pos_p, jnp.zeros((bp, POOL_PAST, POOL_DIM), f32),
                                       jnp.zeros((bp, CONV_W - 1, CONV_DIM), f32),
                                       jnp.zeros((bp, SSM_H, SSM_P, SSM_N), f32), *prm)
            os_, ps, cs, hs = odd_mixer(ns_, pos_s, state_pool[j], state_conv[j], state_ssm[j], *prm)
            pp_l.append(pp); cp_l.append(cp); hp_l.append(hp)
            ps_l.append(ps); cs_l.append(cs); hs_l.append(hs)
        xp = xp + op
        xs = xs + os_
        xp = xp + swiglu(rmsnorm(xp, norm_ffn[l]), w_gate[l], w_up[l], w_down[l])
        xs = xs + swiglu(rmsnorm(xs, norm_ffn[l]), w_gate[l], w_up[l], w_down[l])
    return (xp, xs,
            jnp.stack(kp_l), jnp.stack(vp_l), jnp.stack(kip_l), jnp.stack(rp_l),
            jnp.stack(pp_l), jnp.stack(cp_l), jnp.stack(hp_l),
            jnp.stack(ks_l), jnp.stack(vs_l), jnp.stack(kis_l), jnp.stack(rs_l),
            jnp.stack(ps_l), jnp.stack(cs_l), jnp.stack(hs_l))


_drawn_inputs = setup_inputs


def setup_inputs(seed=0):
    import zlib

    import numpy as np

    out = dict(_drawn_inputs(seed))
    spreads = {}
    factors = {'q_norm': 8.0,
     'k_norm': 2.893,
     'rel_bias': 3.581,
     'pool_scale': 6.566,
     'd_skip': 6.392,
     'ssm_norm': 6.064}
    for name, (base, spread) in spreads.items():
        noise = np.random.default_rng([zlib.crc32(name.encode()), seed]).standard_normal(out[name].shape)
        drawn = base * np.exp(spread * noise) if base else spread * noise
        out[name] = __import__('jax').numpy.asarray(drawn.astype(out[name].dtype))
    for name, factor in factors.items():
        out[name] = (out[name] * factor).astype(out[name].dtype)
    return out
```

```python
import math
from contextlib import ExitStack

import numpy as np

import concourse.bass as bass
from concourse import mybir

F32 = mybir.dt.float32
F32R = mybir.dt.float32r
I32 = mybir.dt.int32
U32 = mybir.dt.uint32
ALU = mybir.AluOpType
ACT = mybir.ActivationFunctionType
AX = mybir.AxisListType

P = 128
D = 1024
KD = D // P
SEQ = 1024
NB, NT = 8, 4
NS = NB * NT
T = SEQ + NS
TILES = SEQ // P + 1
SMP = TILES - 1
THIRD = T // 3
H = 4
PAGE = 128
PAST = 512
NPAGE = PAST // PAGE
KEYS = PAST + NS
IH, ID = 8, 64
TOPK = 256
TOPK_S = 129
FF = 2816
KF = FF // P
PW = 512
PPAST = 15
DI = 512
SH, SP, SN = 8, 64, 128
CW = 4
CD = 1024
EPS = 1e-6
NEG = -1e30
TAKEN = -3e38
EVEN_TM = 7
IDX_COL = 3584
ODD_Z, ODD_XBC, ODD_DT = 512, 1024, 2048


def rows(t):
    return P if t < SMP else NS


def host_constants():
    parts, place, at = [], {}, 0

    def put(name, a):
        nonlocal at
        full = np.zeros((P, a.shape[1]), np.float32)
        full[:a.shape[0]] = a
        parts.append(full)
        place[name] = (at, a.shape[1])
        at += a.shape[1]

    i = np.arange(P)
    put("ident", np.eye(P))
    put("flip", np.eye(P)[::-1])
    put("ones", np.ones((P, P)))
    put("upper", (i[:, None] <= i[None, :]) * 1.0)
    put("causal", np.where(i[None, :] <= i[:, None], 0.0, NEG))
    r = np.arange(NS)
    b, t = r // NT, r % NT
    same = b[:, None] == b[None, :]
    put("upper_s", (same & (t[:, None] <= t[None, :])) * 1.0)
    put("new_ok", np.where(same & (t[None, :] <= t[:, None]), 0.0, NEG))
    put("same_s", same * 1.0)
    put("seq_of", (b[:, None] == np.arange(NB)[None, :]) * 1.0)
    put("col_seq", np.tile((np.arange(NB)[:, None] == b[None, :]).reshape(1, -1) * 1.0, (P, 1)))
    def bucket(n):
        n = np.maximum(n, 0)
        nf = np.maximum(n, 1).astype(np.float32)
        large = 16 + (np.log(nf / np.float32(16)) / np.float32(math.log(8.0)) * np.float32(16)).astype(np.int32)
        return np.where(n < 16, n, np.minimum(large, 31))

    def onehot(n):
        k = np.arange(32)[:, None]
        return (bucket(n)[None, :] == k) * 1.0 - (k == 31) * 1.0

    put("bias_p", onehot(255 - np.arange(384)))
    dist = []
    for tt in range(NT):
        new = tt - (np.arange(NS) % NT)
        dist.append(onehot(np.concatenate([PAST + tt - np.arange(PAST), new])))
    put("bias_s", np.concatenate(dist, 0))
    put("t_of", (i[:, None] // 32 == np.arange(NT)[None, :]) * 1.0)
    q = np.arange(P)
    put("row_bht", (r[:, None] == (q // 16 * NT + q % NT)[None, :]) * 1.0)
    for g in range(2):
        tok = (4 * g + q // 32) * NT + q % NT
        put(f"row_idx{g}", (r[:, None] == tok[None, :]) * 1.0)
        put(f"sum_idx{g}", (tok[:, None] == r[None, :]) * 1.0)
    head = 2 * ((q % 16) // 4) + (q % 32) // 16
    put("head_idx", (head[:, None] == np.arange(IH)[None, :]) * 1.0)
    put("page_row", i[:, None] * 1.0)
    cnt = np.stack([1.0 / np.minimum(np.arange(PPAST) + 1, 2 ** (g + 1)) for g in range(4)])
    put("pool_head", np.tile(cnt.reshape(1, -1), (P, 1)))
    kept = at
    gam = (1.0 - 2.0 ** (-5.0 - np.arange(H))).astype(np.float64)
    where = np.zeros((P, TILES))
    where[:, :SMP] = i[:, None]
    where[:NS, SMP] = t
    put("ret_q", (gam[None, None, :] ** (where[:, :, None] + 1)).reshape(P, -1))
    put("ret_k", (gam[None, None, :] ** -(where[:, :, None] + 1) * P ** -0.5).reshape(P, -1))
    put("ret_step", np.tile(gam[None, :] ** P, (P, 1)))
    put("ret_step_s", np.tile(gam[None, :] ** NT, (P, 1)))
    pos = np.zeros((P, TILES), np.float32)
    pos[:, :SMP] = np.arange(SEQ).reshape(SMP, P).T
    pos[:NS, SMP] = PAST + t
    inv = np.float32(10000.0) ** (-np.linspace(0.0, 1.0, 64, dtype=np.float32))
    ang = (pos[:, :, None] * inv.astype(np.float32)[None, None, :]).astype(np.float32)
    put("cos", np.cos(ang.astype(np.float64)).reshape(P, -1))
    put("sin", np.sin(ang.astype(np.float64)).reshape(P, -1))

    return place, kept, np.ascontiguousarray(np.concatenate(parts, 1), np.float32)


def spread(ap, at, n):
    dims = list(ap.ap)
    dims.insert(1 + at, [0, n])
    return bass.AP(ap.tensor, ap.offset, dims)


class Room:
    pass


def build_program(nc, ins, outs, const_dram, place, kept):
    with ExitStack() as whole:
        g = Room()
        g.nc = nc
        g.ins, g.outs = ins, outs
        g.sems = []

        def new_semaphore(name):
            g.sems.append(nc.alloc_semaphore(name))
            return g.sems[-1]
        g.sem = new_semaphore
        g.slot_sems = lambda name, n: [new_semaphore(f"{name}{i}") for i in range(n)]
        g.ps = whole.enter_context(nc.psum_tensor("ps", [P, 8, 512], F32))
        g.cst = whole.enter_context(nc.sbuf_tensor("cst", [P, kept], F32))
        g.kept = kept
        g.c = lambda name: g.cst[:, place[name][0]:place[name][0] + place[name][1]]
        g.const_dram, g.place = const_dram, place

        def scratch(name, shape):
            return nc.dram_tensor(name, shape, F32).ap()

        g.proj = scratch("proj", [EVEN_TM, T, 512])
        g.xt_spill = scratch("xt_spill", [P, KD, T])
        g.bias_row = scratch("bias_row", [H, 384])
        g.gain = whole.enter_context(nc.sbuf_tensor("gain", [P, 4, KD], F32))

        def room(stack, name, shape, dt=F32, side=None):
            return stack.enter_context(nc.sbuf_tensor(name, shape, dt, side=side))
        g.room = room

        def halves(stack, name, side=None):
            g.hh = room(stack, f"{name}_high", [P, KD, T], F32R, side)
            g.hl = room(stack, f"{name}_low", [P, KD, T], F32R, side)

        g.halves = halves

        with ExitStack() as even:
            with ExitStack() as att:
                with ExitStack() as normed:
                    halves(normed, "even", "right")
                    with ExitStack() as st:
                        g.xt = room(st, "xt0", [P, KD, T])
                        stage_load(g)
                        stage_norm(g, 0, "n0", spill=True)
                    g.score = room(att, "score", [P, 6, SEQ])
                    g.score_s = room(att, "score_s", [NS, KEYS])
                    stage_index(g)
                    stage_project_even(g)
                g.ht = room(even, "ht_even", [P, KD, T], F32, "right")
                stage_retention(g)
                with ExitStack() as kv:
                    g.qt = room(kv, "qt", [P, H, T])
                    g.kt = room(kv, "kt", [P, H, T])
                    g.va = room(kv, "va", [P, TILES, 512])
                    g.hank = room(kv, "hank", [P, H, 256])
                    stage_attention_prep(g)
                    stage_attention_prompt(g)
                    stage_attention_sample(g)
            free_semaphores(g)
            g.xt = room(whole, "xt", [P, KD, T])
            halves(even, "ffn0")
            stage_project_out(g, ins["w_out_even"][0], "oe", reload=True)
            stage_ffn(g, 0)
        free_semaphores(g)
        with ExitStack() as odd:
            stage_odd(g, odd)
            free_semaphores(g)
            halves(odd, "ffn1")
            stage_project_out(g, ins["w_out_odd"][0], "oo", reload=False)
            stage_ffn(g, 1)
        stage_store(g)
        free_semaphores(g)


def free_semaphores(g):
    g.nc.clear_and_free_semaphores(g.sems)
    g.sems.clear()
    g.nc.all_engine_barrier()


def stage_load(g):
    nc = g.nc
    consts_in, gains_in = g.sem("consts_in"), g.sem("gains_in")
    rows_in, rows_turned, rows_placed = g.slot_sems("rows_in", 3), g.sem("rows_turned"), g.sem("rows_placed")
    with ExitStack() as st:
        ring = g.room(st, "x_rows", [P, 3, D])
        block = st.enter_context(nc.Block())

        @block.sync
        def _(sp):
            sp.dma_start(g.cst[:, :], g.const_dram[:, 0:g.kept]).then_inc(consts_in, 16)
            for t in range(TILES):
                if t >= 3:
                    sp.wait_ge(rows_turned, 2 * (t - 2))
                src = g.ins["x_prompt"][0, t * P:(t + 1) * P, :] if t < SMP else \
                    g.ins["x_sample"].rearrange("b t d -> (b t) d")
                sp.dma_start(ring[0:rows(t), t % 3, :], src).then_inc(rows_in[t % 3], 16)

        @block.gpsimd
        def _(pool):
            for n, (w, l) in enumerate((("norm_mix", 0), ("norm_mix", 1), ("norm_ffn", 0), ("norm_ffn", 1))):
                with nc.allow_non_contiguous_dma("a vector of 1024 across the partitions"):
                    pool.dma_start(g.gain[:, n, :], g.ins[w][l].rearrange("(k p) -> p k", p=P)).then_inc(gains_in, 16)
            pool.wait_ge(gains_in, 64)

        @block.tensor
        def _(pe):
            pe.wait_ge(consts_in, 16)
            for t in range(TILES):
                pe.wait_ge(rows_in[t % 3], 16 * (t // 3 + 1))
                for half in range(2):
                    n = 2 * t + half
                    if n >= 4:
                        pe.wait_ge(rows_placed, n - 3)
                    for k in range(4):
                        last = pe.transpose(g.ps[:, n % 4, k * P:k * P + rows(t)],
                                            ring[0:rows(t), t % 3, (4 * half + k) * P:(4 * half + k + 1) * P],
                                            g.c("ident")[0:rows(t), 0:rows(t)])
                    last.then_inc(rows_turned, 1)

        @block.vector
        def _(dve):
            for n in range(2 * TILES):
                t, half = n // 2, n % 2
                dve.wait_ge(rows_turned, n + 1)
                dve.tensor_copy(g.xt[:, 4 * half:4 * half + 4, t * P:t * P + rows(t)],
                                g.ps[:, n % 4, :].rearrange("p (k i) -> p k i", k=4)[:, :, 0:rows(t)]
                                ).then_inc(rows_placed, 1)


def stage_norm(g, which, tag, spill=False):
    with ExitStack() as st:
        spilled = g.sem(f"{tag}_spilled")
        sq = g.room(st, f"{tag}_sq", [P, 2, T])
        total = g.room(st, f"{tag}_total", [P, T])
        n_scalar, n_tensor, n_vector, _ = split_norm(g, which, tag, sq, total[:, :])
        block = st.enter_context(g.nc.Block())

        @block.sync
        def _(sp):
            if spill:
                for k in range(KD):
                    sp.dma_start(g.xt_spill[:, k, :], g.xt[:, k, :]).then_inc(spilled, 16)
                sp.wait_ge(spilled, 16 * KD)

        @block.scalar
        def _(act):
            n_scalar(act)

        @block.tensor
        def _(pe):
            n_tensor(pe)

        @block.vector
        def _(dve):
            n_vector(dve)


def stage_index(g):
    nc = g.nc
    w_in, w_rounded, w_split = g.slot_sems("ix_weights", 2), g.sem("ix_rounded"), g.sem("ix_split")
    w_pages, keys_doubled = g.sem("ix_pages"), g.sem("ix_doubled")
    table_in, placed_rows = g.sem("ix_table"), g.sem("ix_row_ids")
    projected, copied = g.sem("ix_projected"), g.sem("ix_copied")
    stored = g.sem("ix_stored")
    scored, rectified, weighted = g.sem("ix_scored"), g.sem("ix_rectified"), g.sem("ix_weighted")
    pages_turned, pages_placed = g.sem("ix_turned"), g.sem("ix_placed")
    chain = g.sem("ix_chain")
    s_spread, s_ready, s_scored, s_rect, s_summed = (g.sem(f"ix_s_{n}") for n in
                                                     ("spread", "ready", "scored", "rect", "summed"))
    w_idx = g.ins["w_in_even"][0][:, IDX_COL:IDX_COL + IH * ID + ID + IH].rearrange("(k p) n -> p k n", p=P)
    WI = IH * ID + ID + IH
    LP = 5
    with ExitStack() as st:
        w = g.room(st, "ix_w", [P, 2, KD * P])
        wh = g.room(st, "ix_wh", [P, 2, KD * P], F32R)
        wl = g.room(st, "ix_wl", [P, 2, KD * P], F32R)
        kwt = g.room(st, "ix_kwt", [P, T])
        qi = g.room(st, "ix_q", [P, LP, T])
        kw = g.room(st, "ix_kw", [P, TILES, ID + IH])
        relu = g.room(st, "ix_relu", [P, 3, SEQ])
        pages = g.room(st, "ix_pg", [P, NB * NPAGE, 2, ID])
        past = g.room(st, "ix_past", [P, NB, PAST])
        qz = g.room(st, "ix_qz", [P, NB, 2, NT, NT])
        table = g.room(st, "ix_tab", [P, NB * NPAGE], I32)
        ids = g.room(st, "ix_ids", [P, NB * NPAGE], I32)
        relu_s = g.room(st, "ix_relu_s", [P, 2, KEYS])
        wcol = g.room(st, "ix_wcol", [P, 2, IH + 1])
        wsum = g.room(st, "ix_wsum", [P, 2, NS])
        block = st.enter_context(nc.Block())
        key_rows = g.ins["cache_kidx"][0].rearrange("n p d -> (n p) d")
        units = [(t, h) for t in range(2, SMP) for h in range(IH)]

        def width(m):
            return P if m < 4 else ID + IH

        @block.sync
        def _(sp):
            with nc.allow_non_contiguous_dma("short rows"):
                sp.dma_start(table[:, :], g.ins["page_table"].rearrange("b n -> (b n)").partition_broadcast(P)
                             ).then_inc(table_in, 16)
            for m in range(LP):
                if m >= 2:
                    sp.wait_ge(w_split, m - 1)
                sp.dma_start(w[:, m % 2, 0:KD * width(m)].rearrange("p (k n) -> p k n", k=KD),
                             w_idx[:, :, m * P:m * P + width(m)]).then_inc(w_in[m % 2], 16)
            sp.wait_ge(copied, LP)
            sp.dma_start(qi[ID:2 * ID, 4, :], kwt[0:ID, :]).then_inc(keys_doubled, 16)
            sp.wait_ge(copied, LP + TILES)
            sp.dma_start(g.outs["kidx_prompt"][0, 0].rearrange("(t p) d -> p t d", p=P), kw[:, 0:SMP, 0:ID]
                         ).then_inc(stored, 16)
            sp.dma_start(g.outs["kidx_sample"][0].rearrange("b t d -> (b t) d"), kw[0:NS, SMP, 0:ID]
                         ).then_inc(stored, 16)
            sp.wait_ge(stored, 32)

        @block.gpsimd
        def _(pool):
            pool.memset(qz[:, :, :, :, :], 0.0).then_inc(placed_rows, 1)
            pool.wait_ge(table_in, 16)
            pool.tensor_scalar(ids[:, :], table[:, :], float(PAGE), g.c("page_row"), ALU.mult, ALU.add
                               ).then_inc(placed_rows, 1)
            pool.wait_ge(placed_rows, 2)
            for n in range(NB * NPAGE):
                for c in range(2):
                    pool.indirect_dma_start(out=pages[:, n, c, :], out_offset=None, in_=key_rows,
                                            in_offset=bass.IndirectOffsetOnAxis(ap=ids[:, n:n + 1], axis=0)
                                            ).then_inc(w_pages, 16)

        @block.tensor
        def _(pe):
            for m in range(LP):
                b0 = 4 * (m % 2)
                pe.wait_ge(w_split, m + 1)
                if m >= 2:
                    pe.wait_ge(copied, m - 1)
                for k in range(KD):
                    cols = slice(k * width(m), (k + 1) * width(m))
                    last = split_passes(g, pe, b0, wh[:, m % 2, cols], wl[:, m % 2, cols], g.hh[:, k, :],
                                        g.hl[:, k, :], k == 0, k == KD - 1, width(m))
                last.then_inc(projected, 1)
            pe.wait_ge(copied, LP)
            for t in range(TILES):
                if t >= 2:
                    pe.wait_ge(copied, LP + t - 1)
                pe.transpose(g.ps[0:rows(t), 3 + 4 * (t % 2), 0:ID + IH], kwt[0:ID + IH, t * P:t * P + rows(t)],
                             g.c("ident")[0:ID + IH, 0:ID + IH]).then_inc(projected, 1)
            pe.wait_ge(copied, LP + TILES)
            pe.wait_ge(keys_doubled, 16)
            for n, (t, h) in enumerate(units):
                if n >= 4:
                    pe.wait_ge(rectified, n - 3)
                half = slice(64 * (h % 2), 64 * (h % 2) + 64)
                keys = (t + 1) * P
                for c in range(-(-keys // 512)):
                    hi = min(keys, (c + 1) * 512)
                    last = pe.matmul(g.ps[:, 2 * (n % 4) + c, 0:hi - c * 512], qi[half, h // 2, t * P:(t + 1) * P],
                                     qi[half, 4, c * 512:hi], start=True, stop=True)
                last.then_inc(scored, 1)
            pe.wait_ge(w_pages, 16 * 2 * NB * NPAGE)
            pe.wait_ge(rectified, len(units))
            for b in range(NB):
                if b >= 4:
                    pe.wait_ge(pages_placed, b - 3)
                for p in range(NPAGE):
                    last = pe.transpose(g.ps[:, b % 4, p * P:(p + 1) * P],
                                        pages[:, b * NPAGE + p, :, :].rearrange("p c d -> p (c d)"), g.c("ident"))
                last.then_inc(pages_turned, 1)
            for q in range(2):
                last = pe.matmul(g.ps[:, 4 + q, 0:IH], g.c(f"row_idx{q}")[0:NS, :], kw[0:NS, SMP, ID:ID + IH],
                                 start=True, stop=True)
            last.then_inc(s_spread, 1)
            pe.wait_ge(s_ready, 1)
            for b in range(NB):
                band = slice(32 * (b % 4), 32 * (b % 4) + 32)
                lhs = qz[:, b, :, :, :].rearrange("p a h t -> p (a h t)")
                pe.matmul(g.ps[band, b // 4, :], lhs, past[:, b, :], start=True, stop=True)
                last = pe.matmul(g.ps[band, 2 + b // 4, 0:NS], lhs, qi[:, 4, SEQ:T], start=True, stop=True)
            last.then_inc(s_scored, 1)
            pe.wait_ge(s_rect, 2)
            for q in range(2):
                pe.matmul(g.ps[0:NS, 6, :], wsum[:, q, :], relu_s[:, q, 0:PAST], start=(q == 0), stop=(q == 1))
            for q in range(2):
                last = pe.matmul(g.ps[0:NS, 7, 0:NS], wsum[:, q, :], relu_s[:, q, PAST:KEYS],
                                 start=(q == 0), stop=(q == 1))
            last.then_inc(s_summed, 1)

        @block.scalar
        def _(act):
            def high(m):
                act.wait_ge(w_in[m % 2], 16 * (m // 2 + 1))
                if m >= 2:
                    act.wait_ge(projected, m - 1)
                act.copy(wh[:, m % 2, 0:KD * width(m)], w[:, m % 2, 0:KD * width(m)]).then_inc(w_rounded, 1)

            high(0)
            high(1)
            for m in range(LP):
                act.wait_ge(projected, m + 1)
                b0 = 4 * (m % 2)
                if m < 4:
                    act.activation(qi[:, m, :].rearrange("p (c n) -> p c n", c=3), g.ps[:, b0:b0 + 3, 0:THIRD],
                                   ACT.Copy, scale=ID ** -0.5).then_inc(copied, 1)
                else:
                    act.copy(qi[0:ID, 4, :].rearrange("p (c n) -> p c n", c=3), g.ps[0:ID, b0:b0 + 3, 0:THIRD])
                    act.copy(kwt[0:ID + IH, :].rearrange("p (c n) -> p c n", c=3),
                             g.ps[0:ID + IH, b0:b0 + 3, 0:THIRD]).then_inc(copied, 1)
                if m + 2 < LP:
                    high(m + 2)
            for t in range(TILES):
                act.wait_ge(projected, LP + t + 1)
                act.copy(kw[0:rows(t), t, :], g.ps[0:rows(t), 3 + 4 * (t % 2), 0:ID + IH]).then_inc(copied, 1)
            for n, (t, h) in enumerate(units):
                act.wait_ge(scored, n + 1)
                if n >= 3:
                    act.wait_ge(weighted, n - 2)
                keys = (t + 1) * P
                two = g.ps[:, 2 * (n % 4):2 * (n % 4) + 2, :].rearrange("p c n -> p (c n)")
                act.activation(relu[:, n % 3, 0:keys], two[:, 0:keys], ACT.Relu).then_inc(rectified, 1)
            for q in range(2):
                act.wait_ge(s_scored, 1)
                act.activation(relu_s[:, q, 0:PAST], g.ps[:, q, :], ACT.Relu)
                act.activation(relu_s[:, q, PAST:KEYS], g.ps[:, 2 + q, 0:NS], ACT.Relu).then_inc(s_rect, 1)

        @block.vector
        def _(dve):
            done = [0]

            def link(op):
                done[0] += 1
                op.then_inc(chain, 1)
                dve.wait_ge(chain, done[0])

            for m in range(LP):
                dve.wait_ge(w_rounded, m + 1)
                part = slice(0, KD * width(m))
                dve.tensor_tensor(wl[:, m % 2, part], w[:, m % 2, part], wh[:, m % 2, part].bitcast(F32), ALU.subtract
                                  ).then_inc(w_split, 1)
            dve.wait_ge(copied, LP + TILES)
            link(dve.tensor_scalar(kw[:, 0:SMP, ID:], kw[:, 0:SMP, ID:], IH ** -0.5, None, ALU.mult))
            for n, (t, h) in enumerate(units):
                keys = (t + 1) * P
                out = g.score[:, t - 2, 0:keys]
                wi = kw[:, t, ID + h:ID + h + 1]
                dve.wait_ge(rectified, n + 1)
                if h == 0:
                    dve.tensor_scalar(out, relu[:, n % 3, 0:keys], wi, None, ALU.mult).then_inc(weighted, 1)
                else:
                    dve.wait_ge(weighted, n)
                    dve.scalar_tensor_tensor(out=out, in0=relu[:, n % 3, 0:keys], scalar=wi, in1=out,
                                             op0=ALU.mult, op1=ALU.add).then_inc(weighted, 1)
                if h == IH - 1:
                    dve.wait_ge(weighted, n + 1)
                    link(dve.tensor_tensor(g.score[:, t - 2, keys - P:keys], g.score[:, t - 2, keys - P:keys],
                                           g.c("causal"), ALU.add))
            for b in range(NB):
                dve.wait_ge(pages_turned, b + 1)
                dve.tensor_copy(past[:, b, :], g.ps[:, b % 4, :]).then_inc(pages_placed, 1)
            dve.wait_ge(placed_rows, 1)
            for par in range(2):
                half = slice(64 * par, 64 * par + 64)
                for hh in range(4):
                    link(dve.tensor_copy(qz[half, :, par, hh, :],
                                         qi[half, hh, SEQ:T].rearrange("p (b t) -> p b t", b=NB)))
            dve.wait_ge(s_spread, 1)
            for q in range(2):
                link(dve.tensor_tensor(wcol[:, q, 0:IH], g.ps[:, 4 + q, 0:IH], g.c("head_idx"), ALU.mult))
                link(dve.tensor_reduce(wcol[:, q, IH:IH + 1], wcol[:, q, 0:IH], AX.X, ALU.add))
                link(dve.tensor_scalar(wsum[:, q, :], g.c(f"sum_idx{q}"), wcol[:, q, IH:IH + 1], IH ** -0.5,
                                       ALU.mult, ALU.mult))
            dve.wait_ge(pages_placed, NB)
            dve.wait_ge(copied, LP + TILES)
            dve.tensor_copy(wcol[:, 0, 0:1], wcol[:, 0, 1:2]).then_inc(s_ready, 1)
            dve.wait_ge(s_summed, 1)
            dve.tensor_copy(g.score_s[:, 0:PAST], g.ps[0:NS, 6, :])
            dve.tensor_tensor(g.score_s[:, PAST:KEYS], g.ps[0:NS, 7, 0:NS], g.c("new_ok")[0:NS, :], ALU.add)


def stage_project_even(g):
    nc = g.nc
    projected, copied = g.sem("pe_projected"), g.sem("pe_copied")
    w_in, w_rounded, w_split = g.sem("pe_weights"), g.sem("pe_rounded"), g.sem("pe_split")
    stored = g.slot_sems("pe_stored", 4)
    found, replaced = g.sem("pe_found"), g.sem("pe_replaced")
    with ExitStack() as st:
        w = g.room(st, "pe_w", [P, KD, 512])
        wh = g.room(st, "pe_wh", [P, 2, KD, 512], F32R)
        wl = g.room(st, "pe_wl", [P, 2, KD, 512], F32R)
        out = g.room(st, "pe_out", [P, 4, 512])
        best = g.room(st, "pe_best", [P, 8])
        block = st.enter_context(nc.Block())

        @block.sync
        def _(sp):
            def load(m):
                sp.dma_start(w[:, :, :], g.ins["w_in_even"][0][:, m * 512:(m + 1) * 512]
                             .rearrange("(k p) n -> p k n", p=P)).then_inc(w_in, 16)

            load(0)
            for n in range(EVEN_TM * TILES):
                m, t = n // TILES, n % TILES
                if t == 0 and m + 1 < EVEN_TM:
                    sp.wait_ge(w_split, KD * (m + 1))
                    load(m + 1)
                sp.wait_ge(copied, n + 1)
                sp.dma_start(g.proj[m, t * P:t * P + rows(t), :], out[0:rows(t), n % 4, :]).then_inc(stored[n % 4], 16)
            for slot in range(4):
                sp.wait_ge(stored[slot], 16 * len(range(slot, EVEN_TM * TILES, 4)))

        @block.tensor
        def _(pe):
            for m in range(EVEN_TM):
                for t in range(TILES):
                    n = m * TILES + t
                    if n >= 8:
                        pe.wait_ge(copied, n - 7)
                    for k in range(KD):
                        if t == 0:
                            pe.wait_ge(w_split, KD * m + k + 1)
                        high, low = (h[:, k, t * P:t * P + rows(t)] for h in (g.hh, g.hl))
                        to = g.ps[0:rows(t), n % 8, :]
                        pe.matmul(to, high, wh[:, m % 2, k, :], start=(k == 0), stop=False)
                        pe.matmul(to, high, wl[:, m % 2, k, :], start=False, stop=False)
                        last = pe.matmul(to, low, wh[:, m % 2, k, :], start=False, stop=(k == KD - 1))
                    last.then_inc(projected, 1)

        @block.scalar
        def _(act):
            def high(m, k):
                if k == 0:
                    act.wait_ge(w_in, 16 * (m + 1))
                    if m >= 2:
                        act.wait_ge(projected, TILES * (m - 1))
                act.copy(wh[:, m % 2, k, :], w[:, k, :]).then_inc(w_rounded, 1)

            for k in range(KD):
                high(0, k)
            for n in range(EVEN_TM * TILES):
                m, t = n // TILES, n % TILES
                act.wait_ge(projected, n + 1)
                if n >= 4:
                    act.wait_ge(stored[n % 4], 16 * (n // 4))
                act.copy(out[0:rows(t), n % 4, :], g.ps[0:rows(t), n % 8, :]).then_inc(copied, 1)
                if t < KD and m + 1 < EVEN_TM:
                    high(m + 1, t)

        @block.gpsimd
        def _(pool):
            for n in range(EVEN_TM * KD):
                m, k = n // KD, n % KD
                pool.wait_ge(w_rounded, n + 1)
                pool.tensor_tensor(wl[:, m % 2, k, :], w[:, k, :], wh[:, m % 2, k, :].bitcast(F32), ALU.subtract
                                   ).then_inc(w_split, 1)

        @block.vector
        def _(dve):
            done = [0, 0]
            for t in range(2, TILES):
                area = g.score[:, t - 2, 0:(t + 1) * P] if t < SMP else g.score_s[:, :]
                top = best[0:rows(t), :]
                want = TOPK if t < SMP else TOPK_S
                for r in range(-(-want // 8)):
                    dve.max(top, area).then_inc(found, 1)
                    done[0] += 1
                    dve.wait_ge(found, done[0])
                    if want - 8 * r < 8:
                        dve.memset(best[0:rows(t), want - 8 * r:8], 3e38).then_inc(found, 1)
                        done[0] += 1
                        dve.wait_ge(found, done[0])
                    dve.match_replace(area, top, area, TAKEN).then_inc(replaced, 1)
                    done[1] += 1
                    dve.wait_ge(replaced, done[1])
                dve.tensor_scalar(area, area, TAKEN, NEG, ALU.not_equal, ALU.mult)


def stage_retention(g):
    nc = g.nc
    heads_in, state_in, v_in, g_in = (g.sem(f"rt_{n}") for n in ("qk_in", "state_in", "v_in", "gate_in"))
    zeroed, turned_in = g.sem("rt_zeroed"), g.sem("rt_rotated")
    turned, copied, scored, masked, made, state = (g.sem(f"rt_{n}") for n in
                                                   ("turned", "copied", "scored", "masked", "made", "state"))
    s_turned, s_copied, s_laid, s_scored, s_masked, s_made, s_out, s_kv, s_kv_read = (
        g.sem(f"rt_s_{n}") for n in ("turned", "copied", "laid", "scored", "masked", "made", "out", "kv", "kv_read"))
    gated, mixed, placed, state_out, chain = (g.sem(f"rt_{n}") for n in
                                              ("gated", "mixed", "placed", "state_out", "chain"))
    rms_ready, root_ready = g.sem("rt_rms"), g.sem("rt_root")
    with ExitStack() as st:
        q = g.room(st, "rt_q", [P, TILES, 512])
        k = g.room(st, "rt_k", [P, TILES, 512])
        v = g.room(st, "rt_v", [P, TILES, 512])
        tmp = g.room(st, "rt_tmp", [P, 4, 3 * H * 64])
        qr = g.room(st, "rt_qr", [P, 2, 512])
        kr = g.room(st, "rt_kr", [P, 2, 512])
        sr = g.room(st, "rt_sr", [P, 2, 512])
        R = g.room(st, "rt_state", [P, H, P])
        S0 = g.room(st, "rt_s0", [P, NB, H, P])
        qs = g.room(st, "rt_qs", [P, 2, H, NS])
        qz = g.room(st, "rt_qz", [P, H, NB, NS])
        ss = g.room(st, "rt_ss", [NS, H, NS])
        kb = g.room(st, "rt_kb", [NS, 2, 512])
        ms = g.room(st, "rt_ms", [P, TILES * H])
        tables = g.room(st, "rt_tables", [P, g.const_dram.shape[1] - g.kept])
        tables_in = g.sem("rt_tables_in")
        block = st.enter_context(nc.Block())
        ident = g.c("ident")

        def table(name):
            at, width = g.place[name]
            return tables[:, at - g.kept:at - g.kept + width]

        def src(m):
            return g.proj[m, 0:SEQ, :].rearrange("(c p) n -> p c n", p=P)

        @block.sync
        def _(sp):
            sp.dma_start(tables[:, :], g.const_dram[:, g.kept:]).then_inc(tables_in, 16)
            sp.wait_ge(zeroed, 3)
            for buf, m, s in ((q, 0, heads_in), (k, 1, heads_in), (v, 2, v_in)):
                sp.dma_start(buf[:, 0:SMP, :], src(m)).then_inc(s, 16)
                sp.dma_start(buf[0:NS, SMP, :], g.proj[m, SEQ:T, :]).then_inc(s, 16)
            sp.dma_start(S0[:, :, :, :], g.ins["state_ret"][0].rearrange("b h d e -> d b h e")).then_inc(state_in, 16)
            sp.wait_ge(state, SMP)
            sp.dma_start(g.outs["ret_prompt"][0, 0].rearrange("h d e -> d h e"), R[:, :, :]).then_inc(state_out, 16)
            sp.wait_ge(s_kv_read, NB + 1)
            sp.dma_start(g.outs["ret_sample"][0].rearrange("b h d e -> d b h e"), S0[:, :, :, :]).then_inc(state_out, 16)
            sp.wait_ge(s_kv, NB)
            sp.wait_ge(made, SMP)
            sp.dma_start(k[:, 0:SMP, :], src(3)).then_inc(g_in, 16)
            sp.dma_start(k[0:NS, SMP, :], g.proj[3, SEQ:T, :]).then_inc(g_in, 16)
            sp.wait_ge(state_out, 32)

        @block.gpsimd
        def _(pool):
            for buf in (q, k, v):
                pool.memset(buf[:, SMP, :], 0.0).then_inc(zeroed, 1)

        @block.tensor
        def _(pe):
            def turn(c):
                if c >= 2:
                    pe.wait_ge(copied, 2 * (c - 1))
                for n, buf in enumerate((q, k)):
                    for h in range(H):
                        last = pe.transpose(g.ps[:, 2 * n + c % 2, h * P:(h + 1) * P],
                                            buf[:, c, h * P:(h + 1) * P], ident)
                last.then_inc(turned, 1)

            pe.wait_ge(turned_in, 1)
            pe.wait_ge(v_in, 32)
            turn(0)
            for c in range(SMP):
                if c + 1 < SMP:
                    turn(c + 1)
                pe.wait_ge(copied, 2 * (c + 1))
                if c >= 1:
                    pe.wait_ge(masked, c)
                for h in range(H):
                    cols = slice(h * P, (h + 1) * P)
                    last = pe.matmul(g.ps[:, 4, cols], kr[:, c % 2, cols], qr[:, c % 2, cols], start=True, stop=True)
                last.then_inc(scored, 1)
                pe.wait_ge(masked, c + 1)
                if c >= 1:
                    pe.wait_ge(state, c)
                for h in range(H):
                    cols = slice(h * P, (h + 1) * P)
                    pe.matmul(g.ps[:, 5, cols], sr[:, c % 2, cols], v[:, c, cols], start=True, stop=(c == 0))
                    if c >= 1:
                        pe.matmul(g.ps[:, 5, cols], qr[:, c % 2, cols], R[:, h, :], start=False, stop=True)
                for h in range(H):
                    cols = slice(h * P, (h + 1) * P)
                    last = pe.matmul(g.ps[:, 6, cols], k[:, c, cols], v[:, c, cols], start=True, stop=True)
                last.then_inc(made, 1)
            pe.wait_ge(copied, 2 * SMP)
            for n, buf in enumerate((q, k)):
                for h in range(H):
                    last = pe.transpose(g.ps[:, n, h * NS:(h + 1) * NS], buf[0:NS, SMP, h * P:(h + 1) * P],
                                        ident[0:NS, 0:NS])
            last.then_inc(s_turned, 1)
            pe.wait_ge(s_copied, 2)
            for h in range(H):
                last = pe.matmul(g.ps[0:NS, 2, h * NS:(h + 1) * NS], qs[:, 1, h, :], qs[:, 0, h, :],
                                 start=True, stop=True)
            last.then_inc(s_scored, 1)
            pe.wait_ge(s_masked, 1)
            pe.wait_ge(s_laid, 1)
            pe.wait_ge(state_in, 16)
            for h in range(H):
                cols = slice(h * P, (h + 1) * P)
                pe.matmul(g.ps[0:NS, 3, cols], ss[:, h, :], v[0:NS, SMP, cols], start=True, stop=False)
                for b in range(NB):
                    last = pe.matmul(g.ps[0:NS, 3, cols], qz[:, h, b, :], S0[:, b, h, :],
                                     start=False, stop=(b == NB - 1))
            last.then_inc(s_out, 1)
            pe.wait_ge(state, SMP)
            for b in range(NB):
                pe.wait_ge(s_made, b + 1)
                if b >= 2:
                    pe.wait_ge(s_kv_read, b - 1)
                for h in range(H):
                    cols = slice(h * P, (h + 1) * P)
                    last = pe.matmul(g.ps[:, 4 + b % 2, cols], kb[:, b % 2, cols], v[0:NS, SMP, cols],
                                     start=True, stop=True)
                last.then_inc(s_kv, 1)
            for t in range(TILES):
                pe.wait_ge(mixed, 1)
                if t == 0:
                    pe.wait_ge(s_kv_read, NB)
                if t >= 4:
                    pe.wait_ge(placed, t - 3)
                for h in range(H):
                    last = pe.transpose(g.ps[:, t % 4, h * P:h * P + rows(t)], q[0:rows(t), t, h * P:(h + 1) * P],
                                        ident[0:rows(t), 0:rows(t)])
                last.then_inc(gated, 1)

        @block.scalar
        def _(act):
            for c in range(SMP):
                act.wait_ge(turned, c + 1)
                if c >= 2:
                    act.wait_ge(made, c - 1)
                act.copy(qr[:, c % 2, :], g.ps[:, c % 2, :]).then_inc(copied, 1)
                act.copy(kr[:, c % 2, :], g.ps[:, 2 + c % 2, :]).then_inc(copied, 1)
            act.wait_ge(s_turned, 1)
            for n in range(2):
                act.copy(qs[:, n, :, :].rearrange("p h t -> p (h t)"), g.ps[:, n, 0:H * NS]).then_inc(s_copied, 1)
            act.wait_ge(rms_ready, 1)
            act.activation(ms[:, :], ms[:, :], ACT.Sqrt).then_inc(root_ready, 1)
            act.wait_ge(g_in, 32)
            act.activation(k[:, :, :], k[:, :, :], ACT.Silu).then_inc(root_ready, 1)
            for t in range(TILES):
                act.wait_ge(gated, t + 1)
                act.copy(g.ht[:, 0:H, t * P:t * P + rows(t)],
                         g.ps[:, t % 4, :].rearrange("p (h i) -> p h i", h=H)[:, :, 0:rows(t)]).then_inc(placed, 1)

        @block.vector
        def _(dve):
            done = [0]

            def link(op):
                done[0] += 1
                op.then_inc(chain, 1)
                dve.wait_ge(chain, done[0])

            dve.wait_ge(heads_in, 64)
            dve.wait_ge(tables_in, 16)
            dve.wait_ge(zeroed, 3)
            cos = table("cos").rearrange("p (t i) -> p t i", t=TILES)
            sin = table("sin").rearrange("p (t i) -> p t i", t=TILES)
            last = None
            for buf, decay in ((q, "ret_q"), (k, "ret_k")):
                scale = table(decay).rearrange("p (t h) -> p t h", h=H)
                for t0 in range(0, TILES, 3):
                    part = buf[:, t0:t0 + 3, :].rearrange("p t (h s i) -> p t h s i", h=H, s=2)
                    cs, sn = spread(cos[:, t0:t0 + 3, :], 1, H), spread(sin[:, t0:t0 + 3, :], 1, H)
                    tv = [tmp[:, n, :].rearrange("p (t h i) -> p t h i", t=3, h=H) for n in range(4)]
                    dve.tensor_tensor(tv[0], part[:, :, :, 0, :], cs, ALU.mult)
                    dve.tensor_tensor(tv[1], part[:, :, :, 1, :], sn, ALU.mult)
                    dve.tensor_tensor(tv[2], part[:, :, :, 0, :], sn, ALU.mult)
                    link(dve.tensor_tensor(tv[3], part[:, :, :, 1, :], cs, ALU.mult))
                    dve.tensor_tensor(part[:, :, :, 0, :], tv[0], tv[1], ALU.subtract)
                    link(dve.tensor_tensor(part[:, :, :, 1, :], tv[2], tv[3], ALU.add))
                    whole = buf[:, t0:t0 + 3, :].rearrange("p t (h d) -> p t h d", h=H)
                    last = dve.tensor_tensor(whole, whole, spread(scale[:, t0:t0 + 3, :], 2, P), ALU.mult)
                    if not (buf is k and t0 == 6):
                        link(last)
            last.then_inc(turned_in, 1)
            upper = spread(g.c("upper"), 0, H)
            for c in range(SMP):
                dve.wait_ge(scored, c + 1)
                dve.tensor_tensor(sr[:, c % 2, :].rearrange("p (h i) -> p h i", h=H),
                                  g.ps[:, 4, :].rearrange("p (h i) -> p h i", h=H), upper, ALU.mult
                                  ).then_inc(masked, 1)
                dve.wait_ge(made, c + 1)
                dve.tensor_copy(q[:, c, :], g.ps[:, 5, :])
                kv = g.ps[:, 6, :].rearrange("p (h e) -> p h e", h=H)
                step = spread(table("ret_step"), 1, P)
                if c == 0:
                    dve.tensor_tensor(R[:, :, :], kv, step, ALU.mult).then_inc(state, 1)
                else:
                    link(dve.tensor_tensor(R[:, :, :], kv, R[:, :, :], ALU.add))
                    dve.tensor_tensor(R[:, :, :], R[:, :, :], step, ALU.mult).then_inc(state, 1)
            dve.wait_ge(s_copied, 2)
            col = g.c("col_seq").rearrange("p (b t) -> p b t", b=NB)
            for h in range(H):
                last = dve.tensor_tensor(qz[:, h, :, :], spread(qs[:, 0, h, :], 0, NB), col, ALU.mult)
            last.then_inc(s_laid, 1)
            dve.wait_ge(s_scored, 1)
            dve.tensor_tensor(ss[:, :, :], g.ps[0:NS, 2, 0:H * NS].rearrange("p (h i) -> p h i", h=H),
                              spread(g.c("upper_s")[0:NS, :], 0, H), ALU.mult).then_inc(s_masked, 1)
            dve.wait_ge(s_out, 1)
            link(dve.tensor_copy(q[0:NS, SMP, :], g.ps[0:NS, 3, :]))
            for b in range(NB):
                if b >= 2:
                    dve.wait_ge(s_kv, b - 1)
                dve.tensor_scalar(kb[:, b % 2, :], k[0:NS, SMP, :], g.c("seq_of")[0:NS, b:b + 1], None, ALU.mult
                                  ).then_inc(s_made, 1)
                if b >= 1:
                    dve.wait_ge(s_kv, b)
                    dve.tensor_tensor(S0[:, b - 1, :, :].rearrange("p h e -> p (h e)"), g.ps[:, 4 + (b - 1) % 2, :],
                                      S0[:, b - 1, :, :].rearrange("p h e -> p (h e)"), ALU.add
                                      ).then_inc(s_kv_read, 1)
            dve.wait_ge(s_kv, NB)
            dve.tensor_tensor(S0[:, NB - 1, :, :].rearrange("p h e -> p (h e)"), g.ps[:, 4 + (NB - 1) % 2, :],
                              S0[:, NB - 1, :, :].rearrange("p h e -> p (h e)"), ALU.add).then_inc(s_kv_read, 1)
            dve.wait_ge(s_kv_read, NB)
            dve.tensor_tensor(S0[:, :, :, :], S0[:, :, :, :],
                              spread(spread(table("ret_step_s"), 0, NB), 2, P), ALU.mult).then_inc(s_kv_read, 1)
            dve.wait_ge(s_kv_read, NB + 1)
            qf = q[:, :, :].rearrange("p t (h e) -> p (t h) e", h=H)
            vf = v[:, :, :].rearrange("p t (h e) -> p (t h) e", h=H)
            link(dve.tensor_tensor(vf, qf, qf, ALU.mult))
            link(dve.tensor_reduce(ms[:, :], vf, AX.X, ALU.add))
            dve.tensor_scalar(ms[:, :], ms[:, :], 1.0 / P, EPS, ALU.mult, ALU.add).then_inc(rms_ready, 1)
            dve.wait_ge(root_ready, 1)
            link(dve.reciprocal(ms[:, :], ms[:, :]))
            link(dve.tensor_tensor(qf, qf, spread(ms[:, :], 1, P), ALU.mult))
            dve.wait_ge(root_ready, 2)
            dve.tensor_tensor(q[:, :, :], q[:, :, :], k[:, :, :], ALU.mult).then_inc(mixed, 1)


def stage_attention_prep(g):
    nc = g.nc
    zeroed, q_in, k_in, v_in, small_in = (g.sem(f"ap_{n}") for n in ("zeroed", "q_in", "k_in", "v_in", "small_in"))
    rms, root, chain = g.sem("ap_rms"), g.sem("ap_root"), g.sem("ap_chain")
    normed_q, normed_k, stored = g.sem("ap_normed_q"), g.sem("ap_normed_k"), g.sem("ap_stored")
    turned, placed = g.sem("ap_turned"), g.sem("ap_placed")
    bias_made, bias_read, bias_out, hank_in = (g.sem(f"ap_bias_{n}") for n in ("made", "read", "out", "in"))
    with ExitStack() as st:
        q = g.room(st, "ap_q", [P, TILES, 512])
        k = g.room(st, "ap_k", [P, TILES, 512])
        sq = g.room(st, "ap_sq", [P, TILES, 512])
        ms = g.room(st, "ap_ms", [P, 2, TILES * H])
        gains = g.room(st, "ap_gains", [P, 2, P])
        rb = g.room(st, "ap_rb", [32, H])
        row = g.room(st, "ap_row", [H, 384])
        block = st.enter_context(nc.Block())
        jobs = [(buf, t) for t in range(TILES) for buf in (0, 1)]

        @block.sync
        def _(sp):
            with nc.allow_non_contiguous_dma("small tables"):
                sp.dma_start(rb[:, :], g.ins["rel_bias"]).then_inc(small_in, 16)
                sp.dma_start(gains[:, 0, :], g.ins["q_norm"][0].partition_broadcast(P)).then_inc(small_in, 16)
                sp.dma_start(gains[:, 1, :], g.ins["k_norm"][0].partition_broadcast(P)).then_inc(small_in, 16)
            sp.wait_ge(zeroed, 3)
            for buf, m, s in ((k, 5, k_in), (q, 4, q_in), (g.va, 6, v_in)):
                sp.dma_start(buf[:, 0:SMP, :], g.proj[m, 0:SEQ, :].rearrange("(c p) n -> p c n", p=P)).then_inc(s, 16)
                sp.dma_start(buf[0:NS, SMP, :], g.proj[m, SEQ:T, :]).then_inc(s, 16)
            sp.wait_ge(bias_read, 1)
            sp.dma_start(g.bias_row, row[:, :]).then_inc(bias_out, 16)
            sp.wait_ge(bias_out, 16)
            sp.dma_start(g.hank[:, :, :], bass.AP(g.bias_row.tensor, 0, [[1, P], [384, H], [1, 256]])
                         ).then_inc(hank_in, 16)
            sp.wait_ge(v_in, 32)
            for buf, name, s in ((g.va, "v", None), (k, "k", normed_k)):
                if s is not None:
                    sp.wait_ge(s, 1)
                sp.dma_start(g.outs[f"{name}_prompt"][0, 0].rearrange("(c p) h d -> p c (h d)", p=P),
                             buf[:, 0:SMP, :]).then_inc(stored, 16)
                sp.dma_start(g.outs[f"{name}_sample"][0].rearrange("b t h d -> (b t) (h d)"),
                             buf[0:NS, SMP, :]).then_inc(stored, 16)
            sp.wait_ge(stored, 64)
            sp.wait_ge(hank_in, 16)

        @block.gpsimd
        def _(pool):
            for buf in (q, k, g.va):
                pool.memset(buf[:, SMP, :], 0.0).then_inc(zeroed, 1)

        @block.tensor
        def _(pe):
            pe.wait_ge(small_in, 48)
            pe.matmul(g.ps[0:H, 7, 0:384], rb[:, :], g.c("bias_p")[0:32, :], start=True, stop=True
                      ).then_inc(bias_made, 1)
            pe.wait_ge(normed_k, 1)
            pe.wait_ge(normed_q, 1)
            for n, (which, t) in enumerate(jobs):
                if n >= 4:
                    pe.wait_ge(placed, n - 3)
                for h in range(H):
                    last = pe.transpose(g.ps[:, n % 4, h * P:h * P + rows(t)],
                                        (q, k)[which][0:rows(t), t, h * P:(h + 1) * P],
                                        g.c("ident")[0:rows(t), 0:rows(t)])
                last.then_inc(turned, 1)

        @block.scalar
        def _(act):
            act.wait_ge(bias_made, 1)
            act.copy(row[:, :], g.ps[0:H, 7, 0:384]).then_inc(bias_read, 1)
            for n in range(2):
                act.wait_ge(rms, n + 1)
                act.activation(ms[:, n, :], ms[:, n, :], ACT.Sqrt).then_inc(root, 1)
            for n, (which, t) in enumerate(jobs):
                act.wait_ge(turned, n + 1)
                act.copy((g.qt, g.kt)[which][:, :, t * P:t * P + rows(t)],
                         g.ps[:, n % 4, :].rearrange("p (h i) -> p h i", h=H)[:, :, 0:rows(t)]).then_inc(placed, 1)

        @block.vector
        def _(dve):
            done = [0]

            def link(op):
                done[0] += 1
                op.then_inc(chain, 1)
                dve.wait_ge(chain, done[0])

            dve.wait_ge(zeroed, 3)
            dve.wait_ge(small_in, 48)
            link(dve.tensor_scalar(gains[:, 0, :], gains[:, 0, :], P ** -0.5, None, ALU.mult))
            sv = sq[:, :, :].rearrange("p t (h e) -> p (t h) e", h=H)
            for n, (buf, arrived, normed) in enumerate(((k, k_in, normed_k), (q, q_in, normed_q))):
                dve.wait_ge(arrived, 32)
                xv = buf[:, :, :].rearrange("p t (h e) -> p (t h) e", h=H)
                link(dve.tensor_tensor(sv, xv, xv, ALU.mult))
                link(dve.tensor_reduce(ms[:, n, :], sv, AX.X, ALU.add))
                dve.tensor_scalar(ms[:, n, :], ms[:, n, :], 1.0 / P, EPS, ALU.mult, ALU.add).then_inc(rms, 1)
                dve.wait_ge(root, n + 1)
                link(dve.reciprocal(ms[:, n, :], ms[:, n, :]))
                link(dve.tensor_tensor(xv, xv, spread(ms[:, n, :], 1, P), ALU.mult))
                dve.tensor_tensor(xv, xv, spread(gains[:, 1 - n, :], 0, TILES * H), ALU.mult).then_inc(normed, 1)


def stage_attention_prompt(g):
    nc = g.nc
    logits, summed, negated, powered, total, scaled = (g.sem(f"at_{n}") for n in
                                                       ("logits", "masked", "negated", "powered", "total", "scaled"))
    turned, copied, made, placed = (g.sem(f"at_{n}") for n in ("turned", "copied", "made", "placed"))
    units = [(t, h) for t in range(SMP) for h in range(H)]
    with ExitStack() as st:
        lg = g.room(st, "at_logits", [P, 2, SEQ])
        pt = g.room(st, "at_probs_t", [P, 2, SMP, P])
        near = g.room(st, "at_near", [P, 2 * P])
        stat = g.room(st, "at_stat", [P, 2, 4])
        block = st.enter_context(nc.Block())
        near_ready = g.sem("at_near")

        def spans(keys):
            return [(c, c * 512, min(keys, (c + 1) * 512)) for c in range(-(-keys // 512))]

        @block.tensor
        def _(pe):
            def logit(n):
                t, h = units[n]
                b0 = 2 * (n % 2)
                if n >= 2:
                    pe.wait_ge(summed, n - 1)
                for c, lo, hi in spans((t + 1) * P):
                    blocks = [(j, x) for j, x in ((t - 1, 0), (t, 1)) if lo <= j * P < hi and j >= 0]
                    for x, (j, which) in enumerate(blocks):
                        pe.matmul(g.ps[:, b0 + c, j * P - lo:(j + 1) * P - lo], g.c("flip"),
                                  g.hank[:, h, which * P:(which + 1) * P], start=(x == 0), stop=False,
                                  skip_group_check=True)
                    last = pe.matmul(g.ps[:, b0 + c, 0:hi - lo], g.qt[:, h, t * P:(t + 1) * P], g.kt[:, h, lo:hi],
                                     start=not blocks, stop=True, skip_group_check=True)
                last.then_inc(logits, 1)

            logit(0)
            m = 0
            for n, (t, h) in enumerate(units):
                if n + 1 < len(units):
                    logit(n + 1)
                pe.wait_ge(scaled, n + 1)
                for j0 in range(0, t + 1, 4):
                    if m >= 2:
                        pe.wait_ge(copied, m - 1)
                    for j in range(j0, min(j0 + 4, t + 1)):
                        last = pe.transpose(g.ps[:, 4 + m % 2, (j - j0) * P:(j - j0 + 1) * P],
                                            lg[:, n % 2, j * P:(j + 1) * P], g.c("ident"))
                    last.then_inc(turned, 1)
                    m += 1
                if n >= 2:
                    pe.wait_ge(placed, n - 1)
                pe.wait_ge(copied, m)
                for j in range(t + 1):
                    last = pe.matmul(g.ps[:, 6 + n % 2, 0:P], g.va[:, j, h * P:(h + 1) * P], pt[:, n % 2, j, :],
                                     start=(j == 0), stop=(j == t))
                last.then_inc(made, 1)

        def drain(act, n, m):
            t, h = units[n]
            if n >= 2:
                act.wait_ge(made, n - 1)
            for j0 in range(0, t + 1, 4):
                nb = min(4, t + 1 - j0)
                act.wait_ge(turned, m + 1)
                act.copy(pt[:, n % 2, j0:j0 + nb, :].rearrange("p j i -> p (j i)"), g.ps[:, 4 + m % 2, 0:nb * P]
                         ).then_inc(copied, 1)
                m += 1
            return m

        @block.scalar
        def _(act):
            m = 0
            for n, (t, h) in enumerate(units):
                keys = (t + 1) * P
                act.wait_ge(negated, n + 1)
                act.activation(lg[:, n % 2, 0:keys], lg[:, n % 2, 0:keys], ACT.Exp, bias=stat[:, n % 2, 1:2],
                               accum_out=stat[:, n % 2, 2:3]).then_inc(powered, 1)
                if n >= 1:
                    m = drain(act, n - 1, m)
            drain(act, len(units) - 1, m)

        @block.vector
        def _(dve):
            dve.memset(near[:, 0:P], 0.0).then_inc(near_ready, 1)
            dve.tensor_copy(near[:, P:2 * P], g.c("causal")).then_inc(near_ready, 1)
            dve.wait_ge(near_ready, 2)

            def place(n):
                t, h = units[n]
                dve.wait_ge(made, n + 1)
                dve.tensor_copy(g.ht[:, H + h, t * P:(t + 1) * P], g.ps[:, 6 + n % 2, 0:P]).then_inc(placed, 1)

            for n, (t, h) in enumerate(units):
                keys = (t + 1) * P
                mask = near[:, P:] if t == 0 else near[:, :] if t == 1 else g.score[:, t - 2, 0:keys]
                two = g.ps[:, 2 * (n % 2):2 * (n % 2) + 2, :].rearrange("p c n -> p (c n)")[:, 0:keys]
                dve.wait_ge(logits, n + 1)
                if n >= 2:
                    dve.wait_ge(turned, sum(-(-(u[0] + 1) // 4) for u in units[:n - 1]))
                dve.tensor_tensor_reduce(lg[:, n % 2, 0:keys], two, mask, 1.0, -3e38, ALU.add, ALU.max,
                                         stat[:, n % 2, 0:1]).then_inc(summed, 1)
                dve.wait_ge(summed, n + 1)
                dve.tensor_scalar(stat[:, n % 2, 1:2], stat[:, n % 2, 0:1], -1.0, None, ALU.mult
                                  ).then_inc(negated, 1)
                if n >= 1:
                    place(n - 1)
                dve.wait_ge(powered, n + 1)
                dve.reciprocal(stat[:, n % 2, 3:4], stat[:, n % 2, 2:3]).then_inc(total, 1)
                dve.wait_ge(total, n + 1)
                dve.tensor_scalar(lg[:, n % 2, 0:keys], lg[:, n % 2, 0:keys], stat[:, n % 2, 3:4], None, ALU.mult
                                  ).then_inc(scaled, 1)
            place(len(units) - 1)


def stage_attention_sample(g):
    nc = g.nc
    table_in, ids_ready, rb_in = (g.sem(f"as_{n}") for n in ("table", "ids", "rb_in"))
    k_in, v_in = g.slot_sems("as_k_in", 2), g.slot_sems("as_v_in", 2)
    laid, turned, placed, logits = (g.sem(f"as_{n}") for n in ("laid", "turned", "placed", "logits"))
    masked, negated, powered, scaled = (g.sem(f"as_{n}") for n in ("masked", "negated", "powered", "scaled"))
    p_turned, p_placed, made, chain = (g.sem(f"as_{n}") for n in ("p_turned", "p_placed", "made", "chain"))
    with ExitStack() as st:
        kp = g.room(st, "as_k", [P, 2, NPAGE, 512])
        vp = g.room(st, "as_v", [P, 2, NPAGE, 512])
        kts = g.room(st, "as_kt", [P, 2, H, PAST])
        qz = g.room(st, "as_qz", [P, NB, H, 2, H, NT])
        rb = g.room(st, "as_rb", [P, H])
        rbt = g.room(st, "as_rbt", [P, NB, H, NT])
        lg = g.room(st, "as_logits", [P, KEYS])
        pt = g.room(st, "as_pt", [P, NPAGE + 1, P])
        stat = g.room(st, "as_stat", [P, 4])
        table = g.room(st, "as_tab", [P, NB * NPAGE], I32)
        ids = g.room(st, "as_ids", [P, NB * NPAGE], I32)
        block = st.enter_context(nc.Block())

        @block.sync
        def _(sp):
            with nc.allow_non_contiguous_dma("small tables"):
                sp.dma_start(table[:, :], g.ins["page_table"].rearrange("b n -> (b n)").partition_broadcast(P)
                             ).then_inc(table_in, 16)
                for t in range(NT):
                    sp.dma_start(rb[32 * t:32 * t + 32, :], g.ins["rel_bias"]).then_inc(rb_in, 16)

        @block.gpsimd
        def _(pool):
            pool.memset(qz[:, :, :, :, :, :], 0.0).then_inc(ids_ready, 1)
            pool.wait_ge(table_in, 16)
            pool.tensor_scalar(ids[:, :], table[:, :], float(PAGE), g.c("page_row"), ALU.mult, ALU.add
                               ).then_inc(ids_ready, 1)
            pool.wait_ge(ids_ready, 2)

            def load(buf, name, b, s):
                for p in range(NPAGE):
                    n = b * NPAGE + p
                    pool.indirect_dma_start(out=buf[:, b % 2, p, :], out_offset=None,
                                            in_=g.ins[name][0].rearrange("n p h d -> (n p) (h d)"),
                                            in_offset=bass.IndirectOffsetOnAxis(ap=ids[:, n:n + 1], axis=0)
                                            ).then_inc(s[b % 2], 16)

            for b in range(NB):
                if b >= 2:
                    pool.wait_ge(turned, H * (b - 1))
                load(kp, "cache_k", b, k_in)
            for b in range(NB):
                if b >= 2:
                    pool.wait_ge(made, b - 1)
                load(vp, "cache_v", b, v_in)

        @block.tensor
        def _(pe):
            pe.wait_ge(laid, 1)
            for (bank, lo, hi) in ((4, 0, PAST), (5, PAST, KEYS)):
                pe.matmul(g.ps[:, bank, 0:hi - lo], rbt[:, :, :, :].rearrange("p b h t -> p (b h t)"),
                          g.c("bias_s")[:, lo:hi], start=True, stop=False, skip_group_check=True)
                pe.matmul(g.ps[:, bank, 0:hi - lo], g.c("row_bht")[0:NS, :], g.score_s[:, lo:hi],
                          start=False, stop=False, skip_group_check=True)
            for b in range(NB):
                pe.wait_ge(k_in[b % 2], 16 * NPAGE * (b // 2 + 1))
                for h in range(H):
                    n = b * H + h
                    if n >= 4:
                        pe.wait_ge(placed, n - 3)
                    for p in range(NPAGE):
                        last = pe.transpose(g.ps[:, n % 4, p * P:(p + 1) * P], kp[:, b % 2, p, h * P:(h + 1) * P],
                                            g.c("ident"))
                    last.then_inc(turned, 1)
                band = slice(32 * (b // 2), 32 * (b // 2) + 32)
                pe.wait_ge(placed, H * (b + 1))
                for h in range(H):
                    lhs = qz[:, b, h, :, :, :].rearrange("p a h t -> p (a h t)")
                    pe.matmul(g.ps[band, 4, :], lhs, kts[:, b % 2, h, :], start=False, stop=(b == NB - 1 and h == 3),
                              skip_group_check=True)
                    last = pe.matmul(g.ps[band, 5, 0:NS], lhs, g.kt[:, h, SEQ:T], start=False,
                                     stop=(b == NB - 1 and h == 3), skip_group_check=True)
                last.then_inc(logits, 1)
            pe.wait_ge(scaled, 1)
            for c in range(NPAGE):
                pe.transpose(g.ps[:, 6, c * P:(c + 1) * P], lg[:, c * P:(c + 1) * P], g.c("ident"))
            pe.transpose(g.ps[0:NS, 7, 0:P], lg[:, PAST:KEYS], g.c("ident")).then_inc(p_turned, 1)
            pe.wait_ge(p_placed, 2)
            for b in range(NB):
                pe.wait_ge(v_in[b % 2], 16 * NPAGE * (b // 2 + 1))
                for h in range(H):
                    r0 = (b * H + h) * NT
                    for p in range(NPAGE):
                        pe.matmul(g.ps[:, 0, r0:r0 + NT], vp[:, b % 2, p, h * P:(h + 1) * P], pt[:, p, r0:r0 + NT],
                                  start=(p == 0), stop=False)
                    last = pe.matmul(g.ps[:, 0, r0:r0 + NT], g.va[0:NS, SMP, h * P:(h + 1) * P],
                                     pt[0:NS, NPAGE, r0:r0 + NT], start=False, stop=True)
                last.then_inc(made, 1)

        @block.scalar
        def _(act):
            for n in range(NB * H):
                b, h = n // H, n % H
                act.wait_ge(turned, n + 1)
                if b >= 2:
                    act.wait_ge(logits, b - 1)
                act.copy(kts[:, b % 2, h, :], g.ps[:, n % 4, :]).then_inc(placed, 1)
            act.wait_ge(negated, 1)
            act.activation(lg[:, :], lg[:, :], ACT.Exp, bias=stat[:, 1:2], accum_out=stat[:, 2:3]
                           ).then_inc(powered, 1)

        @block.vector
        def _(dve):
            done = [0]

            def link(op):
                done[0] += 1
                op.then_inc(chain, 1)
                dve.wait_ge(chain, done[0])

            dve.wait_ge(rb_in, 64)
            link(dve.tensor_tensor(rbt[:, :, :, :], spread(spread(rb[:, :], 0, NB), 2, NT),
                                   spread(spread(g.c("t_of"), 0, H), 0, NB), ALU.mult))
            dve.wait_ge(ids_ready, 1)
            for par in range(2):
                for h in range(H):
                    new = g.qt[:, h, SEQ:T].rearrange("p (b a t) -> p b a t", a=2, t=NT)[:, :, par, :]
                    last = dve.tensor_copy(
                        qz[:, :, h, par, h, :].rearrange("p (b a) t -> p b a t", a=2)[:, :, par, :], new)
            last.then_inc(laid, 1)
            dve.wait_ge(logits, NB)
            link(dve.tensor_copy(lg[:, 0:PAST], g.ps[:, 4, :]))
            link(dve.tensor_copy(lg[:, PAST:KEYS], g.ps[:, 5, 0:NS]))
            link(dve.tensor_reduce(stat[:, 0:1], lg[:, :], AX.X, ALU.max))
            dve.tensor_scalar(stat[:, 1:2], stat[:, 0:1], -1.0, None, ALU.mult).then_inc(negated, 1)
            dve.wait_ge(powered, 1)
            link(dve.reciprocal(stat[:, 3:4], stat[:, 2:3]))
            dve.tensor_scalar(lg[:, :], lg[:, :], stat[:, 3:4], None, ALU.mult).then_inc(scaled, 1)
            dve.wait_ge(p_turned, 1)
            dve.tensor_copy(pt[:, 0:NPAGE, :].rearrange("p c r -> p (c r)"), g.ps[:, 6, :]).then_inc(p_placed, 1)
            dve.tensor_copy(pt[0:NS, NPAGE, :], g.ps[0:NS, 7, 0:P]).then_inc(p_placed, 1)
            dve.wait_ge(made, NB)
            dve.tensor_copy(g.ht[:, H:2 * H, SEQ:T].rearrange("p h (b t) -> p b h t", b=NB),
                            g.ps[:, 0, 0:P].rearrange("p (b h t) -> p b h t", b=NB, h=H))


def stage_project_out(g, weight, tag, reload):
    nc = g.nc
    x_in, made, added = (g.sem(f"{tag}_{n}") for n in ("stream", "made", "added"))
    w_in, w_rounded, w_split = g.slot_sems(f"{tag}_weights", 2), g.sem(f"{tag}_w_rounded"), g.sem(f"{tag}_w_split")
    rounded, split = g.sem(f"{tag}_rounded"), g.sem(f"{tag}_split")
    with ExitStack() as st:
        w = g.room(st, f"{tag}_w", [P, 2, KD * P])
        wh = g.room(st, f"{tag}_wh", [P, 2, KD * P], F32R)
        wl = g.room(st, f"{tag}_wl", [P, 2, KD * P], F32R)
        block = st.enter_context(nc.Block())

        @block.sync
        def _(sp):
            for m in range(KD):
                if m >= 2:
                    sp.wait_ge(w_split, m - 1)
                sp.dma_start(w[:, m % 2, :].rearrange("p (k n) -> p k n", k=KD),
                             weight[:, m * P:(m + 1) * P].rearrange("(k p) n -> p k n", p=P)
                             ).then_inc(w_in[m % 2], 16)

        @block.gpsimd
        def _(pool):
            if reload:
                for k in range(KD):
                    pool.dma_start(g.xt[:, k, :], g.xt_spill[:, k, :]).then_inc(x_in, 16)

        @block.tensor
        def _(pe):
            for m in range(KD):
                pe.wait_ge(w_split, m + 1)
                if m >= 2:
                    pe.wait_ge(added, m - 1)
                for k in range(KD):
                    if m == 0:
                        pe.wait_ge(split, k + 1)
                    cols = slice(k * P, (k + 1) * P)
                    last = split_passes(g, pe, 4 * (m % 2), wh[:, m % 2, cols], wl[:, m % 2, cols], g.hh[:, k, :],
                                        g.hl[:, k, :], k == 0, k == KD - 1)
                last.then_inc(made, 1)

        @block.scalar
        def _(act):
            def high(m):
                act.wait_ge(w_in[m % 2], 16 * (m // 2 + 1))
                if m >= 2:
                    act.wait_ge(made, m - 1)
                act.copy(wh[:, m % 2, :], w[:, m % 2, :]).then_inc(w_rounded, 1)

            act.copy(g.hh[:, 0, :], g.ht[:, 0, :]).then_inc(rounded, 1)
            high(0)
            for k in range(1, KD):
                act.copy(g.hh[:, k, :], g.ht[:, k, :]).then_inc(rounded, 1)
            for m in range(1, KD):
                high(m)

        @block.vector
        def _(dve):
            def low(m):
                dve.wait_ge(w_rounded, m + 1)
                dve.tensor_tensor(wl[:, m % 2, :], w[:, m % 2, :], wh[:, m % 2, :].bitcast(F32), ALU.subtract
                                  ).then_inc(w_split, 1)

            for k in range(KD):
                dve.wait_ge(rounded, k + 1)
                dve.tensor_tensor(g.hl[:, k, :], g.ht[:, k, :], g.hh[:, k, :].bitcast(F32), ALU.subtract
                                  ).then_inc(split, 1)
                if k == 0:
                    low(0)
            low(1)
            for m in range(KD):
                dve.wait_ge(made, m + 1)
                if reload and m == 0:
                    dve.wait_ge(x_in, 16 * KD)
                if m + 2 < KD:
                    low(m + 2)
                xv = g.xt[:, m, :].rearrange("p (c n) -> p c n", c=3)
                dve.tensor_tensor(xv, g.ps[:, 4 * (m % 2):4 * (m % 2) + 3, 0:THIRD], xv, ALU.add).then_inc(added, 1)


def split_norm(g, which, tag, sq, total):
    squared, added, summed, mean_ready, root_ready, inverted = (
        g.sem(f"{tag}_{n}") for n in ("squared", "added", "summed", "mean", "root", "inverse"))
    scaled, rounded, normed = g.sem(f"{tag}_scaled"), g.sem(f"{tag}_rounded"), g.sem(f"{tag}_normed")

    def scalar(act):
        for k in range(KD):
            if k >= 2:
                act.wait_ge(added, k - 1)
            act.activation(sq[:, k % 2, :], g.xt[:, k, :], ACT.Square).then_inc(squared, 1)
        act.wait_ge(mean_ready, 1)
        act.activation(total, total, ACT.Sqrt).then_inc(root_ready, 1)
        for k in range(KD):
            act.wait_ge(scaled, k + 1)
            act.copy(g.hh[:, k, :], sq[:, k % 2, :]).then_inc(rounded, 1)

    def tensor(pe):
        pe.wait_ge(added, KD)
        for c in range(3):
            last = pe.matmul(g.ps[:, c, 0:THIRD], g.c("ones"), total[:, c * THIRD:(c + 1) * THIRD],
                             start=True, stop=True)
        last.then_inc(summed, 1)

    def vector(dve):
        for k in range(KD):
            dve.wait_ge(squared, k + 1)
            if k == 0:
                dve.tensor_copy(total, sq[:, 0, :]).then_inc(added, 1)
            else:
                dve.wait_ge(added, k)
                dve.tensor_tensor(total, total, sq[:, k % 2, :], ALU.add).then_inc(added, 1)
        dve.wait_ge(summed, 1)
        dve.tensor_scalar(total.rearrange("p (c n) -> p c n", c=3), g.ps[:, 0:3, 0:THIRD], 1.0 / D, EPS,
                          ALU.mult, ALU.add).then_inc(mean_ready, 1)
        dve.wait_ge(root_ready, 1)
        dve.reciprocal(total, total).then_inc(inverted, 1)
        dve.wait_ge(inverted, 1)

        def low(k):
            dve.wait_ge(rounded, k + 1)
            dve.tensor_tensor(g.hl[:, k, :], sq[:, k % 2, :], g.hh[:, k, :].bitcast(F32), ALU.subtract
                              ).then_inc(normed, 1)

        for k in range(KD):
            if k >= 2:
                dve.wait_ge(normed, k - 1)
            dve.scalar_tensor_tensor(out=sq[:, k % 2, :], in0=g.xt[:, k, :], scalar=g.gain[:, which, k:k + 1],
                                     in1=total, op0=ALU.mult, op1=ALU.mult).then_inc(scaled, 1)
            if k >= 1:
                low(k - 1)
        low(KD - 1)

    return scalar, tensor, vector, normed


def split_passes(g, pe, b0, weight_high, weight_low, high, low, first, final, out_rows=P):
    for n, (lhs, rhs) in enumerate(((weight_high, high), (weight_high, low), (weight_low, high))):
        for c in range(3):
            last = pe.matmul(g.ps[0:out_rows, b0 + c, 0:THIRD], lhs, rhs[:, c * THIRD:(c + 1) * THIRD],
                             start=(first and n == 0), stop=(final and n == 2))
    return last


def stage_ffn(g, layer):
    nc = g.nc
    tag = f"f{layer}"
    CHUNKS = KF // 2
    KINDS = "GUD"
    raw_in = dict(zip(KINDS, g.slot_sems(f"{tag}_raw_in", 3)))
    rounded = dict(zip(KINDS, g.slot_sems(f"{tag}_rounded", 3)))
    split = dict(zip(KINDS, g.slot_sems(f"{tag}_split", 3)))
    made = dict(zip(KINDS, g.slot_sems(f"{tag}_made", 3)))
    silu, joined, hid_high, hid_low, added = (g.sem(f"{tag}_{n}") for n in
                                              ("silu", "joined", "hid_high", "hid_low", "added"))
    source = {"G": g.ins["w_gate"][layer], "U": g.ins["w_up"][layer], "D": g.ins["w_down"][layer]}

    with ExitStack() as st:
        n_scalar, n_tensor, n_vector, normed = split_norm(g, 2 + layer, f"{tag}n", g.ht[:, 5:7, :], g.ht[:, 7, :])
        raw = {k: g.ht[:, 2 + n, 0:1024] for n, k in enumerate(KINDS)}
        wh = {k: g.room(st, f"{tag}_wh{k}", [P, 1024], F32R) for k in KINDS}
        wl = {k: g.room(st, f"{tag}_wl{k}", [P, 1024], F32R) for k in KINDS}
        hidh = g.room(st, f"{tag}_hidh", [P, 2, 2, T], F32R)
        hidl = g.room(st, f"{tag}_hidl", [P, 2, 2, T], F32R)
        gate, prod = g.ht[:, 0, :], g.ht[:, 1, :]
        block = st.enter_context(nc.Block())

        def thirds(ap):
            return ap.rearrange("p (c n) -> p c n", c=3)

        def chunks(fori, chunk):
            for c in range(3):
                chunk(c, c % 2)
            with fori(0, (CHUNKS - 5) // 2) as i:
                for u in range(2):
                    chunk(2 * i + (3 + u), (3 + u) % 2)
            for c in range(CHUNKS - 2, CHUNKS):
                chunk(c, c % 2)

        def at(c, n):
            return isinstance(c, int) and c == n

        @block.sync
        def _(sp):
            def load(kind, x, first=False):
                if not first:
                    sp.wait_ge(split[kind], x)
                if kind == "D":
                    c, half = x
                    src = source["D"][bass.ds(c * 2 * P, 2 * P), half * 512:(half + 1) * 512]
                    sp.dma_start(raw["D"].rearrange("p (k n) -> p k n", k=2),
                                 src.rearrange("(k p) n -> p k n", p=P)).then_inc(raw_in["D"], 16)
                else:
                    sp.dma_start(raw[kind].rearrange("p (k n) -> p k n", k=KD),
                                 source[kind][:, bass.ds(x * P, P)].rearrange("(k p) n -> p k n", p=P)
                                 ).then_inc(raw_in[kind], 16)

            def load_down(c, half, first=False):
                if not first:
                    sp.wait_ge(split["D"], 2 * c + half)
                load("D", (c, half), True)

            def chunk(c, par):
                if at(c, 0):
                    load("G", 0, True)
                    load("U", 0, True)
                    load("D", (0, 0), True)
                else:
                    load_down(c - 1, 1)
                load("G", 2 * c + 1)
                load("U", 2 * c + 1)
                if not at(c, 0) and not at(c, CHUNKS - 1):
                    load_down(c, 0)
                elif at(c, CHUNKS - 1):
                    load_down(c, 0)
                    load_down(c, 1)
                if not at(c, CHUNKS - 1):
                    load("G", 2 * c + 2)
                    load("U", 2 * c + 2)

            chunks(sp.Fori, chunk)

        @block.tensor
        def _(pe):
            def hidden(kind, f, first=False):
                pe.wait_ge(split[kind], f + 1)
                for k in range(KD):
                    if first:
                        pe.wait_ge(normed, k + 1)
                    last = split_passes(g, pe, 0 if kind == "G" else 3, wh[kind][:, k * P:(k + 1) * P],
                                        wl[kind][:, k * P:(k + 1) * P], g.hh[:, k, :], g.hl[:, k, :],
                                        k == 0, k == KD - 1)
                last.then_inc(made[kind], 1)

            def down(c, par, half, tail=False):
                pe.wait_ge(split["D"], 2 * c - 1 + half)
                if half == 0:
                    pe.wait_ge(hid_low, 2 * c)
                for m in range(4):
                    if tail or m >= 2:
                        pe.wait_ge(added, 8 * c - 9 + 4 * half + m)
                    else:
                        pe.wait_ge((silu, joined)[m], 2 * c + half + 1)
                    for k in range(2):
                        cols = slice((4 * k + m) * P, (4 * k + m + 1) * P)
                        last = split_passes(g, pe, 3 * (m % 2), wh["D"][:, cols], wl["D"][:, cols],
                                            hidh[:, 1 - par, k, :], hidl[:, 1 - par, k, :], k == 0, k == 1)
                    last.then_inc(made["D"], 1)

            def chunk(c, par):
                for half in range(2):
                    for n, kind in enumerate("GU"):
                        if at(c, 0) or at(c, 1):
                            if 2 * c + half:
                                if c == 1 and half == 1:
                                    pe.wait_ge(added, 3 + n)
                                else:
                                    pe.wait_ge((silu, joined)[n], 2 * c + half)
                        else:
                            pe.wait_ge(added, 8 * c - 9 + 4 * half + n)
                        hidden(kind, 2 * c + half, first=at(c, 0) and half == 0 and n == 0)
                    if not at(c, 0):
                        down(c, par, half)

            n_tensor(pe)
            chunks(pe.Fori, chunk)
            for half in range(2):
                down(CHUNKS, CHUNKS % 2, half, tail=True)

        @block.scalar
        def _(act):
            def high(kind, x, first=False):
                act.wait_ge(raw_in[kind], 16 * x + 16)
                if not first:
                    act.wait_ge(made[kind], 4 * x if kind == "D" else x)
                act.copy(wh[kind][:, :], raw[kind]).then_inc(rounded[kind], 1)

            def activate(f, first=False):
                act.wait_ge(made["G"], f + 1)
                if not first:
                    act.wait_ge(joined, f)
                act.activation(thirds(gate), g.ps[:, 0:3, 0:THIRD], ACT.Silu).then_inc(silu, 1)

            def hid(par, half, f):
                act.wait_ge(joined, f + 1)
                act.copy(hidh[:, par, half, :], prod).then_inc(hid_high, 1)

            def chunk(c, par):
                final = at(c, CHUNKS - 1)
                if not at(c, 0):
                    high("D", 2 * c - 2, first=at(c, 1))
                activate(2 * c, first=at(c, 0))
                high("G", 2 * c + 1)
                high("U", 2 * c + 1)
                hid(par, 0, 2 * c)
                if not at(c, 0):
                    high("D", 2 * c - 1)
                activate(2 * c + 1)
                if not final:
                    high("G", 2 * c + 2)
                    high("U", 2 * c + 2)
                hid(par, 1, 2 * c + 1)

            high("G", 0, True)
            high("U", 0, True)
            n_scalar(act)
            chunks(act.Fori, chunk)
            for half in range(2):
                high("D", 2 * CHUNKS - 2 + half)

        @block.vector
        def _(dve):
            def low(kind, x):
                dve.wait_ge(rounded[kind], x + 1)
                dve.tensor_tensor(wl[kind][:, :], raw[kind], wh[kind][:, :].bitcast(F32), ALU.subtract
                                  ).then_inc(split[kind], 1)

            def join(f, first=False):
                dve.wait_ge(silu, f + 1)
                dve.wait_ge(made["U"], f + 1)
                if not first:
                    dve.wait_ge(hid_high, f)
                    dve.wait_ge(hid_low, f)
                dve.tensor_tensor(thirds(prod), g.ps[:, 3:6, 0:THIRD], thirds(gate), ALU.mult
                                  ).then_inc(joined, 1)

            def hid(par, half, f):
                dve.wait_ge(hid_high, f + 1)
                dve.tensor_tensor(hidl[:, par, half, :], prod, hidh[:, par, half, :].bitcast(F32), ALU.subtract
                                  ).then_inc(hid_low, 1)

            def add(c, half):
                for m in range(4):
                    dve.wait_ge(made["D"], 8 * c - 7 + 4 * half + m)
                    xv = thirds(g.xt[:, 4 * half + m, :])
                    dve.tensor_tensor(xv, g.ps[:, 3 * (m % 2):3 * (m % 2) + 3, 0:THIRD], xv, ALU.add
                                      ).then_inc(added, 1)

            def chunk(c, par):
                final = at(c, CHUNKS - 1)
                if not at(c, 0):
                    low("D", 2 * c - 2)
                low("G", 2 * c + 1)
                join(2 * c, first=at(c, 0))
                low("U", 2 * c + 1)
                hid(par, 0, 2 * c)
                if not at(c, 0):
                    add(c, 0)
                    low("D", 2 * c - 1)
                if not final:
                    low("G", 2 * c + 2)
                join(2 * c + 1)
                if not final:
                    low("U", 2 * c + 2)
                hid(par, 1, 2 * c + 1)
                if not at(c, 0):
                    add(c, 1)

            low("G", 0)
            low("U", 0)
            n_vector(dve)
            chunks(dve.Fori, chunk)
            for half in range(2):
                low("D", 2 * CHUNKS - 2 + half)
                add(CHUNKS, half)


def stage_store(g):
    nc = g.nc
    turned, copied, stored = g.sem("out_turned"), g.sem("out_copied"), g.slot_sems("out_stored", 4)
    with ExitStack() as st:
        ring = g.room(st, "out_rows", [P, 4, 512])
        block = st.enter_context(nc.Block())

        @block.tensor
        def _(pe):
            for n in range(2 * TILES):
                t, half = n // 2, n % 2
                if n >= 4:
                    pe.wait_ge(copied, n - 3)
                for k in range(4):
                    last = pe.transpose(g.ps[0:rows(t), n % 4, k * P:(k + 1) * P],
                                        g.xt[:, 4 * half + k, t * P:t * P + rows(t)], g.c("ident"))
                last.then_inc(turned, 1)

        @block.vector
        def _(dve):
            for n in range(2 * TILES):
                t = n // 2
                dve.wait_ge(turned, n + 1)
                if n >= 4:
                    dve.wait_ge(stored[n % 4], 16 * (n // 4))
                dve.tensor_copy(ring[0:rows(t), n % 4, :], g.ps[0:rows(t), n % 4, :]).then_inc(copied, 1)

        @block.sync
        def _(sp):
            for n in range(2 * TILES):
                t, half = n // 2, n % 2
                sp.wait_ge(copied, n + 1)
                dst = g.outs["y_prompt"][0, t * P:(t + 1) * P, half * 512:(half + 1) * 512] if t < SMP else \
                    g.outs["y_sample"].rearrange("b t d -> (b t) d")[:, half * 512:(half + 1) * 512]
                sp.dma_start(dst, ring[0:rows(t), n % 4, :]).then_inc(stored[n % 4], 16)
            for slot in range(4):
                sp.wait_ge(stored[slot], 16 * len(range(slot, 2 * TILES, 4)))


XW = CW - 1 + SEQ + NB * (CW - 1 + NT)
UW = PPAST + SEQ


def stage_odd(g, keep):
    with ExitStack() as st:
        g.z = g.room(st, "od_z", [P, TILES, 512], F32, "right")
        g.dt = g.room(st, "od_dt", [P, TILES, SH], F32, "right")
        g.xb = g.room(st, "od_xb", [P, CD // P, XW], F32, "right")
        with ExitStack() as pool_room:
            g.up = g.room(pool_room, "od_up", [P, 4, UW], F32, "right")
            g.us = g.room(pool_room, "od_us", [P, 4, PPAST + NT, NB], F32, "right")
            with ExitStack() as normed:
                g.halves(normed, "odd")
                stage_norm(g, 1, "n2")
                stage_odd_project(g)
            g.ht = g.room(keep, "ht_odd", [P, KD, T])
            stage_pool(g)
        stage_conv(g)
        g.xtm = g.room(st, "od_xtm", [P, TILES, 512])
        g.btm = g.room(st, "od_btm", [P, TILES, 2 * SN])
        stage_ssd(g)


def stage_odd_project(g):
    nc = g.nc
    made, copied = g.sem("op_made"), g.sem("op_copied")
    w_in, w_rounded, w_split = (g.sem(f"op_{n}") for n in ("weights", "rounded", "split"))
    hist_in, hist_turned, hist_placed, cleared = (g.sem(f"op_{n}") for n in
                                                  ("hist_in", "hist_turned", "hist_placed", "cleared"))
    turned, placed = g.sem("op_turned"), g.sem("op_placed")
    weight = g.ins["w_in_odd"][0]
    NF = 17
    ZF = 12
    UROWS, XROWS = NB * PPAST, NB * (CW - 1)

    def first_col(m):
        return m * P if m < 4 else ODD_XBC + (m - 4) * P if m < ZF else ODD_Z + (m - ZF) * P if m < NF - 1 else ODD_DT

    def width(m):
        return P if m < NF - 1 else SH

    with ExitStack() as st:
        w = g.room(st, "op_w", [P, KD * P])
        wh = g.room(st, "op_wh", [P, 2, KD * P], F32R)
        wl = g.room(st, "op_wl", [P, 2, KD * P], F32R)
        hu = g.room(st, "op_hu", [UROWS, PW])
        zt = g.room(st, "op_zt", [P, T])
        hx = zt[0:XROWS, 0:CD]
        block = st.enter_context(nc.Block())

        @block.sync
        def _(sp):
            for m in range(NF):
                if m >= 1:
                    sp.wait_ge(w_split, m)
                with nc.allow_non_contiguous_dma("the last block has eight columns"):
                    sp.dma_start(w[:, 0:KD * width(m)].rearrange("p (k n) -> p k n", k=KD),
                                 weight[:, first_col(m):first_col(m) + width(m)].rearrange("(k p) n -> p k n", p=P)
                                 ).then_inc(w_in, 16)
                if m == 1:
                    sp.dma_start(hu[:, :], g.ins["state_pool"][0].rearrange("b r c -> (b r) c")).then_inc(hist_in, 16)
                    sp.dma_start(hx, g.ins["state_conv"][0].rearrange("b r c -> (b r) c")).then_inc(hist_in, 16)

        @block.gpsimd
        def _(pool):
            pool.memset(g.up[:, :, 0:PPAST], 0.0)
            pool.memset(g.xb[:, :, 0:CW - 1], 0.0)
            pool.memset(g.z[:, SMP, :], 0.0)
            pool.memset(g.dt[:, SMP, :], 0.0).then_inc(cleared, 1)

        @block.tensor
        def _(pe):
            def turn(m):
                pe.wait_ge(copied, m + 1)
                for b in range(3):
                    n = 3 * (m - ZF) + b
                    if n >= 2:
                        pe.wait_ge(placed, n - 1)
                    for t in range(4 * b, min(4 * b + 4, TILES)):
                        at = (t - 4 * b) * P
                        last = pe.transpose(g.ps[0:rows(t), 3 + 4 * (n % 2), at:at + width(m)],
                                            zt[0:width(m), t * P:t * P + rows(t)],
                                            g.c("ident")[0:width(m), 0:width(m)])
                    last.then_inc(turned, 1)

            for m in range(NF):
                pe.wait_ge(w_split, m + 1)
                if m >= 2:
                    pe.wait_ge(copied, m - 1)
                for k in range(KD):
                    cols = slice(k * width(m), (k + 1) * width(m))
                    last = split_passes(g, pe, 4 * (m % 2), wh[:, m % 2, cols], wl[:, m % 2, cols], g.hh[:, k, :],
                                        g.hl[:, k, :], k == 0, k == KD - 1, width(m))
                last.then_inc(made, 1)
                if m == 4:
                    pe.wait_ge(hist_in, 32)
                    for n in range(12):
                        if n >= 2:
                            pe.wait_ge(hist_placed, n - 1)
                        src, r = (hu[:, n * P:(n + 1) * P], UROWS) if n < 4 else (hx[:, (n - 4) * P:(n - 3) * P], XROWS)
                        pe.transpose(g.ps[:, 3 + 4 * (n % 2), 0:r], src, g.c("ident")[0:r, 0:r]
                                     ).then_inc(hist_turned, 1)
                    pe.wait_ge(hist_placed, 12)
                if m > ZF:
                    turn(m - 1)
            turn(NF - 1)

        @block.scalar
        def _(act):
            def high(m):
                act.wait_ge(w_in, 16 * (m + 1))
                if m >= 2:
                    act.wait_ge(made, m - 1)
                act.copy(wh[:, m % 2, 0:KD * width(m)], w[:, 0:KD * width(m)]).then_inc(w_rounded, 1)

            high(0)
            high(1)
            act.wait_ge(cleared, 1)
            for m in range(NF):
                act.wait_ge(made, m + 1)
                b0 = 4 * (m % 2)
                third = SEQ - 2 * THIRD
                if m < ZF:
                    if m < 4:
                        dst, at = g.up[:, m, :], PPAST
                        smp = g.us[:, m, PPAST:PPAST + NT, :]
                    else:
                        dst, at = g.xb[:, m - 4, :], CW - 1
                        smp = g.xb[:, m - 4, CW - 1 + SEQ:XW].rearrange("p (r b) -> p r b", b=NB)[:, CW - 1:, :]
                    act.copy(dst[:, at:at + 2 * THIRD].rearrange("p (c n) -> p c n", c=2), g.ps[:, b0:b0 + 2, 0:THIRD])
                    act.copy(dst[:, at + 2 * THIRD:at + SEQ], g.ps[:, b0 + 2, 0:third])
                    act.copy(smp, g.ps[:, b0 + 2, third:THIRD].rearrange("p (b t) -> p t b", b=NB)
                             ).then_inc(copied, 1)
                else:
                    if m == ZF:
                        act.wait_ge(hist_turned, 12)
                    else:
                        act.wait_ge(turned, 3 * (m - ZF))
                    act.copy(zt[0:width(m), :].rearrange("p (c n) -> p c n", c=3),
                             g.ps[0:width(m), b0:b0 + 3, 0:THIRD]).then_inc(copied, 1)
                if m + 2 < NF:
                    high(m + 2)

        @block.vector
        def _(dve):
            def low(m):
                dve.wait_ge(w_rounded, m + 1)
                part = slice(0, KD * width(m))
                dve.tensor_tensor(wl[:, m % 2, part], w[:, part], wh[:, m % 2, part].bitcast(F32), ALU.subtract
                                  ).then_inc(w_split, 1)

            for m in range(7):
                low(m)
                if m == 5:
                    for n in range(12):
                        dve.wait_ge(hist_turned, n + 1)
                        if n < 4:
                            dst = g.us[:, n, 0:PPAST, :]
                            src = g.ps[:, 3 + 4 * (n % 2), 0:UROWS].rearrange("p (b r) -> p r b", b=NB)
                        else:
                            dst = g.xb[:, n - 4, CW - 1 + SEQ:XW].rearrange("p (r b) -> p r b", b=NB)[:, 0:CW - 1, :]
                            src = g.ps[:, 3 + 4 * (n % 2), 0:XROWS].rearrange("p (b r) -> p r b", b=NB)
                        dve.tensor_copy(dst, src).then_inc(hist_placed, 1)
            for m in range(7, ZF + 2):
                low(m)
            dve.wait_ge(cleared, 1)
            for m in range(ZF, NF):
                if m + 2 < NF:
                    low(m + 2)
                for b in range(3):
                    n = 3 * (m - ZF) + b
                    dve.wait_ge(turned, n + 1)
                    at, tiles = (m - ZF) * P, slice(4 * b, min(4 * b + 4, SMP))
                    room = g.z[:, :, at:at + P] if m < NF - 1 else g.dt
                    src = g.ps[:, 3 + 4 * (n % 2), :].rearrange("p (t i) -> p t i", t=4)[:, :, 0:width(m)]
                    if b < 2:
                        dve.tensor_copy(room[:, tiles, :], src).then_inc(placed, 1)
                    else:
                        dve.tensor_copy(room[0:NS, SMP, :], src[0:NS, 0, :]).then_inc(placed, 1)


def stage_pool(g):
    nc = g.nc
    w_in, diff, mixed, placed = (g.sem(f"po_{n}") for n in ("weights", "diff", "mixed", "placed"))
    turned, copied, stored, chain = (g.sem(f"po_{n}") for n in ("turned", "copied", "stored", "chain"))
    with ExitStack() as st:
        pw = g.room(st, "po_w", [P, 4, P])
        scale = g.room(st, "po_scale", [P, 4])
        sums = g.room(st, "po_sums", [P, 2, UW])
        ssum = g.room(st, "po_ssum", [P, 2, PPAST + NT, NB])
        d = g.room(st, "po_d", [P, 2, T])
        tail = g.room(st, "po_tail", [NS, 2, PW])
        block = st.enter_context(nc.Block())

        @block.sync
        def _(sp):
            sp.dma_start(pw[:, :, :], g.ins["pool_w"][0].rearrange("g c d -> c g d")).then_inc(w_in, 16)
            with nc.allow_non_contiguous_dma("a vector of 512 across the partitions"):
                sp.dma_start(scale[:, :], g.ins["pool_scale"][0].rearrange("(g p) -> p g", p=P)).then_inc(w_in, 16)
            sp.dma_start(g.outs["pool_sample"][0][:, 0:PPAST - NT, :], g.ins["state_pool"][0][:, NT:PPAST, :]
                         ).then_inc(stored, 16)
            sp.wait_ge(copied, 2)
            sp.dma_start(g.outs["pool_prompt"][0, 0], tail[0:PPAST, 0, :]).then_inc(stored, 16)
            for t in range(NT):
                sp.dma_start(g.outs["pool_sample"][0][:, PPAST - NT + t, :], tail[t * NB:(t + 1) * NB, 1, :]
                             ).then_inc(stored, 16)
            sp.wait_ge(stored, 16 * (NT + 2))

        @block.tensor
        def _(pe):
            for m in range(4):
                pe.transpose(g.ps[0:PPAST, 6, m * P:(m + 1) * P], g.up[:, m, SEQ:UW], g.c("ident"))
                last = pe.transpose(g.ps[0:NS, 7, m * P:(m + 1) * P], g.us[:, m, PPAST:, :].rearrange("p t b -> p (t b)"),
                                    g.c("ident"))
            last.then_inc(turned, 1)
            pe.wait_ge(w_in, 32)
            for m in range(4):
                pe.wait_ge(diff, m + 1)
                if m >= 2:
                    pe.wait_ge(placed, m - 1)
                for c in range(3):
                    last = pe.matmul(g.ps[:, 3 * (m % 2) + c, 0:THIRD], pw[:, m, :],
                                     d[:, m % 2, c * THIRD:(c + 1) * THIRD], start=True, stop=True)
                last.then_inc(mixed, 1)

        @block.scalar
        def _(act):
            act.wait_ge(turned, 1)
            act.copy(tail[0:PPAST, 0, :], g.ps[0:PPAST, 6, :]).then_inc(copied, 1)
            act.copy(tail[0:NS, 1, :], g.ps[0:NS, 7, :]).then_inc(copied, 1)
            act.wait_ge(w_in, 32)
            for m in range(4):
                act.wait_ge(mixed, m + 1)
                act.activation(g.ht[:, m, :].rearrange("p (c n) -> p c n", c=3),
                               g.ps[:, 3 * (m % 2):3 * (m % 2) + 3, 0:THIRD], ACT.Copy, scale=scale[:, m:m + 1]
                               ).then_inc(placed, 1)

        @block.vector
        def _(dve):
            done = [0]

            def link(op):
                done[0] += 1
                op.then_inc(chain, 1)
                dve.wait_ge(chain, done[0])

            for m in range(4):
                if m >= 1:
                    dve.wait_ge(diff, m)
                if m >= 2:
                    dve.wait_ge(mixed, m - 1)
                src, ssrc = g.up[:, m, :], g.us[:, m, :, :]
                for s in range(m + 1):
                    sh = 2 ** s
                    dst, sdst = sums[:, s % 2, :], ssum[:, s % 2, :, :]
                    lo = 2 * sh - 1
                    dve.tensor_tensor(dst[:, lo:UW], src[:, lo:UW], src[:, lo - sh:UW - sh], ALU.add)
                    link(dve.tensor_tensor(sdst[:, lo:, :], ssrc[:, lo:, :], ssrc[:, lo - sh:PPAST + NT - sh, :],
                                           ALU.add))
                    src, ssrc = dst, sdst
                head = g.c("pool_head")[:, m * PPAST:(m + 1) * PPAST]
                link(dve.tensor_tensor(src[:, PPAST:2 * PPAST], src[:, PPAST:2 * PPAST], head, ALU.mult))
                inv = 1.0 / 2 ** (m + 1)
                dve.tensor_tensor(d[:, m % 2, 0:PPAST], src[:, PPAST:2 * PPAST], g.up[:, m, PPAST:2 * PPAST],
                                  ALU.subtract)
                dve.scalar_tensor_tensor(out=d[:, m % 2, PPAST:SEQ], in0=src[:, 2 * PPAST:UW], scalar=inv,
                                         in1=g.up[:, m, 2 * PPAST:UW], op0=ALU.mult, op1=ALU.subtract)
                dve.scalar_tensor_tensor(out=d[:, m % 2, SEQ:T].rearrange("p (b t) -> p t b", b=NB),
                                         in0=ssrc[:, PPAST:, :], scalar=inv, in1=g.us[:, m, PPAST:, :],
                                         op0=ALU.mult, op1=ALU.subtract).then_inc(diff, 1)


def stage_conv(g):
    nc = g.nc
    w_in, turned, copied, stored = (g.sem(f"cv_{n}") for n in ("weights", "turned", "copied", "stored"))
    summed, rectified, chain = g.sem("cv_summed"), g.sem("cv_silu"), g.sem("cv_chain")
    MT = CD // P
    with ExitStack() as st:
        taps = g.room(st, "cv_taps", [P, MT, CW + 1])
        acc = g.room(st, "cv_acc", [P, 2, T])
        tail = g.room(st, "cv_tail", [NS, 2, CD])
        block = st.enter_context(nc.Block())

        @block.sync
        def _(sp):
            with nc.allow_non_contiguous_dma("vectors of 1024 across the partitions"):
                for j in range(CW):
                    sp.dma_start(taps[:, :, j], g.ins["conv_w"][0][j].rearrange("(k p) -> p k", p=P)
                                 ).then_inc(w_in, 16)
                sp.dma_start(taps[:, :, CW], g.ins["conv_b"][0].rearrange("(k p) -> p k", p=P)).then_inc(w_in, 16)
            sp.wait_ge(copied, 2)
            sp.dma_start(g.outs["conv_prompt"][0, 0], tail[0:CW - 1, 0, :]).then_inc(stored, 16)
            for t in range(1, NT):
                sp.dma_start(g.outs["conv_sample"][0][:, t - 1, :], tail[t * NB:(t + 1) * NB, 1, :]).then_inc(stored, 16)
            sp.wait_ge(stored, 16 * NT)

        def sample(m):
            return g.xb[:, m, CW - 1 + SEQ:XW].rearrange("p (r b) -> p r b", b=NB)

        @block.tensor
        def _(pe):
            for m in range(MT):
                pe.transpose(g.ps[0:CW - 1, m // 4, (m % 4) * P:(m % 4 + 1) * P], g.xb[:, m, SEQ:SEQ + CW - 1],
                             g.c("ident"))
                last = pe.transpose(g.ps[0:NS, 2 + m // 4, (m % 4) * P:(m % 4 + 1) * P], g.xb[:, m, SEQ + (CW - 1) * (NB + 1):XW], g.c("ident"))
            last.then_inc(turned, 1)

        @block.scalar
        def _(act):
            act.wait_ge(turned, 1)
            act.copy(tail[0:CW - 1, 0, :].rearrange("p (c n) -> p c n", c=2), g.ps[0:CW - 1, 0:2, :]).then_inc(copied, 1)
            act.copy(tail[0:NS, 1, :].rearrange("p (c n) -> p c n", c=2), g.ps[0:NS, 2:4, :]).then_inc(copied, 1)
            for m in range(MT):
                act.wait_ge(summed, m + 1)
                act.activation(g.xb[:, m, 0:T], acc[:, m % 2, :], ACT.Silu).then_inc(rectified, 1)

        @block.vector
        def _(dve):
            done = [0]

            def link(op):
                done[0] += 1
                op.then_inc(chain, 1)
                dve.wait_ge(chain, done[0])

            dve.wait_ge(w_in, 16 * (CW + 1))
            for m in range(MT):
                if m >= 2:
                    dve.wait_ge(rectified, m - 1)
                out, souts = acc[:, m % 2, 0:SEQ], acc[:, m % 2, SEQ:T].rearrange("p (b t) -> p t b", b=NB)
                for j in range(CW):
                    tap = taps[:, m, j:j + 1]
                    src, ssrc = g.xb[:, m, j:j + SEQ], sample(m)[:, j:j + NT, :]
                    if j == 0:
                        dve.tensor_scalar(out, src, tap, taps[:, m, CW:CW + 1], ALU.mult, ALU.add)
                        link(dve.tensor_scalar(souts, ssrc, tap, taps[:, m, CW:CW + 1], ALU.mult, ALU.add))
                    else:
                        dve.scalar_tensor_tensor(out=out, in0=src, scalar=tap, in1=out, op0=ALU.mult, op1=ALU.add)
                        last = dve.scalar_tensor_tensor(out=souts, in0=ssrc, scalar=tap, in1=souts, op0=ALU.mult,
                                                        op1=ALU.add)
                        if j < CW - 1:
                            link(last)
                last.then_inc(summed, 1)


def stage_ssd(g):
    nc = g.nc
    small_in, cleared = g.sem("sd_small"), g.sem("sd_cleared")
    turned, copied = g.sem("sd_turned"), g.sem("sd_copied")
    dt_abs, dt_exp, dt_one, dt_log, dt_ready = (g.sem(f"sd_dt_{n}") for n in ("abs", "exp", "one", "log", "ready"))
    cum, cum_ready, powers = g.sem("sd_cum"), g.sem("sd_cum_ready"), g.sem("sd_powers")
    diag, spread_done, seg, decay, weighted, xs = (g.sem(f"sd_{n}") for n in
                                                   ("diag", "spread", "seg", "decay", "weighted", "xs"))
    made, state, chain = g.sem("sd_made"), g.sem("sd_state"), g.sem("sd_chain")
    st_in, st_turned, st_placed = g.slot_sems("sd_st_in", 2), g.sem("sd_st_turned"), g.sem("sd_st_placed")
    s_laid, s_made, s_xw, s_up, s_new = (g.sem(f"sd_s_{n}") for n in ("laid", "made", "xw", "up", "new"))
    o_turned, o_copied, o_stored = g.sem("sd_o_turned"), g.sem("sd_o_copied"), g.slot_sems("sd_o_stored", 2)
    gate_ready, rms, root, normed, y_turned, y_placed = (g.sem(f"sd_{n}") for n in
                                                         ("gate", "rms", "root", "normed", "y_turned", "y_placed"))
    BT, CT = 4, 6
    with ExitStack() as st:
        ex = g.room(st, "sd_exp", [P, TILES, SH])
        cs = g.room(st, "sd_cs", [P, TILES, SH])
        wend = g.room(st, "sd_wend", [P, TILES, SH])
        a = g.room(st, "sd_a", [P, TILES, SH])
        tmp = g.room(st, "sd_tmp", [P, TILES, SH])
        eend = g.room(st, "sd_eend", [P, SMP, SH])
        eend_s = g.room(st, "sd_eends", [P, NB, SH])
        ab = g.room(st, "sd_ab", [NS, NB, SH])
        rowv = g.room(st, "sd_rowv", [P, 3, SH])
        cst = g.room(st, "sd_cst", [SH, T])
        dg = g.room(st, "sd_diag", [SH, SH, P])
        ee = g.room(st, "sd_e", [P, SH, P])
        gm = g.room(st, "sd_gm", [P, 2, P])
        xd = g.room(st, "sd_xd", [P, 512])
        xw = g.room(st, "sd_xw", [P, 512])
        t1 = g.room(st, "sd_t1", [P, 512])
        h0 = g.room(st, "sd_h", [P, 512])
        hs = g.room(st, "sd_hs", [P, NB, 512])
        nat = g.room(st, "sd_nat", [P, 2, 4, SN])
        cz = g.room(st, "sd_cz", [P, NB, NS])
        gains = g.room(st, "sd_gains", [P, 4])
        rs = g.room(st, "sd_rs", [P, TILES * 2])
        block = st.enter_context(nc.Block())
        ident = g.c("ident")
        state_rows = g.ins["state_ssm"][0].rearrange("b h p n -> b (h p) n")
        out_rows = g.outs["ssm_sample"][0].rearrange("b h p n -> b (h p) n")

        @block.sync
        def _(sp):
            with nc.allow_non_contiguous_dma("small vectors"):
                for n, name in enumerate(("dt_bias", "a_log", "d_skip")):
                    sp.dma_start(rowv[:, n, :], g.ins[name][0].partition_broadcast(P)).then_inc(small_in, 16)
                sp.dma_start(gains[:, :], g.ins["ssm_norm"][0].rearrange("(k p) -> p k", p=P)).then_inc(small_in, 16)
            for b in range(NB):
                if b >= 2:
                    sp.wait_ge(st_turned, b - 1)
                sp.dma_start(nat[:, b % 2, :, :], state_rows[b].rearrange("(c p) n -> p c n", p=P)).then_inc(st_in[b % 2], 16)
            for n in range(NB + 1):
                sp.wait_ge(o_copied, n + 1)
                dst = g.outs["ssm_prompt"][0, 0].rearrange("h p n -> (h p) n") if n == 0 else out_rows[n - 1]
                sp.dma_start(dst.rearrange("(c p) n -> p c n", p=P), nat[:, n % 2, :, :]).then_inc(o_stored[n % 2], 16)
            for slot in range(2):
                sp.wait_ge(o_stored[slot], 16 * len(range(slot, NB + 1, 2)))

        @block.gpsimd
        def _(pool):
            pool.memset(g.xtm[:, SMP, :], 0.0)
            pool.memset(g.btm[:, SMP, :], 0.0)
            pool.memset(cs[:, SMP, :], 0.0)
            pool.memset(wend[:, SMP, :], 0.0).then_inc(cleared, 1)

        @block.tensor
        def _(pe):
            pe.wait_ge(cleared, 1)
            for t in range(TILES):
                if t >= 2:
                    pe.wait_ge(copied, 2 * (t - 1))
                for m in range(6):
                    last = pe.transpose(g.ps[0:rows(t), 2 * (t % 2) + m // 4, (m % 4) * P:(m % 4 + 1) * P],
                                        g.xb[:, m, t * P:t * P + rows(t)], ident)
                last.then_inc(turned, 1)
            for b in range(NB):
                pe.wait_ge(st_in[b % 2], 16 * (b // 2 + 1))
                if b >= 2:
                    pe.wait_ge(st_placed, b - 1)
                for m in range(4):
                    last = pe.transpose(g.ps[:, 4 + b % 2, m * P:(m + 1) * P], nat[:, b % 2, m, :], ident)
                last.then_inc(st_turned, 1)
            pe.wait_ge(dt_ready, 1)
            pe.wait_ge(copied, 2 * TILES)
            pe.wait_ge(st_placed, NB)
            av = a[:, 0:SMP, :].rearrange("p t h -> p (t h)")
            pe.matmul(g.ps[:, 0, 0:SMP * SH], g.c("upper"), av, start=True, stop=True)
            pe.matmul(g.ps[:, 1, 0:SMP * SH], g.c("ones"), av, start=True, stop=True)
            pe.matmul(g.ps[0:NS, 2, 0:SH], g.c("upper_s")[0:NS, :], a[0:NS, SMP, :], start=True, stop=True)
            pe.matmul(g.ps[0:NS, 3, 0:SH], g.c("same_s")[0:NS, :], a[0:NS, SMP, :], start=True, stop=True)
            pe.matmul(g.ps[:, 4, 0:NB * SH], g.c("ones")[0:NS, :], ab[:, :, :].rearrange("p b h -> p (b h)"),
                      start=True, stop=True)
            for c in range(SMP):
                pe.matmul(g.ps[0:SH, 5 + c // 4, (c % 4) * P:(c % 4 + 1) * P], a[:, c, :], g.c("upper"),
                          start=True, stop=True)
            pe.matmul(g.ps[0:SH, 7, 0:NS], a[0:NS, SMP, :], g.c("upper_s")[0:NS, :], start=True, stop=True
                      ).then_inc(cum, 1)
            pe.wait_ge(cum_ready, 1)
            pe.wait_ge(powers, 1)
            for c in range(TILES):
                n = rows(c)
                cols = slice(c * P, c * P + n)
                pe.wait_ge(diag, c + 1)
                if c >= 1:
                    pe.wait_ge(seg, c)
                for half in range(2):
                    last = pe.matmul(g.ps[0:n, half, 0:4 * n], g.c("ones")[0:SH, 0:n],
                                     dg[:, 4 * half:4 * half + 4, 0:n], start=True, stop=True)
                last.then_inc(spread_done, 1)
                if c >= 1:
                    pe.wait_ge(weighted, c)
                for q in range(2):
                    last = pe.matmul(g.ps[0:n, 2, q * P:q * P + n], g.xb[:, BT + q, cols], g.xb[:, CT + q, cols],
                                     start=True, stop=True)
                last.then_inc(spread_done, 1)
                if c >= 1:
                    pe.wait_ge(state, c)
                if c < SMP:
                    if c >= 1:
                        for q in range(2):
                            pe.matmul(g.ps[:, 4, q * 256:(q + 1) * 256], g.xb[:, CT + q, cols],
                                      h0[:, q * 256:(q + 1) * 256], start=True, stop=True)
                    pe.wait_ge(xs, c + 1)
                    for q in range(2):
                        pe.matmul(g.ps[:, 5, q * 256:(q + 1) * 256], g.btm[:, c, q * P:(q + 1) * P],
                                  xw[:, q * 256:(q + 1) * 256], start=True, stop=True)
                else:
                    for q in range(2):
                        pe.wait_ge(s_laid, q + 1)
                        for b in range(NB):
                            last = pe.matmul(g.ps[0:NS, 4, q * 256:(q + 1) * 256], cz[:, b, :],
                                             hs[:, b, q * 256:(q + 1) * 256], start=(b == 0), stop=(b == NB - 1))
                        last.then_inc(s_made, 1)
                    pe.wait_ge(xs, c + 1)
                pe.wait_ge(weighted, c + 1)
                for h in range(SH):
                    last = pe.matmul(g.ps[0:n, 3, h * SP:(h + 1) * SP], ee[0:n, h, 0:n], xd[0:n, h * SP:(h + 1) * SP],
                                     start=True, stop=True)
                last.then_inc(made, 1)
            for m in range(4):
                last = pe.transpose(g.ps[:, 6, m * P:(m + 1) * P], h0[:, m * P:(m + 1) * P], ident)
            last.then_inc(o_turned, 1)
            for b in range(NB):
                pe.wait_ge(s_xw, b + 1)
                for q in range(2):
                    last = pe.matmul(g.ps[:, b % 2, q * 256:(q + 1) * 256], g.btm[0:NS, SMP, q * P:(q + 1) * P],
                                     (xd, t1)[b % 2][0:NS, q * 256:(q + 1) * 256], start=True, stop=True)
                last.then_inc(s_up, 1)
                pe.wait_ge(s_new, b + 1)
                if b >= 1:
                    pe.wait_ge(o_copied, b)
                for m in range(4):
                    last = pe.transpose(g.ps[:, 6 + (b + 1) % 2, m * P:(m + 1) * P], hs[:, b, m * P:(m + 1) * P], ident)
                last.then_inc(o_turned, 1)
            pe.wait_ge(normed, 1)
            for t in range(TILES):
                if t >= 2:
                    pe.wait_ge(y_placed, t - 1)
                for m in range(4):
                    last = pe.transpose(g.ps[:, 2 + t % 2, m * P:m * P + rows(t)],
                                        g.xtm[0:rows(t), t, m * P:(m + 1) * P], ident[0:rows(t), 0:rows(t)])
                last.then_inc(y_turned, 1)

        @block.scalar
        def _(act):
            act.wait_ge(small_in, 64)
            act.wait_ge(dt_abs, 1)
            act.activation(tmp[:, :, :], tmp[:, :, :], ACT.Exp).then_inc(dt_exp, 1)
            act.activation(rowv[:, 1, :], rowv[:, 1, :], ACT.Exp).then_inc(dt_exp, 1)
            act.wait_ge(dt_one, 1)
            act.activation(tmp[:, :, :], tmp[:, :, :], ACT.Ln).then_inc(dt_log, 1)
            for t in range(TILES):
                act.wait_ge(turned, t + 1)
                act.copy(g.xtm[0:rows(t), t, :], g.ps[0:rows(t), 2 * (t % 2), :]).then_inc(copied, 1)
                act.copy(g.btm[0:rows(t), t, :], g.ps[0:rows(t), 2 * (t % 2) + 1, 0:256]).then_inc(copied, 1)
            for b in range(NB):
                act.wait_ge(st_turned, b + 1)
                act.copy(hs[:, b, :], g.ps[:, 4 + b % 2, :]).then_inc(st_placed, 1)
            act.wait_ge(cum_ready, 1)
            act.activation(ex[:, :, :], cs[:, :, :], ACT.Exp)
            act.activation(wend[:, :, :], wend[:, :, :], ACT.Exp)
            act.activation(eend[:, :, :], eend[:, :, :], ACT.Exp)
            act.activation(eend_s[:, :, :], eend_s[:, :, :], ACT.Exp).then_inc(powers, 1)
            for c in range(TILES):
                n = rows(c)
                act.wait_ge(seg, c + 1)
                act.activation(ee[0:n, :, 0:n], ee[0:n, :, 0:n], ACT.Exp).then_inc(decay, 1)
            for n in range(NB + 1):
                act.wait_ge(o_turned, n + 1)
                if n == 0:
                    act.wait_ge(st_turned, NB)
                if n >= 2:
                    act.wait_ge(o_stored[n % 2], 16 * (n // 2))
                act.copy(nat[:, n % 2, :, :].rearrange("p c n -> p (c n)"), g.ps[:, 6 + n % 2, :]).then_inc(o_copied, 1)
            act.activation(g.z[:, :, :], g.z[:, :, :], ACT.Silu).then_inc(gate_ready, 1)
            act.wait_ge(rms, 1)
            act.activation(rs[:, :], rs[:, :], ACT.Sqrt).then_inc(root, 1)

        @block.vector
        def _(dve):
            done = [0]

            def link(op):
                done[0] += 1
                op.then_inc(chain, 1)
                dve.wait_ge(chain, done[0])

            dve.wait_ge(small_in, 64)
            link(dve.tensor_tensor(g.dt[:, :, :], g.dt[:, :, :], spread(rowv[:, 0, :], 0, TILES), ALU.add))
            dve.scalar_tensor_tensor(out=tmp[:, :, :], in0=g.dt[:, :, :], scalar=-1.0, in1=g.dt[:, :, :], op0=ALU.mult,
                                     op1=ALU.min).then_inc(dt_abs, 1)
            dve.wait_ge(dt_exp, 2)
            dve.tensor_scalar(tmp[:, :, :], tmp[:, :, :], 1.0, None, ALU.add).then_inc(dt_one, 1)
            dve.wait_ge(dt_log, 1)
            link(dve.scalar_tensor_tensor(out=g.dt[:, :, :], in0=g.dt[:, :, :], scalar=0.0, in1=tmp[:, :, :],
                                          op0=ALU.max, op1=ALU.add))
            link(dve.scalar_tensor_tensor(out=a[:, :, :], in0=g.dt[:, :, :], scalar=-1.0,
                                          in1=spread(rowv[:, 1, :], 0, TILES), op0=ALU.mult, op1=ALU.mult))
            dve.tensor_tensor(ab[:, :, :], spread(a[0:NS, SMP, :], 0, NB), spread(g.c("seq_of")[0:NS, :], 1, SH),
                              ALU.mult).then_inc(dt_ready, 1)
            dve.wait_ge(cum, 1)
            dve.wait_ge(cleared, 1)
            dve.tensor_copy(cs[:, 0:SMP, :].rearrange("p t h -> p (t h)"), g.ps[:, 0, 0:SMP * SH])
            link(dve.tensor_copy(cs[0:NS, SMP, :], g.ps[0:NS, 2, 0:SH]))
            dve.tensor_tensor(wend[:, 0:SMP, :].rearrange("p t h -> p (t h)"), g.ps[:, 1, 0:SMP * SH],
                              cs[:, 0:SMP, :].rearrange("p t h -> p (t h)"), ALU.subtract)
            dve.tensor_tensor(wend[0:NS, SMP, :], g.ps[0:NS, 3, 0:SH], cs[0:NS, SMP, :], ALU.subtract)
            dve.tensor_copy(eend[:, :, :].rearrange("p t h -> p (t h)"), g.ps[:, 1, 0:SMP * SH])
            dve.tensor_copy(eend_s[:, :, :].rearrange("p b h -> p (b h)"), g.ps[:, 4, 0:NB * SH])
            dve.tensor_copy(cst[:, 0:SEQ].rearrange("p (c n) -> p c n", c=2), g.ps[0:SH, 5:7, :])
            link(dve.tensor_copy(cst[:, SEQ:T], g.ps[0:SH, 7, 0:NS]))
            dve.tensor_copy(t1[:, 0:1], g.c("ones")[:, 0:1]).then_inc(cum_ready, 1)
            dve.wait_ge(powers, 1)
            link(dve.tensor_tensor(wend[:, :, :], wend[:, :, :], g.dt[:, :, :], ALU.mult))
            dve.wait_ge(copied, 2 * TILES)
            for c in range(TILES):
                n = rows(c)
                heads = lambda ap: ap.rearrange("p (h e) -> p h e", h=SH)
                dve.tensor_tensor(dg[:, :, 0:n], spread(cst[:, c * P:c * P + n], 0, SH), spread(ident[0:SH, 0:SH], 1, n),
                                  ALU.mult).then_inc(diag, 1)
                x = heads(g.xtm[0:n, c, :])
                if c >= 1:
                    dve.wait_ge(made, c)
                dve.tensor_tensor(heads(xd[0:n, :]), x, spread(g.dt[0:n, c, :], 1, SP), ALU.mult)
                dve.tensor_tensor(heads(xw[0:n, :]), x, spread(wend[0:n, c, :], 1, SP), ALU.mult).then_inc(xs, 1)
                dve.wait_ge(spread_done, 2 * c + 1)
                two = g.ps[0:n, 0:2, 0:4 * n].rearrange("p a (h i) -> p a h i", h=4)
                ev = ee[0:n, :, 0:n].rearrange("p (a h) i -> p a h i", a=2)
                csv = spread(cs[0:n, c, :].rearrange("p (a h) -> p a h", a=2), 2, n)
                link(dve.tensor_tensor(ev, two, csv, ALU.subtract))
                dve.tensor_scalar(ee[0:n, :, 0:n], ee[0:n, :, 0:n], 0.0, None, ALU.min).then_inc(seg, 1)
                dve.wait_ge(spread_done, 2 * c + 2)
                mask = g.c("upper") if c < SMP else g.c("upper_s")[0:NS, :]
                link(dve.tensor_tensor(gm[0:n, :, 0:n], g.ps[0:n, 2, 0:256].rearrange("p (q i) -> p q i", q=2)[:, :, 0:n],
                                       spread(mask, 0, 2), ALU.mult))
                dve.wait_ge(decay, c + 1)
                dve.tensor_tensor(ev, ev, spread(gm[0:n, :, 0:n], 1, 4), ALU.mult).then_inc(weighted, 1)
                if c == SMP:
                    for q in range(2):
                        if q:
                            dve.wait_ge(s_made, 1)
                        dve.tensor_tensor(cz[:, :, :], spread(g.xb[:, CT + q, SEQ:T], 0, NB),
                                          g.c("col_seq").rearrange("p (b t) -> p b t", b=NB), ALU.mult
                                          ).then_inc(s_laid, 1)
                dve.wait_ge(made, c + 1)
                if c >= 1:
                    link(dve.tensor_tensor(heads(t1[0:n, :]), heads(g.ps[0:n, 4, :]), spread(ex[0:n, c, :], 1, SP),
                                           ALU.mult))
                    link(dve.tensor_tensor(t1[0:n, :], g.ps[0:n, 3, :], t1[0:n, :], ALU.add))
                else:
                    link(dve.tensor_copy(t1[0:n, :], g.ps[0:n, 3, :]))
                link(dve.tensor_tensor(x, x, spread(rowv[0:n, 2, :], 1, SP), ALU.mult))
                if c < SMP:
                    dve.tensor_tensor(g.xtm[0:n, c, :], g.xtm[0:n, c, :], t1[0:n, :], ALU.add)
                    if c >= 1:
                        link(dve.tensor_tensor(heads(h0[:, :]), heads(h0[:, :]), spread(eend[:, c, :], 1, SP), ALU.mult))
                        dve.tensor_tensor(h0[:, :], g.ps[:, 5, :], h0[:, :], ALU.add).then_inc(state, 1)
                    else:
                        dve.tensor_copy(h0[:, :], g.ps[:, 5, :]).then_inc(state, 1)
                else:
                    link(dve.tensor_tensor(g.xtm[0:n, c, :], g.xtm[0:n, c, :], t1[0:n, :], ALU.add))
            for b in range(NB):
                if b >= 2:
                    dve.wait_ge(s_up, b - 1)
                dve.tensor_scalar((xd, t1)[b % 2][0:NS, :], xw[0:NS, :], g.c("seq_of")[0:NS, b:b + 1], None, ALU.mult
                                  ).then_inc(s_xw, 1)
                link(dve.tensor_tensor(hs[:, b, :].rearrange("p (h e) -> p h e", h=SH),
                                       hs[:, b, :].rearrange("p (h e) -> p h e", h=SH),
                                       spread(eend_s[:, b, :], 1, SP), ALU.mult))
                dve.wait_ge(s_up, b + 1)
                dve.tensor_tensor(hs[:, b, :], g.ps[:, b % 2, :], hs[:, b, :], ALU.add).then_inc(s_new, 1)
            dve.wait_ge(gate_ready, 1)
            dve.wait_ge(made, TILES)
            link(dve.tensor_tensor(g.xtm[:, :, :], g.xtm[:, :, :], g.z[:, :, :], ALU.mult))
            yv = g.xtm[:, :, :].rearrange("p t (q e) -> p (t q) e", q=2)
            link(dve.tensor_tensor(g.z[:, :, :], g.xtm[:, :, :], g.xtm[:, :, :], ALU.mult))
            link(dve.tensor_reduce(rs[:, :], g.z[:, :, :].rearrange("p t (q e) -> p (t q) e", q=2), AX.X, ALU.add))
            dve.tensor_scalar(rs[:, :], rs[:, :], 1.0 / 256, EPS, ALU.mult, ALU.add).then_inc(rms, 1)
            dve.wait_ge(root, 1)
            link(dve.reciprocal(rs[:, :], rs[:, :]))
            dve.tensor_tensor(yv, yv, spread(rs[:, :], 1, 256), ALU.mult).then_inc(normed, 1)
            for t in range(TILES):
                dve.wait_ge(y_turned, t + 1)
                dve.tensor_tensor(g.ht[:, 4:8, t * P:t * P + rows(t)],
                                  g.ps[:, 2 + t % 2, :].rearrange("p (m i) -> p m i", m=4)[:, :, 0:rows(t)],
                                  spread(gains[:, :], 1, rows(t)), ALU.mult).then_inc(y_placed, 1)


_INS = ['x_prompt', 'x_sample', 'cache_k', 'cache_v', 'cache_kidx', 'state_ret', 'state_pool', 'state_conv',
        'state_ssm', 'page_table', 'norm_mix', 'norm_ffn', 'w_in_even', 'w_out_even', 'q_norm', 'k_norm', 'rel_bias',
        'w_in_odd', 'w_out_odd', 'pool_w', 'pool_scale', 'conv_w', 'conv_b', 'dt_bias', 'a_log', 'd_skip', 'ssm_norm',
        'w_gate', 'w_up', 'w_down']
_OUTS = [('y_prompt', (1, SEQ, D)), ('y_sample', (NB, NT, D)),
         ('k_prompt', (1, 1, SEQ, H, P)), ('v_prompt', (1, 1, SEQ, H, P)), ('kidx_prompt', (1, 1, SEQ, ID)),
         ('ret_prompt', (1, 1, H, P, P)), ('pool_prompt', (1, 1, PPAST, PW)), ('conv_prompt', (1, 1, CW - 1, CD)),
         ('ssm_prompt', (1, 1, SH, SP, SN)),
         ('k_sample', (1, NB, NT, H, P)), ('v_sample', (1, NB, NT, H, P)), ('kidx_sample', (1, NB, NT, ID)),
         ('ret_sample', (1, NB, H, P, P)), ('pool_sample', (1, NB, PPAST, PW)), ('conv_sample', (1, NB, CW - 1, CD)),
         ('ssm_sample', (1, NB, SH, SP, SN))]


def kernel(**inputs):
    import numpy as _np
    import concourse.bacc as _bacc
    from concourse import mybir as _mybir
    from concourse.bass_utils import run_bass_kernel_spmd as _run

    nc = _bacc.Bacc("TRN2", target_bir_lowering=False, num_devices=1)
    arrays, ins, outs = {}, {}, {}
    for name in _INS:
        a = _np.ascontiguousarray(inputs[name])
        arrays[f"in_{name}_dram"] = a
        ins[name] = nc.dram_tensor(f"in_{name}_dram", a.shape, _mybir.dt.from_np(a.dtype), kind="ExternalInput").ap()
    place, kept, table = host_constants()
    arrays["in_tables_dram"] = table
    tables = nc.dram_tensor("in_tables_dram", table.shape, _mybir.dt.float32, kind="ExternalInput").ap()
    for name, shape in _OUTS:
        outs[name] = nc.dram_tensor(f"out_{name}_dram", shape, _mybir.dt.float32, kind="ExternalOutput").ap()
    build_program(nc, ins, outs, tables, place, kept)
    r = _run(nc, [arrays], core_ids=[0])
    return tuple(r.results[0][f"out_{name}_dram"] for name, _ in _OUTS)
```

```python
import math
from contextlib import ExitStack

import numpy as np

import concourse.bass as bass
from concourse import mybir

F32 = mybir.dt.float32
F32R = mybir.dt.float32r
I32 = mybir.dt.int32
U32 = mybir.dt.uint32
ALU = mybir.AluOpType
ACT = mybir.ActivationFunctionType
AX = mybir.AxisListType

P = 128
D = 1024
KD = D // P
SEQ = 1024
NB, NT = 8, 4
NS = NB * NT
T = SEQ + NS
TILES = SEQ // P + 1
SMP = TILES - 1
THIRD = T // 3
H = 4
PAGE = 128
PAST = 512
NPAGE = PAST // PAGE
KEYS = PAST + NS
IH, ID = 8, 64
TOPK = 256
TOPK_S = 129
FF = 2816
KF = FF // P
PW = 512
PPAST = 15
DI = 512
SH, SP, SN = 8, 64, 128
CW = 4
CD = 1024
EPS = 1e-6
NEG = -1e30
TAKEN = -3e38
EVEN_TM = 7
IDX_COL = 3584
ODD_Z, ODD_XBC, ODD_DT = 512, 1024, 2048


HELD = 6


def rows(t):
    return P if t < SMP else NS


def host_constants():
    parts, place, at = [], {}, 0

    def put(name, a):
        nonlocal at
        full = np.zeros((P, a.shape[1]), np.float32)
        full[:a.shape[0]] = a
        parts.append(full)
        place[name] = (at, a.shape[1])
        at += a.shape[1]

    i = np.arange(P)
    put("ident", np.eye(P))
    put("flip", np.eye(P)[::-1])
    put("ones", np.ones((P, P)))
    put("upper", (i[:, None] <= i[None, :]) * 1.0)
    put("causal", np.where(i[None, :] <= i[:, None], 0.0, NEG))
    r = np.arange(NS)
    b, t = r // NT, r % NT
    same = b[:, None] == b[None, :]
    put("upper_s", (same & (t[:, None] <= t[None, :])) * 1.0)
    put("new_ok", np.where(same & (t[None, :] <= t[:, None]), 0.0, NEG))
    put("same_s", same * 1.0)
    put("seq_of", (b[:, None] == np.arange(NB)[None, :]) * 1.0)
    put("col_seq", np.tile((np.arange(NB)[:, None] == b[None, :]).reshape(1, -1) * 1.0, (P, 1)))
    def bucket(n):
        n = np.maximum(n, 0)
        nf = np.maximum(n, 1).astype(np.float32)
        large = 16 + (np.log(nf / np.float32(16)) / np.float32(math.log(8.0)) * np.float32(16)).astype(np.int32)
        return np.where(n < 16, n, np.minimum(large, 31))

    def onehot(n):
        k = np.arange(32)[:, None]
        return (bucket(n)[None, :] == k) * 1.0 - (k == 31) * 1.0

    put("bias_p", onehot(255 - np.arange(384)))
    dist = []
    for tt in range(NT):
        new = tt - (np.arange(NS) % NT)
        dist.append(onehot(np.concatenate([PAST + tt - np.arange(PAST), new])))
    put("bias_s", np.concatenate(dist, 0))
    put("t_of", (i[:, None] // 32 == np.arange(NT)[None, :]) * 1.0)
    q = np.arange(P)
    put("row_bht", (r[:, None] == (q // 16 * NT + q % NT)[None, :]) * 1.0)
    for g in range(2):
        tok = (4 * g + q // 32) * NT + q % NT
        put(f"row_idx{g}", (r[:, None] == tok[None, :]) * 1.0)
        put(f"sum_idx{g}", (tok[:, None] == r[None, :]) * 1.0)
    head = 2 * ((q % 16) // 4) + (q % 32) // 16
    put("head_idx", (head[:, None] == np.arange(IH)[None, :]) * 1.0)
    put("page_row", i[:, None] * 1.0)
    cnt = np.stack([1.0 / np.minimum(np.arange(PPAST) + 1, 2 ** (g + 1)) for g in range(4)])
    put("pool_head", np.tile(cnt.reshape(1, -1), (P, 1)))
    kept = at
    gam = (1.0 - 2.0 ** (-5.0 - np.arange(H))).astype(np.float64)
    where = np.zeros((P, TILES))
    where[:, :SMP] = i[:, None]
    where[:NS, SMP] = t
    put("ret_q", (gam[None, None, :] ** (where[:, :, None] + 1)).reshape(P, -1))
    put("ret_k", (gam[None, None, :] ** -(where[:, :, None] + 1) * P ** -0.5).reshape(P, -1))
    put("ret_step", np.tile(gam[None, :] ** P, (P, 1)))
    put("ret_step_s", np.tile(gam[None, :] ** NT, (P, 1)))
    pos = np.zeros((P, TILES), np.float32)
    pos[:, :SMP] = np.arange(SEQ).reshape(SMP, P).T
    pos[:NS, SMP] = PAST + t
    inv = np.float32(10000.0) ** (-np.linspace(0.0, 1.0, 64, dtype=np.float32))
    ang = (pos[:, :, None] * inv.astype(np.float32)[None, None, :]).astype(np.float32)
    put("cos", np.cos(ang.astype(np.float64)).reshape(P, -1))
    put("sin", np.sin(ang.astype(np.float64)).reshape(P, -1))

    return place, kept, np.ascontiguousarray(np.concatenate(parts, 1), np.float32)


def spread(ap, at, n):
    dims = list(ap.ap)
    dims.insert(1 + at, [0, n])
    return bass.AP(ap.tensor, ap.offset, dims)


class Room:
    pass


def build_program(nc, ins, outs, const_dram, place, kept):
    with ExitStack() as whole:
        g = Room()
        g.nc = nc
        g.ins, g.outs = ins, outs
        g.sems = []

        def new_semaphore(name):
            g.sems.append(nc.alloc_semaphore(name))
            return g.sems[-1]
        g.sem = new_semaphore
        g.slot_sems = lambda name, n: [new_semaphore(f"{name}{i}") for i in range(n)]
        g.ps = whole.enter_context(nc.psum_tensor("ps", [P, 8, 512], F32))
        g.cst = whole.enter_context(nc.sbuf_tensor("cst", [P, kept], F32))
        g.kept = kept
        g.c = lambda name: g.cst[:, place[name][0]:place[name][0] + place[name][1]]
        g.const_dram, g.place = const_dram, place

        def scratch(name, shape):
            return nc.dram_tensor(name, shape, F32).ap()

        g.proj = scratch("proj", [EVEN_TM, T, 512])
        g.xt_spill = scratch("xt_spill", [P, KD, T])
        g.bias_row = scratch("bias_row", [H, 384])
        g.gain = whole.enter_context(nc.sbuf_tensor("gain", [P, 4, KD], F32))

        def room(stack, name, shape, dt=F32, side=None):
            return stack.enter_context(nc.sbuf_tensor(name, shape, dt, side=side))
        g.room = room

        def halves(stack, name, side=None):
            g.hh = room(stack, f"{name}_high", [P, KD, T], F32R, side)
            g.hl = room(stack, f"{name}_low", [P, KD, T], F32R, side)

        g.halves = halves

        with ExitStack() as even:
            with ExitStack() as att:
                with ExitStack() as normed:
                    halves(normed, "even", "right")
                    with ExitStack() as st:
                        g.xt = room(st, "xt0", [P, KD, T])
                        stage_load(g)
                        stage_norm(g, 0, "n0", spill=True)
                    g.score = room(att, "score", [P, 6, SEQ])
                    g.score_s = room(att, "score_s", [NS, KEYS])
                    stage_index(g)
                    stage_project_even(g)
                g.ht = room(even, "ht_even", [P, KD, T], F32, "right")
                stage_retention(g)
                with ExitStack() as kv:
                    g.qt = room(kv, "qt", [P, H, T])
                    g.kt = room(kv, "kt", [P, H, T])
                    g.va = room(kv, "va", [P, TILES, 512])
                    g.hank = room(kv, "hank", [P, H, 256])
                    stage_attention_prep(g)
                    g.pages = room(kv, "pages", [P, HELD, NPAGE, 512])
                    g.ids = room(kv, "page_rows", [P, NB * NPAGE], I32)
                    stage_attention_prompt(g)
                    stage_attention_sample(g)
            free_semaphores(g)
            g.xt = room(whole, "xt", [P, KD, T])
            halves(even, "ffn0")
            stage_project_out(g, ins["w_out_even"][0], "oe", reload=True)
            stage_ffn(g, 0)
        free_semaphores(g)
        with ExitStack() as odd:
            stage_odd(g, odd)
            free_semaphores(g)
            halves(odd, "ffn1")
            stage_project_out(g, ins["w_out_odd"][0], "oo", reload=False)
            stage_ffn(g, 1)
        stage_store(g)
        free_semaphores(g)


def free_semaphores(g):
    g.nc.clear_and_free_semaphores(g.sems)
    g.sems.clear()
    g.nc.all_engine_barrier()


def stage_load(g):
    nc = g.nc
    consts_in, gains_in = g.sem("consts_in"), g.sem("gains_in")
    rows_in, rows_turned, rows_placed = g.slot_sems("rows_in", 3), g.sem("rows_turned"), g.sem("rows_placed")
    with ExitStack() as st:
        ring = g.room(st, "x_rows", [P, 3, D])
        block = st.enter_context(nc.Block())

        @block.sync
        def _(sp):
            sp.dma_start(g.cst[:, :], g.const_dram[:, 0:g.kept]).then_inc(consts_in, 16)
            for t in range(TILES):
                if t >= 3:
                    sp.wait_ge(rows_turned, 2 * (t - 2))
                src = g.ins["x_prompt"][0, t * P:(t + 1) * P, :] if t < SMP else \
                    g.ins["x_sample"].rearrange("b t d -> (b t) d")
                sp.dma_start(ring[0:rows(t), t % 3, :], src).then_inc(rows_in[t % 3], 16)

        @block.gpsimd
        def _(pool):
            for n, (w, l) in enumerate((("norm_mix", 0), ("norm_mix", 1), ("norm_ffn", 0), ("norm_ffn", 1))):
                with nc.allow_non_contiguous_dma("a vector of 1024 across the partitions"):
                    pool.dma_start(g.gain[:, n, :], g.ins[w][l].rearrange("(k p) -> p k", p=P)).then_inc(gains_in, 16)
            pool.wait_ge(gains_in, 64)

        @block.tensor
        def _(pe):
            pe.wait_ge(consts_in, 16)
            for t in range(TILES):
                pe.wait_ge(rows_in[t % 3], 16 * (t // 3 + 1))
                for half in range(2):
                    n = 2 * t + half
                    if n >= 4:
                        pe.wait_ge(rows_placed, n - 3)
                    for k in range(4):
                        last = pe.transpose(g.ps[:, n % 4, k * P:k * P + rows(t)],
                                            ring[0:rows(t), t % 3, (4 * half + k) * P:(4 * half + k + 1) * P],
                                            g.c("ident")[0:rows(t), 0:rows(t)])
                    last.then_inc(rows_turned, 1)

        @block.vector
        def _(dve):
            for n in range(2 * TILES):
                t, half = n // 2, n % 2
                dve.wait_ge(rows_turned, n + 1)
                dve.tensor_copy(g.xt[:, 4 * half:4 * half + 4, t * P:t * P + rows(t)],
                                g.ps[:, n % 4, :].rearrange("p (k i) -> p k i", k=4)[:, :, 0:rows(t)]
                                ).then_inc(rows_placed, 1)


def stage_norm(g, which, tag, spill=False):
    with ExitStack() as st:
        spilled = g.sem(f"{tag}_spilled")
        sq = g.room(st, f"{tag}_sq", [P, 2, T])
        total = g.room(st, f"{tag}_total", [P, T])
        n_scalar, n_tensor, n_vector, _ = split_norm(g, which, tag, sq, total[:, :])
        block = st.enter_context(g.nc.Block())

        @block.sync
        def _(sp):
            if spill:
                for k in range(KD):
                    sp.dma_start(g.xt_spill[:, k, :], g.xt[:, k, :]).then_inc(spilled, 16)
                sp.wait_ge(spilled, 16 * KD)

        @block.scalar
        def _(act):
            n_scalar(act)

        @block.tensor
        def _(pe):
            n_tensor(pe)

        @block.vector
        def _(dve):
            n_vector(dve)


def stage_index(g):
    nc = g.nc
    w_in, w_rounded, w_split = g.slot_sems("ix_weights", 2), g.sem("ix_rounded"), g.sem("ix_split")
    second_split, padded = g.sem("ix_second_split"), g.sem("ix_padded")
    w_pages, keys_doubled, lowered = g.sem("ix_pages"), g.sem("ix_doubled"), g.sem("ix_lowered")
    table_in, placed_rows = g.sem("ix_table"), g.sem("ix_row_ids")
    projected, copied = g.sem("ix_projected"), g.sem("ix_copied")
    stored = g.sem("ix_stored")
    scored, rectified, weighted = g.sem("ix_scored"), g.sem("ix_rectified"), g.sem("ix_weighted")
    pages_turned, pages_placed = g.sem("ix_turned"), g.sem("ix_placed")
    chain = g.sem("ix_chain")
    s_spread, s_ready, s_scored, s_rect, s_summed = (g.sem(f"ix_s_{n}") for n in
                                                     ("spread", "ready", "scored", "rect", "summed"))
    w_idx = g.ins["w_in_even"][0][:, IDX_COL:IDX_COL + IH * ID + ID + IH].rearrange("(k p) n -> p k n", p=P)
    WI = IH * ID + ID + IH
    LP = 5
    with ExitStack() as st:
        past = g.room(st, "ix_past", [P, NB, PAST])
        early = past[:, :, :].rearrange("p b n -> p (b n)")
        w = early[:, 0:2 * KD * P].rearrange("p (s n) -> p s n", s=2)
        wh = g.room(st, "ix_wh", [P, 2, KD * P], F32R)
        wl = g.room(st, "ix_wl", [P, 2, KD * P], F32R)
        odd_h, odd_l = (x[:, :, :].rearrange("p s n -> p (s n)")[:, 0:T] for x in (wh, wl))
        second = early[ID:2 * ID, 0:T]
        kwt = early[:, 2 * KD * P:2 * KD * P + T]
        qh = g.room(st, "ix_qh", [P, LP, T], F32R)
        ql = g.room(st, "ix_ql", [P, LP, T], F32R)
        new_keys = g.room(st, "ix_new_keys", [P, NS])
        kw = g.room(st, "ix_kw", [P, TILES, ID + IH])
        relu = g.room(st, "ix_relu", [P, 3, SEQ])
        pages = g.room(st, "ix_pg", [P, NB * NPAGE, 2, ID])
        qz = g.room(st, "ix_qz", [P, NB, 2, NT, NT])
        table = g.room(st, "ix_tab", [P, NB * NPAGE], I32)
        ids = g.room(st, "ix_ids", [P, NB * NPAGE], I32)
        relu_s = relu[:, 0:2, 0:KEYS]
        wcol = g.room(st, "ix_wcol", [P, 2, IH + 1])
        wsum = g.room(st, "ix_wsum", [P, 2, NS])
        block = st.enter_context(nc.Block())
        key_rows = g.ins["cache_kidx"][0].rearrange("n p d -> (n p) d")
        units = [(t, h) for t in range(2, SMP) for h in range(IH)]

        def width(m):
            return P if m < 4 else ID + IH

        @block.sync
        def _(sp):
            with nc.allow_non_contiguous_dma("short rows"):
                sp.dma_start(table[:, :], g.ins["page_table"].rearrange("b n -> (b n)").partition_broadcast(P)
                             ).then_inc(table_in, 16)
            for m in range(LP):
                if m >= 2:
                    sp.wait_ge(w_split, m - 1)
                sp.dma_start(w[:, m % 2, 0:KD * width(m)].rearrange("p (k n) -> p k n", k=KD),
                             w_idx[:, :, m * P:m * P + width(m)]).then_inc(w_in[m % 2], 16)
            sp.wait_ge(w_split, LP)
            sp.wait_ge(copied, LP)
            sp.dma_start(second, kwt[0:ID, :]).then_inc(keys_doubled, 16)
            sp.wait_ge(copied, LP + TILES)
            sp.dma_start(g.outs["kidx_prompt"][0, 0].rearrange("(t p) d -> p t d", p=P), kw[:, 0:SMP, 0:ID]
                         ).then_inc(stored, 16)
            sp.dma_start(g.outs["kidx_sample"][0].rearrange("b t d -> (b t) d"), kw[0:NS, SMP, 0:ID]
                         ).then_inc(stored, 16)
            sp.wait_ge(stored, 32)

        @block.gpsimd
        def _(pool):
            pool.memset(qz[:, :, :, :, :], 0.0).then_inc(placed_rows, 1)
            pool.wait_ge(table_in, 16)
            pool.tensor_scalar(ids[:, :], table[:, :], float(PAGE), g.c("page_row"), ALU.mult, ALU.add
                               ).then_inc(placed_rows, 1)
            pool.wait_ge(placed_rows, 2)
            for n in range(NB * NPAGE):
                for c in range(2):
                    pool.indirect_dma_start(out=pages[:, n, c, :], out_offset=None, in_=key_rows,
                                            in_offset=bass.IndirectOffsetOnAxis(ap=ids[:, n:n + 1], axis=0)
                                            ).then_inc(w_pages, 16)

        @block.tensor
        def _(pe):
            for m in range(LP):
                b0 = 4 * (m % 2)
                pe.wait_ge(w_split, m + 1)
                if m >= 2:
                    pe.wait_ge(lowered, m - 1)
                for k in range(KD):
                    cols = slice(k * width(m), (k + 1) * width(m))
                    last = split_passes(g, pe, b0, wh[:, m % 2, cols], wl[:, m % 2, cols], g.hh[:, k, :],
                                        g.hl[:, k, :], k == 0, k == KD - 1, width(m))
                last.then_inc(projected, 1)
            pe.wait_ge(lowered, LP)
            for t in range(TILES):
                if t >= 2:
                    pe.wait_ge(copied, LP + t - 1)
                pe.transpose(g.ps[0:rows(t), 3 + 4 * (t % 2), 0:ID + IH], kwt[0:ID + IH, t * P:t * P + rows(t)],
                             g.c("ident")[0:ID + IH, 0:ID + IH]).then_inc(projected, 1)
            pe.wait_ge(copied, LP + TILES)
            pe.wait_ge(second_split, 2)
            pe.wait_ge(padded, 2)
            for n, (t, h) in enumerate(units):
                if n >= 4:
                    pe.wait_ge(rectified, n - 3)
                keys = (t + 1) * P
                kh, kl = (qh[:, 4, :], ql[:, 4, :]) if h % 2 == 0 else (odd_h, odd_l)
                for c in range(-(-keys // 512)):
                    hi = min(keys, (c + 1) * 512)
                    for x, (queries, known) in enumerate(((qh, kh), (qh, kl), (ql, kh))):
                        last = pe.matmul(g.ps[:, 2 * (n % 4) + c, 0:hi - c * 512],
                                         queries[:, h // 2, t * P:(t + 1) * P], known[:, c * 512:hi],
                                         start=(x == 0), stop=(x == 2))
                last.then_inc(scored, 1)
            pe.wait_ge(w_pages, 16 * 2 * NB * NPAGE)
            pe.wait_ge(rectified, len(units))
            for b in range(NB):
                if b >= 4:
                    pe.wait_ge(pages_placed, b - 3)
                for p in range(NPAGE):
                    last = pe.transpose(g.ps[:, b % 4, p * P:(p + 1) * P],
                                        pages[:, b * NPAGE + p, :, :].rearrange("p c d -> p (c d)"), g.c("ident"))
                last.then_inc(pages_turned, 1)
            for q in range(2):
                last = pe.matmul(g.ps[:, 4 + q, 0:IH], g.c(f"row_idx{q}")[0:NS, :], kw[0:NS, SMP, ID:ID + IH],
                                 start=True, stop=True)
            last.then_inc(s_spread, 1)
            pe.wait_ge(s_ready, 1)
            for b in range(NB):
                band = slice(32 * (b % 4), 32 * (b % 4) + 32)
                lhs = qz[:, b, :, :, :].rearrange("p a h t -> p (a h t)")
                pe.matmul(g.ps[band, b // 4, :], lhs, past[:, b, :], start=True, stop=True)
                last = pe.matmul(g.ps[band, 2 + b // 4, 0:NS], lhs, new_keys[:, :], start=True, stop=True)
            last.then_inc(s_scored, 1)
            pe.wait_ge(s_rect, 2)
            for q in range(2):
                pe.matmul(g.ps[0:NS, 6, :], wsum[:, q, :], relu_s[:, q, 0:PAST], start=(q == 0), stop=(q == 1))
            for q in range(2):
                last = pe.matmul(g.ps[0:NS, 7, 0:NS], wsum[:, q, :], relu_s[:, q, PAST:KEYS],
                                 start=(q == 0), stop=(q == 1))
            last.then_inc(s_summed, 1)

        @block.scalar
        def _(act):
            def high(m):
                act.wait_ge(w_in[m % 2], 16 * (m // 2 + 1))
                if m >= 2:
                    act.wait_ge(projected, m - 1)
                act.copy(wh[:, m % 2, 0:KD * width(m)], w[:, m % 2, 0:KD * width(m)]).then_inc(w_rounded, 1)

            high(0)
            high(1)
            for m in range(LP):
                act.wait_ge(projected, m + 1)
                b0 = 4 * (m % 2)
                if m < 4:
                    act.activation(qh[:, m, :].rearrange("p (c n) -> p c n", c=3), g.ps[:, b0:b0 + 3, 0:THIRD],
                                   ACT.Copy, scale=ID ** -0.5).then_inc(copied, 1)
                else:
                    act.copy(qh[0:ID, 4, :].rearrange("p (c n) -> p c n", c=3), g.ps[0:ID, b0:b0 + 3, 0:THIRD])
                    act.copy(kwt[0:ID + IH, :].rearrange("p (c n) -> p c n", c=3),
                             g.ps[0:ID + IH, b0:b0 + 3, 0:THIRD]).then_inc(copied, 1)
                if m + 2 < LP:
                    high(m + 2)
            act.wait_ge(keys_doubled, 16)
            act.copy(odd_h[ID:2 * ID, :], second).then_inc(second_split, 1)
            for t in range(TILES):
                act.wait_ge(projected, LP + t + 1)
                act.copy(kw[0:rows(t), t, :], g.ps[0:rows(t), 3 + 4 * (t % 2), 0:ID + IH]).then_inc(copied, 1)
            for n, (t, h) in enumerate(units):
                act.wait_ge(scored, n + 1)
                if n >= 3:
                    act.wait_ge(weighted, n - 2)
                keys = (t + 1) * P
                two = g.ps[:, 2 * (n % 4):2 * (n % 4) + 2, :].rearrange("p c n -> p (c n)")
                act.activation(relu[:, n % 3, 0:keys], two[:, 0:keys], ACT.Relu).then_inc(rectified, 1)
            act.wait_ge(weighted, len(units))
            for q in range(2):
                act.wait_ge(s_scored, 1)
                act.activation(relu_s[:, q, 0:PAST], g.ps[:, q, :], ACT.Relu)
                act.activation(relu_s[:, q, PAST:KEYS], g.ps[:, 2 + q, 0:NS], ACT.Relu).then_inc(s_rect, 1)

        @block.vector
        def _(dve):
            done = [0]

            def link(op):
                done[0] += 1
                op.then_inc(chain, 1)
                dve.wait_ge(chain, done[0])

            def lower(m):
                r = slice(0, P if m < 4 else ID)
                dve.wait_ge(copied, m + 1)
                dve.scalar_tensor_tensor(out=ql[r, m, :].rearrange("p (c n) -> p c n", c=3),
                                         in0=g.ps[r, 4 * (m % 2):4 * (m % 2) + 3, 0:THIRD],
                                         scalar=ID ** -0.5 if m < 4 else 1.0,
                                         in1=qh[r, m, :].bitcast(F32).rearrange("p (c n) -> p c n", c=3),
                                         op0=ALU.mult, op1=ALU.subtract).then_inc(lowered, 1)

            dve.memset(qh[ID:2 * ID, 4, :].bitcast(F32), 0.0)
            dve.memset(ql[ID:2 * ID, 4, :].bitcast(F32), 0.0).then_inc(padded, 1)
            for m in range(LP):
                dve.wait_ge(w_rounded, m + 1)
                part = slice(0, KD * width(m))
                dve.tensor_tensor(wl[:, m % 2, part], w[:, m % 2, part], wh[:, m % 2, part].bitcast(F32), ALU.subtract
                                  ).then_inc(w_split, 1)
                if m >= 1:
                    lower(m - 1)
            lower(LP - 1)
            dve.memset(odd_h[0:ID, :].bitcast(F32), 0.0)
            dve.memset(odd_l[0:ID, :].bitcast(F32), 0.0).then_inc(padded, 1)
            dve.wait_ge(keys_doubled, 16)
            dve.wait_ge(second_split, 1)
            dve.tensor_tensor(odd_l[ID:2 * ID, :], second, odd_h[ID:2 * ID, :].bitcast(F32), ALU.subtract
                              ).then_inc(second_split, 1)
            dve.wait_ge(copied, LP + TILES)
            link(dve.tensor_scalar(kw[:, 0:SMP, ID:], kw[:, 0:SMP, ID:], IH ** -0.5, None, ALU.mult))
            for n, (t, h) in enumerate(units):
                keys = (t + 1) * P
                out = g.score[:, t - 2, 0:keys]
                wi = kw[:, t, ID + h:ID + h + 1]
                dve.wait_ge(rectified, n + 1)
                if h == 0:
                    dve.tensor_scalar(out, relu[:, n % 3, 0:keys], wi, None, ALU.mult).then_inc(weighted, 1)
                else:
                    dve.wait_ge(weighted, n)
                    dve.scalar_tensor_tensor(out=out, in0=relu[:, n % 3, 0:keys], scalar=wi, in1=out,
                                             op0=ALU.mult, op1=ALU.add).then_inc(weighted, 1)
                if h == IH - 1:
                    dve.wait_ge(weighted, n + 1)
                    link(dve.tensor_tensor(g.score[:, t - 2, keys - P:keys], g.score[:, t - 2, keys - P:keys],
                                           g.c("causal"), ALU.add))
            for b in range(NB):
                dve.wait_ge(pages_turned, b + 1)
                dve.tensor_copy(past[:, b, :], g.ps[:, b % 4, :]).then_inc(pages_placed, 1)
            dve.wait_ge(placed_rows, 1)
            for par in range(2):
                half = slice(64 * par, 64 * par + 64)
                for hh in range(4):
                    link(dve.tensor_tensor(qz[half, :, par, hh, :],
                                           qh[half, hh, SEQ:T].bitcast(F32).rearrange("p (b t) -> p b t", b=NB),
                                           ql[half, hh, SEQ:T].bitcast(F32).rearrange("p (b t) -> p b t", b=NB),
                                           ALU.add))
            dve.wait_ge(second_split, 2)
            for high, low in ((qh[:, 4, :], ql[:, 4, :]), (odd_h, odd_l)):
                part = slice(0, ID) if high is not odd_h else slice(ID, 2 * ID)
                link(dve.tensor_tensor(new_keys[part, :], high[part, SEQ:T].bitcast(F32), low[part, SEQ:T].bitcast(F32),
                                       ALU.add))
            dve.wait_ge(s_spread, 1)
            for q in range(2):
                link(dve.tensor_tensor(wcol[:, q, 0:IH], g.ps[:, 4 + q, 0:IH], g.c("head_idx"), ALU.mult))
                link(dve.tensor_reduce(wcol[:, q, IH:IH + 1], wcol[:, q, 0:IH], AX.X, ALU.add))
                link(dve.tensor_scalar(wsum[:, q, :], g.c(f"sum_idx{q}"), wcol[:, q, IH:IH + 1], IH ** -0.5,
                                       ALU.mult, ALU.mult))
            dve.wait_ge(pages_placed, NB)
            dve.wait_ge(copied, LP + TILES)
            dve.tensor_copy(wcol[:, 0, 0:1], wcol[:, 0, 1:2]).then_inc(s_ready, 1)
            dve.wait_ge(s_summed, 1)
            dve.tensor_copy(g.score_s[:, 0:PAST], g.ps[0:NS, 6, :])
            dve.tensor_tensor(g.score_s[:, PAST:KEYS], g.ps[0:NS, 7, 0:NS], g.c("new_ok")[0:NS, :], ALU.add)


def stage_project_even(g):
    nc = g.nc
    projected, copied = g.sem("pe_projected"), g.sem("pe_copied")
    w_in, w_rounded, w_split = g.sem("pe_weights"), g.sem("pe_rounded"), g.sem("pe_split")
    stored = g.slot_sems("pe_stored", 4)
    found, replaced = g.sem("pe_found"), g.sem("pe_replaced")
    with ExitStack() as st:
        w = g.room(st, "pe_w", [P, KD, 512])
        wh = g.room(st, "pe_wh", [P, 2, KD, 512], F32R)
        wl = g.room(st, "pe_wl", [P, 2, KD, 512], F32R)
        out = g.room(st, "pe_out", [P, 4, 512])
        best = g.room(st, "pe_best", [P, 8])
        block = st.enter_context(nc.Block())

        @block.sync
        def _(sp):
            def load(m):
                sp.dma_start(w[:, :, :], g.ins["w_in_even"][0][:, m * 512:(m + 1) * 512]
                             .rearrange("(k p) n -> p k n", p=P)).then_inc(w_in, 16)

            load(0)
            for n in range(EVEN_TM * TILES):
                m, t = n // TILES, n % TILES
                if t == 0 and m + 1 < EVEN_TM:
                    sp.wait_ge(w_split, KD * (m + 1))
                    load(m + 1)
                sp.wait_ge(copied, n + 1)
                sp.dma_start(g.proj[m, t * P:t * P + rows(t), :], out[0:rows(t), n % 4, :]).then_inc(stored[n % 4], 16)
            for slot in range(4):
                sp.wait_ge(stored[slot], 16 * len(range(slot, EVEN_TM * TILES, 4)))

        @block.tensor
        def _(pe):
            for m in range(EVEN_TM):
                for t in range(TILES):
                    n = m * TILES + t
                    if n >= 8:
                        pe.wait_ge(copied, n - 7)
                    for k in range(KD):
                        if t == 0:
                            pe.wait_ge(w_split, KD * m + k + 1)
                        high, low = (h[:, k, t * P:t * P + rows(t)] for h in (g.hh, g.hl))
                        to = g.ps[0:rows(t), n % 8, :]
                        pe.matmul(to, high, wh[:, m % 2, k, :], start=(k == 0), stop=False)
                        pe.matmul(to, high, wl[:, m % 2, k, :], start=False, stop=False)
                        last = pe.matmul(to, low, wh[:, m % 2, k, :], start=False, stop=(k == KD - 1))
                    last.then_inc(projected, 1)

        @block.scalar
        def _(act):
            def high(m, k):
                if k == 0:
                    act.wait_ge(w_in, 16 * (m + 1))
                    if m >= 2:
                        act.wait_ge(projected, TILES * (m - 1))
                act.copy(wh[:, m % 2, k, :], w[:, k, :]).then_inc(w_rounded, 1)

            for k in range(KD):
                high(0, k)
            for n in range(EVEN_TM * TILES):
                m, t = n // TILES, n % TILES
                act.wait_ge(projected, n + 1)
                if n >= 4:
                    act.wait_ge(stored[n % 4], 16 * (n // 4))
                act.copy(out[0:rows(t), n % 4, :], g.ps[0:rows(t), n % 8, :]).then_inc(copied, 1)
                if t < KD and m + 1 < EVEN_TM:
                    high(m + 1, t)

        @block.gpsimd
        def _(pool):
            for n in range(EVEN_TM * KD):
                m, k = n // KD, n % KD
                pool.wait_ge(w_rounded, n + 1)
                pool.tensor_tensor(wl[:, m % 2, k, :], w[:, k, :], wh[:, m % 2, k, :].bitcast(F32), ALU.subtract
                                   ).then_inc(w_split, 1)

        @block.vector
        def _(dve):
            done = [0, 0]
            for t in range(2, TILES):
                area = g.score[:, t - 2, 0:(t + 1) * P] if t < SMP else g.score_s[:, :]
                top = best[0:rows(t), :]
                want = TOPK if t < SMP else TOPK_S
                for r in range(-(-want // 8)):
                    dve.max(top, area).then_inc(found, 1)
                    done[0] += 1
                    dve.wait_ge(found, done[0])
                    if want - 8 * r < 8:
                        dve.memset(best[0:rows(t), want - 8 * r:8], 3e38).then_inc(found, 1)
                        done[0] += 1
                        dve.wait_ge(found, done[0])
                    dve.match_replace(area, top, area, TAKEN).then_inc(replaced, 1)
                    done[1] += 1
                    dve.wait_ge(replaced, done[1])
                dve.tensor_scalar(area, area, TAKEN, NEG, ALU.not_equal, ALU.mult)


def stage_retention(g):
    nc = g.nc
    heads_in, state_in, v_in, g_in = (g.sem(f"rt_{n}") for n in ("qk_in", "state_in", "v_in", "gate_in"))
    zeroed, turned_in = g.sem("rt_zeroed"), g.sem("rt_rotated")
    turned, copied, scored, masked, made, state = (g.sem(f"rt_{n}") for n in
                                                   ("turned", "copied", "scored", "masked", "made", "state"))
    s_turned, s_copied, s_laid, s_scored, s_masked, s_made, s_out, s_kv, s_kv_read = (
        g.sem(f"rt_s_{n}") for n in ("turned", "copied", "laid", "scored", "masked", "made", "out", "kv", "kv_read"))
    gated, mixed, placed, state_out, chain = (g.sem(f"rt_{n}") for n in
                                              ("gated", "mixed", "placed", "state_out", "chain"))
    rms_ready, root_ready = g.sem("rt_rms"), g.sem("rt_root")
    with ExitStack() as st:
        q = g.room(st, "rt_q", [P, TILES, 512])
        k = g.room(st, "rt_k", [P, TILES, 512])
        v = g.room(st, "rt_v", [P, TILES, 512])
        tmp = g.room(st, "rt_tmp", [P, 4, 3 * H * 64])
        qr = g.room(st, "rt_qr", [P, 2, 512])
        kr = g.room(st, "rt_kr", [P, 2, 512])
        sr = g.room(st, "rt_sr", [P, 2, 512])
        R = g.room(st, "rt_state", [P, H, P])
        S0 = g.room(st, "rt_s0", [P, NB, H, P])
        qs = g.room(st, "rt_qs", [P, 2, H, NS])
        qz = g.room(st, "rt_qz", [P, H, NB, NS])
        ss = g.room(st, "rt_ss", [NS, H, NS])
        kb = g.room(st, "rt_kb", [NS, 2, 512])
        ms = g.room(st, "rt_ms", [P, TILES * H])
        tables = g.room(st, "rt_tables", [P, g.const_dram.shape[1] - g.kept])
        tables_in = g.sem("rt_tables_in")
        block = st.enter_context(nc.Block())
        ident = g.c("ident")

        def table(name):
            at, width = g.place[name]
            return tables[:, at - g.kept:at - g.kept + width]

        def src(m):
            return g.proj[m, 0:SEQ, :].rearrange("(c p) n -> p c n", p=P)

        @block.sync
        def _(sp):
            sp.dma_start(tables[:, :], g.const_dram[:, g.kept:]).then_inc(tables_in, 16)
            sp.wait_ge(zeroed, 3)
            for buf, m, s in ((q, 0, heads_in), (k, 1, heads_in), (v, 2, v_in)):
                sp.dma_start(buf[:, 0:SMP, :], src(m)).then_inc(s, 16)
                sp.dma_start(buf[0:NS, SMP, :], g.proj[m, SEQ:T, :]).then_inc(s, 16)
            sp.dma_start(S0[:, :, :, :], g.ins["state_ret"][0].rearrange("b h d e -> d b h e")).then_inc(state_in, 16)
            sp.wait_ge(state, SMP)
            sp.dma_start(g.outs["ret_prompt"][0, 0].rearrange("h d e -> d h e"), R[:, :, :]).then_inc(state_out, 16)
            sp.wait_ge(s_kv_read, NB + 1)
            sp.dma_start(g.outs["ret_sample"][0].rearrange("b h d e -> d b h e"), S0[:, :, :, :]).then_inc(state_out, 16)
            sp.wait_ge(s_kv, NB)
            sp.wait_ge(made, SMP)
            sp.dma_start(k[:, 0:SMP, :], src(3)).then_inc(g_in, 16)
            sp.dma_start(k[0:NS, SMP, :], g.proj[3, SEQ:T, :]).then_inc(g_in, 16)
            sp.wait_ge(state_out, 32)

        @block.gpsimd
        def _(pool):
            for buf in (q, k, v):
                pool.memset(buf[:, SMP, :], 0.0).then_inc(zeroed, 1)

        @block.tensor
        def _(pe):
            def turn(c):
                if c >= 2:
                    pe.wait_ge(copied, 2 * (c - 1))
                for n, buf in enumerate((q, k)):
                    for h in range(H):
                        last = pe.transpose(g.ps[:, 2 * n + c % 2, h * P:(h + 1) * P],
                                            buf[:, c, h * P:(h + 1) * P], ident)
                last.then_inc(turned, 1)

            pe.wait_ge(turned_in, 1)
            pe.wait_ge(v_in, 32)
            turn(0)
            for c in range(SMP):
                if c + 1 < SMP:
                    turn(c + 1)
                pe.wait_ge(copied, 2 * (c + 1))
                if c >= 1:
                    pe.wait_ge(masked, c)
                for h in range(H):
                    cols = slice(h * P, (h + 1) * P)
                    last = pe.matmul(g.ps[:, 4, cols], kr[:, c % 2, cols], qr[:, c % 2, cols], start=True, stop=True)
                last.then_inc(scored, 1)
                pe.wait_ge(masked, c + 1)
                if c >= 1:
                    pe.wait_ge(state, c)
                for h in range(H):
                    cols = slice(h * P, (h + 1) * P)
                    pe.matmul(g.ps[:, 5, cols], sr[:, c % 2, cols], v[:, c, cols], start=True, stop=(c == 0))
                    if c >= 1:
                        pe.matmul(g.ps[:, 5, cols], qr[:, c % 2, cols], R[:, h, :], start=False, stop=True)
                for h in range(H):
                    cols = slice(h * P, (h + 1) * P)
                    last = pe.matmul(g.ps[:, 6, cols], k[:, c, cols], v[:, c, cols], start=True, stop=True)
                last.then_inc(made, 1)
            pe.wait_ge(copied, 2 * SMP)
            for n, buf in enumerate((q, k)):
                for h in range(H):
                    last = pe.transpose(g.ps[:, n, h * NS:(h + 1) * NS], buf[0:NS, SMP, h * P:(h + 1) * P],
                                        ident[0:NS, 0:NS])
            last.then_inc(s_turned, 1)
            pe.wait_ge(s_copied, 2)
            for h in range(H):
                last = pe.matmul(g.ps[0:NS, 2, h * NS:(h + 1) * NS], qs[:, 1, h, :], qs[:, 0, h, :],
                                 start=True, stop=True)
            last.then_inc(s_scored, 1)
            pe.wait_ge(s_masked, 1)
            pe.wait_ge(s_laid, 1)
            pe.wait_ge(state_in, 16)
            for h in range(H):
                cols = slice(h * P, (h + 1) * P)
                pe.matmul(g.ps[0:NS, 3, cols], ss[:, h, :], v[0:NS, SMP, cols], start=True, stop=False)
                for b in range(NB):
                    last = pe.matmul(g.ps[0:NS, 3, cols], qz[:, h, b, :], S0[:, b, h, :],
                                     start=False, stop=(b == NB - 1))
            last.then_inc(s_out, 1)
            pe.wait_ge(state, SMP)
            for b in range(NB):
                pe.wait_ge(s_made, b + 1)
                if b >= 2:
                    pe.wait_ge(s_kv_read, b - 1)
                for h in range(H):
                    cols = slice(h * P, (h + 1) * P)
                    last = pe.matmul(g.ps[:, 4 + b % 2, cols], kb[:, b % 2, cols], v[0:NS, SMP, cols],
                                     start=True, stop=True)
                last.then_inc(s_kv, 1)
            for t in range(TILES):
                pe.wait_ge(mixed, 1)
                if t == 0:
                    pe.wait_ge(s_kv_read, NB)
                if t >= 4:
                    pe.wait_ge(placed, t - 3)
                for h in range(H):
                    last = pe.transpose(g.ps[:, t % 4, h * P:h * P + rows(t)], q[0:rows(t), t, h * P:(h + 1) * P],
                                        ident[0:rows(t), 0:rows(t)])
                last.then_inc(gated, 1)

        @block.scalar
        def _(act):
            for c in range(SMP):
                act.wait_ge(turned, c + 1)
                if c >= 2:
                    act.wait_ge(made, c - 1)
                act.copy(qr[:, c % 2, :], g.ps[:, c % 2, :]).then_inc(copied, 1)
                act.copy(kr[:, c % 2, :], g.ps[:, 2 + c % 2, :]).then_inc(copied, 1)
            act.wait_ge(s_turned, 1)
            for n in range(2):
                act.copy(qs[:, n, :, :].rearrange("p h t -> p (h t)"), g.ps[:, n, 0:H * NS]).then_inc(s_copied, 1)
            act.wait_ge(rms_ready, 1)
            act.activation(ms[:, :], ms[:, :], ACT.Sqrt).then_inc(root_ready, 1)
            act.wait_ge(g_in, 32)
            act.activation(k[:, :, :], k[:, :, :], ACT.Silu).then_inc(root_ready, 1)
            for t in range(TILES):
                act.wait_ge(gated, t + 1)
                act.copy(g.ht[:, 0:H, t * P:t * P + rows(t)],
                         g.ps[:, t % 4, :].rearrange("p (h i) -> p h i", h=H)[:, :, 0:rows(t)]).then_inc(placed, 1)

        @block.vector
        def _(dve):
            done = [0]

            def link(op):
                done[0] += 1
                op.then_inc(chain, 1)
                dve.wait_ge(chain, done[0])

            dve.wait_ge(heads_in, 64)
            dve.wait_ge(tables_in, 16)
            dve.wait_ge(zeroed, 3)
            cos = table("cos").rearrange("p (t i) -> p t i", t=TILES)
            sin = table("sin").rearrange("p (t i) -> p t i", t=TILES)
            last = None
            for buf, decay in ((q, "ret_q"), (k, "ret_k")):
                scale = table(decay).rearrange("p (t h) -> p t h", h=H)
                for t0 in range(0, TILES, 3):
                    part = buf[:, t0:t0 + 3, :].rearrange("p t (h s i) -> p t h s i", h=H, s=2)
                    cs, sn = spread(cos[:, t0:t0 + 3, :], 1, H), spread(sin[:, t0:t0 + 3, :], 1, H)
                    tv = [tmp[:, n, :].rearrange("p (t h i) -> p t h i", t=3, h=H) for n in range(4)]
                    dve.tensor_tensor(tv[0], part[:, :, :, 0, :], cs, ALU.mult)
                    dve.tensor_tensor(tv[1], part[:, :, :, 1, :], sn, ALU.mult)
                    dve.tensor_tensor(tv[2], part[:, :, :, 0, :], sn, ALU.mult)
                    link(dve.tensor_tensor(tv[3], part[:, :, :, 1, :], cs, ALU.mult))
                    dve.tensor_tensor(part[:, :, :, 0, :], tv[0], tv[1], ALU.subtract)
                    link(dve.tensor_tensor(part[:, :, :, 1, :], tv[2], tv[3], ALU.add))
                    whole = buf[:, t0:t0 + 3, :].rearrange("p t (h d) -> p t h d", h=H)
                    last = dve.tensor_tensor(whole, whole, spread(scale[:, t0:t0 + 3, :], 2, P), ALU.mult)
                    if not (buf is k and t0 == 6):
                        link(last)
            last.then_inc(turned_in, 1)
            upper = spread(g.c("upper"), 0, H)
            for c in range(SMP):
                dve.wait_ge(scored, c + 1)
                dve.tensor_tensor(sr[:, c % 2, :].rearrange("p (h i) -> p h i", h=H),
                                  g.ps[:, 4, :].rearrange("p (h i) -> p h i", h=H), upper, ALU.mult
                                  ).then_inc(masked, 1)
                dve.wait_ge(made, c + 1)
                dve.tensor_copy(q[:, c, :], g.ps[:, 5, :])
                kv = g.ps[:, 6, :].rearrange("p (h e) -> p h e", h=H)
                step = spread(table("ret_step"), 1, P)
                if c == 0:
                    dve.tensor_tensor(R[:, :, :], kv, step, ALU.mult).then_inc(state, 1)
                else:
                    link(dve.tensor_tensor(R[:, :, :], kv, R[:, :, :], ALU.add))
                    dve.tensor_tensor(R[:, :, :], R[:, :, :], step, ALU.mult).then_inc(state, 1)
            dve.wait_ge(s_copied, 2)
            col = g.c("col_seq").rearrange("p (b t) -> p b t", b=NB)
            for h in range(H):
                last = dve.tensor_tensor(qz[:, h, :, :], spread(qs[:, 0, h, :], 0, NB), col, ALU.mult)
            last.then_inc(s_laid, 1)
            dve.wait_ge(s_scored, 1)
            dve.tensor_tensor(ss[:, :, :], g.ps[0:NS, 2, 0:H * NS].rearrange("p (h i) -> p h i", h=H),
                              spread(g.c("upper_s")[0:NS, :], 0, H), ALU.mult).then_inc(s_masked, 1)
            dve.wait_ge(s_out, 1)
            link(dve.tensor_copy(q[0:NS, SMP, :], g.ps[0:NS, 3, :]))
            for b in range(NB):
                if b >= 2:
                    dve.wait_ge(s_kv, b - 1)
                dve.tensor_scalar(kb[:, b % 2, :], k[0:NS, SMP, :], g.c("seq_of")[0:NS, b:b + 1], None, ALU.mult
                                  ).then_inc(s_made, 1)
                if b >= 1:
                    dve.wait_ge(s_kv, b)
                    dve.tensor_tensor(S0[:, b - 1, :, :].rearrange("p h e -> p (h e)"), g.ps[:, 4 + (b - 1) % 2, :],
                                      S0[:, b - 1, :, :].rearrange("p h e -> p (h e)"), ALU.add
                                      ).then_inc(s_kv_read, 1)
            dve.wait_ge(s_kv, NB)
            dve.tensor_tensor(S0[:, NB - 1, :, :].rearrange("p h e -> p (h e)"), g.ps[:, 4 + (NB - 1) % 2, :],
                              S0[:, NB - 1, :, :].rearrange("p h e -> p (h e)"), ALU.add).then_inc(s_kv_read, 1)
            dve.wait_ge(s_kv_read, NB)
            dve.tensor_tensor(S0[:, :, :, :], S0[:, :, :, :],
                              spread(spread(table("ret_step_s"), 0, NB), 2, P), ALU.mult).then_inc(s_kv_read, 1)
            dve.wait_ge(s_kv_read, NB + 1)
            qf = q[:, :, :].rearrange("p t (h e) -> p (t h) e", h=H)
            vf = v[:, :, :].rearrange("p t (h e) -> p (t h) e", h=H)
            link(dve.tensor_tensor(vf, qf, qf, ALU.mult))
            link(dve.tensor_reduce(ms[:, :], vf, AX.X, ALU.add))
            dve.tensor_scalar(ms[:, :], ms[:, :], 1.0 / P, EPS, ALU.mult, ALU.add).then_inc(rms_ready, 1)
            dve.wait_ge(root_ready, 1)
            link(dve.reciprocal(ms[:, :], ms[:, :]))
            link(dve.tensor_tensor(qf, qf, spread(ms[:, :], 1, P), ALU.mult))
            dve.wait_ge(root_ready, 2)
            dve.tensor_tensor(q[:, :, :], q[:, :, :], k[:, :, :], ALU.mult).then_inc(mixed, 1)


def stage_attention_prep(g):
    nc = g.nc
    zeroed, q_in, k_in, v_in, small_in = (g.sem(f"ap_{n}") for n in ("zeroed", "q_in", "k_in", "v_in", "small_in"))
    rms, root, chain = g.sem("ap_rms"), g.sem("ap_root"), g.sem("ap_chain")
    normed_q, normed_k, stored = g.sem("ap_normed_q"), g.sem("ap_normed_k"), g.sem("ap_stored")
    turned, placed = g.sem("ap_turned"), g.sem("ap_placed")
    bias_made, bias_read, bias_out, hank_in = (g.sem(f"ap_bias_{n}") for n in ("made", "read", "out", "in"))
    with ExitStack() as st:
        q = g.room(st, "ap_q", [P, TILES, 512])
        k = g.room(st, "ap_k", [P, TILES, 512])
        sq = g.room(st, "ap_sq", [P, TILES, 512])
        ms = g.room(st, "ap_ms", [P, 2, TILES * H])
        gains = g.room(st, "ap_gains", [P, 2, P])
        rb = g.room(st, "ap_rb", [32, H])
        row = g.room(st, "ap_row", [H, 384])
        block = st.enter_context(nc.Block())
        jobs = [(buf, t) for t in range(TILES) for buf in (0, 1)]

        @block.sync
        def _(sp):
            with nc.allow_non_contiguous_dma("small tables"):
                sp.dma_start(rb[:, :], g.ins["rel_bias"]).then_inc(small_in, 16)
                sp.dma_start(gains[:, 0, :], g.ins["q_norm"][0].partition_broadcast(P)).then_inc(small_in, 16)
                sp.dma_start(gains[:, 1, :], g.ins["k_norm"][0].partition_broadcast(P)).then_inc(small_in, 16)
            sp.wait_ge(zeroed, 3)
            for buf, m, s in ((k, 5, k_in), (q, 4, q_in), (g.va, 6, v_in)):
                sp.dma_start(buf[:, 0:SMP, :], g.proj[m, 0:SEQ, :].rearrange("(c p) n -> p c n", p=P)).then_inc(s, 16)
                sp.dma_start(buf[0:NS, SMP, :], g.proj[m, SEQ:T, :]).then_inc(s, 16)
            sp.wait_ge(bias_read, 1)
            sp.dma_start(g.bias_row, row[:, :]).then_inc(bias_out, 16)
            sp.wait_ge(bias_out, 16)
            sp.dma_start(g.hank[:, :, :], bass.AP(g.bias_row.tensor, 0, [[1, P], [384, H], [1, 256]])
                         ).then_inc(hank_in, 16)
            sp.wait_ge(v_in, 32)
            for buf, name, s in ((g.va, "v", None), (k, "k", normed_k)):
                if s is not None:
                    sp.wait_ge(s, 1)
                sp.dma_start(g.outs[f"{name}_prompt"][0, 0].rearrange("(c p) h d -> p c (h d)", p=P),
                             buf[:, 0:SMP, :]).then_inc(stored, 16)
                sp.dma_start(g.outs[f"{name}_sample"][0].rearrange("b t h d -> (b t) (h d)"),
                             buf[0:NS, SMP, :]).then_inc(stored, 16)
            sp.wait_ge(stored, 64)
            sp.wait_ge(hank_in, 16)

        @block.gpsimd
        def _(pool):
            for buf in (q, k, g.va):
                pool.memset(buf[:, SMP, :], 0.0).then_inc(zeroed, 1)

        @block.tensor
        def _(pe):
            pe.wait_ge(small_in, 48)
            pe.matmul(g.ps[0:H, 7, 0:384], rb[:, :], g.c("bias_p")[0:32, :], start=True, stop=True
                      ).then_inc(bias_made, 1)
            pe.wait_ge(normed_k, 1)
            pe.wait_ge(normed_q, 1)
            for n, (which, t) in enumerate(jobs):
                if n >= 4:
                    pe.wait_ge(placed, n - 3)
                for h in range(H):
                    last = pe.transpose(g.ps[:, n % 4, h * P:h * P + rows(t)],
                                        (q, k)[which][0:rows(t), t, h * P:(h + 1) * P],
                                        g.c("ident")[0:rows(t), 0:rows(t)])
                last.then_inc(turned, 1)

        @block.scalar
        def _(act):
            act.wait_ge(bias_made, 1)
            act.copy(row[:, :], g.ps[0:H, 7, 0:384]).then_inc(bias_read, 1)
            for n in range(2):
                act.wait_ge(rms, n + 1)
                act.activation(ms[:, n, :], ms[:, n, :], ACT.Sqrt).then_inc(root, 1)
            for n, (which, t) in enumerate(jobs):
                act.wait_ge(turned, n + 1)
                act.copy((g.qt, g.kt)[which][:, :, t * P:t * P + rows(t)],
                         g.ps[:, n % 4, :].rearrange("p (h i) -> p h i", h=H)[:, :, 0:rows(t)]).then_inc(placed, 1)

        @block.vector
        def _(dve):
            done = [0]

            def link(op):
                done[0] += 1
                op.then_inc(chain, 1)
                dve.wait_ge(chain, done[0])

            dve.wait_ge(zeroed, 3)
            dve.wait_ge(small_in, 48)
            link(dve.tensor_scalar(gains[:, 0, :], gains[:, 0, :], P ** -0.5, None, ALU.mult))
            sv = sq[:, :, :].rearrange("p t (h e) -> p (t h) e", h=H)
            for n, (buf, arrived, normed) in enumerate(((k, k_in, normed_k), (q, q_in, normed_q))):
                dve.wait_ge(arrived, 32)
                xv = buf[:, :, :].rearrange("p t (h e) -> p (t h) e", h=H)
                link(dve.tensor_tensor(sv, xv, xv, ALU.mult))
                link(dve.tensor_reduce(ms[:, n, :], sv, AX.X, ALU.add))
                dve.tensor_scalar(ms[:, n, :], ms[:, n, :], 1.0 / P, EPS, ALU.mult, ALU.add).then_inc(rms, 1)
                dve.wait_ge(root, n + 1)
                link(dve.reciprocal(ms[:, n, :], ms[:, n, :]))
                link(dve.tensor_tensor(xv, xv, spread(ms[:, n, :], 1, P), ALU.mult))
                dve.tensor_tensor(xv, xv, spread(gains[:, 1 - n, :], 0, TILES * H), ALU.mult).then_inc(normed, 1)


def page_slot(name, b):
    return (b if name == "cache_k" else NB + b) % HELD


def gather_pages(g, pool, name, b, arrived):
    slot = page_slot(name, b)
    for p in range(NPAGE):
        n = b * NPAGE + p
        pool.indirect_dma_start(out=g.pages[:, slot, p, :], out_offset=None,
                                in_=g.ins[name][0].rearrange("n p h d -> (n p) (h d)"),
                                in_offset=bass.IndirectOffsetOnAxis(ap=g.ids[:, n:n + 1], axis=0)
                                ).then_inc(arrived, 16)


def stage_attention_prompt(g):
    nc = g.nc
    logits, summed, negated, powered, total, scaled = (g.sem(f"at_{n}") for n in
                                                       ("logits", "masked", "negated", "powered", "total", "scaled"))
    turned, copied, made, placed = (g.sem(f"at_{n}") for n in ("turned", "copied", "made", "placed"))
    units = [(t, h) for t in range(SMP) for h in range(H)]
    with ExitStack() as st:
        lg = g.room(st, "at_logits", [P, 3, SEQ])
        pt = g.room(st, "at_probs_t", [P, 2, SMP, P])
        near = g.room(st, "at_near", [P, 2 * P])
        stat = g.room(st, "at_stat", [P, 3, 4])
        table = g.room(st, "at_tab", [P, NB * NPAGE], I32)
        block = st.enter_context(nc.Block())
        near_ready, table_in, ids_ready = g.sem("at_near"), g.sem("at_table"), g.sem("at_ids")
        g.k_in = g.slot_sems("at_k_in", NB)

        def banks(n):
            return sum(-(-(t + 1) // 4) for t, h in units[:n])

        @block.sync
        def _(sp):
            with nc.allow_non_contiguous_dma("a small table"):
                sp.dma_start(table[:, :], g.ins["page_table"].rearrange("b n -> (b n)").partition_broadcast(P)
                             ).then_inc(table_in, 16)

        @block.gpsimd
        def _(pool):
            pool.wait_ge(table_in, 16)
            pool.tensor_scalar(g.ids[:, :], table[:, :], float(PAGE), g.c("page_row"), ALU.mult, ALU.add
                               ).then_inc(ids_ready, 1)
            pool.wait_ge(ids_ready, 1)
            for b in range(HELD):
                gather_pages(g, pool, "cache_k", b, g.k_in[b])

        def spans(keys):
            return [(c, c * 512, min(keys, (c + 1) * 512)) for c in range(-(-keys // 512))]

        @block.tensor
        def _(pe):
            def logit(n):
                t, h = units[n]
                b0 = 2 * (n % 2)
                if n >= 2:
                    pe.wait_ge(summed, n - 1)
                for c, lo, hi in spans((t + 1) * P):
                    blocks = [(j, x) for j, x in ((t - 1, 0), (t, 1)) if lo <= j * P < hi and j >= 0]
                    for x, (j, which) in enumerate(blocks):
                        pe.matmul(g.ps[:, b0 + c, j * P - lo:(j + 1) * P - lo], g.c("flip"),
                                  g.hank[:, h, which * P:(which + 1) * P], start=(x == 0), stop=False,
                                  skip_group_check=True)
                    last = pe.matmul(g.ps[:, b0 + c, 0:hi - lo], g.qt[:, h, t * P:(t + 1) * P], g.kt[:, h, lo:hi],
                                     start=not blocks, stop=True, skip_group_check=True)
                last.then_inc(logits, 1)

            def turn(n, m):
                t, h = units[n]
                pe.wait_ge(scaled, n + 1)
                for j0 in range(0, t + 1, 4):
                    if m >= 2:
                        pe.wait_ge(copied, m - 1)
                    for j in range(j0, min(j0 + 4, t + 1)):
                        last = pe.transpose(g.ps[:, 4 + m % 2, (j - j0) * P:(j - j0 + 1) * P],
                                            lg[:, n % 3, j * P:(j + 1) * P], g.c("ident"))
                    last.then_inc(turned, 1)
                    m += 1

            def values(n):
                t, h = units[n]
                if n >= 2:
                    pe.wait_ge(placed, n - 1)
                pe.wait_ge(copied, banks(n + 1))
                for j in range(t + 1):
                    last = pe.matmul(g.ps[:, 6 + n % 2, 0:P], g.va[:, j, h * P:(h + 1) * P], pt[:, n % 2, j, :],
                                     start=(j == 0), stop=(j == t))
                last.then_inc(made, 1)

            logit(0)
            for n in range(len(units) + 2):
                if n + 1 < len(units):
                    logit(n + 1)
                if n >= 2:
                    values(n - 2)
                if 1 <= n <= len(units):
                    turn(n - 1, banks(n - 1))

        @block.scalar
        def _(act):
            def drain(n, m):
                t, h = units[n]
                if n >= 2:
                    act.wait_ge(made, n - 1)
                for j0 in range(0, t + 1, 4):
                    nb = min(4, t + 1 - j0)
                    act.wait_ge(turned, m + 1)
                    act.copy(pt[:, n % 2, j0:j0 + nb, :].rearrange("p j i -> p (j i)"), g.ps[:, 4 + m % 2, 0:nb * P]
                             ).then_inc(copied, 1)
                    m += 1

            for n in range(len(units) + 1):
                if n < len(units):
                    keys = (units[n][0] + 1) * P
                    act.wait_ge(negated, n + 1)
                    act.activation(lg[:, n % 3, 0:keys], lg[:, n % 3, 0:keys], ACT.Exp, bias=stat[:, n % 3, 1:2],
                                   accum_out=stat[:, n % 3, 2:3]).then_inc(powered, 1)
                if n >= 1:
                    drain(n - 1, banks(n - 1))

        @block.vector
        def _(dve):
            dve.memset(near[:, 0:P], 0.0).then_inc(near_ready, 1)
            dve.tensor_copy(near[:, P:2 * P], g.c("causal")).then_inc(near_ready, 1)
            dve.wait_ge(near_ready, 2)

            def mask(n):
                t, h = units[n]
                keys = (t + 1) * P
                chosen = near[:, P:] if t == 0 else near[:, :] if t == 1 else g.score[:, t - 2, 0:keys]
                two = g.ps[:, 2 * (n % 2):2 * (n % 2) + 2, :].rearrange("p c n -> p (c n)")[:, 0:keys]
                dve.wait_ge(logits, n + 1)
                if n >= 3:
                    dve.wait_ge(turned, banks(n - 2))
                dve.tensor_tensor_reduce(lg[:, n % 3, 0:keys], two, chosen, 1.0, -3e38, ALU.add, ALU.max,
                                         stat[:, n % 3, 0:1]).then_inc(summed, 1)
                dve.wait_ge(summed, n + 1)
                dve.tensor_scalar(stat[:, n % 3, 1:2], stat[:, n % 3, 0:1], -1.0, None, ALU.mult
                                  ).then_inc(negated, 1)

            def finish(n):
                keys = (units[n][0] + 1) * P
                dve.wait_ge(powered, n + 1)
                dve.reciprocal(stat[:, n % 3, 3:4], stat[:, n % 3, 2:3]).then_inc(total, 1)
                dve.wait_ge(total, n + 1)
                dve.tensor_scalar(lg[:, n % 3, 0:keys], lg[:, n % 3, 0:keys], stat[:, n % 3, 3:4], None, ALU.mult
                                  ).then_inc(scaled, 1)

            def place(n):
                t, h = units[n]
                dve.wait_ge(made, n + 1)
                dve.tensor_copy(g.ht[:, H + h, t * P:(t + 1) * P], g.ps[:, 6 + n % 2, 0:P]).then_inc(placed, 1)

            for n in range(len(units) + 2):
                if n < len(units):
                    mask(n)
                if 1 <= n <= len(units):
                    finish(n - 1)
                if n >= 2:
                    place(n - 2)


def stage_attention_sample(g):
    nc = g.nc
    cleared, rb_in = g.sem("as_cleared"), g.sem("as_rb_in")
    k_in, v_in = g.k_in, g.slot_sems("as_v_in", NB)
    laid, turned, placed, logits = (g.sem(f"as_{n}") for n in ("laid", "turned", "placed", "logits"))
    masked, negated, powered, scaled = (g.sem(f"as_{n}") for n in ("masked", "negated", "powered", "scaled"))
    p_turned, p_placed, made, chain = (g.sem(f"as_{n}") for n in ("p_turned", "p_placed", "made", "chain"))
    ptz_cleared, out_read, out_turned = g.sem("as_ptz_cleared"), g.sem("as_out_read"), g.sem("as_out_turned")
    with ExitStack() as st:
        kts = g.room(st, "as_kt", [P, 2, H, PAST])
        qz = g.room(st, "as_qz", [P, NB, H, 2, H, NT])
        rb = g.room(st, "as_rb", [P, H])
        rbt = g.room(st, "as_rbt", [P, NB, H, NT])
        lg = g.room(st, "as_logits", [P, KEYS])
        ptn = g.room(st, "as_ptn", [NS, P])
        ptz = kts[:, :, :, :].rearrange("p a h n -> p (a h n)").rearrange("p (b c r) -> p b c r", b=NB, c=NPAGE)
        ptz_own = bass.AP(ptz.tensor, ptz.offset, [list(ptz.ap[0]), [NPAGE * P + H * NT, NB], [P, NPAGE],
                                                   [1, H * NT]])
        ov = g.room(st, "as_out", [P, 512])
        stat = g.room(st, "as_stat", [P, 4])
        block = st.enter_context(nc.Block())

        @block.sync
        def _(sp):
            with nc.allow_non_contiguous_dma("small tables"):
                for t in range(NT):
                    sp.dma_start(rb[32 * t:32 * t + 32, :], g.ins["rel_bias"]).then_inc(rb_in, 16)

        @block.gpsimd
        def _(pool):
            pool.memset(qz[:, :, :, :, :, :], 0.0).then_inc(cleared, 1)
            for n in range(HELD, 2 * NB):
                before = n - HELD
                if before < NB:
                    pool.wait_ge(turned, H * (before + 1))
                else:
                    pool.wait_ge(made, before - NB + 1)
                if n < NB:
                    gather_pages(g, pool, "cache_k", n, k_in[n])
                else:
                    gather_pages(g, pool, "cache_v", n - NB, v_in[n - NB])

        @block.tensor
        def _(pe):
            pe.wait_ge(laid, 1)
            for (bank, lo, hi) in ((4, 0, PAST), (5, PAST, KEYS)):
                pe.matmul(g.ps[:, bank, 0:hi - lo], rbt[:, :, :, :].rearrange("p b h t -> p (b h t)"),
                          g.c("bias_s")[:, lo:hi], start=True, stop=False, skip_group_check=True)
                pe.matmul(g.ps[:, bank, 0:hi - lo], g.c("row_bht")[0:NS, :], g.score_s[:, lo:hi],
                          start=False, stop=False, skip_group_check=True)
            for b in range(NB):
                pe.wait_ge(k_in[b], 16 * NPAGE)
                for h in range(H):
                    n = b * H + h
                    if n >= 4:
                        pe.wait_ge(placed, n - 3)
                    for p in range(NPAGE):
                        last = pe.transpose(g.ps[:, n % 4, p * P:(p + 1) * P],
                                            g.pages[:, page_slot("cache_k", b), p, h * P:(h + 1) * P], g.c("ident"))
                    last.then_inc(turned, 1)
                band = slice(32 * (b // 2), 32 * (b // 2) + 32)
                pe.wait_ge(placed, H * (b + 1))
                for h in range(H):
                    lhs = qz[:, b, h, :, :, :].rearrange("p a h t -> p (a h t)")
                    pe.matmul(g.ps[band, 4, :], lhs, kts[:, b % 2, h, :], start=False, stop=(b == NB - 1 and h == 3),
                              skip_group_check=True)
                    last = pe.matmul(g.ps[band, 5, 0:NS], lhs, g.kt[:, h, SEQ:T], start=False,
                                     stop=(b == NB - 1 and h == 3), skip_group_check=True)
                last.then_inc(logits, 1)
            pe.wait_ge(scaled, 1)
            for c in range(NPAGE):
                pe.transpose(g.ps[:, 6, c * P:(c + 1) * P], lg[:, c * P:(c + 1) * P], g.c("ident"))
            pe.transpose(g.ps[0:NS, 7, 0:P], lg[:, PAST:KEYS], g.c("ident")).then_inc(p_turned, 1)
            pe.wait_ge(p_placed, 2)
            pe.matmul(g.ps[:, 0, :], ptn[:, :], g.va[0:NS, SMP, :], start=True, stop=False)
            for b in range(NB):
                pe.wait_ge(v_in[b], 16 * NPAGE)
                for p in range(NPAGE):
                    last = pe.matmul(g.ps[:, 0, :], ptz[:, b, p, :], g.pages[:, page_slot("cache_v", b), p, :],
                                     start=False, stop=(b == NB - 1 and p == NPAGE - 1))
                last.then_inc(made, 1)
            pe.wait_ge(out_read, 1)
            for h in range(H):
                last = pe.transpose(g.ps[:, 1, h * P:(h + 1) * P], ov[:, h * P:(h + 1) * P], g.c("ident"))
            last.then_inc(out_turned, 1)

        @block.scalar
        def _(act):
            for n in range(NB * H):
                b, h = n // H, n % H
                act.wait_ge(turned, n + 1)
                if b >= 2:
                    act.wait_ge(logits, b - 1)
                act.copy(kts[:, b % 2, h, :], g.ps[:, n % 4, :]).then_inc(placed, 1)
            act.wait_ge(negated, 1)
            act.activation(lg[:, :], lg[:, :], ACT.Exp, bias=stat[:, 1:2], accum_out=stat[:, 2:3]
                           ).then_inc(powered, 1)

        @block.vector
        def _(dve):
            done = [0]

            def link(op):
                done[0] += 1
                op.then_inc(chain, 1)
                dve.wait_ge(chain, done[0])

            dve.wait_ge(rb_in, 64)
            link(dve.tensor_tensor(rbt[:, :, :, :], spread(spread(rb[:, :], 0, NB), 2, NT),
                                   spread(spread(g.c("t_of"), 0, H), 0, NB), ALU.mult))
            dve.wait_ge(cleared, 1)
            for par in range(2):
                for h in range(H):
                    new = g.qt[:, h, SEQ:T].rearrange("p (b a t) -> p b a t", a=2, t=NT)[:, :, par, :]
                    last = dve.tensor_copy(
                        qz[:, :, h, par, h, :].rearrange("p (b a) t -> p b a t", a=2)[:, :, par, :], new)
            last.then_inc(laid, 1)
            dve.wait_ge(logits, NB)
            link(dve.tensor_copy(lg[:, 0:PAST], g.ps[:, 4, :]))
            link(dve.tensor_copy(lg[:, PAST:KEYS], g.ps[:, 5, 0:NS]))
            link(dve.tensor_reduce(stat[:, 0:1], lg[:, :], AX.X, ALU.max))
            dve.tensor_scalar(stat[:, 1:2], stat[:, 0:1], -1.0, None, ALU.mult).then_inc(negated, 1)
            dve.memset(ptz, 0.0).then_inc(ptz_cleared, 1)
            dve.wait_ge(powered, 1)
            link(dve.reciprocal(stat[:, 3:4], stat[:, 2:3]))
            dve.tensor_scalar(lg[:, :], lg[:, :], stat[:, 3:4], None, ALU.mult).then_inc(scaled, 1)
            dve.wait_ge(p_turned, 1)
            dve.wait_ge(ptz_cleared, 1)
            dve.tensor_copy(ptz_own, g.ps[:, 6, :].rearrange("p (c b r) -> p b c r", c=NPAGE, b=NB)).then_inc(p_placed, 1)
            dve.tensor_copy(ptn[:, :], g.ps[0:NS, 7, 0:P]).then_inc(p_placed, 1)
            dve.wait_ge(made, NB)
            dve.tensor_copy(ov[:, :], g.ps[:, 0, :]).then_inc(out_read, 1)
            dve.wait_ge(out_turned, 1)
            turned_out = g.ps[:, 1, :]
            dve.tensor_copy(g.ht[:, H:2 * H, SEQ:T].rearrange("p h (b t) -> p h b t", b=NB),
                            bass.AP(turned_out.tensor, turned_out.offset,
                                    [list(turned_out.ap[0]), [P + NT, H], [H * NT, NB], [1, NT]]))


def stage_project_out(g, weight, tag, reload):
    nc = g.nc
    x_in, made, added = (g.sem(f"{tag}_{n}") for n in ("stream", "made", "added"))
    w_in, w_rounded, w_split = g.slot_sems(f"{tag}_weights", 2), g.sem(f"{tag}_w_rounded"), g.sem(f"{tag}_w_split")
    rounded, split = g.sem(f"{tag}_rounded"), g.sem(f"{tag}_split")
    with ExitStack() as st:
        w = g.room(st, f"{tag}_w", [P, 2, KD * P])
        wh = g.room(st, f"{tag}_wh", [P, 2, KD * P], F32R)
        wl = g.room(st, f"{tag}_wl", [P, 2, KD * P], F32R)
        block = st.enter_context(nc.Block())

        @block.sync
        def _(sp):
            for m in range(KD):
                if m >= 2:
                    sp.wait_ge(w_split, m - 1)
                sp.dma_start(w[:, m % 2, :].rearrange("p (k n) -> p k n", k=KD),
                             weight[:, m * P:(m + 1) * P].rearrange("(k p) n -> p k n", p=P)
                             ).then_inc(w_in[m % 2], 16)

        @block.gpsimd
        def _(pool):
            if reload:
                for k in range(KD):
                    pool.dma_start(g.xt[:, k, :], g.xt_spill[:, k, :]).then_inc(x_in, 16)

        @block.tensor
        def _(pe):
            for m in range(KD):
                pe.wait_ge(w_split, m + 1)
                if m >= 2:
                    pe.wait_ge(added, m - 1)
                for k in range(KD):
                    if m == 0:
                        pe.wait_ge(split, k + 1)
                    cols = slice(k * P, (k + 1) * P)
                    last = split_passes(g, pe, 4 * (m % 2), wh[:, m % 2, cols], wl[:, m % 2, cols], g.hh[:, k, :],
                                        g.hl[:, k, :], k == 0, k == KD - 1)
                last.then_inc(made, 1)

        @block.scalar
        def _(act):
            def high(m):
                act.wait_ge(w_in[m % 2], 16 * (m // 2 + 1))
                if m >= 2:
                    act.wait_ge(made, m - 1)
                act.copy(wh[:, m % 2, :], w[:, m % 2, :]).then_inc(w_rounded, 1)

            act.copy(g.hh[:, 0, :], g.ht[:, 0, :]).then_inc(rounded, 1)
            high(0)
            for k in range(1, KD):
                act.copy(g.hh[:, k, :], g.ht[:, k, :]).then_inc(rounded, 1)
            for m in range(1, KD):
                high(m)

        @block.vector
        def _(dve):
            def low(m):
                dve.wait_ge(w_rounded, m + 1)
                dve.tensor_tensor(wl[:, m % 2, :], w[:, m % 2, :], wh[:, m % 2, :].bitcast(F32), ALU.subtract
                                  ).then_inc(w_split, 1)

            for k in range(KD):
                dve.wait_ge(rounded, k + 1)
                dve.tensor_tensor(g.hl[:, k, :], g.ht[:, k, :], g.hh[:, k, :].bitcast(F32), ALU.subtract
                                  ).then_inc(split, 1)
                if k == 0:
                    low(0)
            low(1)
            for m in range(KD):
                dve.wait_ge(made, m + 1)
                if reload and m == 0:
                    dve.wait_ge(x_in, 16 * KD)
                if m + 2 < KD:
                    low(m + 2)
                xv = g.xt[:, m, :].rearrange("p (c n) -> p c n", c=3)
                dve.tensor_tensor(xv, g.ps[:, 4 * (m % 2):4 * (m % 2) + 3, 0:THIRD], xv, ALU.add).then_inc(added, 1)


def split_norm(g, which, tag, sq, total):
    squared, added, summed, mean_ready, root_ready, inverted = (
        g.sem(f"{tag}_{n}") for n in ("squared", "added", "summed", "mean", "root", "inverse"))
    scaled, rounded, normed = g.sem(f"{tag}_scaled"), g.sem(f"{tag}_rounded"), g.sem(f"{tag}_normed")

    def scalar(act):
        for k in range(KD):
            if k >= 2:
                act.wait_ge(added, k - 1)
            act.activation(sq[:, k % 2, :], g.xt[:, k, :], ACT.Square).then_inc(squared, 1)
        act.wait_ge(mean_ready, 1)
        act.activation(total, total, ACT.Sqrt).then_inc(root_ready, 1)
        for k in range(KD):
            act.wait_ge(scaled, k + 1)
            act.copy(g.hh[:, k, :], sq[:, k % 2, :]).then_inc(rounded, 1)

    def tensor(pe):
        pe.wait_ge(added, KD)
        for c in range(3):
            last = pe.matmul(g.ps[:, c, 0:THIRD], g.c("ones"), total[:, c * THIRD:(c + 1) * THIRD],
                             start=True, stop=True)
        last.then_inc(summed, 1)

    def vector(dve):
        for k in range(KD):
            dve.wait_ge(squared, k + 1)
            if k == 0:
                dve.tensor_copy(total, sq[:, 0, :]).then_inc(added, 1)
            else:
                dve.wait_ge(added, k)
                dve.tensor_tensor(total, total, sq[:, k % 2, :], ALU.add).then_inc(added, 1)
        dve.wait_ge(summed, 1)
        dve.tensor_scalar(total.rearrange("p (c n) -> p c n", c=3), g.ps[:, 0:3, 0:THIRD], 1.0 / D, EPS,
                          ALU.mult, ALU.add).then_inc(mean_ready, 1)
        dve.wait_ge(root_ready, 1)
        dve.reciprocal(total, total).then_inc(inverted, 1)
        dve.wait_ge(inverted, 1)

        def low(k):
            dve.wait_ge(rounded, k + 1)
            dve.tensor_tensor(g.hl[:, k, :], sq[:, k % 2, :], g.hh[:, k, :].bitcast(F32), ALU.subtract
                              ).then_inc(normed, 1)

        for k in range(KD):
            if k >= 2:
                dve.wait_ge(normed, k - 1)
            dve.scalar_tensor_tensor(out=sq[:, k % 2, :], in0=g.xt[:, k, :], scalar=g.gain[:, which, k:k + 1],
                                     in1=total, op0=ALU.mult, op1=ALU.mult).then_inc(scaled, 1)
            if k >= 1:
                low(k - 1)
        low(KD - 1)

    return scalar, tensor, vector, normed


def split_passes(g, pe, b0, weight_high, weight_low, high, low, first, final, out_rows=P):
    for n, (lhs, rhs) in enumerate(((weight_high, high), (weight_high, low), (weight_low, high))):
        for c in range(3):
            last = pe.matmul(g.ps[0:out_rows, b0 + c, 0:THIRD], lhs, rhs[:, c * THIRD:(c + 1) * THIRD],
                             start=(first and n == 0), stop=(final and n == 2))
    return last


def stage_ffn(g, layer):
    nc = g.nc
    tag = f"f{layer}"
    CHUNKS = KF // 2
    KINDS = "GUD"
    raw_in = dict(zip(KINDS, g.slot_sems(f"{tag}_raw_in", 3)))
    rounded = dict(zip(KINDS, g.slot_sems(f"{tag}_rounded", 3)))
    split = dict(zip(KINDS, g.slot_sems(f"{tag}_split", 3)))
    made = dict(zip(KINDS, g.slot_sems(f"{tag}_made", 3)))
    silu, joined, hid_high, hid_low, added = (g.sem(f"{tag}_{n}") for n in
                                              ("silu", "joined", "hid_high", "hid_low", "added"))
    source = {"G": g.ins["w_gate"][layer], "U": g.ins["w_up"][layer], "D": g.ins["w_down"][layer]}

    with ExitStack() as st:
        n_scalar, n_tensor, n_vector, normed = split_norm(g, 2 + layer, f"{tag}n", g.ht[:, 5:7, :], g.ht[:, 7, :])
        raw = {k: g.ht[:, 2 + n, 0:1024] for n, k in enumerate(KINDS)}
        wh = {k: g.room(st, f"{tag}_wh{k}", [P, 1024], F32R) for k in KINDS}
        wl = {k: g.room(st, f"{tag}_wl{k}", [P, 1024], F32R) for k in KINDS}
        hidh = g.room(st, f"{tag}_hidh", [P, 2, 2, T], F32R)
        hidl = g.room(st, f"{tag}_hidl", [P, 2, 2, T], F32R)
        gate, prod = g.ht[:, 0, :], g.ht[:, 1, :]
        block = st.enter_context(nc.Block())

        def thirds(ap):
            return ap.rearrange("p (c n) -> p c n", c=3)

        def chunks(fori, chunk):
            for c in range(3):
                chunk(c, c % 2)
            with fori(0, (CHUNKS - 5) // 2) as i:
                for u in range(2):
                    chunk(2 * i + (3 + u), (3 + u) % 2)
            for c in range(CHUNKS - 2, CHUNKS):
                chunk(c, c % 2)

        def at(c, n):
            return isinstance(c, int) and c == n

        @block.sync
        def _(sp):
            def load(kind, x, first=False):
                if not first:
                    sp.wait_ge(split[kind], x)
                if kind == "D":
                    c, half = x
                    src = source["D"][bass.ds(c * 2 * P, 2 * P), half * 512:(half + 1) * 512]
                    sp.dma_start(raw["D"].rearrange("p (k n) -> p k n", k=2),
                                 src.rearrange("(k p) n -> p k n", p=P)).then_inc(raw_in["D"], 16)
                else:
                    sp.dma_start(raw[kind].rearrange("p (k n) -> p k n", k=KD),
                                 source[kind][:, bass.ds(x * P, P)].rearrange("(k p) n -> p k n", p=P)
                                 ).then_inc(raw_in[kind], 16)

            def load_down(c, half, first=False):
                if not first:
                    sp.wait_ge(split["D"], 2 * c + half)
                load("D", (c, half), True)

            def chunk(c, par):
                if at(c, 0):
                    load("G", 0, True)
                    load("U", 0, True)
                    load("D", (0, 0), True)
                else:
                    load_down(c - 1, 1)
                load("G", 2 * c + 1)
                load("U", 2 * c + 1)
                if not at(c, 0) and not at(c, CHUNKS - 1):
                    load_down(c, 0)
                elif at(c, CHUNKS - 1):
                    load_down(c, 0)
                    load_down(c, 1)
                if not at(c, CHUNKS - 1):
                    load("G", 2 * c + 2)
                    load("U", 2 * c + 2)

            chunks(sp.Fori, chunk)

        @block.tensor
        def _(pe):
            def hidden(kind, f, first=False):
                pe.wait_ge(split[kind], f + 1)
                for k in range(KD):
                    if first:
                        pe.wait_ge(normed, k + 1)
                    last = split_passes(g, pe, 0 if kind == "G" else 3, wh[kind][:, k * P:(k + 1) * P],
                                        wl[kind][:, k * P:(k + 1) * P], g.hh[:, k, :], g.hl[:, k, :],
                                        k == 0, k == KD - 1)
                last.then_inc(made[kind], 1)

            def down(c, par, half, tail=False):
                pe.wait_ge(split["D"], 2 * c - 1 + half)
                if half == 0:
                    pe.wait_ge(hid_low, 2 * c)
                for m in range(4):
                    if tail or m >= 2:
                        pe.wait_ge(added, 8 * c - 9 + 4 * half + m)
                    else:
                        pe.wait_ge((silu, joined)[m], 2 * c + half + 1)
                    for k in range(2):
                        cols = slice((4 * k + m) * P, (4 * k + m + 1) * P)
                        last = split_passes(g, pe, 3 * (m % 2), wh["D"][:, cols], wl["D"][:, cols],
                                            hidh[:, 1 - par, k, :], hidl[:, 1 - par, k, :], k == 0, k == 1)
                    last.then_inc(made["D"], 1)

            def chunk(c, par):
                for half in range(2):
                    for n, kind in enumerate("GU"):
                        if at(c, 0) or at(c, 1):
                            if 2 * c + half:
                                if c == 1 and half == 1:
                                    pe.wait_ge(added, 3 + n)
                                else:
                                    pe.wait_ge((silu, joined)[n], 2 * c + half)
                        else:
                            pe.wait_ge(added, 8 * c - 9 + 4 * half + n)
                        hidden(kind, 2 * c + half, first=at(c, 0) and half == 0 and n == 0)
                    if not at(c, 0):
                        down(c, par, half)

            n_tensor(pe)
            chunks(pe.Fori, chunk)
            for half in range(2):
                down(CHUNKS, CHUNKS % 2, half, tail=True)

        @block.scalar
        def _(act):
            def high(kind, x, first=False):
                act.wait_ge(raw_in[kind], 16 * x + 16)
                if not first:
                    act.wait_ge(made[kind], 4 * x if kind == "D" else x)
                act.copy(wh[kind][:, :], raw[kind]).then_inc(rounded[kind], 1)

            def activate(f, first=False):
                act.wait_ge(made["G"], f + 1)
                if not first:
                    act.wait_ge(joined, f)
                act.activation(thirds(gate), g.ps[:, 0:3, 0:THIRD], ACT.Silu).then_inc(silu, 1)

            def hid(par, half, f):
                act.wait_ge(joined, f + 1)
                act.copy(hidh[:, par, half, :], prod).then_inc(hid_high, 1)

            def chunk(c, par):
                final = at(c, CHUNKS - 1)
                if not at(c, 0):
                    high("D", 2 * c - 2, first=at(c, 1))
                activate(2 * c, first=at(c, 0))
                high("G", 2 * c + 1)
                high("U", 2 * c + 1)
                hid(par, 0, 2 * c)
                if not at(c, 0):
                    high("D", 2 * c - 1)
                activate(2 * c + 1)
                if not final:
                    high("G", 2 * c + 2)
                    high("U", 2 * c + 2)
                hid(par, 1, 2 * c + 1)

            high("G", 0, True)
            high("U", 0, True)
            n_scalar(act)
            chunks(act.Fori, chunk)
            for half in range(2):
                high("D", 2 * CHUNKS - 2 + half)

        @block.vector
        def _(dve):
            def low(kind, x):
                dve.wait_ge(rounded[kind], x + 1)
                dve.tensor_tensor(wl[kind][:, :], raw[kind], wh[kind][:, :].bitcast(F32), ALU.subtract
                                  ).then_inc(split[kind], 1)

            def join(f, first=False):
                dve.wait_ge(silu, f + 1)
                dve.wait_ge(made["U"], f + 1)
                if not first:
                    dve.wait_ge(hid_high, f)
                    dve.wait_ge(hid_low, f)
                dve.tensor_tensor(thirds(prod), g.ps[:, 3:6, 0:THIRD], thirds(gate), ALU.mult
                                  ).then_inc(joined, 1)

            def hid(par, half, f):
                dve.wait_ge(hid_high, f + 1)
                dve.tensor_tensor(hidl[:, par, half, :], prod, hidh[:, par, half, :].bitcast(F32), ALU.subtract
                                  ).then_inc(hid_low, 1)

            def add(c, half):
                for m in range(4):
                    dve.wait_ge(made["D"], 8 * c - 7 + 4 * half + m)
                    xv = thirds(g.xt[:, 4 * half + m, :])
                    dve.tensor_tensor(xv, g.ps[:, 3 * (m % 2):3 * (m % 2) + 3, 0:THIRD], xv, ALU.add
                                      ).then_inc(added, 1)

            def chunk(c, par):
                final = at(c, CHUNKS - 1)
                if not at(c, 0):
                    low("D", 2 * c - 2)
                low("G", 2 * c + 1)
                join(2 * c, first=at(c, 0))
                low("U", 2 * c + 1)
                hid(par, 0, 2 * c)
                if not at(c, 0):
                    add(c, 0)
                    low("D", 2 * c - 1)
                if not final:
                    low("G", 2 * c + 2)
                join(2 * c + 1)
                if not final:
                    low("U", 2 * c + 2)
                hid(par, 1, 2 * c + 1)
                if not at(c, 0):
                    add(c, 1)

            low("G", 0)
            low("U", 0)
            n_vector(dve)
            chunks(dve.Fori, chunk)
            for half in range(2):
                low("D", 2 * CHUNKS - 2 + half)
                add(CHUNKS, half)


def stage_store(g):
    nc = g.nc
    turned, copied, stored = g.sem("out_turned"), g.sem("out_copied"), g.slot_sems("out_stored", 4)
    with ExitStack() as st:
        ring = g.room(st, "out_rows", [P, 4, 512])
        block = st.enter_context(nc.Block())

        @block.tensor
        def _(pe):
            for n in range(2 * TILES):
                t, half = n // 2, n % 2
                if n >= 4:
                    pe.wait_ge(copied, n - 3)
                for k in range(4):
                    last = pe.transpose(g.ps[0:rows(t), n % 4, k * P:(k + 1) * P],
                                        g.xt[:, 4 * half + k, t * P:t * P + rows(t)], g.c("ident"))
                last.then_inc(turned, 1)

        @block.vector
        def _(dve):
            for n in range(2 * TILES):
                t = n // 2
                dve.wait_ge(turned, n + 1)
                if n >= 4:
                    dve.wait_ge(stored[n % 4], 16 * (n // 4))
                dve.tensor_copy(ring[0:rows(t), n % 4, :], g.ps[0:rows(t), n % 4, :]).then_inc(copied, 1)

        @block.sync
        def _(sp):
            for n in range(2 * TILES):
                t, half = n // 2, n % 2
                sp.wait_ge(copied, n + 1)
                dst = g.outs["y_prompt"][0, t * P:(t + 1) * P, half * 512:(half + 1) * 512] if t < SMP else \
                    g.outs["y_sample"].rearrange("b t d -> (b t) d")[:, half * 512:(half + 1) * 512]
                sp.dma_start(dst, ring[0:rows(t), n % 4, :]).then_inc(stored[n % 4], 16)
            for slot in range(4):
                sp.wait_ge(stored[slot], 16 * len(range(slot, 2 * TILES, 4)))


XW = CW - 1 + SEQ + NB * (CW - 1 + NT)
UW = PPAST + SEQ


def stage_odd(g, keep):
    with ExitStack() as st:
        g.z = g.room(st, "od_z", [P, TILES, 512], F32, "right")
        g.dt = g.room(st, "od_dt", [P, TILES, SH], F32, "right")
        g.xb = g.room(st, "od_xb", [P, CD // P, XW], F32, "right")
        with ExitStack() as pool_room:
            g.up = g.room(pool_room, "od_up", [P, 4, UW], F32, "right")
            g.us = g.room(pool_room, "od_us", [P, 4, PPAST + NT, NB], F32, "right")
            with ExitStack() as normed:
                g.halves(normed, "odd")
                stage_norm(g, 1, "n2")
                stage_odd_project(g)
            g.ht = g.room(keep, "ht_odd", [P, KD, T])
            stage_pool(g)
        stage_conv(g)
        g.xtm = g.room(st, "od_xtm", [P, TILES, 512])
        g.btm = g.room(st, "od_btm", [P, TILES, 2 * SN])
        stage_ssd(g)


def stage_odd_project(g):
    nc = g.nc
    made, copied = g.sem("op_made"), g.sem("op_copied")
    w_in, w_rounded, w_split = (g.sem(f"op_{n}") for n in ("weights", "rounded", "split"))
    hist_in, hist_turned, hist_placed, cleared = (g.sem(f"op_{n}") for n in
                                                  ("hist_in", "hist_turned", "hist_placed", "cleared"))
    turned, placed = g.sem("op_turned"), g.sem("op_placed")
    weight = g.ins["w_in_odd"][0]
    NF = 17
    ZF = 12
    UROWS, XROWS = NB * PPAST, NB * (CW - 1)

    def first_col(m):
        return m * P if m < 4 else ODD_XBC + (m - 4) * P if m < ZF else ODD_Z + (m - ZF) * P if m < NF - 1 else ODD_DT

    def width(m):
        return P if m < NF - 1 else SH

    with ExitStack() as st:
        w = g.room(st, "op_w", [P, KD * P])
        wh = g.room(st, "op_wh", [P, 2, KD * P], F32R)
        wl = g.room(st, "op_wl", [P, 2, KD * P], F32R)
        hu = g.room(st, "op_hu", [UROWS, PW])
        zt = g.room(st, "op_zt", [P, T])
        hx = zt[0:XROWS, 0:CD]
        block = st.enter_context(nc.Block())

        @block.sync
        def _(sp):
            for m in range(NF):
                if m >= 1:
                    sp.wait_ge(w_split, m)
                with nc.allow_non_contiguous_dma("the last block has eight columns"):
                    sp.dma_start(w[:, 0:KD * width(m)].rearrange("p (k n) -> p k n", k=KD),
                                 weight[:, first_col(m):first_col(m) + width(m)].rearrange("(k p) n -> p k n", p=P)
                                 ).then_inc(w_in, 16)
                if m == 1:
                    sp.dma_start(hu[:, :], g.ins["state_pool"][0].rearrange("b r c -> (b r) c")).then_inc(hist_in, 16)
                    sp.dma_start(hx, g.ins["state_conv"][0].rearrange("b r c -> (b r) c")).then_inc(hist_in, 16)

        @block.gpsimd
        def _(pool):
            pool.memset(g.up[:, :, 0:PPAST], 0.0)
            pool.memset(g.xb[:, :, 0:CW - 1], 0.0)
            pool.memset(g.z[:, SMP, :], 0.0)
            pool.memset(g.dt[:, SMP, :], 0.0).then_inc(cleared, 1)

        @block.tensor
        def _(pe):
            def turn(m):
                pe.wait_ge(copied, m + 1)
                for b in range(3):
                    n = 3 * (m - ZF) + b
                    if n >= 2:
                        pe.wait_ge(placed, n - 1)
                    for t in range(4 * b, min(4 * b + 4, TILES)):
                        at = (t - 4 * b) * P
                        last = pe.transpose(g.ps[0:rows(t), 3 + 4 * (n % 2), at:at + width(m)],
                                            zt[0:width(m), t * P:t * P + rows(t)],
                                            g.c("ident")[0:width(m), 0:width(m)])
                    last.then_inc(turned, 1)

            for m in range(NF):
                pe.wait_ge(w_split, m + 1)
                if m >= 2:
                    pe.wait_ge(copied, m - 1)
                for k in range(KD):
                    cols = slice(k * width(m), (k + 1) * width(m))
                    last = split_passes(g, pe, 4 * (m % 2), wh[:, m % 2, cols], wl[:, m % 2, cols], g.hh[:, k, :],
                                        g.hl[:, k, :], k == 0, k == KD - 1, width(m))
                last.then_inc(made, 1)
                if m == 4:
                    pe.wait_ge(hist_in, 32)
                    for n in range(12):
                        if n >= 2:
                            pe.wait_ge(hist_placed, n - 1)
                        src, r = (hu[:, n * P:(n + 1) * P], UROWS) if n < 4 else (hx[:, (n - 4) * P:(n - 3) * P], XROWS)
                        pe.transpose(g.ps[:, 3 + 4 * (n % 2), 0:r], src, g.c("ident")[0:r, 0:r]
                                     ).then_inc(hist_turned, 1)
                    pe.wait_ge(hist_placed, 12)
                if m > ZF:
                    turn(m - 1)
            turn(NF - 1)

        @block.scalar
        def _(act):
            def high(m):
                act.wait_ge(w_in, 16 * (m + 1))
                if m >= 2:
                    act.wait_ge(made, m - 1)
                act.copy(wh[:, m % 2, 0:KD * width(m)], w[:, 0:KD * width(m)]).then_inc(w_rounded, 1)

            high(0)
            high(1)
            act.wait_ge(cleared, 1)
            for m in range(NF):
                act.wait_ge(made, m + 1)
                b0 = 4 * (m % 2)
                third = SEQ - 2 * THIRD
                if m < ZF:
                    if m < 4:
                        dst, at = g.up[:, m, :], PPAST
                        smp = g.us[:, m, PPAST:PPAST + NT, :]
                    else:
                        dst, at = g.xb[:, m - 4, :], CW - 1
                        smp = g.xb[:, m - 4, CW - 1 + SEQ:XW].rearrange("p (r b) -> p r b", b=NB)[:, CW - 1:, :]
                    act.copy(dst[:, at:at + 2 * THIRD].rearrange("p (c n) -> p c n", c=2), g.ps[:, b0:b0 + 2, 0:THIRD])
                    act.copy(dst[:, at + 2 * THIRD:at + SEQ], g.ps[:, b0 + 2, 0:third])
                    act.copy(smp, g.ps[:, b0 + 2, third:THIRD].rearrange("p (b t) -> p t b", b=NB)
                             ).then_inc(copied, 1)
                else:
                    if m == ZF:
                        act.wait_ge(hist_turned, 12)
                    else:
                        act.wait_ge(turned, 3 * (m - ZF))
                    act.copy(zt[0:width(m), :].rearrange("p (c n) -> p c n", c=3),
                             g.ps[0:width(m), b0:b0 + 3, 0:THIRD]).then_inc(copied, 1)
                if m + 2 < NF:
                    high(m + 2)

        @block.vector
        def _(dve):
            def low(m):
                dve.wait_ge(w_rounded, m + 1)
                part = slice(0, KD * width(m))
                dve.tensor_tensor(wl[:, m % 2, part], w[:, part], wh[:, m % 2, part].bitcast(F32), ALU.subtract
                                  ).then_inc(w_split, 1)

            for m in range(7):
                low(m)
                if m == 5:
                    for n in range(12):
                        dve.wait_ge(hist_turned, n + 1)
                        if n < 4:
                            dst = g.us[:, n, 0:PPAST, :]
                            src = g.ps[:, 3 + 4 * (n % 2), 0:UROWS].rearrange("p (b r) -> p r b", b=NB)
                        else:
                            dst = g.xb[:, n - 4, CW - 1 + SEQ:XW].rearrange("p (r b) -> p r b", b=NB)[:, 0:CW - 1, :]
                            src = g.ps[:, 3 + 4 * (n % 2), 0:XROWS].rearrange("p (b r) -> p r b", b=NB)
                        dve.tensor_copy(dst, src).then_inc(hist_placed, 1)
            for m in range(7, ZF + 2):
                low(m)
            dve.wait_ge(cleared, 1)
            for m in range(ZF, NF):
                if m + 2 < NF:
                    low(m + 2)
                for b in range(3):
                    n = 3 * (m - ZF) + b
                    dve.wait_ge(turned, n + 1)
                    at, tiles = (m - ZF) * P, slice(4 * b, min(4 * b + 4, SMP))
                    room = g.z[:, :, at:at + P] if m < NF - 1 else g.dt
                    src = g.ps[:, 3 + 4 * (n % 2), :].rearrange("p (t i) -> p t i", t=4)[:, :, 0:width(m)]
                    if b < 2:
                        dve.tensor_copy(room[:, tiles, :], src).then_inc(placed, 1)
                    else:
                        dve.tensor_copy(room[0:NS, SMP, :], src[0:NS, 0, :]).then_inc(placed, 1)


def stage_pool(g):
    nc = g.nc
    w_in, diff, mixed, placed = (g.sem(f"po_{n}") for n in ("weights", "diff", "mixed", "placed"))
    turned, copied, stored, chain = (g.sem(f"po_{n}") for n in ("turned", "copied", "stored", "chain"))
    with ExitStack() as st:
        pw = g.room(st, "po_w", [P, 4, P])
        scale = g.room(st, "po_scale", [P, 4])
        sums = g.room(st, "po_sums", [P, 2, UW])
        ssum = g.room(st, "po_ssum", [P, 2, PPAST + NT, NB])
        d = g.room(st, "po_d", [P, 2, T])
        tail = g.room(st, "po_tail", [NS, 2, PW])
        block = st.enter_context(nc.Block())

        @block.sync
        def _(sp):
            sp.dma_start(pw[:, :, :], g.ins["pool_w"][0].rearrange("g c d -> c g d")).then_inc(w_in, 16)
            with nc.allow_non_contiguous_dma("a vector of 512 across the partitions"):
                sp.dma_start(scale[:, :], g.ins["pool_scale"][0].rearrange("(g p) -> p g", p=P)).then_inc(w_in, 16)
            sp.dma_start(g.outs["pool_sample"][0][:, 0:PPAST - NT, :], g.ins["state_pool"][0][:, NT:PPAST, :]
                         ).then_inc(stored, 16)
            sp.wait_ge(copied, 2)
            sp.dma_start(g.outs["pool_prompt"][0, 0], tail[0:PPAST, 0, :]).then_inc(stored, 16)
            for t in range(NT):
                sp.dma_start(g.outs["pool_sample"][0][:, PPAST - NT + t, :], tail[t * NB:(t + 1) * NB, 1, :]
                             ).then_inc(stored, 16)
            sp.wait_ge(stored, 16 * (NT + 2))

        @block.tensor
        def _(pe):
            for m in range(4):
                pe.transpose(g.ps[0:PPAST, 6, m * P:(m + 1) * P], g.up[:, m, SEQ:UW], g.c("ident"))
                last = pe.transpose(g.ps[0:NS, 7, m * P:(m + 1) * P], g.us[:, m, PPAST:, :].rearrange("p t b -> p (t b)"),
                                    g.c("ident"))
            last.then_inc(turned, 1)
            pe.wait_ge(w_in, 32)
            for m in range(4):
                pe.wait_ge(diff, m + 1)
                if m >= 2:
                    pe.wait_ge(placed, m - 1)
                for c in range(3):
                    last = pe.matmul(g.ps[:, 3 * (m % 2) + c, 0:THIRD], pw[:, m, :],
                                     d[:, m % 2, c * THIRD:(c + 1) * THIRD], start=True, stop=True)
                last.then_inc(mixed, 1)

        @block.scalar
        def _(act):
            act.wait_ge(turned, 1)
            act.copy(tail[0:PPAST, 0, :], g.ps[0:PPAST, 6, :]).then_inc(copied, 1)
            act.copy(tail[0:NS, 1, :], g.ps[0:NS, 7, :]).then_inc(copied, 1)
            act.wait_ge(w_in, 32)
            for m in range(4):
                act.wait_ge(mixed, m + 1)
                act.activation(g.ht[:, m, :].rearrange("p (c n) -> p c n", c=3),
                               g.ps[:, 3 * (m % 2):3 * (m % 2) + 3, 0:THIRD], ACT.Copy, scale=scale[:, m:m + 1]
                               ).then_inc(placed, 1)

        @block.vector
        def _(dve):
            done = [0]

            def link(op):
                done[0] += 1
                op.then_inc(chain, 1)
                dve.wait_ge(chain, done[0])

            for m in range(4):
                if m >= 1:
                    dve.wait_ge(diff, m)
                if m >= 2:
                    dve.wait_ge(mixed, m - 1)
                src, ssrc = g.up[:, m, :], g.us[:, m, :, :]
                for s in range(m + 1):
                    sh = 2 ** s
                    dst, sdst = sums[:, s % 2, :], ssum[:, s % 2, :, :]
                    lo = 2 * sh - 1
                    dve.tensor_tensor(dst[:, lo:UW], src[:, lo:UW], src[:, lo - sh:UW - sh], ALU.add)
                    link(dve.tensor_tensor(sdst[:, lo:, :], ssrc[:, lo:, :], ssrc[:, lo - sh:PPAST + NT - sh, :],
                                           ALU.add))
                    src, ssrc = dst, sdst
                head = g.c("pool_head")[:, m * PPAST:(m + 1) * PPAST]
                link(dve.tensor_tensor(src[:, PPAST:2 * PPAST], src[:, PPAST:2 * PPAST], head, ALU.mult))
                inv = 1.0 / 2 ** (m + 1)
                dve.tensor_tensor(d[:, m % 2, 0:PPAST], src[:, PPAST:2 * PPAST], g.up[:, m, PPAST:2 * PPAST],
                                  ALU.subtract)
                dve.scalar_tensor_tensor(out=d[:, m % 2, PPAST:SEQ], in0=src[:, 2 * PPAST:UW], scalar=inv,
                                         in1=g.up[:, m, 2 * PPAST:UW], op0=ALU.mult, op1=ALU.subtract)
                dve.scalar_tensor_tensor(out=d[:, m % 2, SEQ:T].rearrange("p (b t) -> p t b", b=NB),
                                         in0=ssrc[:, PPAST:, :], scalar=inv, in1=g.us[:, m, PPAST:, :],
                                         op0=ALU.mult, op1=ALU.subtract).then_inc(diff, 1)


def stage_conv(g):
    nc = g.nc
    w_in, turned, copied, stored = (g.sem(f"cv_{n}") for n in ("weights", "turned", "copied", "stored"))
    summed, rectified, chain = g.sem("cv_summed"), g.sem("cv_silu"), g.sem("cv_chain")
    MT = CD // P
    with ExitStack() as st:
        taps = g.room(st, "cv_taps", [P, MT, CW + 1])
        acc = g.room(st, "cv_acc", [P, 2, T])
        tail = g.room(st, "cv_tail", [NS, 2, CD])
        block = st.enter_context(nc.Block())

        @block.sync
        def _(sp):
            with nc.allow_non_contiguous_dma("vectors of 1024 across the partitions"):
                for j in range(CW):
                    sp.dma_start(taps[:, :, j], g.ins["conv_w"][0][j].rearrange("(k p) -> p k", p=P)
                                 ).then_inc(w_in, 16)
                sp.dma_start(taps[:, :, CW], g.ins["conv_b"][0].rearrange("(k p) -> p k", p=P)).then_inc(w_in, 16)
            sp.wait_ge(copied, 2)
            sp.dma_start(g.outs["conv_prompt"][0, 0], tail[0:CW - 1, 0, :]).then_inc(stored, 16)
            for t in range(1, NT):
                sp.dma_start(g.outs["conv_sample"][0][:, t - 1, :], tail[t * NB:(t + 1) * NB, 1, :]).then_inc(stored, 16)
            sp.wait_ge(stored, 16 * NT)

        def sample(m):
            return g.xb[:, m, CW - 1 + SEQ:XW].rearrange("p (r b) -> p r b", b=NB)

        @block.tensor
        def _(pe):
            for m in range(MT):
                pe.transpose(g.ps[0:CW - 1, m // 4, (m % 4) * P:(m % 4 + 1) * P], g.xb[:, m, SEQ:SEQ + CW - 1],
                             g.c("ident"))
                last = pe.transpose(g.ps[0:NS, 2 + m // 4, (m % 4) * P:(m % 4 + 1) * P], g.xb[:, m, SEQ + (CW - 1) * (NB + 1):XW], g.c("ident"))
            last.then_inc(turned, 1)

        @block.scalar
        def _(act):
            act.wait_ge(turned, 1)
            act.copy(tail[0:CW - 1, 0, :].rearrange("p (c n) -> p c n", c=2), g.ps[0:CW - 1, 0:2, :]).then_inc(copied, 1)
            act.copy(tail[0:NS, 1, :].rearrange("p (c n) -> p c n", c=2), g.ps[0:NS, 2:4, :]).then_inc(copied, 1)
            for m in range(MT):
                act.wait_ge(summed, m + 1)
                act.activation(g.xb[:, m, 0:T], acc[:, m % 2, :], ACT.Silu).then_inc(rectified, 1)

        @block.vector
        def _(dve):
            done = [0]

            def link(op):
                done[0] += 1
                op.then_inc(chain, 1)
                dve.wait_ge(chain, done[0])

            dve.wait_ge(w_in, 16 * (CW + 1))
            for m in range(MT):
                if m >= 2:
                    dve.wait_ge(rectified, m - 1)
                out, souts = acc[:, m % 2, 0:SEQ], acc[:, m % 2, SEQ:T].rearrange("p (b t) -> p t b", b=NB)
                for j in range(CW):
                    tap = taps[:, m, j:j + 1]
                    src, ssrc = g.xb[:, m, j:j + SEQ], sample(m)[:, j:j + NT, :]
                    if j == 0:
                        dve.tensor_scalar(out, src, tap, taps[:, m, CW:CW + 1], ALU.mult, ALU.add)
                        link(dve.tensor_scalar(souts, ssrc, tap, taps[:, m, CW:CW + 1], ALU.mult, ALU.add))
                    else:
                        dve.scalar_tensor_tensor(out=out, in0=src, scalar=tap, in1=out, op0=ALU.mult, op1=ALU.add)
                        last = dve.scalar_tensor_tensor(out=souts, in0=ssrc, scalar=tap, in1=souts, op0=ALU.mult,
                                                        op1=ALU.add)
                        if j < CW - 1:
                            link(last)
                last.then_inc(summed, 1)


def stage_ssd(g):
    nc = g.nc
    small_in, cleared = g.sem("sd_small"), g.sem("sd_cleared")
    turned, copied = g.sem("sd_turned"), g.sem("sd_copied")
    dt_abs, dt_exp, dt_one, dt_log, dt_ready = (g.sem(f"sd_dt_{n}") for n in ("abs", "exp", "one", "log", "ready"))
    cum, cum_ready, powers = g.sem("sd_cum"), g.sem("sd_cum_ready"), g.sem("sd_powers")
    spread_done, decay, weighted, xs, xs_w = (g.sem(f"sd_{n}") for n in ("spread", "decay", "weighted", "xs", "xs_w"))
    made, state, chain = g.sem("sd_made"), g.sem("sd_state"), g.sem("sd_chain")
    st_in, st_turned, st_placed = g.slot_sems("sd_st_in", 2), g.sem("sd_st_turned"), g.sem("sd_st_placed")
    s_laid, s_xw, s_up, s_new = (g.sem(f"sd_s_{n}") for n in ("laid", "xw", "up", "new"))
    tables_ready, cum_high, cum_split, negative = (g.sem(f"sd_{n}") for n in
                                                   ("tables", "cum_high", "cum_split", "negative"))
    products, updated, y_read, skipped = (g.sem(f"sd_{n}") for n in ("products", "updated", "y_read", "skipped"))
    diag_made, w_ready = g.sem("sd_diag_made"), g.sem("sd_w_ready")
    o_turned, o_copied, o_stored = g.sem("sd_o_turned"), g.sem("sd_o_copied"), g.slot_sems("sd_o_stored", 2)
    gate_ready, rms, root, normed, y_turned, y_placed = (g.sem(f"sd_{n}") for n in
                                                         ("gate", "rms", "root", "normed", "y_turned", "y_placed"))
    BT, CT = 4, 6
    with ExitStack() as st:
        ex = g.room(st, "sd_exp", [P, TILES, SH])
        cs = g.room(st, "sd_cs", [P, TILES, SH])
        wend = g.room(st, "sd_wend", [P, TILES, SH])
        a = g.room(st, "sd_a", [P, TILES, SH])
        tmp = g.room(st, "sd_tmp", [P, TILES, SH])
        eend = g.room(st, "sd_eend", [P, SMP, SH])
        eend_s = g.room(st, "sd_eends", [P, NB, SH])
        ab = g.room(st, "sd_ab", [NS, NB, SH])
        rowv = g.room(st, "sd_rowv", [P, 3, SH])
        csth = g.room(st, "sd_cst_high", [SH, T], F32R)
        cstl = g.room(st, "sd_cst_low", [SH, T], F32R)
        dgh = g.room(st, "sd_diag_high", [SH, SH, P], F32R)
        dgl = g.room(st, "sd_diag_low", [SH, SH, P], F32R)
        onesr = g.room(st, "sd_ones", [SH, P], F32R)
        identr = g.room(st, "sd_ident", [P, P], F32R)
        causalr = g.room(st, "sd_causal", [P, P], F32R)
        newr = g.room(st, "sd_new", [NS, NS], F32R)
        ncs = g.room(st, "sd_ncs", [P, TILES, SH])
        ee = g.room(st, "sd_e", [P, 2, SH, P])
        xd = g.room(st, "sd_xd", [P, 2, 512])
        xw = g.room(st, "sd_xw", [P, 2, 512])
        t1 = g.room(st, "sd_t1", [P, 512])
        h0 = g.room(st, "sd_h", [P, 512])
        hs = g.ht[:, 4:8, :].rearrange("p k n -> p (k n)")[:, 0:NB * 512].rearrange("p (b n) -> p b n", b=NB)
        nat = g.room(st, "sd_nat", [P, 2, 4, SN])
        cz = g.room(st, "sd_cz", [P, 2, NB, NS])
        gains = g.room(st, "sd_gains", [P, 4])
        rs = g.room(st, "sd_rs", [P, TILES * 2])
        block = st.enter_context(nc.Block())
        ident = g.c("ident")

        def heads(ap):
            return ap.rearrange("p (h e) -> p h e", h=SH)

        state_rows = g.ins["state_ssm"][0].rearrange("b h p n -> b (h p) n")
        out_rows = g.outs["ssm_sample"][0].rearrange("b h p n -> b (h p) n")

        @block.sync
        def _(sp):
            with nc.allow_non_contiguous_dma("small vectors"):
                for n, name in enumerate(("dt_bias", "a_log", "d_skip")):
                    sp.dma_start(rowv[:, n, :], g.ins[name][0].partition_broadcast(P)).then_inc(small_in, 16)
                sp.dma_start(gains[:, :], g.ins["ssm_norm"][0].rearrange("(k p) -> p k", p=P)).then_inc(small_in, 16)
            for b in range(NB):
                if b >= 2:
                    sp.wait_ge(st_turned, b - 1)
                sp.dma_start(nat[:, b % 2, :, :], state_rows[b].rearrange("(c p) n -> p c n", p=P)).then_inc(st_in[b % 2], 16)
            for n in range(NB + 1):
                sp.wait_ge(o_copied, n + 1)
                dst = g.outs["ssm_prompt"][0, 0].rearrange("h p n -> (h p) n") if n == 0 else out_rows[n - 1]
                sp.dma_start(dst.rearrange("(c p) n -> p c n", p=P), nat[:, n % 2, :, :]).then_inc(o_stored[n % 2], 16)
            for slot in range(2):
                sp.wait_ge(o_stored[slot], 16 * len(range(slot, NB + 1, 2)))

        @block.gpsimd
        def _(pool):
            pool.memset(g.xtm[:, SMP, :], 0.0)
            pool.memset(g.btm[:, SMP, :], 0.0)
            pool.memset(cs[:, SMP, :], 0.0)
            pool.memset(wend[:, SMP, :], 0.0).then_inc(cleared, 1)
            pool.tensor_copy(onesr[:, :], g.c("ones")[0:SH, :])
            pool.tensor_copy(identr[:, :], ident)
            pool.tensor_copy(causalr[:, :], g.c("causal"))
            pool.tensor_copy(newr[:, :], g.c("new_ok")[0:NS, :]).then_inc(tables_ready, 1)
            for q in range(2):
                pool.tensor_tensor(cz[:, q, :, :], spread(g.xb[:, CT + q, SEQ:T], 0, NB),
                                   g.c("col_seq").rearrange("p (b t) -> p b t", b=NB), ALU.mult).then_inc(s_laid, 1)
            pool.wait_ge(cum_split, 1)
            own = ident[0:SH, 0:SH]

            def diagonal(c):
                n = rows(c)
                if c >= 1:
                    pool.wait_ge(spread_done, c)
                for to, part in ((dgh, csth), (dgl, cstl)):
                    last = pool.tensor_tensor(to[:, :, 0:n], spread(part[:, c * P:c * P + n].bitcast(F32), 0, SH),
                                              spread(own, 1, n), ALU.mult)
                last.then_inc(diag_made, 1)

            def ends(c):
                n = rows(c)
                if c >= 2:
                    pool.wait_ge(updated, c - 1)
                pool.tensor_tensor(heads(xw[0:n, c % 2, :]), heads(g.xtm[0:n, c, :]), spread(wend[0:n, c, :], 1, SP),
                                   ALU.mult).then_inc(xs_w, 1)

            diagonal(0)
            pool.wait_ge(w_ready, 1)
            ends(0)
            for c in range(TILES):
                n = rows(c)
                if c + 1 < TILES:
                    diagonal(c + 1)
                    ends(c + 1)
                pool.wait_ge(xs, c + 1)
                pool.wait_ge(xs_w, c + 1)
                x = heads(g.xtm[0:n, c, :])
                pool.tensor_tensor(x, x, spread(rowv[0:n, 2, :], 1, SP), ALU.mult).then_inc(skipped, 1)

        @block.tensor
        def _(pe):
            pe.wait_ge(cleared, 1)
            for t in range(TILES):
                if t >= 2:
                    pe.wait_ge(copied, 2 * (t - 1))
                for m in range(6):
                    last = pe.transpose(g.ps[0:rows(t), 2 * (t % 2) + m // 4, (m % 4) * P:(m % 4 + 1) * P],
                                        g.xb[:, m, t * P:t * P + rows(t)], ident)
                last.then_inc(turned, 1)
            for b in range(NB):
                pe.wait_ge(st_in[b % 2], 16 * (b // 2 + 1))
                if b >= 2:
                    pe.wait_ge(st_placed, b - 1)
                for m in range(4):
                    last = pe.transpose(g.ps[:, 4 + b % 2, m * P:(m + 1) * P], nat[:, b % 2, m, :], ident)
                last.then_inc(st_turned, 1)
            pe.wait_ge(dt_ready, 1)
            pe.wait_ge(copied, 2 * TILES)
            pe.wait_ge(st_placed, NB)
            av = a[:, 0:SMP, :].rearrange("p t h -> p (t h)")
            pe.matmul(g.ps[:, 0, 0:SMP * SH], g.c("upper"), av, start=True, stop=True)
            pe.matmul(g.ps[:, 1, 0:SMP * SH], g.c("ones"), av, start=True, stop=True)
            pe.matmul(g.ps[0:NS, 2, 0:SH], g.c("upper_s")[0:NS, :], a[0:NS, SMP, :], start=True, stop=True)
            pe.matmul(g.ps[0:NS, 3, 0:SH], g.c("same_s")[0:NS, :], a[0:NS, SMP, :], start=True, stop=True)
            pe.matmul(g.ps[:, 4, 0:NB * SH], g.c("ones")[0:NS, :], ab[:, :, :].rearrange("p b h -> p (b h)"),
                      start=True, stop=True)
            for c in range(SMP):
                pe.matmul(g.ps[0:SH, 5 + c // 4, (c % 4) * P:(c % 4 + 1) * P], a[:, c, :], g.c("upper"),
                          start=True, stop=True)
            pe.matmul(g.ps[0:SH, 7, 0:NS], a[0:NS, SMP, :], g.c("upper_s")[0:NS, :], start=True, stop=True
                      ).then_inc(cum, 1)
            pe.wait_ge(cum_ready, 1)
            pe.wait_ge(powers, 1)
            pe.wait_ge(tables_ready, 1)

            def sums(c):
                n = rows(c)
                pe.wait_ge(diag_made, c + 1)
                if c >= 2:
                    pe.wait_ge(decay, c - 1)
                apart = causalr[:, :] if c < SMP else newr[:, :]
                for half in range(2):
                    to = g.ps[0:n, 6 * (c % 2) + half, 0:4 * n]
                    pe.matmul(to, apart, spread(identr[0:n, 0:n], 0, 4), start=True, stop=False)
                    for part in (dgh, dgl):
                        last = pe.matmul(to, onesr[:, 0:n], part[:, 4 * half:4 * half + 4, 0:n],
                                         start=False, stop=(part is dgl))
                last.then_inc(spread_done, 1)

            def pairs(c):
                n, cols = rows(c), slice(c * P, c * P + rows(c))
                for q in range(2):
                    last = pe.matmul(g.ps[0:n, 2, q * P:q * P + n], g.xb[:, BT + q, cols], g.xb[:, CT + q, cols],
                                     start=True, stop=True)
                last.then_inc(products, 1)

            sums(0)
            pairs(0)
            for c in range(TILES):
                n = rows(c)
                cols = slice(c * P, c * P + n)
                if c + 1 < TILES:
                    sums(c + 1)
                if c >= 1:
                    pe.wait_ge(state, c)
                    pe.wait_ge(y_read, c)
                if c < SMP:
                    if c >= 1:
                        for q in range(2):
                            pe.matmul(g.ps[:, 4, q * 256:(q + 1) * 256], g.xb[:, CT + q, cols],
                                      h0[:, q * 256:(q + 1) * 256], start=True, stop=True)
                    pe.wait_ge(xs_w, c + 1)
                    for q in range(2):
                        last = pe.matmul(g.ps[:, 5, q * 256:(q + 1) * 256], g.btm[:, c, q * P:(q + 1) * P],
                                         xw[:, c % 2, q * 256:(q + 1) * 256], start=True, stop=True)
                    last.then_inc(updated, 1)
                else:
                    pe.wait_ge(s_laid, 2)
                    for q in range(2):
                        for b in range(NB):
                            pe.matmul(g.ps[0:NS, 4, q * 256:(q + 1) * 256], cz[:, q, b, :],
                                      hs[:, b, q * 256:(q + 1) * 256], start=(b == 0), stop=(b == NB - 1))
                pe.wait_ge(weighted, c + 1)
                if c + 1 < TILES:
                    pairs(c + 1)
                for h in range(SH):
                    last = pe.matmul(g.ps[0:n, 3, h * SP:(h + 1) * SP], ee[0:n, c % 2, h, 0:n],
                                     xd[0:n, c % 2, h * SP:(h + 1) * SP], start=True, stop=True)
                last.then_inc(made, 1)
            pe.wait_ge(decay, TILES)
            for m in range(4):
                last = pe.transpose(g.ps[:, 6, m * P:(m + 1) * P], h0[:, m * P:(m + 1) * P], ident)
            last.then_inc(o_turned, 1)
            for b in range(NB):
                pe.wait_ge(s_xw, b + 1)
                for q in range(2):
                    last = pe.matmul(g.ps[:, b % 2, q * 256:(q + 1) * 256], g.btm[0:NS, SMP, q * P:(q + 1) * P],
                                     xd[0:NS, b % 2, q * 256:(q + 1) * 256], start=True, stop=True)
                last.then_inc(s_up, 1)
                pe.wait_ge(s_new, b + 1)
                if b >= 1:
                    pe.wait_ge(o_copied, b)
                for m in range(4):
                    last = pe.transpose(g.ps[:, 6 + (b + 1) % 2, m * P:(m + 1) * P], hs[:, b, m * P:(m + 1) * P], ident)
                last.then_inc(o_turned, 1)
            for t in range(TILES):
                pe.wait_ge(normed, t + 1)
                if t >= 2:
                    pe.wait_ge(y_placed, t - 1)
                for m in range(4):
                    last = pe.transpose(g.ps[:, 2 + t % 2, m * P:m * P + rows(t)],
                                        g.xtm[0:rows(t), t, m * P:(m + 1) * P], ident[0:rows(t), 0:rows(t)])
                last.then_inc(y_turned, 1)

        @block.scalar
        def _(act):
            act.wait_ge(small_in, 64)
            act.wait_ge(dt_abs, 1)
            act.activation(tmp[:, :, :], tmp[:, :, :], ACT.Exp).then_inc(dt_exp, 1)
            act.activation(rowv[:, 1, :], rowv[:, 1, :], ACT.Exp).then_inc(dt_exp, 1)
            act.wait_ge(dt_one, 1)
            act.activation(tmp[:, :, :], tmp[:, :, :], ACT.Ln).then_inc(dt_log, 1)
            for t in range(TILES):
                act.wait_ge(turned, t + 1)
                act.copy(g.xtm[0:rows(t), t, :], g.ps[0:rows(t), 2 * (t % 2), :]).then_inc(copied, 1)
                act.copy(g.btm[0:rows(t), t, :], g.ps[0:rows(t), 2 * (t % 2) + 1, 0:256]).then_inc(copied, 1)
            act.activation(g.z[:, :, :], g.z[:, :, :], ACT.Silu).then_inc(gate_ready, 1)
            act.wait_ge(cum_ready, 1)
            act.activation(ex[:, :, :], cs[:, :, :], ACT.Exp)
            act.activation(wend[:, :, :], wend[:, :, :], ACT.Exp)
            act.activation(eend[:, :, :], eend[:, :, :], ACT.Exp)
            act.activation(eend_s[:, :, :], eend_s[:, :, :], ACT.Exp).then_inc(powers, 1)
            act.wait_ge(negative, 1)
            for c in range(TILES):
                n = rows(c)
                act.wait_ge(spread_done, c + 1)
                if c >= 2:
                    act.wait_ge(made, c - 1)
                for h in range(SH):
                    last = act.activation(ee[0:n, c % 2, h, 0:n],
                                          g.ps[0:n, 6 * (c % 2) + h // 4, (h % 4) * n:(h % 4 + 1) * n], ACT.Exp,
                                          bias=ncs[0:n, c, h:h + 1])
                last.then_inc(decay, 1)
            for n in range(NB + 1):
                act.wait_ge(o_turned, n + 1)
                if n == 0:
                    act.wait_ge(st_turned, NB)
                if n >= 2:
                    act.wait_ge(o_stored[n % 2], 16 * (n // 2))
                act.copy(nat[:, n % 2, :, :].rearrange("p c n -> p (c n)"), g.ps[:, 6 + n % 2, :]).then_inc(o_copied, 1)
            act.wait_ge(rms, 1)
            act.activation(rs[:, :], rs[:, :], ACT.Sqrt).then_inc(root, 1)
            for t in range(TILES):
                act.wait_ge(y_turned, t + 1)
                for m in range(4):
                    last = act.activation(g.ht[:, 4 + m, t * P:t * P + rows(t)], g.ps[:, 2 + t % 2, m * P:m * P + rows(t)],
                                          ACT.Copy, scale=gains[:, m:m + 1])
                last.then_inc(y_placed, 1)

        @block.vector
        def _(dve):
            done = [0]

            def link(op):
                done[0] += 1
                op.then_inc(chain, 1)
                dve.wait_ge(chain, done[0])

            dve.wait_ge(small_in, 64)
            link(dve.tensor_tensor(g.dt[:, :, :], g.dt[:, :, :], spread(rowv[:, 0, :], 0, TILES), ALU.add))
            dve.scalar_tensor_tensor(out=tmp[:, :, :], in0=g.dt[:, :, :], scalar=-1.0, in1=g.dt[:, :, :], op0=ALU.mult,
                                     op1=ALU.min).then_inc(dt_abs, 1)
            dve.wait_ge(dt_exp, 2)
            dve.tensor_scalar(tmp[:, :, :], tmp[:, :, :], 1.0, None, ALU.add).then_inc(dt_one, 1)
            dve.wait_ge(dt_log, 1)
            link(dve.scalar_tensor_tensor(out=g.dt[:, :, :], in0=g.dt[:, :, :], scalar=0.0, in1=tmp[:, :, :],
                                          op0=ALU.max, op1=ALU.add))
            link(dve.scalar_tensor_tensor(out=a[:, :, :], in0=g.dt[:, :, :], scalar=-1.0,
                                          in1=spread(rowv[:, 1, :], 0, TILES), op0=ALU.mult, op1=ALU.mult))
            dve.tensor_tensor(ab[:, :, :], spread(a[0:NS, SMP, :], 0, NB), spread(g.c("seq_of")[0:NS, :], 1, SH),
                              ALU.mult).then_inc(dt_ready, 1)
            for b in range(NB):
                dve.wait_ge(st_turned, b + 1)
                dve.tensor_copy(hs[:, b, :], g.ps[:, 4 + b % 2, :]).then_inc(st_placed, 1)
            dve.wait_ge(cum, 1)
            dve.wait_ge(cleared, 1)
            dve.tensor_copy(cs[:, 0:SMP, :].rearrange("p t h -> p (t h)"), g.ps[:, 0, 0:SMP * SH])
            link(dve.tensor_copy(cs[0:NS, SMP, :], g.ps[0:NS, 2, 0:SH]))
            dve.tensor_tensor(wend[:, 0:SMP, :].rearrange("p t h -> p (t h)"), g.ps[:, 1, 0:SMP * SH],
                              cs[:, 0:SMP, :].rearrange("p t h -> p (t h)"), ALU.subtract)
            dve.tensor_tensor(wend[0:NS, SMP, :], g.ps[0:NS, 3, 0:SH], cs[0:NS, SMP, :], ALU.subtract)
            dve.tensor_copy(eend[:, :, :].rearrange("p t h -> p (t h)"), g.ps[:, 1, 0:SMP * SH])
            dve.tensor_copy(eend_s[:, :, :].rearrange("p b h -> p (b h)"), g.ps[:, 4, 0:NB * SH])
            by_head = ((csth[:, 0:SEQ], cstl[:, 0:SEQ], g.ps[0:SH, 5:7, :].rearrange("p c n -> p (c n)")),
                       (csth[:, SEQ:T], cstl[:, SEQ:T], g.ps[0:SH, 7, 0:NS]))
            for high, low, sums in by_head:
                last = dve.tensor_copy(high, sums)
            last.then_inc(cum_high, 1)
            dve.wait_ge(cum_high, 1)
            for high, low, sums in by_head:
                last = dve.tensor_tensor(low, sums, high.bitcast(F32), ALU.subtract)
            last.then_inc(cum_split, 1)
            dve.wait_ge(cum_split, 1)
            dve.tensor_copy(t1[:, 0:1], g.c("ones")[:, 0:1]).then_inc(cum_ready, 1)
            dve.tensor_scalar(ncs[:, :, :], cs[:, :, :], -1.0, None, ALU.mult).then_inc(negative, 1)
            dve.wait_ge(powers, 1)
            dve.tensor_tensor(wend[:, :, :], wend[:, :, :], g.dt[:, :, :], ALU.mult).then_inc(w_ready, 1)
            dve.wait_ge(copied, 2 * TILES)

            def steps(c):
                n = rows(c)
                if c >= 2:
                    dve.wait_ge(made, c - 1)
                dve.tensor_tensor(heads(xd[0:n, c % 2, :]), heads(g.xtm[0:n, c, :]), spread(g.dt[0:n, c, :], 1, SP),
                                  ALU.mult).then_inc(xs, 1)

            def weight(c):
                n = rows(c)
                dve.wait_ge(decay, c + 1)
                dve.wait_ge(products, c + 1)
                ev = ee[0:n, c % 2, :, 0:n].rearrange("p (a h) i -> p a h i", a=2)
                bc = g.ps[0:n, 2, 0:256].rearrange("p (q i) -> p q i", q=2)[:, :, 0:n]
                dve.tensor_tensor(ev, ev, spread(bc, 1, 4), ALU.mult).then_inc(weighted, 1)

            steps(0)
            weight(0)
            dve.wait_ge(gate_ready, 1)
            for c in range(TILES):
                n = rows(c)
                if c + 1 < TILES:
                    steps(c + 1)
                if c < SMP:
                    dve.wait_ge(updated, c + 1)
                    if c >= 1:
                        link(dve.tensor_tensor(heads(h0[:, :]), heads(h0[:, :]), spread(eend[:, c, :], 1, SP), ALU.mult))
                        dve.tensor_tensor(h0[:, :], g.ps[:, 5, :], h0[:, :], ALU.add).then_inc(state, 1)
                    else:
                        dve.tensor_copy(h0[:, :], g.ps[:, 5, :]).then_inc(state, 1)
                dve.wait_ge(made, c + 1)
                if c + 1 < TILES:
                    weight(c + 1)
                if c >= 1:
                    link(dve.tensor_tensor(heads(t1[0:n, :]), heads(g.ps[0:n, 4, :]), spread(ex[0:n, c, :], 1, SP),
                                           ALU.mult))
                    dve.tensor_tensor(t1[0:n, :], g.ps[0:n, 3, :], t1[0:n, :], ALU.add).then_inc(y_read, 1)
                else:
                    dve.tensor_copy(t1[0:n, :], g.ps[0:n, 3, :]).then_inc(y_read, 1)
                dve.wait_ge(y_read, c + 1)
                dve.wait_ge(skipped, c + 1)
                link(dve.tensor_tensor(g.xtm[0:n, c, :], g.xtm[0:n, c, :], t1[0:n, :], ALU.add))
                link(dve.tensor_tensor(g.xtm[:, c, :], g.xtm[:, c, :], g.z[:, c, :], ALU.mult))
                for q in range(2):
                    part = slice(q * 256, (q + 1) * 256)
                    last = dve.tensor_tensor_reduce(g.z[:, c, part], g.xtm[:, c, part], g.xtm[:, c, part], 1.0, 0.0,
                                                    ALU.mult, ALU.add, rs[:, 2 * c + q:2 * c + q + 1])
                link(last)
            for b in range(NB):
                if b >= 2:
                    dve.wait_ge(s_up, b - 1)
                dve.tensor_scalar(xd[0:NS, b % 2, :], xw[0:NS, SMP % 2, :], g.c("seq_of")[0:NS, b:b + 1], None, ALU.mult
                                  ).then_inc(s_xw, 1)
                link(dve.tensor_tensor(heads(hs[:, b, :]), heads(hs[:, b, :]), spread(eend_s[:, b, :], 1, SP), ALU.mult))
                dve.wait_ge(s_up, b + 1)
                dve.tensor_tensor(hs[:, b, :], g.ps[:, b % 2, :], hs[:, b, :], ALU.add).then_inc(s_new, 1)
            dve.tensor_scalar(rs[:, :], rs[:, :], 1.0 / 256, EPS, ALU.mult, ALU.add).then_inc(rms, 1)
            dve.wait_ge(root, 1)
            link(dve.reciprocal(rs[:, :], rs[:, :]))
            for c in range(TILES):
                y = g.xtm[:, c, :].rearrange("p (q e) -> p q e", q=2)
                dve.tensor_tensor(y, y, spread(rs[:, 2 * c:2 * c + 2], 1, 256), ALU.mult).then_inc(normed, 1)


_INS = ['x_prompt', 'x_sample', 'cache_k', 'cache_v', 'cache_kidx', 'state_ret', 'state_pool', 'state_conv',
        'state_ssm', 'page_table', 'norm_mix', 'norm_ffn', 'w_in_even', 'w_out_even', 'q_norm', 'k_norm', 'rel_bias',
        'w_in_odd', 'w_out_odd', 'pool_w', 'pool_scale', 'conv_w', 'conv_b', 'dt_bias', 'a_log', 'd_skip', 'ssm_norm',
        'w_gate', 'w_up', 'w_down']
_OUTS = [('y_prompt', (1, SEQ, D)), ('y_sample', (NB, NT, D)),
         ('k_prompt', (1, 1, SEQ, H, P)), ('v_prompt', (1, 1, SEQ, H, P)), ('kidx_prompt', (1, 1, SEQ, ID)),
         ('ret_prompt', (1, 1, H, P, P)), ('pool_prompt', (1, 1, PPAST, PW)), ('conv_prompt', (1, 1, CW - 1, CD)),
         ('ssm_prompt', (1, 1, SH, SP, SN)),
         ('k_sample', (1, NB, NT, H, P)), ('v_sample', (1, NB, NT, H, P)), ('kidx_sample', (1, NB, NT, ID)),
         ('ret_sample', (1, NB, H, P, P)), ('pool_sample', (1, NB, PPAST, PW)), ('conv_sample', (1, NB, CW - 1, CD)),
         ('ssm_sample', (1, NB, SH, SP, SN))]


def kernel(**inputs):
    import numpy as _np
    import concourse.bacc as _bacc
    from concourse import mybir as _mybir
    from concourse.bass_utils import run_bass_kernel_spmd as _run

    nc = _bacc.Bacc("TRN2", target_bir_lowering=False, num_devices=1)
    arrays, ins, outs = {}, {}, {}
    for name in _INS:
        a = _np.ascontiguousarray(inputs[name])
        arrays[f"in_{name}_dram"] = a
        ins[name] = nc.dram_tensor(f"in_{name}_dram", a.shape, _mybir.dt.from_np(a.dtype), kind="ExternalInput").ap()
    place, kept, table = host_constants()
    arrays["in_tables_dram"] = table
    tables = nc.dram_tensor("in_tables_dram", table.shape, _mybir.dt.float32, kind="ExternalInput").ap()
    for name, shape in _OUTS:
        outs[name] = nc.dram_tensor(f"out_{name}_dram", shape, _mybir.dt.float32, kind="ExternalOutput").ap()
    build_program(nc, ins, outs, tables, place, kept)
    r = _run(nc, [arrays], core_ids=[0])
    return tuple(r.results[0][f"out_{name}_dram"] for name, _ in _OUTS)
```

```python
import math
from contextlib import ExitStack

import numpy as np

import concourse.bass as bass
from concourse import mybir

F32 = mybir.dt.float32
F32R = mybir.dt.float32r
I32 = mybir.dt.int32
U32 = mybir.dt.uint32
ALU = mybir.AluOpType
ACT = mybir.ActivationFunctionType
AX = mybir.AxisListType

P = 128
D = 1024
KD = D // P
SEQ = 1024
NB, NT = 8, 4
NS = NB * NT
T = SEQ + NS
TILES = SEQ // P + 1
SMP = TILES - 1
THIRD = T // 3
H = 4
PAGE = 128
PAST = 512
NPAGE = PAST // PAGE
KEYS = PAST + NS
IH, ID = 8, 64
TOPK = 256
TOPK_S = 129
FF = 2816
KF = FF // P
PW = 512
PPAST = 15
DI = 512
SH, SP, SN = 8, 64, 128
CW = 4
CD = 1024
EPS = 1e-6
NEG = -1e30
TAKEN = -3e38
EVEN_TM = 7
IDX_COL = 3584
ODD_Z, ODD_XBC, ODD_DT = 512, 1024, 2048


SQUARES, TOTAL = slice(3, 7), 7
ROUNDS_2 = (0, 8, 16, 26, 32)
HELD = 6


def rows(t):
    return P if t < SMP else NS


def host_constants():
    parts, place, at = [], {}, 0

    def put(name, a):
        nonlocal at
        full = np.zeros((P, a.shape[1]), np.float32)
        full[:a.shape[0]] = a
        parts.append(full)
        place[name] = (at, a.shape[1])
        at += a.shape[1]

    i = np.arange(P)
    put("ident", np.eye(P))
    put("flip", np.eye(P)[::-1])
    put("ones", np.ones((P, P)))
    put("upper", (i[:, None] <= i[None, :]) * 1.0)
    put("causal", np.where(i[None, :] <= i[:, None], 0.0, NEG))
    r = np.arange(NS)
    b, t = r // NT, r % NT
    same = b[:, None] == b[None, :]
    put("upper_s", (same & (t[:, None] <= t[None, :])) * 1.0)
    put("new_ok", np.where(same & (t[None, :] <= t[:, None]), 0.0, NEG))
    put("same_s", same * 1.0)
    put("seq_of", (b[:, None] == np.arange(NB)[None, :]) * 1.0)
    put("col_seq", np.tile((np.arange(NB)[:, None] == b[None, :]).reshape(1, -1) * 1.0, (P, 1)))
    def bucket(n):
        n = np.maximum(n, 0)
        nf = np.maximum(n, 1).astype(np.float32)
        large = 16 + (np.log(nf / np.float32(16)) / np.float32(math.log(8.0)) * np.float32(16)).astype(np.int32)
        return np.where(n < 16, n, np.minimum(large, 31))

    def onehot(n):
        k = np.arange(32)[:, None]
        return (bucket(n)[None, :] == k) * 1.0 - (k == 31) * 1.0

    put("bias_p", onehot(255 - np.arange(384)))
    dist = []
    for tt in range(NT):
        new = tt - (np.arange(NS) % NT)
        dist.append(onehot(np.concatenate([PAST + tt - np.arange(PAST), new])))
    put("bias_s", np.concatenate(dist, 0))
    put("t_of", (i[:, None] // 32 == np.arange(NT)[None, :]) * 1.0)
    q = np.arange(P)
    put("row_bht", (r[:, None] == (q // 16 * NT + q % NT)[None, :]) * 1.0)
    for g in range(2):
        tok = (4 * g + q // 32) * NT + q % NT
        put(f"row_idx{g}", (r[:, None] == tok[None, :]) * 1.0)
        put(f"sum_idx{g}", (tok[:, None] == r[None, :]) * 1.0)
    head = 2 * ((q % 16) // 4) + (q % 32) // 16
    put("head_idx", (head[:, None] == np.arange(IH)[None, :]) * 1.0)
    put("page_row", i[:, None] * 1.0)
    cnt = np.stack([1.0 / np.minimum(np.arange(PPAST) + 1, 2 ** (g + 1)) for g in range(4)])
    put("pool_head", np.tile(cnt.reshape(1, -1), (P, 1)))
    kept = at
    gam = (1.0 - 2.0 ** (-5.0 - np.arange(H))).astype(np.float64)
    where = np.zeros((P, TILES))
    where[:, :SMP] = i[:, None]
    where[:NS, SMP] = t
    put("ret_q", (gam[None, None, :] ** (where[:, :, None] + 1)).reshape(P, -1))
    put("ret_k", (gam[None, None, :] ** -(where[:, :, None] + 1) * P ** -0.5).reshape(P, -1))
    put("ret_step", np.tile(gam[None, :] ** P, (P, 1)))
    put("ret_step_s", np.tile(gam[None, :] ** NT, (P, 1)))
    pos = np.zeros((P, TILES), np.float32)
    pos[:, :SMP] = np.arange(SEQ).reshape(SMP, P).T
    pos[:NS, SMP] = PAST + t
    inv = np.float32(10000.0) ** (-np.linspace(0.0, 1.0, 64, dtype=np.float32))
    ang = (pos[:, :, None] * inv.astype(np.float32)[None, None, :]).astype(np.float32)
    put("cos", np.cos(ang.astype(np.float64)).reshape(P, -1))
    put("sin", np.sin(ang.astype(np.float64)).reshape(P, -1))

    return place, kept, np.ascontiguousarray(np.concatenate(parts, 1), np.float32)


def spread(ap, at, n):
    dims = list(ap.ap)
    dims.insert(1 + at, [0, n])
    return bass.AP(ap.tensor, ap.offset, dims)


class Room:
    pass


def build_program(nc, ins, outs, const_dram, place, kept):
    with ExitStack() as whole:
        g = Room()
        g.nc = nc
        g.ins, g.outs = ins, outs
        g.sems = []

        def new_semaphore(name):
            g.sems.append(nc.alloc_semaphore(name))
            return g.sems[-1]
        g.sem = new_semaphore
        g.slot_sems = lambda name, n: [new_semaphore(f"{name}{i}") for i in range(n)]
        g.ps = whole.enter_context(nc.psum_tensor("ps", [P, 8, 512], F32))
        g.cst = whole.enter_context(nc.sbuf_tensor("cst", [P, kept], F32))
        g.kept = kept
        g.c = lambda name: g.cst[:, place[name][0]:place[name][0] + place[name][1]]
        g.const_dram, g.place = const_dram, place

        def scratch(name, shape):
            return nc.dram_tensor(name, shape, F32).ap()

        g.proj = scratch("proj", [EVEN_TM, T, 512])
        g.xt_spill = scratch("xt_spill", [P, KD, T])
        g.bias_row = scratch("bias_row", [H, 384])
        g.gain = whole.enter_context(nc.sbuf_tensor("gain", [P, 4, KD], F32))

        def room(stack, name, shape, dt=F32, side=None):
            return stack.enter_context(nc.sbuf_tensor(name, shape, dt, side=side))
        g.room = room

        def halves(stack, name, side=None):
            g.hh = room(stack, f"{name}_high", [P, KD, T], F32R, side)
            g.hl = room(stack, f"{name}_low", [P, KD, T], F32R, side)

        g.halves = halves

        with ExitStack() as even:
            with ExitStack() as att:
                with ExitStack() as normed:
                    halves(normed, "even", "right")
                    with ExitStack() as st:
                        g.xt = room(st, "xt0", [P, KD, T])
                        stage_load(g)
                        stage_norm(g, 0, "n0", spill=True)
                    g.score = room(att, "score", [P, 6, SEQ])
                    g.score_s = room(att, "score_s", [NS, KEYS])
                    stage_index(g)
                    stage_project_even(g)
                g.ht = room(even, "ht_even", [P, KD, T], F32, "right")
                free_semaphores(g)
                stage_retention(g)
                with ExitStack() as kv:
                    g.qt = room(kv, "qt", [P, H, T])
                    g.kt = room(kv, "kt", [P, H, T])
                    g.va = room(kv, "va", [P, TILES, 512])
                    g.hank = room(kv, "hank", [P, H, 256])
                    stage_attention_prep(g)
                    g.pages = room(kv, "pages", [P, HELD, NPAGE, 512])
                    g.ids = room(kv, "page_rows", [P, NB * NPAGE], I32)
                    stage_attention_prompt(g)
                    stage_attention_sample(g)
            free_semaphores(g)
            g.xt = room(whole, "xt", [P, KD, T])
            halves(even, "ffn0")
            stage_project_out(g, ins["w_out_even"][0], "oe", reload=True)
            stage_ffn(g, 0)
        free_semaphores(g)
        with ExitStack() as odd:
            stage_odd(g, odd)
            free_semaphores(g)
            halves(odd, "ffn1")
            stage_project_out(g, ins["w_out_odd"][0], "oo", reload=False)
            stage_ffn(g, 1)
        stage_store(g)
        free_semaphores(g)


def free_semaphores(g):
    g.nc.clear_and_free_semaphores(g.sems)
    g.sems.clear()
    g.nc.all_engine_barrier()


def stage_load(g):
    nc = g.nc
    consts_in, gains_in = g.sem("consts_in"), g.sem("gains_in")
    rows_in, rows_turned, rows_placed = g.slot_sems("rows_in", 3), g.sem("rows_turned"), g.sem("rows_placed")
    with ExitStack() as st:
        ring = g.room(st, "x_rows", [P, 3, D])
        block = st.enter_context(nc.Block())

        @block.sync
        def _(sp):
            sp.dma_start(g.cst[:, :], g.const_dram[:, 0:g.kept]).then_inc(consts_in, 16)
            for t in range(TILES):
                if t >= 3:
                    sp.wait_ge(rows_turned, 2 * (t - 2))
                src = g.ins["x_prompt"][0, t * P:(t + 1) * P, :] if t < SMP else \
                    g.ins["x_sample"].rearrange("b t d -> (b t) d")
                sp.dma_start(ring[0:rows(t), t % 3, :], src).then_inc(rows_in[t % 3], 16)

        @block.gpsimd
        def _(pool):
            for n, (w, l) in enumerate((("norm_mix", 0), ("norm_mix", 1), ("norm_ffn", 0), ("norm_ffn", 1))):
                with nc.allow_non_contiguous_dma("a vector of 1024 across the partitions"):
                    pool.dma_start(g.gain[:, n, :], g.ins[w][l].rearrange("(k p) -> p k", p=P)).then_inc(gains_in, 16)
            pool.wait_ge(gains_in, 64)

        @block.tensor
        def _(pe):
            pe.wait_ge(consts_in, 16)
            for t in range(TILES):
                pe.wait_ge(rows_in[t % 3], 16 * (t // 3 + 1))
                for half in range(2):
                    n = 2 * t + half
                    if n >= 4:
                        pe.wait_ge(rows_placed, n - 3)
                    for k in range(4):
                        last = pe.transpose(g.ps[:, n % 4, k * P:k * P + rows(t)],
                                            ring[0:rows(t), t % 3, (4 * half + k) * P:(4 * half + k + 1) * P],
                                            g.c("ident")[0:rows(t), 0:rows(t)])
                    last.then_inc(rows_turned, 1)

        @block.vector
        def _(dve):
            for n in range(2 * TILES):
                t, half = n // 2, n % 2
                dve.wait_ge(rows_turned, n + 1)
                dve.tensor_copy(g.xt[:, 4 * half:4 * half + 4, t * P:t * P + rows(t)],
                                g.ps[:, n % 4, :].rearrange("p (k i) -> p k i", k=4)[:, :, 0:rows(t)]
                                ).then_inc(rows_placed, 1)


def stage_norm(g, which, tag, spill=False):
    with ExitStack() as st:
        spilled = g.sem(f"{tag}_spilled")
        sq = g.room(st, f"{tag}_sq", [P, 3, T])
        total = g.room(st, f"{tag}_total", [P, T])
        inverse = g.room(st, f"{tag}_inverse", [P, TILES])
        n_scalar, n_tensor, n_vector, n_gpsimd, _ = split_norm(g, which, tag, sq[:, :, :], total[:, :], inverse[:, :])
        block = st.enter_context(g.nc.Block())

        @block.sync
        def _(sp):
            if spill:
                for k in range(KD):
                    sp.dma_start(g.xt_spill[:, k, :], g.xt[:, k, :]).then_inc(spilled, 16)
                sp.wait_ge(spilled, 16 * KD)

        @block.scalar
        def _(act):
            for part in n_scalar:
                part(act)

        @block.tensor
        def _(pe):
            n_tensor(pe)

        @block.vector
        def _(dve):
            for part in n_vector:
                part(dve)

        @block.gpsimd
        def _(pool):
            n_gpsimd(pool)


def stage_index(g):
    nc = g.nc
    w_in, w_rounded, w_split = g.slot_sems("ix_weights", 2), g.sem("ix_rounded"), g.sem("ix_split")
    second_split, padded = g.sem("ix_second_split"), g.sem("ix_padded")
    w_pages, keys_doubled, lowered = g.sem("ix_pages"), g.sem("ix_doubled"), g.sem("ix_lowered")
    table_in, placed_rows = g.sem("ix_table"), g.sem("ix_row_ids")
    projected, copied = g.sem("ix_projected"), g.sem("ix_copied")
    stored = g.sem("ix_stored")
    scored, rectified, weighted = g.sem("ix_scored"), g.sem("ix_rectified"), g.sem("ix_weighted")
    pages_turned, pages_placed = g.sem("ix_turned"), g.sem("ix_placed")
    chain = g.sem("ix_chain")
    s_spread, s_ready, s_scored, s_rect, s_summed = (g.sem(f"ix_s_{n}") for n in
                                                     ("spread", "ready", "scored", "rect", "summed"))
    w_idx = g.ins["w_in_even"][0][:, IDX_COL:IDX_COL + IH * ID + ID + IH].rearrange("(k p) n -> p k n", p=P)
    WI = IH * ID + ID + IH
    LP = 5
    with ExitStack() as st:
        past = g.room(st, "ix_past", [P, NB, PAST])
        early = past[:, :, :].rearrange("p b n -> p (b n)")
        w = early[:, 0:2 * KD * P].rearrange("p (s n) -> p s n", s=2)
        wh = g.room(st, "ix_wh", [P, 2, KD * P], F32R)
        wl = g.room(st, "ix_wl", [P, 2, KD * P], F32R)
        odd_h, odd_l = (x[:, :, :].rearrange("p s n -> p (s n)")[:, 0:T] for x in (wh, wl))
        second = early[ID:2 * ID, 0:T]
        kwt = early[:, 2 * KD * P:2 * KD * P + T]
        qh = g.room(st, "ix_qh", [P, LP, T], F32R)
        ql = g.room(st, "ix_ql", [P, LP, T], F32R)
        new_keys = g.room(st, "ix_new_keys", [P, NS])
        kw = g.room(st, "ix_kw", [P, TILES, ID + IH])
        relu = g.room(st, "ix_relu", [P, 3, SEQ])
        pages = g.room(st, "ix_pg", [P, NB * NPAGE, 2, ID])
        qz = g.room(st, "ix_qz", [P, NB, 2, NT, NT])
        table = g.room(st, "ix_tab", [P, NB * NPAGE], I32)
        ids = g.room(st, "ix_ids", [P, NB * NPAGE], I32)
        relu_s = relu[:, 0:2, 0:KEYS]
        wcol = g.room(st, "ix_wcol", [P, 2, IH + 1])
        wsum = g.room(st, "ix_wsum", [P, 2, NS])
        block = st.enter_context(nc.Block())
        key_rows = g.ins["cache_kidx"][0].rearrange("n p d -> (n p) d")
        units = [(t, h) for t in range(2, SMP) for h in range(IH)]

        def width(m):
            return P if m < 4 else ID + IH

        @block.sync
        def _(sp):
            with nc.allow_non_contiguous_dma("short rows"):
                sp.dma_start(table[:, :], g.ins["page_table"].rearrange("b n -> (b n)").partition_broadcast(P)
                             ).then_inc(table_in, 16)
            for m in range(LP):
                if m >= 2:
                    sp.wait_ge(w_split, m - 1)
                sp.dma_start(w[:, m % 2, 0:KD * width(m)].rearrange("p (k n) -> p k n", k=KD),
                             w_idx[:, :, m * P:m * P + width(m)]).then_inc(w_in[m % 2], 16)
            sp.wait_ge(w_split, LP)
            sp.wait_ge(copied, LP)
            sp.dma_start(second, kwt[0:ID, :]).then_inc(keys_doubled, 16)
            sp.wait_ge(copied, LP + TILES)
            sp.dma_start(g.outs["kidx_prompt"][0, 0].rearrange("(t p) d -> p t d", p=P), kw[:, 0:SMP, 0:ID]
                         ).then_inc(stored, 16)
            sp.dma_start(g.outs["kidx_sample"][0].rearrange("b t d -> (b t) d"), kw[0:NS, SMP, 0:ID]
                         ).then_inc(stored, 16)
            sp.wait_ge(stored, 32)

        @block.gpsimd
        def _(pool):
            pool.memset(qz[:, :, :, :, :], 0.0).then_inc(placed_rows, 1)
            pool.wait_ge(table_in, 16)
            pool.tensor_scalar(ids[:, :], table[:, :], float(PAGE), g.c("page_row"), ALU.mult, ALU.add
                               ).then_inc(placed_rows, 1)
            pool.wait_ge(placed_rows, 2)
            for n in range(NB * NPAGE):
                for c in range(2):
                    pool.indirect_dma_start(out=pages[:, n, c, :], out_offset=None, in_=key_rows,
                                            in_offset=bass.IndirectOffsetOnAxis(ap=ids[:, n:n + 1], axis=0)
                                            ).then_inc(w_pages, 16)

        @block.tensor
        def _(pe):
            for m in range(LP):
                b0 = 4 * (m % 2)
                pe.wait_ge(w_split, m + 1)
                if m >= 2:
                    pe.wait_ge(lowered, m - 1)
                for k in range(KD):
                    cols = slice(k * width(m), (k + 1) * width(m))
                    last = split_passes(g, pe, b0, wh[:, m % 2, cols], wl[:, m % 2, cols], g.hh[:, k, :],
                                        g.hl[:, k, :], k == 0, k == KD - 1, width(m))
                last.then_inc(projected, 1)
            pe.wait_ge(lowered, LP)
            for t in range(TILES):
                if t >= 2:
                    pe.wait_ge(copied, LP + t - 1)
                pe.transpose(g.ps[0:rows(t), 3 + 4 * (t % 2), 0:ID + IH], kwt[0:ID + IH, t * P:t * P + rows(t)],
                             g.c("ident")[0:ID + IH, 0:ID + IH]).then_inc(projected, 1)
            pe.wait_ge(copied, LP + TILES)
            pe.wait_ge(second_split, 2)
            pe.wait_ge(padded, 2)
            for n, (t, h) in enumerate(units):
                if n >= 4:
                    pe.wait_ge(rectified, n - 3)
                keys = (t + 1) * P
                kh, kl = (qh[:, 4, :], ql[:, 4, :]) if h % 2 == 0 else (odd_h, odd_l)
                for c in range(-(-keys // 512)):
                    hi = min(keys, (c + 1) * 512)
                    for x, (queries, known) in enumerate(((qh, kh), (qh, kl), (ql, kh))):
                        last = pe.matmul(g.ps[:, 2 * (n % 4) + c, 0:hi - c * 512],
                                         queries[:, h // 2, t * P:(t + 1) * P], known[:, c * 512:hi],
                                         start=(x == 0), stop=(x == 2))
                last.then_inc(scored, 1)
            pe.wait_ge(w_pages, 16 * 2 * NB * NPAGE)
            pe.wait_ge(rectified, len(units))
            for b in range(NB):
                if b >= 4:
                    pe.wait_ge(pages_placed, b - 3)
                for p in range(NPAGE):
                    last = pe.transpose(g.ps[:, b % 4, p * P:(p + 1) * P],
                                        pages[:, b * NPAGE + p, :, :].rearrange("p c d -> p (c d)"), g.c("ident"))
                last.then_inc(pages_turned, 1)
            for q in range(2):
                last = pe.matmul(g.ps[:, 4 + q, 0:IH], g.c(f"row_idx{q}")[0:NS, :], kw[0:NS, SMP, ID:ID + IH],
                                 start=True, stop=True)
            last.then_inc(s_spread, 1)
            pe.wait_ge(s_ready, 1)
            for b in range(NB):
                band = slice(32 * (b % 4), 32 * (b % 4) + 32)
                lhs = qz[:, b, :, :, :].rearrange("p a h t -> p (a h t)")
                pe.matmul(g.ps[band, b // 4, :], lhs, past[:, b, :], start=True, stop=True)
                last = pe.matmul(g.ps[band, 2 + b // 4, 0:NS], lhs, new_keys[:, :], start=True, stop=True)
            last.then_inc(s_scored, 1)
            pe.wait_ge(s_rect, 2)
            for q in range(2):
                pe.matmul(g.ps[0:NS, 6, :], wsum[:, q, :], relu_s[:, q, 0:PAST], start=(q == 0), stop=(q == 1))
            for q in range(2):
                last = pe.matmul(g.ps[0:NS, 7, 0:NS], wsum[:, q, :], relu_s[:, q, PAST:KEYS],
                                 start=(q == 0), stop=(q == 1))
            last.then_inc(s_summed, 1)

        @block.scalar
        def _(act):
            def high(m):
                act.wait_ge(w_in[m % 2], 16 * (m // 2 + 1))
                if m >= 2:
                    act.wait_ge(projected, m - 1)
                act.copy(wh[:, m % 2, 0:KD * width(m)], w[:, m % 2, 0:KD * width(m)]).then_inc(w_rounded, 1)

            high(0)
            high(1)
            for m in range(LP):
                act.wait_ge(projected, m + 1)
                b0 = 4 * (m % 2)
                if m < 4:
                    act.activation(qh[:, m, :].rearrange("p (c n) -> p c n", c=3), g.ps[:, b0:b0 + 3, 0:THIRD],
                                   ACT.Copy, scale=ID ** -0.5).then_inc(copied, 1)
                else:
                    act.copy(qh[0:ID, 4, :].rearrange("p (c n) -> p c n", c=3), g.ps[0:ID, b0:b0 + 3, 0:THIRD])
                    act.copy(kwt[0:ID + IH, :].rearrange("p (c n) -> p c n", c=3),
                             g.ps[0:ID + IH, b0:b0 + 3, 0:THIRD]).then_inc(copied, 1)
                if m + 2 < LP:
                    high(m + 2)
            act.wait_ge(keys_doubled, 16)
            act.copy(odd_h[ID:2 * ID, :], second).then_inc(second_split, 1)
            for t in range(TILES):
                act.wait_ge(projected, LP + t + 1)
                act.copy(kw[0:rows(t), t, :], g.ps[0:rows(t), 3 + 4 * (t % 2), 0:ID + IH]).then_inc(copied, 1)
            for n, (t, h) in enumerate(units):
                act.wait_ge(scored, n + 1)
                if n >= 3:
                    act.wait_ge(weighted, n - 2)
                keys = (t + 1) * P
                two = g.ps[:, 2 * (n % 4):2 * (n % 4) + 2, :].rearrange("p c n -> p (c n)")
                act.activation(relu[:, n % 3, 0:keys], two[:, 0:keys], ACT.Relu).then_inc(rectified, 1)
            act.wait_ge(weighted, len(units))
            for q in range(2):
                act.wait_ge(s_scored, 1)
                act.activation(relu_s[:, q, 0:PAST], g.ps[:, q, :], ACT.Relu)
                act.activation(relu_s[:, q, PAST:KEYS], g.ps[:, 2 + q, 0:NS], ACT.Relu).then_inc(s_rect, 1)

        @block.vector
        def _(dve):
            done = [0]

            def link(op):
                done[0] += 1
                op.then_inc(chain, 1)
                dve.wait_ge(chain, done[0])

            def lower(m):
                r = slice(0, P if m < 4 else ID)
                dve.wait_ge(copied, m + 1)
                dve.scalar_tensor_tensor(out=ql[r, m, :].rearrange("p (c n) -> p c n", c=3),
                                         in0=g.ps[r, 4 * (m % 2):4 * (m % 2) + 3, 0:THIRD],
                                         scalar=ID ** -0.5 if m < 4 else 1.0,
                                         in1=qh[r, m, :].bitcast(F32).rearrange("p (c n) -> p c n", c=3),
                                         op0=ALU.mult, op1=ALU.subtract).then_inc(lowered, 1)

            dve.memset(qh[ID:2 * ID, 4, :].bitcast(F32), 0.0)
            dve.memset(ql[ID:2 * ID, 4, :].bitcast(F32), 0.0).then_inc(padded, 1)
            for m in range(LP):
                dve.wait_ge(w_rounded, m + 1)
                part = slice(0, KD * width(m))
                dve.tensor_tensor(wl[:, m % 2, part], w[:, m % 2, part], wh[:, m % 2, part].bitcast(F32), ALU.subtract
                                  ).then_inc(w_split, 1)
                if m >= 1:
                    lower(m - 1)
            lower(LP - 1)
            dve.memset(odd_h[0:ID, :].bitcast(F32), 0.0)
            dve.memset(odd_l[0:ID, :].bitcast(F32), 0.0).then_inc(padded, 1)
            dve.wait_ge(keys_doubled, 16)
            dve.wait_ge(second_split, 1)
            dve.tensor_tensor(odd_l[ID:2 * ID, :], second, odd_h[ID:2 * ID, :].bitcast(F32), ALU.subtract
                              ).then_inc(second_split, 1)
            dve.wait_ge(copied, LP + TILES)
            link(dve.tensor_scalar(kw[:, 0:SMP, ID:], kw[:, 0:SMP, ID:], IH ** -0.5, None, ALU.mult))
            for n, (t, h) in enumerate(units):
                keys = (t + 1) * P
                out = g.score[:, t - 2, 0:keys]
                wi = kw[:, t, ID + h:ID + h + 1]
                dve.wait_ge(rectified, n + 1)
                if h == 0:
                    dve.tensor_scalar(out, relu[:, n % 3, 0:keys], wi, None, ALU.mult).then_inc(weighted, 1)
                else:
                    dve.wait_ge(weighted, n)
                    dve.scalar_tensor_tensor(out=out, in0=relu[:, n % 3, 0:keys], scalar=wi, in1=out,
                                             op0=ALU.mult, op1=ALU.add).then_inc(weighted, 1)
                if h == IH - 1:
                    dve.wait_ge(weighted, n + 1)
                    link(dve.tensor_tensor(g.score[:, t - 2, keys - P:keys], g.score[:, t - 2, keys - P:keys],
                                           g.c("causal"), ALU.add))
            for b in range(NB):
                dve.wait_ge(pages_turned, b + 1)
                dve.tensor_copy(past[:, b, :], g.ps[:, b % 4, :]).then_inc(pages_placed, 1)
            dve.wait_ge(placed_rows, 1)
            for par in range(2):
                half = slice(64 * par, 64 * par + 64)
                for hh in range(4):
                    link(dve.tensor_tensor(qz[half, :, par, hh, :],
                                           qh[half, hh, SEQ:T].bitcast(F32).rearrange("p (b t) -> p b t", b=NB),
                                           ql[half, hh, SEQ:T].bitcast(F32).rearrange("p (b t) -> p b t", b=NB),
                                           ALU.add))
            dve.wait_ge(second_split, 2)
            for high, low in ((qh[:, 4, :], ql[:, 4, :]), (odd_h, odd_l)):
                part = slice(0, ID) if high is not odd_h else slice(ID, 2 * ID)
                link(dve.tensor_tensor(new_keys[part, :], high[part, SEQ:T].bitcast(F32), low[part, SEQ:T].bitcast(F32),
                                       ALU.add))
            dve.wait_ge(s_spread, 1)
            for q in range(2):
                link(dve.tensor_tensor(wcol[:, q, 0:IH], g.ps[:, 4 + q, 0:IH], g.c("head_idx"), ALU.mult))
                link(dve.tensor_reduce(wcol[:, q, IH:IH + 1], wcol[:, q, 0:IH], AX.X, ALU.add))
                link(dve.tensor_scalar(wsum[:, q, :], g.c(f"sum_idx{q}"), wcol[:, q, IH:IH + 1], IH ** -0.5,
                                       ALU.mult, ALU.mult))
            dve.wait_ge(pages_placed, NB)
            dve.wait_ge(copied, LP + TILES)
            dve.tensor_copy(wcol[:, 0, 0:1], wcol[:, 0, 1:2]).then_inc(s_ready, 1)
            dve.wait_ge(s_summed, 1)
            dve.tensor_copy(g.score_s[:, 0:PAST], g.ps[0:NS, 6, :])
            dve.tensor_tensor(g.score_s[:, PAST:KEYS], g.ps[0:NS, 7, 0:NS], g.c("new_ok")[0:NS, :], ALU.add)


def rounds(t):
    return -(-(TOPK if t < SMP else TOPK_S) // 8)


def chooser(g, dve, best, found, replaced):
    done = [0, 0]

    def choose(t, r0, r1):
        area = g.score[:, t - 2, 0:(t + 1) * P] if t < SMP else g.score_s[:, :]
        top = best[0:rows(t), :]
        want = TOPK if t < SMP else TOPK_S
        for r in range(r0, r1):
            dve.max(top, area).then_inc(found, 1)
            done[0] += 1
            dve.wait_ge(found, done[0])
            if want - 8 * r < 8:
                dve.memset(best[0:rows(t), want - 8 * r:8], 3e38).then_inc(found, 1)
                done[0] += 1
                dve.wait_ge(found, done[0])
            dve.match_replace(area, top, area, TAKEN).then_inc(replaced, 1)
            done[1] += 1
            dve.wait_ge(replaced, done[1])
        if r1 == rounds(t):
            dve.tensor_scalar(area, area, TAKEN, NEG, ALU.not_equal, ALU.mult)

    return choose


def stage_project_even(g):
    nc = g.nc
    projected, copied = g.sem("pe_projected"), g.sem("pe_copied")
    w_in, w_rounded, w_split = g.sem("pe_weights"), g.sem("pe_rounded"), g.sem("pe_split")
    stored = g.slot_sems("pe_stored", 4)
    found, replaced = g.sem("pe_found"), g.sem("pe_replaced")
    with ExitStack() as st:
        w = g.room(st, "pe_w", [P, KD, 512])
        wh = g.room(st, "pe_wh", [P, 2, KD, 512], F32R)
        wl = g.room(st, "pe_wl", [P, 2, KD, 512], F32R)
        out = g.room(st, "pe_out", [P, 4, 512])
        best = g.room(st, "pe_best", [P, 8])
        block = st.enter_context(nc.Block())

        @block.sync
        def _(sp):
            def load(m):
                sp.dma_start(w[:, :, :], g.ins["w_in_even"][0][:, m * 512:(m + 1) * 512]
                             .rearrange("(k p) n -> p k n", p=P)).then_inc(w_in, 16)

            load(0)
            for n in range(EVEN_TM * TILES):
                m, t = n // TILES, n % TILES
                if t == 0 and m + 1 < EVEN_TM:
                    sp.wait_ge(w_split, KD * (m + 1))
                    load(m + 1)
                sp.wait_ge(copied, n + 1)
                sp.dma_start(g.proj[m, t * P:t * P + rows(t), :], out[0:rows(t), n % 4, :]).then_inc(stored[n % 4], 16)
            for slot in range(4):
                sp.wait_ge(stored[slot], 16 * len(range(slot, EVEN_TM * TILES, 4)))

        @block.tensor
        def _(pe):
            for m in range(EVEN_TM):
                for t in range(TILES):
                    n = m * TILES + t
                    if n >= 8:
                        pe.wait_ge(copied, n - 7)
                    for k in range(KD):
                        if t == 0:
                            pe.wait_ge(w_split, KD * m + k + 1)
                        high, low = (h[:, k, t * P:t * P + rows(t)] for h in (g.hh, g.hl))
                        to = g.ps[0:rows(t), n % 8, :]
                        pe.matmul(to, high, wh[:, m % 2, k, :], start=(k == 0), stop=False)
                        pe.matmul(to, high, wl[:, m % 2, k, :], start=False, stop=False)
                        last = pe.matmul(to, low, wh[:, m % 2, k, :], start=False, stop=(k == KD - 1))
                    last.then_inc(projected, 1)

        @block.scalar
        def _(act):
            def high(m, k):
                if k == 0:
                    act.wait_ge(w_in, 16 * (m + 1))
                    if m >= 2:
                        act.wait_ge(projected, TILES * (m - 1))
                act.copy(wh[:, m % 2, k, :], w[:, k, :]).then_inc(w_rounded, 1)

            for k in range(KD):
                high(0, k)
            for n in range(EVEN_TM * TILES):
                m, t = n // TILES, n % TILES
                act.wait_ge(projected, n + 1)
                if n >= 4:
                    act.wait_ge(stored[n % 4], 16 * (n // 4))
                act.copy(out[0:rows(t), n % 4, :], g.ps[0:rows(t), n % 8, :]).then_inc(copied, 1)
                if t < KD and m + 1 < EVEN_TM:
                    high(m + 1, t)

        @block.gpsimd
        def _(pool):
            for n in range(EVEN_TM * KD):
                m, k = n // KD, n % KD
                pool.wait_ge(w_rounded, n + 1)
                pool.tensor_tensor(wl[:, m % 2, k, :], w[:, k, :], wh[:, m % 2, k, :].bitcast(F32), ALU.subtract
                                   ).then_inc(w_split, 1)

        @block.vector
        def _(dve):
            choose = chooser(g, dve, best, found, replaced)
            for t in range(3, SMP):
                choose(t, 0, rounds(t))


def stage_retention(g):
    nc = g.nc
    GROUP = 3
    heads_in, v_in = g.slot_sems("rt_qk_in", GROUP), g.slot_sems("rt_v_in", GROUP)
    state_in, g_in = g.sem("rt_state_in"), g.sem("rt_gate_in")
    zeroed, q_rotated, k_rotated = g.sem("rt_zeroed"), g.sem("rt_q_rotated"), g.sem("rt_k_rotated")
    q_chain, k_chain, out_copied, squared = (g.sem(f"rt_{n}") for n in ("q_chain", "k_chain", "out_copied", "squared"))
    turned, copied, scored, masked, made, state = (g.sem(f"rt_{n}") for n in
                                                   ("turned", "copied", "scored", "masked", "made", "state"))
    s_turned, s_copied, s_laid, s_scored, s_masked, s_made, s_out, s_kv, s_kv_read = (
        g.sem(f"rt_s_{n}") for n in ("turned", "copied", "laid", "scored", "masked", "made", "out", "kv", "kv_read"))
    gated, mixed, placed, state_out, chain = (g.sem(f"rt_{n}") for n in
                                              ("gated", "mixed", "placed", "state_out", "chain"))
    rms_ready, root_ready = g.sem("rt_rms"), g.sem("rt_root")
    found, replaced = g.sem("rt_found"), g.sem("rt_replaced")
    with ExitStack() as st:
        q = g.room(st, "rt_q", [P, TILES, 512])
        k = g.room(st, "rt_k", [P, TILES, 512])
        v = g.room(st, "rt_v", [P, TILES, 512])
        gate = g.room(st, "rt_gate", [P, TILES, 512])
        tmp = g.room(st, "rt_tmp", [P, 2, 2, 2, H * 64])
        waste = g.room(st, "rt_waste", [P, P])
        best = g.room(st, "rt_best", [P, 8])
        qr = g.room(st, "rt_qr", [P, 2, 512])
        kr = g.room(st, "rt_kr", [P, 2, 512])
        sr = g.room(st, "rt_sr", [P, 2, 512])
        R = g.room(st, "rt_state", [P, H, P])
        S0 = g.room(st, "rt_s0", [P, NB, H, P])
        qs = g.room(st, "rt_qs", [P, 2, H, NS])
        qz = g.room(st, "rt_qz", [P, H, NB, NS])
        ss = g.room(st, "rt_ss", [NS, H, NS])
        kb = g.room(st, "rt_kb", [NS, 2, 512])
        ms = g.room(st, "rt_ms", [P, TILES * H])
        tables = g.room(st, "rt_tables", [P, g.const_dram.shape[1] - g.kept])
        tables_in = g.sem("rt_tables_in")
        block = st.enter_context(nc.Block())
        ident = g.c("ident")

        def table(name):
            at, width = g.place[name]
            return tables[:, at - g.kept:at - g.kept + width]

        def src(m):
            return g.proj[m, 0:SEQ, :].rearrange("(c p) n -> p c n", p=P)

        def rotate(engine, which, link):
            buf, decay, done = ((q, "ret_q", q_rotated), (k, "ret_k", k_rotated))[which]
            cos = table("cos").rearrange("p (t i) -> p t i", t=TILES)
            sin = table("sin").rearrange("p (t i) -> p t i", t=TILES)
            scale = table(decay).rearrange("p (t h) -> p t h", h=H)

            def tile(t):
                n = t // GROUP
                engine.wait_ge(heads_in[n], 64 if n == 2 else 32)
                part = buf[:, t, :].rearrange("p (h s i) -> p h s i", h=H, s=2)
                cs, sn = spread(cos[:, t, :], 0, H), spread(sin[:, t, :], 0, H)
                first, second = part[:, :, 0, :], part[:, :, 1, :]
                up, down = (tmp[:, which, t % 2, x, :].rearrange("p (h i) -> p h i", h=H) for x in (0, 1))
                engine.tensor_tensor(up, first, sn, ALU.mult)
                link(engine.tensor_tensor(down, second, sn, ALU.mult))
                engine.tensor_tensor(first, first, cs, ALU.mult)
                link(engine.tensor_tensor(second, second, cs, ALU.mult))
                engine.tensor_tensor(first, first, down, ALU.subtract)
                link(engine.tensor_tensor(second, second, up, ALU.add))
                whole = buf[:, t, :].rearrange("p (h d) -> p h d", h=H)
                engine.tensor_tensor(whole, whole, spread(scale[:, t, :], 1, P), ALU.mult).then_inc(done, 1)
            return tile

        @block.sync
        def _(sp):
            def load(buf, m, n, arrived):
                hi = min(GROUP * n + GROUP, SMP)
                sp.dma_start(buf[:, GROUP * n:hi, :], src(m)[:, GROUP * n:hi, :]).then_inc(arrived, 16)
                if n == 2:
                    sp.dma_start(buf[0:NS, SMP, :], g.proj[m, SEQ:T, :]).then_inc(arrived, 16)

            sp.dma_start(tables[:, :], g.const_dram[:, g.kept:]).then_inc(tables_in, 16)
            sp.wait_ge(zeroed, 4)
            for n in range(3):
                load(q, 0, n, heads_in[n])
                load(k, 1, n, heads_in[n])
                load(v, 2, n, v_in[n])
            sp.dma_start(S0[:, :, :, :], g.ins["state_ret"][0].rearrange("b h d e -> d b h e")).then_inc(state_in, 16)
            for n in range(3):
                load(gate, 3, n, g_in)
            sp.wait_ge(state, SMP)
            sp.dma_start(g.outs["ret_prompt"][0, 0].rearrange("h d e -> d h e"), R[:, :, :]).then_inc(state_out, 16)
            sp.wait_ge(s_kv_read, NB + 1)
            sp.dma_start(g.outs["ret_sample"][0].rearrange("b h d e -> d b h e"), S0[:, :, :, :]).then_inc(state_out, 16)
            sp.wait_ge(state_out, 32)

        @block.gpsimd
        def _(pool):
            done = [0]

            def link(op):
                done[0] += 1
                op.then_inc(k_chain, 1)
                pool.wait_ge(k_chain, done[0])

            for buf in (q, k, v, gate):
                pool.memset(buf[:, SMP, :], 0.0).then_inc(zeroed, 1)
            pool.wait_ge(tables_in, 16)
            rotate_keys = rotate(pool, 1, link)
            for t in range(TILES):
                rotate_keys(t)
            pool.wait_ge(k_rotated, TILES)
            for b in range(NB):
                if b >= 2:
                    pool.wait_ge(s_kv, b - 1)
                pool.tensor_scalar(kb[:, b % 2, :], k[0:NS, SMP, :], g.c("seq_of")[0:NS, b:b + 1], None, ALU.mult
                                   ).then_inc(s_made, 1)

        @block.tensor
        def _(pe):
            def turn(c):
                pe.wait_ge(q_rotated, c + 1)
                pe.wait_ge(k_rotated, c + 1)
                if c >= 2:
                    pe.wait_ge(copied, 2 * (c - 1))
                for n, buf in enumerate((q, k)):
                    for h in range(H):
                        last = pe.transpose(g.ps[:, 2 * n + c % 2, h * P:(h + 1) * P],
                                            buf[:, c, h * P:(h + 1) * P], ident)
                last.then_inc(turned, 1)

            turn(0)
            for c in range(SMP):
                if c % GROUP == 0:
                    pe.wait_ge(v_in[c // GROUP], 32 if c // GROUP == 2 else 16)
                if c + 1 < SMP:
                    turn(c + 1)
                pe.wait_ge(copied, 2 * (c + 1))
                if c >= 1:
                    pe.wait_ge(masked, c)
                for h in range(H):
                    cols = slice(h * P, (h + 1) * P)
                    last = pe.matmul(g.ps[:, 4, cols], kr[:, c % 2, cols], qr[:, c % 2, cols], start=True, stop=True)
                last.then_inc(scored, 1)
                pe.wait_ge(masked, c + 1)
                if c >= 1:
                    pe.wait_ge(state, c)
                for h in range(H):
                    cols = slice(h * P, (h + 1) * P)
                    pe.matmul(g.ps[:, 5, cols], sr[:, c % 2, cols], v[:, c, cols], start=True, stop=(c == 0))
                    if c >= 1:
                        pe.matmul(g.ps[:, 5, cols], qr[:, c % 2, cols], R[:, h, :], start=False, stop=True)
                for h in range(H):
                    cols = slice(h * P, (h + 1) * P)
                    last = pe.matmul(g.ps[:, 6, cols], k[:, c, cols], v[:, c, cols], start=True, stop=True)
                last.then_inc(made, 1)
            pe.wait_ge(copied, 2 * SMP)
            pe.wait_ge(q_rotated, TILES)
            pe.wait_ge(k_rotated, TILES)
            for n, buf in enumerate((q, k)):
                for h in range(H):
                    last = pe.transpose(g.ps[:, n, h * NS:(h + 1) * NS], buf[0:NS, SMP, h * P:(h + 1) * P],
                                        ident[0:NS, 0:NS])
            last.then_inc(s_turned, 1)
            pe.wait_ge(s_copied, 2)
            for h in range(H):
                last = pe.matmul(g.ps[0:NS, 2, h * NS:(h + 1) * NS], qs[:, 1, h, :], qs[:, 0, h, :],
                                 start=True, stop=True)
            last.then_inc(s_scored, 1)
            pe.wait_ge(s_masked, 1)
            pe.wait_ge(s_laid, 1)
            pe.wait_ge(state_in, 16)
            for h in range(H):
                cols = slice(h * P, (h + 1) * P)
                pe.matmul(g.ps[0:NS, 3, cols], ss[:, h, :], v[0:NS, SMP, cols], start=True, stop=False)
                for b in range(NB):
                    last = pe.matmul(g.ps[0:NS, 3, cols], qz[:, h, b, :], S0[:, b, h, :],
                                     start=False, stop=(b == NB - 1))
            last.then_inc(s_out, 1)
            pe.wait_ge(state, SMP)
            for b in range(NB):
                pe.wait_ge(s_made, b + 1)
                if b >= 2:
                    pe.wait_ge(s_kv_read, b - 1)
                for h in range(H):
                    cols = slice(h * P, (h + 1) * P)
                    last = pe.matmul(g.ps[:, 4 + b % 2, cols], kb[:, b % 2, cols], v[0:NS, SMP, cols],
                                     start=True, stop=True)
                last.then_inc(s_kv, 1)
            for t in range(TILES):
                pe.wait_ge(mixed, t + 1)
                if t >= 4:
                    pe.wait_ge(placed, t - 3)
                for h in range(H):
                    last = pe.transpose(g.ps[:, t % 4, h * P:h * P + rows(t)], q[0:rows(t), t, h * P:(h + 1) * P],
                                        ident[0:rows(t), 0:rows(t)])
                last.then_inc(gated, 1)

        @block.scalar
        def _(act):
            def squares(c):
                act.wait_ge(out_copied, c + 1)
                for h in range(H):
                    act.activation(waste[:, :], q[:, c, h * P:(h + 1) * P], ACT.Square,
                                   accum_out=ms[:, c * H + h:c * H + h + 1]).then_inc(squared, 1)
                    act.wait_ge(squared, c * H + h + 1)

            for c in range(SMP):
                act.wait_ge(turned, c + 1)
                if c >= 2:
                    act.wait_ge(made, c - 1)
                act.copy(qr[:, c % 2, :], g.ps[:, c % 2, :]).then_inc(copied, 1)
                act.copy(kr[:, c % 2, :], g.ps[:, 2 + c % 2, :]).then_inc(copied, 1)
                if c >= 2:
                    squares(c - 2)
            act.wait_ge(s_turned, 1)
            for n in range(2):
                act.copy(qs[:, n, :, :].rearrange("p h t -> p (h t)"), g.ps[:, n, 0:H * NS]).then_inc(s_copied, 1)
            for c in range(SMP - 2, TILES):
                squares(c)
            act.wait_ge(rms_ready, 1)
            act.activation(ms[:, :], ms[:, :], ACT.Sqrt).then_inc(root_ready, 1)
            act.wait_ge(g_in, 64)
            act.activation(gate[:, :, :], gate[:, :, :], ACT.Silu).then_inc(root_ready, 1)
            for t in range(TILES):
                act.wait_ge(gated, t + 1)
                act.copy(g.ht[:, 0:H, t * P:t * P + rows(t)],
                         g.ps[:, t % 4, :].rearrange("p (h i) -> p h i", h=H)[:, :, 0:rows(t)]).then_inc(placed, 1)

        @block.vector
        def _(dve):
            done = [0]

            def link(op):
                done[0] += 1
                op.then_inc(chain, 1)
                dve.wait_ge(chain, done[0])

            choose = chooser(g, dve, best, found, replaced)
            choose(2, ROUNDS_2[0], ROUNDS_2[1])
            dve.wait_ge(tables_in, 16)
            dve.wait_ge(zeroed, 4)
            rotate_queries = rotate(dve, 0, link)
            for t in range(2):
                rotate_queries(t)
            upper = spread(g.c("upper"), 0, H)
            for c in range(SMP):
                dve.wait_ge(scored, c + 1)
                dve.tensor_tensor(sr[:, c % 2, :].rearrange("p (h i) -> p h i", h=H),
                                  g.ps[:, 4, :].rearrange("p (h i) -> p h i", h=H), upper, ALU.mult
                                  ).then_inc(masked, 1)
                if c + 2 < TILES:
                    rotate_queries(c + 2)
                dve.wait_ge(made, c + 1)
                dve.tensor_copy(q[:, c, :], g.ps[:, 5, :]).then_inc(out_copied, 1)
                kv = g.ps[:, 6, :].rearrange("p (h e) -> p h e", h=H)
                step = spread(table("ret_step"), 1, P)
                if c == 0:
                    dve.tensor_tensor(R[:, :, :], kv, step, ALU.mult).then_inc(state, 1)
                else:
                    link(dve.tensor_tensor(R[:, :, :], kv, R[:, :, :], ALU.add))
                    dve.tensor_tensor(R[:, :, :], R[:, :, :], step, ALU.mult).then_inc(state, 1)
            dve.wait_ge(s_copied, 2)
            col = g.c("col_seq").rearrange("p (b t) -> p b t", b=NB)
            for h in range(H):
                last = dve.tensor_tensor(qz[:, h, :, :], spread(qs[:, 0, h, :], 0, NB), col, ALU.mult)
            last.then_inc(s_laid, 1)
            dve.wait_ge(s_scored, 1)
            dve.tensor_tensor(ss[:, :, :], g.ps[0:NS, 2, 0:H * NS].rearrange("p (h i) -> p h i", h=H),
                              spread(g.c("upper_s")[0:NS, :], 0, H), ALU.mult).then_inc(s_masked, 1)
            dve.wait_ge(s_out, 1)
            dve.tensor_copy(q[0:NS, SMP, :], g.ps[0:NS, 3, :]).then_inc(out_copied, 1)
            for b in range(NB):
                dve.wait_ge(s_kv, b + 1)
                dve.tensor_tensor(S0[:, b, :, :].rearrange("p h e -> p (h e)"), g.ps[:, 4 + b % 2, :],
                                  S0[:, b, :, :].rearrange("p h e -> p (h e)"), ALU.add).then_inc(s_kv_read, 1)
                if b < ROUNDS_2[2] - ROUNDS_2[1]:
                    choose(2, ROUNDS_2[1] + b, ROUNDS_2[1] + b + 1)
            dve.wait_ge(s_kv_read, NB)
            dve.tensor_tensor(S0[:, :, :, :], S0[:, :, :, :],
                              spread(spread(table("ret_step_s"), 0, NB), 2, P), ALU.mult).then_inc(s_kv_read, 1)
            dve.wait_ge(squared, TILES * H)
            dve.tensor_scalar(ms[:, :], ms[:, :], 1.0 / P, EPS, ALU.mult, ALU.add).then_inc(rms_ready, 1)
            dve.wait_ge(root_ready, 1)
            link(dve.reciprocal(ms[:, :], ms[:, :]))
            dve.wait_ge(root_ready, 2)
            dve.wait_ge(out_copied, TILES)
            for t in range(TILES):
                heads = q[:, t, :].rearrange("p (h e) -> p h e", h=H)
                link(dve.tensor_tensor(heads, heads, spread(ms[:, t * H:(t + 1) * H], 1, P), ALU.mult))
                dve.tensor_tensor(q[:, t, :], q[:, t, :], gate[:, t, :], ALU.mult).then_inc(mixed, 1)


def stage_attention_prep(g):
    nc = g.nc
    zeroed, q_in, k_in, v_in, small_in = (g.sem(f"ap_{n}") for n in ("zeroed", "q_in", "k_in", "v_in", "small_in"))
    squared, gain_ready = g.sem("ap_squared"), g.sem("ap_gain")
    found, replaced = g.sem("ap_found"), g.sem("ap_replaced")
    rms, root, chain = g.sem("ap_rms"), g.sem("ap_root"), g.sem("ap_chain")
    normed_q, normed_k, stored = g.sem("ap_normed_q"), g.sem("ap_normed_k"), g.sem("ap_stored")
    turned, placed = g.sem("ap_turned"), g.sem("ap_placed")
    bias_made, bias_read, bias_out, hank_in = (g.sem(f"ap_bias_{n}") for n in ("made", "read", "out", "in"))
    with ExitStack() as st:
        q = g.room(st, "ap_q", [P, TILES, 512])
        k = g.room(st, "ap_k", [P, TILES, 512])
        sq = g.room(st, "ap_sq", [P, TILES, 512])
        ms = g.room(st, "ap_ms", [P, 2, TILES * H])
        waste = g.room(st, "ap_waste", [P, P])
        best = g.room(st, "ap_best", [P, 8])
        q_gain = g.room(st, "ap_q_gain", [P, 1])
        k_gain = g.room(st, "ap_k_gain", [P, P])
        rb = g.room(st, "ap_rb", [32, H])
        row = g.room(st, "ap_row", [H, 384])
        block = st.enter_context(nc.Block())
        jobs = [(which, t) for which in (1, 0) for t in range(TILES)]

        @block.sync
        def _(sp):
            with nc.allow_non_contiguous_dma("small tables"):
                sp.dma_start(rb[:, :], g.ins["rel_bias"]).then_inc(small_in, 16)
                sp.dma_start(q_gain[:, :], g.ins["q_norm"][0].rearrange("(p o) -> p o", o=1)).then_inc(small_in, 16)
                sp.dma_start(k_gain[:, :], g.ins["k_norm"][0].partition_broadcast(P)).then_inc(small_in, 16)
            sp.wait_ge(zeroed, 3)
            for buf, m, s in ((k, 5, k_in), (q, 4, q_in), (g.va, 6, v_in)):
                sp.dma_start(buf[:, 0:SMP, :], g.proj[m, 0:SEQ, :].rearrange("(c p) n -> p c n", p=P)).then_inc(s, 16)
                sp.dma_start(buf[0:NS, SMP, :], g.proj[m, SEQ:T, :]).then_inc(s, 16)
            sp.wait_ge(bias_read, 1)
            sp.dma_start(g.bias_row, row[:, :]).then_inc(bias_out, 16)
            sp.wait_ge(bias_out, 16)
            sp.dma_start(g.hank[:, :, :], bass.AP(g.bias_row.tensor, 0, [[1, P], [384, H], [1, 256]])
                         ).then_inc(hank_in, 16)
            sp.wait_ge(v_in, 32)
            for buf, name, s in ((g.va, "v", None), (k, "k", normed_k)):
                if s is not None:
                    sp.wait_ge(s, 1)
                sp.dma_start(g.outs[f"{name}_prompt"][0, 0].rearrange("(c p) h d -> p c (h d)", p=P),
                             buf[:, 0:SMP, :]).then_inc(stored, 16)
                sp.dma_start(g.outs[f"{name}_sample"][0].rearrange("b t h d -> (b t) (h d)"),
                             buf[0:NS, SMP, :]).then_inc(stored, 16)
            sp.wait_ge(stored, 64)
            sp.wait_ge(hank_in, 16)

        @block.gpsimd
        def _(pool):
            for buf in (q, k, g.va):
                pool.memset(buf[:, SMP, :], 0.0).then_inc(zeroed, 1)

        @block.tensor
        def _(pe):
            pe.wait_ge(small_in, 48)
            pe.matmul(g.ps[0:H, 7, 0:384], rb[:, :], g.c("bias_p")[0:32, :], start=True, stop=True
                      ).then_inc(bias_made, 1)
            pe.wait_ge(normed_k, 1)
            for n, (which, t) in enumerate(jobs):
                if which == 0:
                    pe.wait_ge(normed_q, t // 3 + 1)
                if n >= 4:
                    pe.wait_ge(placed, n - 3)
                for h in range(H):
                    last = pe.transpose(g.ps[:, n % 4, h * P:h * P + rows(t)],
                                        (q, k)[which][0:rows(t), t, h * P:(h + 1) * P],
                                        g.c("ident")[0:rows(t), 0:rows(t)])
                last.then_inc(turned, 1)

        @block.scalar
        def _(act):
            act.wait_ge(bias_made, 1)
            act.copy(row[:, :], g.ps[0:H, 7, 0:384]).then_inc(bias_read, 1)
            act.wait_ge(q_in, 32)
            act.wait_ge(zeroed, 3)
            for n in range(TILES * H):
                t, h = n // H, n % H
                act.activation(waste[:, :], q[:, t, h * P:(h + 1) * P], ACT.Square, accum_out=ms[:, 1, n:n + 1]
                               ).then_inc(squared, 1)
                act.wait_ge(squared, n + 1)
            for n in range(2):
                act.wait_ge(rms, n + 1)
                act.activation(ms[:, n, :], ms[:, n, :], ACT.Sqrt).then_inc(root, 1)
            act.wait_ge(gain_ready, 1)
            for n, (which, t) in enumerate(jobs):
                act.wait_ge(turned, n + 1)
                act.activation((g.qt, g.kt)[which][:, :, t * P:t * P + rows(t)],
                               g.ps[:, n % 4, :].rearrange("p (h i) -> p h i", h=H)[:, :, 0:rows(t)], ACT.Copy,
                               scale=(q_gain[:, 0:1], 1.0)[which]).then_inc(placed, 1)

        @block.vector
        def _(dve):
            done = [0]

            def link(op):
                done[0] += 1
                op.then_inc(chain, 1)
                dve.wait_ge(chain, done[0])

            dve.wait_ge(zeroed, 3)
            dve.wait_ge(small_in, 48)
            dve.tensor_scalar(q_gain[:, :], q_gain[:, :], P ** -0.5, None, ALU.mult).then_inc(gain_ready, 1)
            sv, kv = (x[:, :, :].rearrange("p t (h e) -> p (t h) e", h=H) for x in (sq, k))
            choose = chooser(g, dve, best, found, replaced)
            choose(2, ROUNDS_2[2], ROUNDS_2[3])
            dve.wait_ge(k_in, 32)
            link(dve.tensor_tensor(sv, kv, kv, ALU.mult))
            link(dve.tensor_reduce(ms[:, 0, :], sv, AX.X, ALU.add))
            dve.tensor_scalar(ms[:, 0, :], ms[:, 0, :], 1.0 / P, EPS, ALU.mult, ALU.add).then_inc(rms, 1)
            dve.wait_ge(squared, TILES * H)
            dve.tensor_scalar(ms[:, 1, :], ms[:, 1, :], 1.0 / P, EPS, ALU.mult, ALU.add).then_inc(rms, 1)
            dve.wait_ge(root, 1)
            link(dve.reciprocal(ms[:, 0, :], ms[:, 0, :]))
            link(dve.tensor_tensor(kv, kv, spread(ms[:, 0, :], 1, P), ALU.mult))
            dve.tensor_tensor(kv, kv, spread(k_gain[:, :], 0, TILES * H), ALU.mult).then_inc(normed_k, 1)
            dve.wait_ge(root, 2)
            link(dve.reciprocal(ms[:, 1, :], ms[:, 1, :]))
            for t0 in range(0, TILES, 3):
                part = q[:, t0:t0 + 3, :].rearrange("p t (h e) -> p (t h) e", h=H)
                dve.tensor_tensor(part, part, spread(ms[:, 1, t0 * H:(t0 + 3) * H], 1, P), ALU.mult).then_inc(normed_q, 1)
            choose(2, ROUNDS_2[3], ROUNDS_2[4])


def page_slot(name, b):
    return (b if name == "cache_k" else NB + b) % HELD


def gather_pages(g, pool, name, b, arrived):
    slot = page_slot(name, b)
    for p in range(NPAGE):
        n = b * NPAGE + p
        pool.indirect_dma_start(out=g.pages[:, slot, p, :], out_offset=None,
                                in_=g.ins[name][0].rearrange("n p h d -> (n p) (h d)"),
                                in_offset=bass.IndirectOffsetOnAxis(ap=g.ids[:, n:n + 1], axis=0)
                                ).then_inc(arrived, 16)


def stage_attention_prompt(g):
    nc = g.nc
    logits, summed, negated, powered, total, scaled = (g.sem(f"at_{n}") for n in
                                                       ("logits", "masked", "negated", "powered", "total", "scaled"))
    turned, copied, made, placed = (g.sem(f"at_{n}") for n in ("turned", "copied", "made", "placed"))
    found, replaced = g.sem("at_found"), g.sem("at_replaced")
    units = [(t, h) for t in range(SMP) for h in range(H)]
    FIRST = len(units) - rounds(SMP) - 1
    with ExitStack() as st:
        best = g.room(st, "at_best", [P, 8])
        lg = g.room(st, "at_logits", [P, 3, SEQ])
        pt = g.room(st, "at_probs_t", [P, 2, SMP, P])
        near = g.room(st, "at_near", [P, 2 * P])
        stat = g.room(st, "at_stat", [P, 3, 4])
        table = g.room(st, "at_tab", [P, NB * NPAGE], I32)
        block = st.enter_context(nc.Block())
        near_ready, table_in, ids_ready = g.sem("at_near"), g.sem("at_table"), g.sem("at_ids")
        g.k_in = g.slot_sems("at_k_in", NB)

        def banks(n):
            return sum(-(-(t + 1) // 4) for t, h in units[:n])

        @block.sync
        def _(sp):
            with nc.allow_non_contiguous_dma("a small table"):
                sp.dma_start(table[:, :], g.ins["page_table"].rearrange("b n -> (b n)").partition_broadcast(P)
                             ).then_inc(table_in, 16)

        @block.gpsimd
        def _(pool):
            pool.wait_ge(table_in, 16)
            pool.tensor_scalar(g.ids[:, :], table[:, :], float(PAGE), g.c("page_row"), ALU.mult, ALU.add
                               ).then_inc(ids_ready, 1)
            pool.wait_ge(ids_ready, 1)
            for b in range(HELD):
                gather_pages(g, pool, "cache_k", b, g.k_in[b])

        def spans(keys):
            return [(c, c * 512, min(keys, (c + 1) * 512)) for c in range(-(-keys // 512))]

        @block.tensor
        def _(pe):
            def logit(n):
                t, h = units[n]
                b0 = 2 * (n % 2)
                if n >= 2:
                    pe.wait_ge(summed, n - 1)
                for c, lo, hi in spans((t + 1) * P):
                    blocks = [(j, x) for j, x in ((t - 1, 0), (t, 1)) if lo <= j * P < hi and j >= 0]
                    for x, (j, which) in enumerate(blocks):
                        pe.matmul(g.ps[:, b0 + c, j * P - lo:(j + 1) * P - lo], g.c("flip"),
                                  g.hank[:, h, which * P:(which + 1) * P], start=(x == 0), stop=False,
                                  skip_group_check=True)
                    last = pe.matmul(g.ps[:, b0 + c, 0:hi - lo], g.qt[:, h, t * P:(t + 1) * P], g.kt[:, h, lo:hi],
                                     start=not blocks, stop=True, skip_group_check=True)
                last.then_inc(logits, 1)

            def turn(n, m):
                t, h = units[n]
                pe.wait_ge(scaled, n + 1)
                for j0 in range(0, t + 1, 4):
                    if m >= 2:
                        pe.wait_ge(copied, m - 1)
                    for j in range(j0, min(j0 + 4, t + 1)):
                        last = pe.transpose(g.ps[:, 4 + m % 2, (j - j0) * P:(j - j0 + 1) * P],
                                            lg[:, n % 3, j * P:(j + 1) * P], g.c("ident"))
                    last.then_inc(turned, 1)
                    m += 1

            def values(n):
                t, h = units[n]
                if n >= 2:
                    pe.wait_ge(placed, n - 1)
                pe.wait_ge(copied, banks(n + 1))
                for j in range(t + 1):
                    last = pe.matmul(g.ps[:, 6 + n % 2, 0:P], g.va[:, j, h * P:(h + 1) * P], pt[:, n % 2, j, :],
                                     start=(j == 0), stop=(j == t))
                last.then_inc(made, 1)

            logit(0)
            for n in range(len(units) + 2):
                if n + 1 < len(units):
                    logit(n + 1)
                if n >= 2:
                    values(n - 2)
                if 1 <= n <= len(units):
                    turn(n - 1, banks(n - 1))

        @block.scalar
        def _(act):
            def drain(n, m):
                t, h = units[n]
                if n >= 2:
                    act.wait_ge(made, n - 1)
                for j0 in range(0, t + 1, 4):
                    nb = min(4, t + 1 - j0)
                    act.wait_ge(turned, m + 1)
                    act.copy(pt[:, n % 2, j0:j0 + nb, :].rearrange("p j i -> p (j i)"), g.ps[:, 4 + m % 2, 0:nb * P]
                             ).then_inc(copied, 1)
                    m += 1

            for n in range(len(units) + 1):
                if n < len(units):
                    keys = (units[n][0] + 1) * P
                    act.wait_ge(negated, n + 1)
                    act.activation(lg[:, n % 3, 0:keys], lg[:, n % 3, 0:keys], ACT.Exp, bias=stat[:, n % 3, 1:2],
                                   accum_out=stat[:, n % 3, 2:3]).then_inc(powered, 1)
                if n >= 1:
                    drain(n - 1, banks(n - 1))

        @block.vector
        def _(dve):
            dve.memset(near[:, 0:P], 0.0).then_inc(near_ready, 1)
            dve.tensor_copy(near[:, P:2 * P], g.c("causal")).then_inc(near_ready, 1)
            dve.wait_ge(near_ready, 2)

            def mask(n):
                t, h = units[n]
                keys = (t + 1) * P
                chosen = near[:, P:] if t == 0 else near[:, :] if t == 1 else g.score[:, t - 2, 0:keys]
                two = g.ps[:, 2 * (n % 2):2 * (n % 2) + 2, :].rearrange("p c n -> p (c n)")[:, 0:keys]
                dve.wait_ge(logits, n + 1)
                if n >= 3:
                    dve.wait_ge(turned, banks(n - 2))
                dve.tensor_tensor_reduce(lg[:, n % 3, 0:keys], two, chosen, 1.0, -3e38, ALU.add, ALU.max,
                                         stat[:, n % 3, 0:1]).then_inc(summed, 1)
                dve.wait_ge(summed, n + 1)
                dve.tensor_scalar(stat[:, n % 3, 1:2], stat[:, n % 3, 0:1], -1.0, None, ALU.mult
                                  ).then_inc(negated, 1)

            def finish(n):
                keys = (units[n][0] + 1) * P
                dve.wait_ge(powered, n + 1)
                dve.reciprocal(stat[:, n % 3, 3:4], stat[:, n % 3, 2:3]).then_inc(total, 1)
                dve.wait_ge(total, n + 1)
                dve.tensor_scalar(lg[:, n % 3, 0:keys], lg[:, n % 3, 0:keys], stat[:, n % 3, 3:4], None, ALU.mult
                                  ).then_inc(scaled, 1)

            def place(n):
                t, h = units[n]
                dve.wait_ge(made, n + 1)
                dve.tensor_copy(g.ht[:, H + h, t * P:(t + 1) * P], g.ps[:, 6 + n % 2, 0:P]).then_inc(placed, 1)

            choose = chooser(g, dve, best, found, replaced)
            for n in range(len(units) + 2):
                if n < len(units):
                    mask(n)
                if FIRST <= n < FIRST + rounds(SMP):
                    choose(SMP, n - FIRST, n - FIRST + 1)
                if 1 <= n <= len(units):
                    finish(n - 1)
                if n >= 2:
                    place(n - 2)


def stage_attention_sample(g):
    nc = g.nc
    cleared, rb_in = g.sem("as_cleared"), g.sem("as_rb_in")
    k_in, v_in = g.k_in, g.slot_sems("as_v_in", NB)
    laid, turned, placed, logits = (g.sem(f"as_{n}") for n in ("laid", "turned", "placed", "logits"))
    masked, negated, powered, scaled = (g.sem(f"as_{n}") for n in ("masked", "negated", "powered", "scaled"))
    p_turned, p_placed, made, chain = (g.sem(f"as_{n}") for n in ("p_turned", "p_placed", "made", "chain"))
    ptz_cleared, out_read, out_turned = g.sem("as_ptz_cleared"), g.sem("as_out_read"), g.sem("as_out_turned")
    with ExitStack() as st:
        kts = g.room(st, "as_kt", [P, 2, H, PAST])
        qz = g.room(st, "as_qz", [P, NB, H, 2, H, NT])
        rb = g.room(st, "as_rb", [P, H])
        rbt = g.room(st, "as_rbt", [P, NB, H, NT])
        lg = g.room(st, "as_logits", [P, KEYS])
        ptn = g.room(st, "as_ptn", [NS, P])
        ptz = kts[:, :, :, :].rearrange("p a h n -> p (a h n)").rearrange("p (b c r) -> p b c r", b=NB, c=NPAGE)
        ptz_own = bass.AP(ptz.tensor, ptz.offset, [list(ptz.ap[0]), [NPAGE * P + H * NT, NB], [P, NPAGE],
                                                   [1, H * NT]])
        ov = g.room(st, "as_out", [P, 512])
        stat = g.room(st, "as_stat", [P, 4])
        block = st.enter_context(nc.Block())

        @block.sync
        def _(sp):
            with nc.allow_non_contiguous_dma("small tables"):
                for t in range(NT):
                    sp.dma_start(rb[32 * t:32 * t + 32, :], g.ins["rel_bias"]).then_inc(rb_in, 16)

        @block.gpsimd
        def _(pool):
            pool.memset(qz[:, :, :, :, :, :], 0.0).then_inc(cleared, 1)
            for n in range(HELD, 2 * NB):
                before = n - HELD
                if before < NB:
                    pool.wait_ge(turned, H * (before + 1))
                else:
                    pool.wait_ge(made, before - NB + 1)
                if n < NB:
                    gather_pages(g, pool, "cache_k", n, k_in[n])
                else:
                    gather_pages(g, pool, "cache_v", n - NB, v_in[n - NB])

        @block.tensor
        def _(pe):
            pe.wait_ge(laid, 1)
            for (bank, lo, hi) in ((4, 0, PAST), (5, PAST, KEYS)):
                pe.matmul(g.ps[:, bank, 0:hi - lo], rbt[:, :, :, :].rearrange("p b h t -> p (b h t)"),
                          g.c("bias_s")[:, lo:hi], start=True, stop=False, skip_group_check=True)
                pe.matmul(g.ps[:, bank, 0:hi - lo], g.c("row_bht")[0:NS, :], g.score_s[:, lo:hi],
                          start=False, stop=False, skip_group_check=True)
            for b in range(NB):
                pe.wait_ge(k_in[b], 16 * NPAGE)
                for h in range(H):
                    n = b * H + h
                    if n >= 4:
                        pe.wait_ge(placed, n - 3)
                    for p in range(NPAGE):
                        last = pe.transpose(g.ps[:, n % 4, p * P:(p + 1) * P],
                                            g.pages[:, page_slot("cache_k", b), p, h * P:(h + 1) * P], g.c("ident"))
                    last.then_inc(turned, 1)
                band = slice(32 * (b // 2), 32 * (b // 2) + 32)
                pe.wait_ge(placed, H * (b + 1))
                for h in range(H):
                    lhs = qz[:, b, h, :, :, :].rearrange("p a h t -> p (a h t)")
                    pe.matmul(g.ps[band, 4, :], lhs, kts[:, b % 2, h, :], start=False, stop=(b == NB - 1 and h == 3),
                              skip_group_check=True)
                    last = pe.matmul(g.ps[band, 5, 0:NS], lhs, g.kt[:, h, SEQ:T], start=False,
                                     stop=(b == NB - 1 and h == 3), skip_group_check=True)
                last.then_inc(logits, 1)
            pe.wait_ge(scaled, 1)
            for c in range(NPAGE):
                pe.transpose(g.ps[:, 6, c * P:(c + 1) * P], lg[:, c * P:(c + 1) * P], g.c("ident"))
            pe.transpose(g.ps[0:NS, 7, 0:P], lg[:, PAST:KEYS], g.c("ident")).then_inc(p_turned, 1)
            pe.wait_ge(p_placed, 2)
            pe.matmul(g.ps[:, 0, :], ptn[:, :], g.va[0:NS, SMP, :], start=True, stop=False)
            for b in range(NB):
                pe.wait_ge(v_in[b], 16 * NPAGE)
                for p in range(NPAGE):
                    last = pe.matmul(g.ps[:, 0, :], ptz[:, b, p, :], g.pages[:, page_slot("cache_v", b), p, :],
                                     start=False, stop=(b == NB - 1 and p == NPAGE - 1))
                last.then_inc(made, 1)
            pe.wait_ge(out_read, 1)
            for h in range(H):
                last = pe.transpose(g.ps[:, 1, h * P:(h + 1) * P], ov[:, h * P:(h + 1) * P], g.c("ident"))
            last.then_inc(out_turned, 1)

        @block.scalar
        def _(act):
            for n in range(NB * H):
                b, h = n // H, n % H
                act.wait_ge(turned, n + 1)
                if b >= 2:
                    act.wait_ge(logits, b - 1)
                act.copy(kts[:, b % 2, h, :], g.ps[:, n % 4, :]).then_inc(placed, 1)
            act.wait_ge(negated, 1)
            act.activation(lg[:, :], lg[:, :], ACT.Exp, bias=stat[:, 1:2], accum_out=stat[:, 2:3]
                           ).then_inc(powered, 1)

        @block.vector
        def _(dve):
            done = [0]

            def link(op):
                done[0] += 1
                op.then_inc(chain, 1)
                dve.wait_ge(chain, done[0])

            dve.wait_ge(rb_in, 64)
            link(dve.tensor_tensor(rbt[:, :, :, :], spread(spread(rb[:, :], 0, NB), 2, NT),
                                   spread(spread(g.c("t_of"), 0, H), 0, NB), ALU.mult))
            dve.wait_ge(cleared, 1)
            for par in range(2):
                for h in range(H):
                    new = g.qt[:, h, SEQ:T].rearrange("p (b a t) -> p b a t", a=2, t=NT)[:, :, par, :]
                    last = dve.tensor_copy(
                        qz[:, :, h, par, h, :].rearrange("p (b a) t -> p b a t", a=2)[:, :, par, :], new)
            last.then_inc(laid, 1)
            dve.wait_ge(logits, NB)
            link(dve.tensor_copy(lg[:, 0:PAST], g.ps[:, 4, :]))
            link(dve.tensor_copy(lg[:, PAST:KEYS], g.ps[:, 5, 0:NS]))
            link(dve.tensor_reduce(stat[:, 0:1], lg[:, :], AX.X, ALU.max))
            dve.tensor_scalar(stat[:, 1:2], stat[:, 0:1], -1.0, None, ALU.mult).then_inc(negated, 1)
            dve.memset(ptz, 0.0).then_inc(ptz_cleared, 1)
            dve.wait_ge(powered, 1)
            link(dve.reciprocal(stat[:, 3:4], stat[:, 2:3]))
            dve.tensor_scalar(lg[:, :], lg[:, :], stat[:, 3:4], None, ALU.mult).then_inc(scaled, 1)
            dve.wait_ge(p_turned, 1)
            dve.wait_ge(ptz_cleared, 1)
            dve.tensor_copy(ptz_own, g.ps[:, 6, :].rearrange("p (c b r) -> p b c r", c=NPAGE, b=NB)).then_inc(p_placed, 1)
            dve.tensor_copy(ptn[:, :], g.ps[0:NS, 7, 0:P]).then_inc(p_placed, 1)
            dve.wait_ge(made, NB)
            dve.tensor_copy(ov[:, :], g.ps[:, 0, :]).then_inc(out_read, 1)
            dve.wait_ge(out_turned, 1)
            turned_out = g.ps[:, 1, :]
            dve.tensor_copy(g.ht[:, H:2 * H, SEQ:T].rearrange("p h (b t) -> p h b t", b=NB),
                            bass.AP(turned_out.tensor, turned_out.offset,
                                    [list(turned_out.ap[0]), [P + NT, H], [H * NT, NB], [1, NT]]))


def stage_project_out(g, weight, tag, reload):
    nc = g.nc
    x_in, made, added = (g.sem(f"{tag}_{n}") for n in ("stream", "made", "added"))
    w_in, w_rounded, w_split = g.slot_sems(f"{tag}_weights", 2), g.sem(f"{tag}_w_rounded"), g.sem(f"{tag}_w_split")
    rounded, split = g.sem(f"{tag}_rounded"), g.sem(f"{tag}_split")
    square, add_square, _ = sum_squares(g, f"{tag}n", g.ht[:, SQUARES, :], g.ht[:, TOTAL, :])
    with ExitStack() as st:
        w = g.room(st, f"{tag}_w", [P, 2, KD * P])
        wh = g.room(st, f"{tag}_wh", [P, 2, KD * P], F32R)
        wl = g.room(st, f"{tag}_wl", [P, 2, KD * P], F32R)
        block = st.enter_context(nc.Block())

        @block.sync
        def _(sp):
            for m in range(KD):
                if m >= 2:
                    sp.wait_ge(w_split, m - 1)
                sp.dma_start(w[:, m % 2, :].rearrange("p (k n) -> p k n", k=KD),
                             weight[:, m * P:(m + 1) * P].rearrange("(k p) n -> p k n", p=P)
                             ).then_inc(w_in[m % 2], 16)

        @block.gpsimd
        def _(pool):
            if reload:
                for k in range(KD):
                    pool.dma_start(g.xt[:, k, :], g.xt_spill[:, k, :]).then_inc(x_in, 16)

        @block.tensor
        def _(pe):
            for m in range(KD):
                pe.wait_ge(w_split, m + 1)
                if m >= 2:
                    pe.wait_ge(added, m - 1)
                for k in range(KD):
                    if m == 0:
                        pe.wait_ge(split, k + 1)
                    cols = slice(k * P, (k + 1) * P)
                    last = split_passes(g, pe, 4 * (m % 2), wh[:, m % 2, cols], wl[:, m % 2, cols], g.hh[:, k, :],
                                        g.hl[:, k, :], k == 0, k == KD - 1)
                last.then_inc(made, 1)

        @block.scalar
        def _(act):
            def high(m):
                act.wait_ge(w_in[m % 2], 16 * (m // 2 + 1))
                if m >= 2:
                    act.wait_ge(made, m - 1)
                act.copy(wh[:, m % 2, :], w[:, m % 2, :]).then_inc(w_rounded, 1)

            act.copy(g.hh[:, 0, :], g.ht[:, 0, :]).then_inc(rounded, 1)
            high(0)
            for k in range(1, KD):
                act.copy(g.hh[:, k, :], g.ht[:, k, :]).then_inc(rounded, 1)
            for m in range(1, KD):
                high(m)
                if m >= 2:
                    if m == 2:
                        act.wait_ge(split, KD)
                    act.wait_ge(added, m - 1)
                    square(act, m - 2)
            for m in range(KD - 2, KD):
                act.wait_ge(added, m + 1)
                square(act, m)

        @block.vector
        def _(dve):
            def low(m):
                dve.wait_ge(w_rounded, m + 1)
                dve.tensor_tensor(wl[:, m % 2, :], w[:, m % 2, :], wh[:, m % 2, :].bitcast(F32), ALU.subtract
                                  ).then_inc(w_split, 1)

            for k in range(KD):
                dve.wait_ge(rounded, k + 1)
                dve.tensor_tensor(g.hl[:, k, :], g.ht[:, k, :], g.hh[:, k, :].bitcast(F32), ALU.subtract
                                  ).then_inc(split, 1)
                if k == 0:
                    low(0)
            low(1)
            for m in range(KD):
                dve.wait_ge(made, m + 1)
                if reload and m == 0:
                    dve.wait_ge(x_in, 16 * KD)
                if m + 2 < KD:
                    low(m + 2)
                xv = g.xt[:, m, :].rearrange("p (c n) -> p c n", c=3)
                dve.tensor_tensor(xv, g.ps[:, 4 * (m % 2):4 * (m % 2) + 3, 0:THIRD], xv, ALU.add).then_inc(added, 1)
                if m >= 1:
                    add_square(dve, m - 1)
            add_square(dve, KD - 1)


def sum_squares(g, tag, sq, total):
    squared, summed = g.sem(f"{tag}_squared"), g.sem(f"{tag}_added")
    slots = sq.shape[1]

    def square(act, k):
        if k >= slots:
            act.wait_ge(summed, k - slots + 1)
        act.activation(sq[:, k % slots, :], g.xt[:, k, :], ACT.Square).then_inc(squared, 1)

    def add(dve, k):
        dve.wait_ge(squared, k + 1)
        if k == 0:
            dve.tensor_copy(total, sq[:, 0, :]).then_inc(summed, 1)
        else:
            dve.wait_ge(summed, k)
            dve.tensor_tensor(total, total, sq[:, k % slots, :], ALU.add).then_inc(summed, 1)

    return square, add, summed


def split_norm(g, which, tag, sq, total, inverse, squares_done=False):
    summed, mean_ready, root_ready, chain, diagonal, spread_out = (
        g.sem(f"{tag}_{n}") for n in ("summed", "mean", "root", "chain", "diagonal", "spread"))
    scaled, rounded = g.sem(f"{tag}_scaled"), g.sem(f"{tag}_rounded")
    normed = g.slot_sems(f"{tag}_normed", 2)
    slots = sq.shape[1]
    if not squares_done:
        square, add, squares_added = sum_squares(g, tag, sq, total)
    diag = bass.AP(sq.tensor, sq.offset, [list(sq.ap[0]), [1, (TILES - 1) * P + NS]])
    replicated = bass.AP(g.ps[:, 5, 0:1].tensor, g.ps[:, 5, 0:1].offset, [list(g.ps[:, 5, 0:1].ap[0]), [1, T]])

    def low(engine, k):
        engine.wait_ge(rounded, k + 1)
        engine.tensor_tensor(g.hl[:, k, :], sq[:, k % slots, :], g.hh[:, k, :].bitcast(F32), ALU.subtract
                             ).then_inc(normed[k % 2], 1)

    def scalar(act):
        if not squares_done:
            for k in range(KD):
                square(act, k)
        act.wait_ge(mean_ready, 1)
        act.activation(inverse, inverse, ACT.Sqrt).then_inc(root_ready, 1)

    def scalar_round(act):
        for k in range(KD):
            act.wait_ge(scaled, k + 1)
            act.copy(g.hh[:, k, :], sq[:, k % slots, :]).then_inc(rounded, 1)

    def tensor(pe):
        if not squares_done:
            pe.wait_ge(squares_added, KD)
        for t in range(TILES):
            last = pe.matmul(g.ps[0:rows(t), 0, t:t + 1], total[:, t * P:t * P + rows(t)], g.c("ones")[:, 0:1],
                             start=True, stop=True)
        last.then_inc(summed, 1)
        for t in range(TILES):
            pe.wait_ge(diagonal, t + 1)
            last = pe.matmul(replicated[:, t * P:t * P + rows(t)], g.c("ones")[0:rows(t), :],
                             diag[0:rows(t), t * P:t * P + rows(t)], start=True, stop=True)
        last.then_inc(spread_out, 1)

    def vector(dve):
        dve.memset(inverse, 1.0).then_inc(chain, 1)
        if not squares_done:
            for k in range(KD):
                add(dve, k)
        dve.wait_ge(summed, 1)
        dve.wait_ge(chain, 1)
        dve.tensor_scalar(inverse[:, 0:SMP], g.ps[:, 0, 0:SMP], 1.0 / D, EPS, ALU.mult, ALU.add)
        dve.tensor_scalar(inverse[0:NS, SMP:TILES], g.ps[0:NS, 0, SMP:TILES], 1.0 / D, EPS, ALU.mult, ALU.add
                          ).then_inc(mean_ready, 1)
        dve.wait_ge(root_ready, 1)
        dve.reciprocal(inverse, inverse).then_inc(chain, 1)
        dve.wait_ge(chain, 2)
        for t in range(TILES):
            n = rows(t)
            dve.tensor_scalar(diag[0:n, t * P:t * P + n], g.c("ident")[0:n, 0:n], inverse[0:n, t:t + 1], None, ALU.mult
                              ).then_inc(diagonal, 1)

    def vector_scale(dve):
        dve.wait_ge(spread_out, 1)
        for k in range(KD):
            if k >= slots:
                dve.wait_ge(normed[(k - slots) % 2], (k - slots) // 2 + 1)
            dve.scalar_tensor_tensor(out=sq[:, k % slots, :], in0=g.xt[:, k, :], scalar=g.gain[:, which, k:k + 1],
                                     in1=replicated, op0=ALU.mult, op1=ALU.mult).then_inc(scaled, 1)
            if k % 2 == 1:
                low(dve, k - 1)

    def gpsimd(pool):
        for k in range(1, KD, 2):
            low(pool, k)

    def wait_normed(pe, k):
        pe.wait_ge(normed[k % 2], k // 2 + 1)

    return (scalar, scalar_round), tensor, (vector, vector_scale), gpsimd, wait_normed


def split_passes(g, pe, b0, weight_high, weight_low, high, low, first, final, out_rows=P):
    for n, (lhs, rhs) in enumerate(((weight_high, high), (weight_high, low), (weight_low, high))):
        for c in range(3):
            last = pe.matmul(g.ps[0:out_rows, b0 + c, 0:THIRD], lhs, rhs[:, c * THIRD:(c + 1) * THIRD],
                             start=(first and n == 0), stop=(final and n == 2))
    return last


def stage_ffn(g, layer):
    nc = g.nc
    tag = f"f{layer}"
    CHUNKS = KF // 2
    KINDS = "GUD"
    raw_in = dict(zip(KINDS, g.slot_sems(f"{tag}_raw_in", 3)))
    rounded = dict(zip(KINDS, g.slot_sems(f"{tag}_rounded", 3)))
    split = dict(zip(KINDS, g.slot_sems(f"{tag}_split", 3)))
    made = dict(zip(KINDS, g.slot_sems(f"{tag}_made", 3)))
    silu, joined, hid_high, hid_low, added = (g.sem(f"{tag}_{n}") for n in
                                              ("silu", "joined", "hid_high", "hid_low", "added"))
    source = {"G": g.ins["w_gate"][layer], "U": g.ins["w_up"][layer], "D": g.ins["w_down"][layer]}

    with ExitStack() as st:
        inverse = g.room(st, f"{tag}_inverse", [P, TILES])
        n_scalar, n_tensor, n_vector, n_gpsimd, wait_normed = split_norm(
            g, 2 + layer, f"{tag}n", g.ht[:, SQUARES, :], g.ht[:, TOTAL, :], inverse[:, :], squares_done=True)
        raw = {k: g.ht[:, n, 0:1024] for n, k in enumerate(KINDS)}
        wh = {k: g.room(st, f"{tag}_wh{k}", [P, 1024], F32R) for k in KINDS}
        wl = {k: g.room(st, f"{tag}_wl{k}", [P, 1024], F32R) for k in KINDS}
        hidh = g.room(st, f"{tag}_hidh", [P, 2, 2, T], F32R)
        hidl = g.room(st, f"{tag}_hidl", [P, 2, 2, T], F32R)
        gate, prod = g.ht[:, 3, :], g.ht[:, 4, :]
        block = st.enter_context(nc.Block())

        def thirds(ap):
            return ap.rearrange("p (c n) -> p c n", c=3)

        def chunks(fori, chunk):
            for c in range(3):
                chunk(c, c % 2)
            with fori(0, (CHUNKS - 5) // 2) as i:
                for u in range(2):
                    chunk(2 * i + (3 + u), (3 + u) % 2)
            for c in range(CHUNKS - 2, CHUNKS):
                chunk(c, c % 2)

        def at(c, n):
            return isinstance(c, int) and c == n

        @block.sync
        def _(sp):
            def load(kind, x, first=False):
                if not first:
                    sp.wait_ge(split[kind], x)
                if kind == "D":
                    c, half = x
                    src = source["D"][bass.ds(c * 2 * P, 2 * P), half * 512:(half + 1) * 512]
                    sp.dma_start(raw["D"].rearrange("p (k n) -> p k n", k=2),
                                 src.rearrange("(k p) n -> p k n", p=P)).then_inc(raw_in["D"], 16)
                else:
                    sp.dma_start(raw[kind].rearrange("p (k n) -> p k n", k=KD),
                                 source[kind][:, bass.ds(x * P, P)].rearrange("(k p) n -> p k n", p=P)
                                 ).then_inc(raw_in[kind], 16)

            def load_down(c, half, first=False):
                if not first:
                    sp.wait_ge(split["D"], 2 * c + half)
                load("D", (c, half), True)

            def chunk(c, par):
                if at(c, 0):
                    load("G", 0, True)
                    load("U", 0, True)
                    load("D", (0, 0), True)
                else:
                    load_down(c - 1, 1)
                load("G", 2 * c + 1)
                load("U", 2 * c + 1)
                if not at(c, 0) and not at(c, CHUNKS - 1):
                    load_down(c, 0)
                elif at(c, CHUNKS - 1):
                    load_down(c, 0)
                    load_down(c, 1)
                if not at(c, CHUNKS - 1):
                    load("G", 2 * c + 2)
                    load("U", 2 * c + 2)

            chunks(sp.Fori, chunk)

        @block.tensor
        def _(pe):
            def hidden(kind, f, first=False):
                pe.wait_ge(split[kind], f + 1)
                for k in range(KD):
                    if first:
                        wait_normed(pe, k)
                    last = split_passes(g, pe, 0 if kind == "G" else 3, wh[kind][:, k * P:(k + 1) * P],
                                        wl[kind][:, k * P:(k + 1) * P], g.hh[:, k, :], g.hl[:, k, :],
                                        k == 0, k == KD - 1)
                last.then_inc(made[kind], 1)

            def down(c, par, half, tail=False):
                pe.wait_ge(split["D"], 2 * c - 1 + half)
                if half == 0:
                    pe.wait_ge(hid_low, 2 * c)
                for m in range(4):
                    if tail or m >= 2:
                        pe.wait_ge(added, 8 * c - 9 + 4 * half + m)
                    else:
                        pe.wait_ge((silu, joined)[m], 2 * c + half + 1)
                    for k in range(2):
                        cols = slice((4 * k + m) * P, (4 * k + m + 1) * P)
                        last = split_passes(g, pe, 3 * (m % 2), wh["D"][:, cols], wl["D"][:, cols],
                                            hidh[:, 1 - par, k, :], hidl[:, 1 - par, k, :], k == 0, k == 1)
                    last.then_inc(made["D"], 1)

            def chunk(c, par):
                for half in range(2):
                    for n, kind in enumerate("GU"):
                        if at(c, 0) or at(c, 1):
                            if 2 * c + half:
                                if c == 1 and half == 1:
                                    pe.wait_ge(added, 3 + n)
                                else:
                                    pe.wait_ge((silu, joined)[n], 2 * c + half)
                        else:
                            pe.wait_ge(added, 8 * c - 9 + 4 * half + n)
                        hidden(kind, 2 * c + half, first=at(c, 0) and half == 0 and n == 0)
                    if not at(c, 0):
                        down(c, par, half)

            n_tensor(pe)
            chunks(pe.Fori, chunk)
            for half in range(2):
                down(CHUNKS, CHUNKS % 2, half, tail=True)

        @block.gpsimd
        def _(pool):
            n_gpsimd(pool)

        @block.scalar
        def _(act):
            def high(kind, x, first=False):
                act.wait_ge(raw_in[kind], 16 * x + 16)
                if not first:
                    act.wait_ge(made[kind], 4 * x if kind == "D" else x)
                act.copy(wh[kind][:, :], raw[kind]).then_inc(rounded[kind], 1)

            def activate(f, first=False):
                act.wait_ge(made["G"], f + 1)
                if not first:
                    act.wait_ge(joined, f)
                act.activation(thirds(gate), g.ps[:, 0:3, 0:THIRD], ACT.Silu).then_inc(silu, 1)

            def hid(par, half, f):
                act.wait_ge(joined, f + 1)
                act.copy(hidh[:, par, half, :], prod).then_inc(hid_high, 1)

            def chunk(c, par):
                final = at(c, CHUNKS - 1)
                if not at(c, 0):
                    high("D", 2 * c - 2, first=at(c, 1))
                activate(2 * c, first=at(c, 0))
                high("G", 2 * c + 1)
                high("U", 2 * c + 1)
                hid(par, 0, 2 * c)
                if not at(c, 0):
                    high("D", 2 * c - 1)
                activate(2 * c + 1)
                if not final:
                    high("G", 2 * c + 2)
                    high("U", 2 * c + 2)
                hid(par, 1, 2 * c + 1)

            n_scalar[0](act)
            high("G", 0, True)
            high("U", 0, True)
            n_scalar[1](act)
            chunks(act.Fori, chunk)
            for half in range(2):
                high("D", 2 * CHUNKS - 2 + half)

        @block.vector
        def _(dve):
            def low(kind, x):
                dve.wait_ge(rounded[kind], x + 1)
                dve.tensor_tensor(wl[kind][:, :], raw[kind], wh[kind][:, :].bitcast(F32), ALU.subtract
                                  ).then_inc(split[kind], 1)

            def join(f, first=False):
                dve.wait_ge(silu, f + 1)
                dve.wait_ge(made["U"], f + 1)
                if not first:
                    dve.wait_ge(hid_high, f)
                    dve.wait_ge(hid_low, f)
                dve.tensor_tensor(thirds(prod), g.ps[:, 3:6, 0:THIRD], thirds(gate), ALU.mult
                                  ).then_inc(joined, 1)

            def hid(par, half, f):
                dve.wait_ge(hid_high, f + 1)
                dve.tensor_tensor(hidl[:, par, half, :], prod, hidh[:, par, half, :].bitcast(F32), ALU.subtract
                                  ).then_inc(hid_low, 1)

            def add(c, half):
                for m in range(4):
                    dve.wait_ge(made["D"], 8 * c - 7 + 4 * half + m)
                    xv = thirds(g.xt[:, 4 * half + m, :])
                    dve.tensor_tensor(xv, g.ps[:, 3 * (m % 2):3 * (m % 2) + 3, 0:THIRD], xv, ALU.add
                                      ).then_inc(added, 1)

            def chunk(c, par):
                final = at(c, CHUNKS - 1)
                if not at(c, 0):
                    low("D", 2 * c - 2)
                low("G", 2 * c + 1)
                join(2 * c, first=at(c, 0))
                low("U", 2 * c + 1)
                hid(par, 0, 2 * c)
                if not at(c, 0):
                    add(c, 0)
                    low("D", 2 * c - 1)
                if not final:
                    low("G", 2 * c + 2)
                join(2 * c + 1)
                if not final:
                    low("U", 2 * c + 2)
                hid(par, 1, 2 * c + 1)
                if not at(c, 0):
                    add(c, 1)

            n_vector[0](dve)
            low("G", 0)
            low("U", 0)
            n_vector[1](dve)
            chunks(dve.Fori, chunk)
            for half in range(2):
                low("D", 2 * CHUNKS - 2 + half)
                add(CHUNKS, half)


def stage_store(g):
    nc = g.nc
    turned, copied, stored = g.sem("out_turned"), g.sem("out_copied"), g.slot_sems("out_stored", 4)
    with ExitStack() as st:
        ring = g.room(st, "out_rows", [P, 4, 512])
        block = st.enter_context(nc.Block())

        @block.tensor
        def _(pe):
            for n in range(2 * TILES):
                t, half = n // 2, n % 2
                if n >= 4:
                    pe.wait_ge(copied, n - 3)
                for k in range(4):
                    last = pe.transpose(g.ps[0:rows(t), n % 4, k * P:(k + 1) * P],
                                        g.xt[:, 4 * half + k, t * P:t * P + rows(t)], g.c("ident"))
                last.then_inc(turned, 1)

        @block.vector
        def _(dve):
            for n in range(2 * TILES):
                t = n // 2
                dve.wait_ge(turned, n + 1)
                if n >= 4:
                    dve.wait_ge(stored[n % 4], 16 * (n // 4))
                dve.tensor_copy(ring[0:rows(t), n % 4, :], g.ps[0:rows(t), n % 4, :]).then_inc(copied, 1)

        @block.sync
        def _(sp):
            for n in range(2 * TILES):
                t, half = n // 2, n % 2
                sp.wait_ge(copied, n + 1)
                dst = g.outs["y_prompt"][0, t * P:(t + 1) * P, half * 512:(half + 1) * 512] if t < SMP else \
                    g.outs["y_sample"].rearrange("b t d -> (b t) d")[:, half * 512:(half + 1) * 512]
                sp.dma_start(dst, ring[0:rows(t), n % 4, :]).then_inc(stored[n % 4], 16)
            for slot in range(4):
                sp.wait_ge(stored[slot], 16 * len(range(slot, 2 * TILES, 4)))


XW = CW - 1 + SEQ + NB * (CW - 1 + NT)
UW = PPAST + SEQ


def stage_odd(g, keep):
    with ExitStack() as st:
        g.z = g.room(st, "od_z", [P, TILES, 512], F32, "right")
        g.dt = g.room(st, "od_dt", [P, TILES, SH], F32, "right")
        g.xb = g.room(st, "od_xb", [P, CD // P, XW], F32, "right")
        with ExitStack() as pool_room:
            g.up = g.room(pool_room, "od_up", [P, 4, UW], F32, "right")
            g.us = g.room(pool_room, "od_us", [P, 4, PPAST + NT, NB], F32, "right")
            with ExitStack() as normed:
                g.halves(normed, "odd")
                stage_odd_project(g)
            g.ht = g.room(keep, "ht_odd", [P, KD, T])
            stage_pool(g)
        g.xtm = g.room(st, "od_xtm", [P, TILES, 512])
        g.btm = g.room(st, "od_btm", [P, TILES, 2 * SN])
        stage_ssd(g)


def stage_odd_project(g):
    nc = g.nc
    made, copied = g.sem("op_made"), g.sem("op_copied")
    w_in, w_rounded, w_split = (g.sem(f"op_{n}") for n in ("weights", "rounded", "split"))
    hist_in, hist_turned, hist_placed, cleared = (g.sem(f"op_{n}") for n in
                                                  ("hist_in", "hist_turned", "hist_placed", "cleared"))
    turned, placed = g.sem("op_turned"), g.sem("op_placed")
    taps_in, tail_turned, tail_copied, tail_stored = (g.sem(f"op_{n}") for n in
                                                      ("taps", "tail_turned", "tail_copied", "tail_stored"))
    summed, rectified, chain = g.sem("op_summed"), g.sem("op_silu"), g.sem("op_chain")
    weight = g.ins["w_in_odd"][0]
    NF = 17
    ZF = 12
    MT = CD // P
    UROWS, XROWS = NB * PPAST, NB * (CW - 1)

    def first_col(m):
        return m * P if m < 4 else ODD_XBC + (m - 4) * P if m < ZF else ODD_Z + (m - ZF) * P if m < NF - 1 else ODD_DT

    def width(m):
        return P if m < NF - 1 else SH

    with ExitStack() as st:
        w = g.room(st, "op_w", [P, KD * P])
        wh = g.room(st, "op_wh", [P, 2, KD * P], F32R)
        wl = g.room(st, "op_wl", [P, 2, KD * P], F32R)
        hu = g.room(st, "op_hu", [UROWS, PW])
        zt = g.room(st, "op_zt", [P, T])
        hx = zt[0:XROWS, 0:CD]
        tail = zt[0:XW - SEQ, 0:CD]
        taps = g.room(st, "op_taps", [P, MT, CW + 1])
        inverse = g.room(st, "op_inverse", [P, TILES])
        ring = g.z[:, :, :].rearrange("p t n -> p (t n)")[:, 0:4 * T].rearrange("p (s n) -> p s n", s=4)
        n_scalar, n_tensor, n_vector, n_gpsimd, wait_normed = split_norm(g, 1, "n2", ring[:, 0:3, :], ring[:, 3, :],
                                                                         inverse[:, :])
        acc = g.z[:, :, :].rearrange("p t n -> p (t n)")[:, 0:2 * T].rearrange("p (s n) -> p s n", s=2)
        block = st.enter_context(nc.Block())

        @block.sync
        def _(sp):
            for m in range(NF):
                if m >= 1:
                    sp.wait_ge(w_split, m)
                with nc.allow_non_contiguous_dma("the last block has eight columns"):
                    sp.dma_start(w[:, 0:KD * width(m)].rearrange("p (k n) -> p k n", k=KD),
                                 weight[:, first_col(m):first_col(m) + width(m)].rearrange("(k p) n -> p k n", p=P)
                                 ).then_inc(w_in, 16)
                if m == 1:
                    sp.dma_start(hu[:, :], g.ins["state_pool"][0].rearrange("b r c -> (b r) c")).then_inc(hist_in, 16)
                    sp.dma_start(hx, g.ins["state_conv"][0].rearrange("b r c -> (b r) c")).then_inc(hist_in, 16)
                    with nc.allow_non_contiguous_dma("vectors of 1024 across the partitions"):
                        for j in range(CW):
                            sp.dma_start(taps[:, :, j], g.ins["conv_w"][0][j].rearrange("(k p) -> p k", p=P)
                                         ).then_inc(taps_in, 16)
                        sp.dma_start(taps[:, :, CW], g.ins["conv_b"][0].rearrange("(k p) -> p k", p=P)
                                     ).then_inc(taps_in, 16)

        @block.gpsimd
        def _(pool):
            n_gpsimd(pool)
            pool.wait_ge(made, 1)
            pool.memset(g.up[:, :, 0:PPAST], 0.0)
            pool.memset(g.xb[:, :, 0:CW - 1], 0.0)
            pool.memset(g.z[:, SMP, :], 0.0)
            pool.memset(g.dt[:, SMP, :], 0.0).then_inc(cleared, 1)
            pool.wait_ge(tail_copied, MT)
            pool.dma_start(g.outs["conv_prompt"][0, 0], tail[0:CW - 1, :]).then_inc(tail_stored, 16)
            for t in range(1, NT):
                first = CW - 1 + (CW - 1 + t) * NB
                pool.dma_start(g.outs["conv_sample"][0][:, t - 1, :], tail[first:first + NB, :]).then_inc(tail_stored, 16)
            pool.wait_ge(tail_stored, 16 * NT)

        @block.tensor
        def _(pe):
            def turn(m):
                pe.wait_ge(copied, m + 1)
                for b in range(3):
                    n = 3 * (m - ZF) + b
                    if n >= 2:
                        pe.wait_ge(placed, n - 1)
                    for t in range(4 * b, min(4 * b + 4, TILES)):
                        at = (t - 4 * b) * P
                        last = pe.transpose(g.ps[0:rows(t), 3 + 4 * (n % 2), at:at + width(m)],
                                            zt[0:width(m), t * P:t * P + rows(t)],
                                            g.c("ident")[0:width(m), 0:width(m)])
                    last.then_inc(turned, 1)

            n_tensor(pe)
            for m in range(NF):
                pe.wait_ge(w_split, m + 1)
                if m >= 2:
                    pe.wait_ge(copied, m - 1)
                for k in range(KD):
                    if m == 0:
                        wait_normed(pe, k)
                    cols = slice(k * width(m), (k + 1) * width(m))
                    last = split_passes(g, pe, 4 * (m % 2), wh[:, m % 2, cols], wl[:, m % 2, cols], g.hh[:, k, :],
                                        g.hl[:, k, :], k == 0, k == KD - 1, width(m))
                last.then_inc(made, 1)
                if m == 4:
                    pe.wait_ge(hist_in, 32)
                    for n in range(12):
                        if n >= 2:
                            pe.wait_ge(hist_placed, n - 1)
                        src, r = (hu[:, n * P:(n + 1) * P], UROWS) if n < 4 else (hx[:, (n - 4) * P:(n - 3) * P], XROWS)
                        pe.transpose(g.ps[:, 3 + 4 * (n % 2), 0:r], src, g.c("ident")[0:r, 0:r]
                                     ).then_inc(hist_turned, 1)
                    pe.wait_ge(hist_placed, 12)
                if 5 <= m < 5 + MT:
                    i = m - 5
                    pe.wait_ge(copied, m)
                    if i >= 2:
                        pe.wait_ge(tail_copied, i - 1)
                    pe.transpose(g.ps[0:XW - SEQ, 3 + 4 * (i % 2), 0:P], g.xb[:, i, SEQ:XW], g.c("ident")
                                 ).then_inc(tail_turned, 1)
                if m == ZF:
                    pe.wait_ge(tail_copied, MT)
                if m > ZF:
                    turn(m - 1)
            turn(NF - 1)

        @block.scalar
        def _(act):
            def high(m):
                act.wait_ge(w_in, 16 * (m + 1))
                if m >= 2:
                    act.wait_ge(made, m - 1)
                act.copy(wh[:, m % 2, 0:KD * width(m)], w[:, 0:KD * width(m)]).then_inc(w_rounded, 1)

            def store_tail(i):
                if i == 0:
                    act.wait_ge(hist_turned, 12)
                act.wait_ge(tail_turned, i + 1)
                act.copy(tail[:, i * P:(i + 1) * P], g.ps[0:XW - SEQ, 3 + 4 * (i % 2), 0:P]).then_inc(tail_copied, 1)

            n_scalar[0](act)
            high(0)
            n_scalar[1](act)
            high(1)
            act.wait_ge(cleared, 1)
            for m in range(NF):
                if 6 <= m < 6 + MT:
                    act.wait_ge(summed, m - 5)
                    act.activation(g.xb[:, m - 6, 0:T], acc[:, m % 2, :], ACT.Silu).then_inc(rectified, 1)
                act.wait_ge(made, m + 1)
                b0 = 4 * (m % 2)
                third = SEQ - 2 * THIRD
                if m < ZF:
                    if m < 4:
                        dst, at = g.up[:, m, :], PPAST
                        smp = g.us[:, m, PPAST:PPAST + NT, :]
                    else:
                        dst, at = g.xb[:, m - 4, :], CW - 1
                        smp = g.xb[:, m - 4, CW - 1 + SEQ:XW].rearrange("p (r b) -> p r b", b=NB)[:, CW - 1:, :]
                    act.copy(dst[:, at:at + 2 * THIRD].rearrange("p (c n) -> p c n", c=2), g.ps[:, b0:b0 + 2, 0:THIRD])
                    act.copy(dst[:, at + 2 * THIRD:at + SEQ], g.ps[:, b0 + 2, 0:third])
                    act.copy(smp, g.ps[:, b0 + 2, third:THIRD].rearrange("p (b t) -> p t b", b=NB)
                             ).then_inc(copied, 1)
                else:
                    if m == ZF:
                        store_tail(MT - 1)
                        act.wait_ge(tail_stored, 16 * NT)
                    else:
                        act.wait_ge(turned, 3 * (m - ZF))
                    act.copy(zt[0:width(m), :].rearrange("p (c n) -> p c n", c=3),
                             g.ps[0:width(m), b0:b0 + 3, 0:THIRD]).then_inc(copied, 1)
                if m + 2 < NF:
                    high(m + 2)
                if 5 <= m < 4 + MT:
                    store_tail(m - 5)

        @block.vector
        def _(dve):
            def low(m):
                dve.wait_ge(w_rounded, m + 1)
                part = slice(0, KD * width(m))
                dve.tensor_tensor(wl[:, m % 2, part], w[:, part], wh[:, m % 2, part].bitcast(F32), ALU.subtract
                                  ).then_inc(w_split, 1)

            done = [0]

            def link(op):
                done[0] += 1
                op.then_inc(chain, 1)
                dve.wait_ge(chain, done[0])

            def convolve(i):
                dve.wait_ge(copied, i + 5)
                if i == 0:
                    dve.wait_ge(hist_placed, 12)
                if i >= 2:
                    dve.wait_ge(rectified, i - 1)
                out, souts = acc[:, i % 2, 0:SEQ], acc[:, i % 2, SEQ:T].rearrange("p (b t) -> p t b", b=NB)
                sample = g.xb[:, i, CW - 1 + SEQ:XW].rearrange("p (r b) -> p r b", b=NB)
                for j in range(CW):
                    tap = taps[:, i, j:j + 1]
                    src, ssrc = g.xb[:, i, j:j + SEQ], sample[:, j:j + NT, :]
                    if j == 0:
                        dve.tensor_scalar(out, src, tap, taps[:, i, CW:CW + 1], ALU.mult, ALU.add)
                        link(dve.tensor_scalar(souts, ssrc, tap, taps[:, i, CW:CW + 1], ALU.mult, ALU.add))
                    else:
                        dve.scalar_tensor_tensor(out=out, in0=src, scalar=tap, in1=out, op0=ALU.mult, op1=ALU.add)
                        last = dve.scalar_tensor_tensor(out=souts, in0=ssrc, scalar=tap, in1=souts, op0=ALU.mult,
                                                        op1=ALU.add)
                        if j < CW - 1:
                            link(last)
                last.then_inc(summed, 1)

            n_vector[0](dve)
            low(0)
            n_vector[1](dve)
            for m in range(1, 6):
                low(m)
                if m == 5:
                    for n in range(12):
                        dve.wait_ge(hist_turned, n + 1)
                        if n < 4:
                            dst = g.us[:, n, 0:PPAST, :]
                            src = g.ps[:, 3 + 4 * (n % 2), 0:UROWS].rearrange("p (b r) -> p r b", b=NB)
                        else:
                            dst = g.xb[:, n - 4, CW - 1 + SEQ:XW].rearrange("p (r b) -> p r b", b=NB)[:, 0:CW - 1, :]
                            src = g.ps[:, 3 + 4 * (n % 2), 0:XROWS].rearrange("p (b r) -> p r b", b=NB)
                        dve.tensor_copy(dst, src).then_inc(hist_placed, 1)
            dve.wait_ge(cleared, 1)
            dve.wait_ge(taps_in, 16 * (CW + 1))
            for m in range(6, ZF + 2):
                low(m)
                convolve(m - 6)
            dve.wait_ge(rectified, MT)
            for m in range(ZF, NF):
                if m + 2 < NF:
                    low(m + 2)
                for b in range(3):
                    n = 3 * (m - ZF) + b
                    dve.wait_ge(turned, n + 1)
                    at, tiles = (m - ZF) * P, slice(4 * b, min(4 * b + 4, SMP))
                    room = g.z[:, :, at:at + P] if m < NF - 1 else g.dt
                    src = g.ps[:, 3 + 4 * (n % 2), :].rearrange("p (t i) -> p t i", t=4)[:, :, 0:width(m)]
                    if b < 2:
                        dve.tensor_copy(room[:, tiles, :], src).then_inc(placed, 1)
                    else:
                        dve.tensor_copy(room[0:NS, SMP, :], src[0:NS, 0, :]).then_inc(placed, 1)


def stage_pool(g):
    nc = g.nc
    w_in, diff, mixed, placed = (g.sem(f"po_{n}") for n in ("weights", "diff", "mixed", "placed"))
    turned, copied, stored, chain = (g.sem(f"po_{n}") for n in ("turned", "copied", "stored", "chain"))
    with ExitStack() as st:
        pw = g.room(st, "po_w", [P, 4, P])
        scale = g.room(st, "po_scale", [P, 4])
        sums = g.room(st, "po_sums", [P, 2, UW])
        ssum = g.room(st, "po_ssum", [P, 2, PPAST + NT, NB])
        d = g.room(st, "po_d", [P, 2, T])
        tail = g.room(st, "po_tail", [NS, 2, PW])
        block = st.enter_context(nc.Block())

        @block.sync
        def _(sp):
            sp.dma_start(pw[:, :, :], g.ins["pool_w"][0].rearrange("g c d -> c g d")).then_inc(w_in, 16)
            with nc.allow_non_contiguous_dma("a vector of 512 across the partitions"):
                sp.dma_start(scale[:, :], g.ins["pool_scale"][0].rearrange("(g p) -> p g", p=P)).then_inc(w_in, 16)
            sp.dma_start(g.outs["pool_sample"][0][:, 0:PPAST - NT, :], g.ins["state_pool"][0][:, NT:PPAST, :]
                         ).then_inc(stored, 16)
            sp.wait_ge(copied, 2)
            sp.dma_start(g.outs["pool_prompt"][0, 0], tail[0:PPAST, 0, :]).then_inc(stored, 16)
            for t in range(NT):
                sp.dma_start(g.outs["pool_sample"][0][:, PPAST - NT + t, :], tail[t * NB:(t + 1) * NB, 1, :]
                             ).then_inc(stored, 16)
            sp.wait_ge(stored, 16 * (NT + 2))

        @block.tensor
        def _(pe):
            for m in range(4):
                pe.transpose(g.ps[0:PPAST, 6, m * P:(m + 1) * P], g.up[:, m, SEQ:UW], g.c("ident"))
                last = pe.transpose(g.ps[0:NS, 7, m * P:(m + 1) * P], g.us[:, m, PPAST:, :].rearrange("p t b -> p (t b)"),
                                    g.c("ident"))
            last.then_inc(turned, 1)
            pe.wait_ge(w_in, 32)
            for m in range(4):
                pe.wait_ge(diff, m + 1)
                if m >= 2:
                    pe.wait_ge(placed, m - 1)
                for c in range(3):
                    last = pe.matmul(g.ps[:, 3 * (m % 2) + c, 0:THIRD], pw[:, m, :],
                                     d[:, m % 2, c * THIRD:(c + 1) * THIRD], start=True, stop=True)
                last.then_inc(mixed, 1)

        @block.scalar
        def _(act):
            act.wait_ge(turned, 1)
            act.copy(tail[0:PPAST, 0, :], g.ps[0:PPAST, 6, :]).then_inc(copied, 1)
            act.copy(tail[0:NS, 1, :], g.ps[0:NS, 7, :]).then_inc(copied, 1)
            act.wait_ge(w_in, 32)
            for m in range(4):
                act.wait_ge(mixed, m + 1)
                act.activation(g.ht[:, m, :].rearrange("p (c n) -> p c n", c=3),
                               g.ps[:, 3 * (m % 2):3 * (m % 2) + 3, 0:THIRD], ACT.Copy, scale=scale[:, m:m + 1]
                               ).then_inc(placed, 1)

        @block.vector
        def _(dve):
            done = [0]

            def link(op):
                done[0] += 1
                op.then_inc(chain, 1)
                dve.wait_ge(chain, done[0])

            for m in range(4):
                if m >= 1:
                    dve.wait_ge(diff, m)
                if m >= 2:
                    dve.wait_ge(mixed, m - 1)
                src, ssrc = g.up[:, m, :], g.us[:, m, :, :]
                for s in range(m + 1):
                    sh = 2 ** s
                    dst, sdst = sums[:, s % 2, :], ssum[:, s % 2, :, :]
                    lo = 2 * sh - 1
                    dve.tensor_tensor(dst[:, lo:UW], src[:, lo:UW], src[:, lo - sh:UW - sh], ALU.add)
                    link(dve.tensor_tensor(sdst[:, lo:, :], ssrc[:, lo:, :], ssrc[:, lo - sh:PPAST + NT - sh, :],
                                           ALU.add))
                    src, ssrc = dst, sdst
                head = g.c("pool_head")[:, m * PPAST:(m + 1) * PPAST]
                link(dve.tensor_tensor(src[:, PPAST:2 * PPAST], src[:, PPAST:2 * PPAST], head, ALU.mult))
                inv = 1.0 / 2 ** (m + 1)
                dve.tensor_tensor(d[:, m % 2, 0:PPAST], src[:, PPAST:2 * PPAST], g.up[:, m, PPAST:2 * PPAST],
                                  ALU.subtract)
                dve.scalar_tensor_tensor(out=d[:, m % 2, PPAST:SEQ], in0=src[:, 2 * PPAST:UW], scalar=inv,
                                         in1=g.up[:, m, 2 * PPAST:UW], op0=ALU.mult, op1=ALU.subtract)
                dve.scalar_tensor_tensor(out=d[:, m % 2, SEQ:T].rearrange("p (b t) -> p t b", b=NB),
                                         in0=ssrc[:, PPAST:, :], scalar=inv, in1=g.us[:, m, PPAST:, :],
                                         op0=ALU.mult, op1=ALU.subtract).then_inc(diff, 1)


def stage_ssd(g):
    nc = g.nc
    small_in, cleared = g.sem("sd_small"), g.sem("sd_cleared")
    turned, copied = g.sem("sd_turned"), g.sem("sd_copied")
    dt_abs, dt_exp, dt_one, dt_log, dt_ready = (g.sem(f"sd_dt_{n}") for n in ("abs", "exp", "one", "log", "ready"))
    cum, cum_ready, powers = g.sem("sd_cum"), g.sem("sd_cum_ready"), g.sem("sd_powers")
    spread_done, decay, weighted, xs, xs_w = (g.sem(f"sd_{n}") for n in ("spread", "decay", "weighted", "xs", "xs_w"))
    made, state, chain = g.sem("sd_made"), g.sem("sd_state"), g.sem("sd_chain")
    st_in, st_turned, st_placed = g.slot_sems("sd_st_in", 2), g.sem("sd_st_turned"), g.sem("sd_st_placed")
    s_laid, s_xw, s_up, s_new = (g.sem(f"sd_s_{n}") for n in ("laid", "xw", "up", "new"))
    tables_ready, cum_high, cum_split, negative = (g.sem(f"sd_{n}") for n in
                                                   ("tables", "cum_high", "cum_split", "negative"))
    products, updated, y_read, skipped = (g.sem(f"sd_{n}") for n in ("products", "updated", "y_read", "skipped"))
    diag_made, w_ready = g.sem("sd_diag_made"), g.sem("sd_w_ready")
    o_turned, o_copied, o_stored = g.sem("sd_o_turned"), g.sem("sd_o_copied"), g.slot_sems("sd_o_stored", 2)
    gate_ready, rms, root, normed, y_turned, y_placed = (g.sem(f"sd_{n}") for n in
                                                         ("gate", "rms", "root", "normed", "y_turned", "y_placed"))
    BT, CT = 4, 6
    with ExitStack() as st:
        ex = g.room(st, "sd_exp", [P, TILES, SH])
        cs = g.room(st, "sd_cs", [P, TILES, SH])
        wend = g.room(st, "sd_wend", [P, TILES, SH])
        a = g.room(st, "sd_a", [P, TILES, SH])
        tmp = g.room(st, "sd_tmp", [P, TILES, SH])
        eend = g.room(st, "sd_eend", [P, SMP, SH])
        eend_s = g.room(st, "sd_eends", [P, NB, SH])
        ab = g.room(st, "sd_ab", [NS, NB, SH])
        rowv = g.room(st, "sd_rowv", [P, 3, SH])
        csth = g.room(st, "sd_cst_high", [SH, T], F32R)
        cstl = g.room(st, "sd_cst_low", [SH, T], F32R)
        dgh = g.room(st, "sd_diag_high", [SH, SH, P], F32R)
        dgl = g.room(st, "sd_diag_low", [SH, SH, P], F32R)
        onesr = g.room(st, "sd_ones", [SH, P], F32R)
        identr = g.room(st, "sd_ident", [P, P], F32R)
        causalr = g.room(st, "sd_causal", [P, P], F32R)
        newr = g.room(st, "sd_new", [NS, NS], F32R)
        ncs = g.room(st, "sd_ncs", [P, TILES, SH])
        ee = g.room(st, "sd_e", [P, 2, SH, P])
        xd = g.room(st, "sd_xd", [P, 2, 512])
        xw = g.room(st, "sd_xw", [P, 2, 512])
        t1 = g.room(st, "sd_t1", [P, 512])
        h0 = g.room(st, "sd_h", [P, 512])
        hs = g.ht[:, 4:8, :].rearrange("p k n -> p (k n)")[:, 0:NB * 512].rearrange("p (b n) -> p b n", b=NB)
        nat = g.room(st, "sd_nat", [P, 2, 4, SN])
        cz = g.room(st, "sd_cz", [P, 2, NB, NS])
        gains = g.room(st, "sd_gains", [P, 4])
        rs = g.room(st, "sd_rs", [P, TILES * 2])
        block = st.enter_context(nc.Block())
        ident = g.c("ident")

        def heads(ap):
            return ap.rearrange("p (h e) -> p h e", h=SH)

        state_rows = g.ins["state_ssm"][0].rearrange("b h p n -> b (h p) n")
        out_rows = g.outs["ssm_sample"][0].rearrange("b h p n -> b (h p) n")

        @block.sync
        def _(sp):
            with nc.allow_non_contiguous_dma("small vectors"):
                for n, name in enumerate(("dt_bias", "a_log", "d_skip")):
                    sp.dma_start(rowv[:, n, :], g.ins[name][0].partition_broadcast(P)).then_inc(small_in, 16)
                sp.dma_start(gains[:, :], g.ins["ssm_norm"][0].rearrange("(k p) -> p k", p=P)).then_inc(small_in, 16)
            for b in range(NB):
                if b >= 2:
                    sp.wait_ge(st_turned, b - 1)
                sp.dma_start(nat[:, b % 2, :, :], state_rows[b].rearrange("(c p) n -> p c n", p=P)).then_inc(st_in[b % 2], 16)
            for n in range(NB + 1):
                sp.wait_ge(o_copied, n + 1)
                dst = g.outs["ssm_prompt"][0, 0].rearrange("h p n -> (h p) n") if n == 0 else out_rows[n - 1]
                sp.dma_start(dst.rearrange("(c p) n -> p c n", p=P), nat[:, n % 2, :, :]).then_inc(o_stored[n % 2], 16)
            for slot in range(2):
                sp.wait_ge(o_stored[slot], 16 * len(range(slot, NB + 1, 2)))

        @block.gpsimd
        def _(pool):
            pool.memset(g.xtm[:, SMP, :], 0.0)
            pool.memset(g.btm[:, SMP, :], 0.0)
            pool.memset(cs[:, SMP, :], 0.0)
            pool.memset(wend[:, SMP, :], 0.0).then_inc(cleared, 1)
            pool.tensor_copy(onesr[:, :], g.c("ones")[0:SH, :])
            pool.tensor_copy(identr[:, :], ident)
            pool.tensor_copy(causalr[:, :], g.c("causal"))
            pool.tensor_copy(newr[:, :], g.c("new_ok")[0:NS, :]).then_inc(tables_ready, 1)
            for q in range(2):
                pool.tensor_tensor(cz[:, q, :, :], spread(g.xb[:, CT + q, SEQ:T], 0, NB),
                                   g.c("col_seq").rearrange("p (b t) -> p b t", b=NB), ALU.mult).then_inc(s_laid, 1)
            pool.wait_ge(cum_split, 1)
            own = ident[0:SH, 0:SH]

            def diagonal(c):
                n = rows(c)
                if c >= 1:
                    pool.wait_ge(spread_done, c)
                for to, part in ((dgh, csth), (dgl, cstl)):
                    last = pool.tensor_tensor(to[:, :, 0:n], spread(part[:, c * P:c * P + n].bitcast(F32), 0, SH),
                                              spread(own, 1, n), ALU.mult)
                last.then_inc(diag_made, 1)

            def ends(c):
                n = rows(c)
                if c >= 2:
                    pool.wait_ge(updated, c - 1)
                pool.tensor_tensor(heads(xw[0:n, c % 2, :]), heads(g.xtm[0:n, c, :]), spread(wend[0:n, c, :], 1, SP),
                                   ALU.mult).then_inc(xs_w, 1)

            diagonal(0)
            pool.wait_ge(w_ready, 1)
            ends(0)
            for c in range(TILES):
                n = rows(c)
                if c + 1 < TILES:
                    diagonal(c + 1)
                    ends(c + 1)
                pool.wait_ge(xs, c + 1)
                pool.wait_ge(xs_w, c + 1)
                x = heads(g.xtm[0:n, c, :])
                pool.tensor_tensor(x, x, spread(rowv[0:n, 2, :], 1, SP), ALU.mult).then_inc(skipped, 1)

        @block.tensor
        def _(pe):
            pe.wait_ge(cleared, 1)
            for t in range(TILES):
                if t >= 2:
                    pe.wait_ge(copied, 2 * (t - 1))
                for m in range(6):
                    last = pe.transpose(g.ps[0:rows(t), 2 * (t % 2) + m // 4, (m % 4) * P:(m % 4 + 1) * P],
                                        g.xb[:, m, t * P:t * P + rows(t)], ident)
                last.then_inc(turned, 1)
            for b in range(NB):
                pe.wait_ge(st_in[b % 2], 16 * (b // 2 + 1))
                if b >= 2:
                    pe.wait_ge(st_placed, b - 1)
                for m in range(4):
                    last = pe.transpose(g.ps[:, 4 + b % 2, m * P:(m + 1) * P], nat[:, b % 2, m, :], ident)
                last.then_inc(st_turned, 1)
            pe.wait_ge(dt_ready, 1)
            pe.wait_ge(copied, 2 * TILES)
            pe.wait_ge(st_placed, NB)
            av = a[:, 0:SMP, :].rearrange("p t h -> p (t h)")
            pe.matmul(g.ps[:, 0, 0:SMP * SH], g.c("upper"), av, start=True, stop=True)
            pe.matmul(g.ps[:, 1, 0:SMP * SH], g.c("ones"), av, start=True, stop=True)
            pe.matmul(g.ps[0:NS, 2, 0:SH], g.c("upper_s")[0:NS, :], a[0:NS, SMP, :], start=True, stop=True)
            pe.matmul(g.ps[0:NS, 3, 0:SH], g.c("same_s")[0:NS, :], a[0:NS, SMP, :], start=True, stop=True)
            pe.matmul(g.ps[:, 4, 0:NB * SH], g.c("ones")[0:NS, :], ab[:, :, :].rearrange("p b h -> p (b h)"),
                      start=True, stop=True)
            for c in range(SMP):
                pe.matmul(g.ps[0:SH, 5 + c // 4, (c % 4) * P:(c % 4 + 1) * P], a[:, c, :], g.c("upper"),
                          start=True, stop=True)
            pe.matmul(g.ps[0:SH, 7, 0:NS], a[0:NS, SMP, :], g.c("upper_s")[0:NS, :], start=True, stop=True
                      ).then_inc(cum, 1)
            pe.wait_ge(cum_ready, 1)
            pe.wait_ge(powers, 1)
            pe.wait_ge(tables_ready, 1)

            def sums(c):
                n = rows(c)
                pe.wait_ge(diag_made, c + 1)
                if c >= 2:
                    pe.wait_ge(decay, c - 1)
                apart = causalr[:, :] if c < SMP else newr[:, :]
                for half in range(2):
                    to = g.ps[0:n, 6 * (c % 2) + half, 0:4 * n]
                    pe.matmul(to, apart, spread(identr[0:n, 0:n], 0, 4), start=True, stop=False)
                    for part in (dgh, dgl):
                        last = pe.matmul(to, onesr[:, 0:n], part[:, 4 * half:4 * half + 4, 0:n],
                                         start=False, stop=(part is dgl))
                last.then_inc(spread_done, 1)

            def pairs(c):
                n, cols = rows(c), slice(c * P, c * P + rows(c))
                for q in range(2):
                    last = pe.matmul(g.ps[0:n, 2, q * P:q * P + n], g.xb[:, BT + q, cols], g.xb[:, CT + q, cols],
                                     start=True, stop=True)
                last.then_inc(products, 1)

            sums(0)
            pairs(0)
            for c in range(TILES):
                n = rows(c)
                cols = slice(c * P, c * P + n)
                if c + 1 < TILES:
                    sums(c + 1)
                if c >= 1:
                    pe.wait_ge(state, c)
                    pe.wait_ge(y_read, c)
                if c < SMP:
                    if c >= 1:
                        for q in range(2):
                            pe.matmul(g.ps[:, 4, q * 256:(q + 1) * 256], g.xb[:, CT + q, cols],
                                      h0[:, q * 256:(q + 1) * 256], start=True, stop=True)
                    pe.wait_ge(xs_w, c + 1)
                    for q in range(2):
                        last = pe.matmul(g.ps[:, 5, q * 256:(q + 1) * 256], g.btm[:, c, q * P:(q + 1) * P],
                                         xw[:, c % 2, q * 256:(q + 1) * 256], start=True, stop=True)
                    last.then_inc(updated, 1)
                else:
                    pe.wait_ge(s_laid, 2)
                    for q in range(2):
                        for b in range(NB):
                            pe.matmul(g.ps[0:NS, 4, q * 256:(q + 1) * 256], cz[:, q, b, :],
                                      hs[:, b, q * 256:(q + 1) * 256], start=(b == 0), stop=(b == NB - 1))
                pe.wait_ge(weighted, c + 1)
                if c + 1 < TILES:
                    pairs(c + 1)
                for h in range(SH):
                    last = pe.matmul(g.ps[0:n, 3, h * SP:(h + 1) * SP], ee[0:n, c % 2, h, 0:n],
                                     xd[0:n, c % 2, h * SP:(h + 1) * SP], start=True, stop=True)
                last.then_inc(made, 1)
            pe.wait_ge(decay, TILES)
            for m in range(4):
                last = pe.transpose(g.ps[:, 6, m * P:(m + 1) * P], h0[:, m * P:(m + 1) * P], ident)
            last.then_inc(o_turned, 1)
            for b in range(NB):
                pe.wait_ge(s_xw, b + 1)
                for q in range(2):
                    last = pe.matmul(g.ps[:, b % 2, q * 256:(q + 1) * 256], g.btm[0:NS, SMP, q * P:(q + 1) * P],
                                     xd[0:NS, b % 2, q * 256:(q + 1) * 256], start=True, stop=True)
                last.then_inc(s_up, 1)
                pe.wait_ge(s_new, b + 1)
                if b >= 1:
                    pe.wait_ge(o_copied, b)
                for m in range(4):
                    last = pe.transpose(g.ps[:, 6 + (b + 1) % 2, m * P:(m + 1) * P], hs[:, b, m * P:(m + 1) * P], ident)
                last.then_inc(o_turned, 1)
            for t in range(TILES):
                pe.wait_ge(normed, t + 1)
                if t >= 2:
                    pe.wait_ge(y_placed, t - 1)
                for m in range(4):
                    last = pe.transpose(g.ps[:, 2 + t % 2, m * P:m * P + rows(t)],
                                        g.xtm[0:rows(t), t, m * P:(m + 1) * P], ident[0:rows(t), 0:rows(t)])
                last.then_inc(y_turned, 1)

        @block.scalar
        def _(act):
            act.wait_ge(small_in, 64)
            act.wait_ge(dt_abs, 1)
            act.activation(tmp[:, :, :], tmp[:, :, :], ACT.Exp).then_inc(dt_exp, 1)
            act.activation(rowv[:, 1, :], rowv[:, 1, :], ACT.Exp).then_inc(dt_exp, 1)
            act.wait_ge(dt_one, 1)
            act.activation(tmp[:, :, :], tmp[:, :, :], ACT.Ln).then_inc(dt_log, 1)
            for t in range(TILES):
                act.wait_ge(turned, t + 1)
                act.copy(g.xtm[0:rows(t), t, :], g.ps[0:rows(t), 2 * (t % 2), :]).then_inc(copied, 1)
                act.copy(g.btm[0:rows(t), t, :], g.ps[0:rows(t), 2 * (t % 2) + 1, 0:256]).then_inc(copied, 1)
            act.activation(g.z[:, :, :], g.z[:, :, :], ACT.Silu).then_inc(gate_ready, 1)
            act.wait_ge(cum_ready, 1)
            act.activation(ex[:, :, :], cs[:, :, :], ACT.Exp)
            act.activation(wend[:, :, :], wend[:, :, :], ACT.Exp)
            act.activation(eend[:, :, :], eend[:, :, :], ACT.Exp)
            act.activation(eend_s[:, :, :], eend_s[:, :, :], ACT.Exp).then_inc(powers, 1)
            act.wait_ge(negative, 1)
            for c in range(TILES):
                n = rows(c)
                act.wait_ge(spread_done, c + 1)
                if c >= 2:
                    act.wait_ge(made, c - 1)
                for h in range(SH):
                    last = act.activation(ee[0:n, c % 2, h, 0:n],
                                          g.ps[0:n, 6 * (c % 2) + h // 4, (h % 4) * n:(h % 4 + 1) * n], ACT.Exp,
                                          bias=ncs[0:n, c, h:h + 1])
                last.then_inc(decay, 1)
            for n in range(NB + 1):
                act.wait_ge(o_turned, n + 1)
                if n == 0:
                    act.wait_ge(st_turned, NB)
                if n >= 2:
                    act.wait_ge(o_stored[n % 2], 16 * (n // 2))
                act.copy(nat[:, n % 2, :, :].rearrange("p c n -> p (c n)"), g.ps[:, 6 + n % 2, :]).then_inc(o_copied, 1)
            act.wait_ge(rms, 1)
            act.activation(rs[:, :], rs[:, :], ACT.Sqrt).then_inc(root, 1)
            for t in range(TILES):
                act.wait_ge(y_turned, t + 1)
                for m in range(4):
                    last = act.activation(g.ht[:, 4 + m, t * P:t * P + rows(t)], g.ps[:, 2 + t % 2, m * P:m * P + rows(t)],
                                          ACT.Copy, scale=gains[:, m:m + 1])
                last.then_inc(y_placed, 1)

        @block.vector
        def _(dve):
            done = [0]

            def link(op):
                done[0] += 1
                op.then_inc(chain, 1)
                dve.wait_ge(chain, done[0])

            dve.wait_ge(small_in, 64)
            link(dve.tensor_tensor(g.dt[:, :, :], g.dt[:, :, :], spread(rowv[:, 0, :], 0, TILES), ALU.add))
            dve.scalar_tensor_tensor(out=tmp[:, :, :], in0=g.dt[:, :, :], scalar=-1.0, in1=g.dt[:, :, :], op0=ALU.mult,
                                     op1=ALU.min).then_inc(dt_abs, 1)
            dve.wait_ge(dt_exp, 2)
            dve.tensor_scalar(tmp[:, :, :], tmp[:, :, :], 1.0, None, ALU.add).then_inc(dt_one, 1)
            dve.wait_ge(dt_log, 1)
            link(dve.scalar_tensor_tensor(out=g.dt[:, :, :], in0=g.dt[:, :, :], scalar=0.0, in1=tmp[:, :, :],
                                          op0=ALU.max, op1=ALU.add))
            link(dve.scalar_tensor_tensor(out=a[:, :, :], in0=g.dt[:, :, :], scalar=-1.0,
                                          in1=spread(rowv[:, 1, :], 0, TILES), op0=ALU.mult, op1=ALU.mult))
            dve.tensor_tensor(ab[:, :, :], spread(a[0:NS, SMP, :], 0, NB), spread(g.c("seq_of")[0:NS, :], 1, SH),
                              ALU.mult).then_inc(dt_ready, 1)
            for b in range(NB):
                dve.wait_ge(st_turned, b + 1)
                dve.tensor_copy(hs[:, b, :], g.ps[:, 4 + b % 2, :]).then_inc(st_placed, 1)
            dve.wait_ge(cum, 1)
            dve.wait_ge(cleared, 1)
            dve.tensor_copy(cs[:, 0:SMP, :].rearrange("p t h -> p (t h)"), g.ps[:, 0, 0:SMP * SH])
            link(dve.tensor_copy(cs[0:NS, SMP, :], g.ps[0:NS, 2, 0:SH]))
            dve.tensor_tensor(wend[:, 0:SMP, :].rearrange("p t h -> p (t h)"), g.ps[:, 1, 0:SMP * SH],
                              cs[:, 0:SMP, :].rearrange("p t h -> p (t h)"), ALU.subtract)
            dve.tensor_tensor(wend[0:NS, SMP, :], g.ps[0:NS, 3, 0:SH], cs[0:NS, SMP, :], ALU.subtract)
            dve.tensor_copy(eend[:, :, :].rearrange("p t h -> p (t h)"), g.ps[:, 1, 0:SMP * SH])
            dve.tensor_copy(eend_s[:, :, :].rearrange("p b h -> p (b h)"), g.ps[:, 4, 0:NB * SH])
            by_head = ((csth[:, 0:SEQ], cstl[:, 0:SEQ], g.ps[0:SH, 5:7, :].rearrange("p c n -> p (c n)")),
                       (csth[:, SEQ:T], cstl[:, SEQ:T], g.ps[0:SH, 7, 0:NS]))
            for high, low, sums in by_head:
                last = dve.tensor_copy(high, sums)
            last.then_inc(cum_high, 1)
            dve.wait_ge(cum_high, 1)
            for high, low, sums in by_head:
                last = dve.tensor_tensor(low, sums, high.bitcast(F32), ALU.subtract)
            last.then_inc(cum_split, 1)
            dve.wait_ge(cum_split, 1)
            dve.tensor_copy(t1[:, 0:1], g.c("ones")[:, 0:1]).then_inc(cum_ready, 1)
            dve.tensor_scalar(ncs[:, :, :], cs[:, :, :], -1.0, None, ALU.mult).then_inc(negative, 1)
            dve.wait_ge(powers, 1)
            dve.tensor_tensor(wend[:, :, :], wend[:, :, :], g.dt[:, :, :], ALU.mult).then_inc(w_ready, 1)
            dve.wait_ge(copied, 2 * TILES)

            def steps(c):
                n = rows(c)
                if c >= 2:
                    dve.wait_ge(made, c - 1)
                dve.tensor_tensor(heads(xd[0:n, c % 2, :]), heads(g.xtm[0:n, c, :]), spread(g.dt[0:n, c, :], 1, SP),
                                  ALU.mult).then_inc(xs, 1)

            def weight(c):
                n = rows(c)
                dve.wait_ge(decay, c + 1)
                dve.wait_ge(products, c + 1)
                ev = ee[0:n, c % 2, :, 0:n].rearrange("p (a h) i -> p a h i", a=2)
                bc = g.ps[0:n, 2, 0:256].rearrange("p (q i) -> p q i", q=2)[:, :, 0:n]
                dve.tensor_tensor(ev, ev, spread(bc, 1, 4), ALU.mult).then_inc(weighted, 1)

            steps(0)
            weight(0)
            dve.wait_ge(gate_ready, 1)
            for c in range(TILES):
                n = rows(c)
                if c + 1 < TILES:
                    steps(c + 1)
                if c < SMP:
                    dve.wait_ge(updated, c + 1)
                    if c >= 1:
                        link(dve.tensor_tensor(heads(h0[:, :]), heads(h0[:, :]), spread(eend[:, c, :], 1, SP), ALU.mult))
                        dve.tensor_tensor(h0[:, :], g.ps[:, 5, :], h0[:, :], ALU.add).then_inc(state, 1)
                    else:
                        dve.tensor_copy(h0[:, :], g.ps[:, 5, :]).then_inc(state, 1)
                dve.wait_ge(made, c + 1)
                if c + 1 < TILES:
                    weight(c + 1)
                if c >= 1:
                    link(dve.tensor_tensor(heads(t1[0:n, :]), heads(g.ps[0:n, 4, :]), spread(ex[0:n, c, :], 1, SP),
                                           ALU.mult))
                    dve.tensor_tensor(t1[0:n, :], g.ps[0:n, 3, :], t1[0:n, :], ALU.add).then_inc(y_read, 1)
                else:
                    dve.tensor_copy(t1[0:n, :], g.ps[0:n, 3, :]).then_inc(y_read, 1)
                dve.wait_ge(y_read, c + 1)
                dve.wait_ge(skipped, c + 1)
                link(dve.tensor_tensor(g.xtm[0:n, c, :], g.xtm[0:n, c, :], t1[0:n, :], ALU.add))
                link(dve.tensor_tensor(g.xtm[:, c, :], g.xtm[:, c, :], g.z[:, c, :], ALU.mult))
                for q in range(2):
                    part = slice(q * 256, (q + 1) * 256)
                    last = dve.tensor_tensor_reduce(g.z[:, c, part], g.xtm[:, c, part], g.xtm[:, c, part], 1.0, 0.0,
                                                    ALU.mult, ALU.add, rs[:, 2 * c + q:2 * c + q + 1])
                link(last)
            for b in range(NB):
                if b >= 2:
                    dve.wait_ge(s_up, b - 1)
                dve.tensor_scalar(xd[0:NS, b % 2, :], xw[0:NS, SMP % 2, :], g.c("seq_of")[0:NS, b:b + 1], None, ALU.mult
                                  ).then_inc(s_xw, 1)
                link(dve.tensor_tensor(heads(hs[:, b, :]), heads(hs[:, b, :]), spread(eend_s[:, b, :], 1, SP), ALU.mult))
                dve.wait_ge(s_up, b + 1)
                dve.tensor_tensor(hs[:, b, :], g.ps[:, b % 2, :], hs[:, b, :], ALU.add).then_inc(s_new, 1)
            dve.tensor_scalar(rs[:, :], rs[:, :], 1.0 / 256, EPS, ALU.mult, ALU.add).then_inc(rms, 1)
            dve.wait_ge(root, 1)
            link(dve.reciprocal(rs[:, :], rs[:, :]))
            for c in range(TILES):
                y = g.xtm[:, c, :].rearrange("p (q e) -> p q e", q=2)
                dve.tensor_tensor(y, y, spread(rs[:, 2 * c:2 * c + 2], 1, 256), ALU.mult).then_inc(normed, 1)


_INS = ['x_prompt', 'x_sample', 'cache_k', 'cache_v', 'cache_kidx', 'state_ret', 'state_pool', 'state_conv',
        'state_ssm', 'page_table', 'norm_mix', 'norm_ffn', 'w_in_even', 'w_out_even', 'q_norm', 'k_norm', 'rel_bias',
        'w_in_odd', 'w_out_odd', 'pool_w', 'pool_scale', 'conv_w', 'conv_b', 'dt_bias', 'a_log', 'd_skip', 'ssm_norm',
        'w_gate', 'w_up', 'w_down']
_OUTS = [('y_prompt', (1, SEQ, D)), ('y_sample', (NB, NT, D)),
         ('k_prompt', (1, 1, SEQ, H, P)), ('v_prompt', (1, 1, SEQ, H, P)), ('kidx_prompt', (1, 1, SEQ, ID)),
         ('ret_prompt', (1, 1, H, P, P)), ('pool_prompt', (1, 1, PPAST, PW)), ('conv_prompt', (1, 1, CW - 1, CD)),
         ('ssm_prompt', (1, 1, SH, SP, SN)),
         ('k_sample', (1, NB, NT, H, P)), ('v_sample', (1, NB, NT, H, P)), ('kidx_sample', (1, NB, NT, ID)),
         ('ret_sample', (1, NB, H, P, P)), ('pool_sample', (1, NB, PPAST, PW)), ('conv_sample', (1, NB, CW - 1, CD)),
         ('ssm_sample', (1, NB, SH, SP, SN))]


def kernel(**inputs):
    import numpy as _np
    import concourse.bacc as _bacc
    from concourse import mybir as _mybir
    from concourse.bass_utils import run_bass_kernel_spmd as _run

    nc = _bacc.Bacc("TRN2", target_bir_lowering=False, num_devices=1)
    arrays, ins, outs = {}, {}, {}
    for name in _INS:
        a = _np.ascontiguousarray(inputs[name])
        arrays[f"in_{name}_dram"] = a
        ins[name] = nc.dram_tensor(f"in_{name}_dram", a.shape, _mybir.dt.from_np(a.dtype), kind="ExternalInput").ap()
    place, kept, table = host_constants()
    arrays["in_tables_dram"] = table
    tables = nc.dram_tensor("in_tables_dram", table.shape, _mybir.dt.float32, kind="ExternalInput").ap()
    for name, shape in _OUTS:
        outs[name] = nc.dram_tensor(f"out_{name}_dram", shape, _mybir.dt.float32, kind="ExternalOutput").ap()
    build_program(nc, ins, outs, tables, place, kept)
    r = _run(nc, [arrays], core_ids=[0])
    return tuple(r.results[0][f"out_{name}_dram"] for name, _ in _OUTS)
```
